# Optimizing a Trainium2 kernel written in Bass

```python
import jax
import jax.numpy as jnp
from jax import lax
import numpy as np
import jax, jax.numpy as jnp

D_MODEL = 1024
BATCH = 1
SEQ = 256
DEPTH = 2

N_HEADS = 16
HEAD_DIM = D_MODEL // N_HEADS
N_KV_GROUPS = 4
HEADS_PER_GROUP = N_HEADS // N_KV_GROUPS
N_BRANCH = 3
CMP_LEN = 32
CMP_STRIDE = 16
CMP_HIDDEN = 4 * HEAD_DIM
SLC_LEN = 64
SLC_TOP_N = 16
WINDOW = 512
Q_BLOCK = 64
D_FF = 2816
CONV_WIDTH = 3
RMS_EPS = 1e-6
NEG_INF = -1e30
FORCE_SCORE = 1e30


def rms_norm(x, g):
    x32 = x.astype(jnp.float32)
    y = x32 * lax.rsqrt(jnp.mean(x32 * x32, axis=-1, keepdims=True) + RMS_EPS)
    return (y * g.astype(jnp.float32)).astype(x.dtype)

def masked_softmax(s, mask):
    s = jnp.where(mask, s, NEG_INF)
    m = jnp.max(s, axis=-1, keepdims=True)
    e = jnp.where(mask, jnp.exp(s - m), 0.0)
    return e / jnp.maximum(jnp.sum(e, axis=-1, keepdims=True), 1e-30)

def alibi_slopes():
    h = jnp.arange(1, N_HEADS + 1, dtype=jnp.float32)
    return jnp.exp2(-8.0 * h / N_HEADS).reshape(N_KV_GROUPS, HEADS_PER_GROUP)

def modulate_pre(x, g_pre, shift, scale):
    return rms_norm(x, g_pre) * (1.0 + scale[:, None, :]) + shift[:, None, :]

def gated_post_add(x, y, g_post, gate, weight):
    return x + weight * gate[:, None, :] * rms_norm(y, g_post)

def swiglu_ffn(h, w_in, w_out):
    g, u = jnp.split(h @ w_in, 2, axis=-1)
    return (jax.nn.silu(g) * u) @ w_out

def causal_shift(v, n):
    if n == 0:
        return v
    return jnp.pad(v[:, :-n], ((0, 0), (n, 0), (0, 0)))

def short_conv_mixer(h, w_in, conv_w, w_out):
    b_gate, c_gate, u = jnp.split(h @ w_in, 3, axis=-1)
    v = c_gate * u
    y = sum(conv_w[k] * causal_shift(v, CONV_WIDTH - 1 - k) for k in range(CONV_WIDTH))
    return (b_gate * y) @ w_out

def build_shared_kv(x, c, kv_norm_g, kv_ada_w, kv_ada_b, kv_w, cmp_pos, cmp_w1, cmp_w2):
    B, S, _ = x.shape
    G, dh = N_KV_GROUPS, HEAD_DIM
    shift, scale = jnp.split(jax.nn.silu(c) @ kv_ada_w + kv_ada_b, 2, axis=-1)
    h = modulate_pre(x, kv_norm_g, shift, scale)
    kv = (h @ kv_w).reshape(B, S, N_BRANCH, 2, G, dh)
    kv = jnp.transpose(kv, (2, 3, 0, 4, 1, 5))
    n_cmp = (S - CMP_LEN) // CMP_STRIDE + 1
    tok = jnp.arange(n_cmp)[:, None] * CMP_STRIDE + jnp.arange(CMP_LEN)[None, :]
    blocks = kv[0][:, :, :, tok] + cmp_pos[:, None, None, None]
    blocks = blocks.reshape(2, B, G, n_cmp, CMP_LEN * dh)
    hid = jax.nn.gelu(jnp.einsum('kbgnf,kfh->kbgnh', blocks, cmp_w1))
    kv_cmp = jnp.einsum('kbgnh,khd->kbgnd', hid, cmp_w2)
    kv_slc = kv[1].reshape(2, B, G, S // SLC_LEN, SLC_LEN, dh)
    kv_win = jnp.pad(kv[2], ((0, 0), (0, 0), (0, 0), (WINDOW, 0), (0, 0)))
    return kv_cmp, kv_slc, kv_win

def nsa_mixer(h, kv_cmp, kv_slc, kv_win, w_in, w_out):
    B, S, _ = h.shape
    G, R, dh = N_KV_GROUPS, HEADS_PER_GROUP, HEAD_DIM
    f32 = jnp.float32
    proj = h @ w_in
    q = proj[..., :N_HEADS * dh].reshape(B, S, G, R, dh) * (dh ** -0.5)
    gates = jax.nn.sigmoid(proj[..., N_HEADS * dh:].astype(f32)).reshape(B, S, N_BRANCH, G, R)
    k_cmp, v_cmp = kv_cmp[0], kv_cmp[1]
    k_slc, v_slc = kv_slc[0], kv_slc[1]
    k_win, v_win = kv_win[0], kv_win[1]
    n_cmp = k_cmp.shape[2]
    n_slc = k_slc.shape[2]
    top_n = min(SLC_TOP_N, n_slc)
    cmp_start = jnp.arange(n_cmp) * CMP_STRIDE
    cmp_end = cmp_start + CMP_LEN - 1
    slc_start = jnp.arange(n_slc) * SLC_LEN
    overlap = ((cmp_start[:, None] < slc_start[None, :] + SLC_LEN)
               & (cmp_end[:, None] >= slc_start[None, :])).astype(f32)
    slopes = alibi_slopes()
    sl5 = slopes[None, :, :, None, None]
    bi = jnp.arange(B)[:, None, None, None]
    gi = jnp.arange(G)[None, :, None, None]
    blk = jnp.arange(n_slc)

    def attend_block(qi):
        q0 = qi * Q_BLOCK
        qb = lax.dynamic_slice_in_dim(q, q0, Q_BLOCK, axis=1)
        t = q0 + jnp.arange(Q_BLOCK)
        d_cmp = t[:, None] - cmp_end[None, :]
        s = jnp.einsum('bqgrd,bgnd->bgrqn', qb, k_cmp, preferred_element_type=f32)
        s = s - sl5 * d_cmp.astype(f32)
        p_cmp = masked_softmax(s, d_cmp >= 0)
        o_cmp = jnp.einsum('bgrqn,bgnd->bqgrd', p_cmp.astype(v_cmp.dtype), v_cmp)
        imp = jnp.einsum('bgrqn,nj->bgqj', p_cmp, overlap)
        cur = t // SLC_LEN
        forced = (blk[None, :] == 0) | (blk[None, :] == cur[:, None]) | (blk[None, :] == cur[:, None] - 1)
        future = slc_start[None, :] > t[:, None]
        imp = jnp.where(forced, FORCE_SCORE, jnp.where(future, NEG_INF, imp))
        _, idx = lax.top_k(imp, top_n)
        k_sel = k_slc[bi, gi, idx]
        v_sel = v_slc[bi, gi, idx]
        d_sel = t[None, None, :, None, None] - (idx[..., None] * SLC_LEN + jnp.arange(SLC_LEN))
        s = jnp.einsum('bqgrd,bgqnld->bgrqnl', qb, k_sel, preferred_element_type=f32)
        s = s - slopes[None, :, :, None, None, None] * d_sel[:, :, None].astype(f32)
        s = s.reshape(B, G, R, Q_BLOCK, top_n * SLC_LEN)
        m_sel = (d_sel >= 0)[:, :, None].reshape(B, G, 1, Q_BLOCK, top_n * SLC_LEN)
        p_sel = masked_softmax(s, m_sel).reshape(B, G, R, Q_BLOCK, top_n, SLC_LEN)
        o_sel = jnp.einsum('bgrqnl,bgqnld->bqgrd', p_sel.astype(v_sel.dtype), v_sel)
        kw = lax.dynamic_slice_in_dim(k_win, q0, WINDOW + Q_BLOCK, axis=2)
        vw = lax.dynamic_slice_in_dim(v_win, q0, WINDOW + Q_BLOCK, axis=2)
        spos = q0 - WINDOW + jnp.arange(WINDOW + Q_BLOCK)
        d_win = t[:, None] - spos[None, :]
        m_win = (d_win >= 0) & (d_win < WINDOW) & (spos[None, :] >= 0)
        s = jnp.einsum('bqgrd,bgkd->bgrqk', qb, kw, preferred_element_type=f32)
        s = s - sl5 * d_win.astype(f32)
        p_win = masked_softmax(s, m_win)
        o_win = jnp.einsum('bgrqk,bgkd->bqgrd', p_win.astype(vw.dtype), vw)
        g = lax.dynamic_slice_in_dim(gates, q0, Q_BLOCK, axis=1)
        o = (g[:, :, 0, :, :, None] * o_cmp.astype(f32)
             + g[:, :, 1, :, :, None] * o_sel.astype(f32)
             + g[:, :, 2, :, :, None] * o_win.astype(f32))
        return o.astype(h.dtype)

    o = lax.map(attend_block, jnp.arange(S // Q_BLOCK))
    o = jnp.moveaxis(o, 0, 1).reshape(B, S, N_HEADS * dh)
    return o @ w_out

def first_inputs(seed: int = 0) -> dict:
    key = jax.random.key(seed)
    ks = jax.random.split(key, 20)
    f32 = jnp.float32
    D = D_MODEL
    n_a = DEPTH // 2
    n_b = DEPTH - n_a
    kv_cols = N_BRANCH * 2 * N_KV_GROUPS * HEAD_DIM

    def dense(k, shape, fan_in):
        return jax.random.normal(k, shape, f32) * fan_in ** -0.5

    def small(k, shape, s):
        return jax.random.normal(k, shape, f32) * s

    return {
        "x": jax.random.normal(ks[0], (BATCH, SEQ, D), f32),
        "c": jax.random.normal(ks[1], (BATCH, D), f32),
        "ada_w": dense(ks[2], (DEPTH, D, 9 * D), D),
        "ada_b": small(ks[3], (DEPTH, 9 * D), 0.01),
        "norm_g": 1.0 + small(ks[4], (DEPTH, 3, 2, D), 0.05),
        "ffn_w_in": dense(ks[5], (DEPTH, 2, D, 2 * D_FF), D),
        "ffn_w_out": dense(ks[6], (DEPTH, 2, D_FF, D), D_FF),
        "a_w_in": dense(ks[7], (n_a, D, 3 * D), D),
        "a_conv": dense(ks[8], (n_a, CONV_WIDTH, D), CONV_WIDTH),
        "a_w_out": dense(ks[9], (n_a, D, D), D),
        "kv_norm_g": 1.0 + small(ks[10], (D,), 0.05),
        "kv_ada_w": dense(ks[11], (D, 2 * D), D),
        "kv_ada_b": small(ks[12], (2 * D,), 0.01),
        "kv_w": dense(ks[13], (D, kv_cols), D),
        "cmp_pos": small(ks[14], (2, CMP_LEN, HEAD_DIM), 0.1),
        "cmp_w1": dense(ks[15], (2, CMP_LEN * HEAD_DIM, CMP_HIDDEN), CMP_LEN * HEAD_DIM),
        "cmp_w2": dense(ks[16], (2, CMP_HIDDEN, HEAD_DIM), CMP_HIDDEN),
        "b_w_in": dense(ks[17], (n_b, D, N_HEADS * HEAD_DIM + N_BRANCH * N_HEADS), D),
        "b_w_out": dense(ks[18], (n_b, N_HEADS * HEAD_DIM, D), N_HEADS * HEAD_DIM),
    }

def first_block(x, c, ada_w, ada_b, norm_g, ffn_w_in, ffn_w_out, a_w_in, a_conv, a_w_out,
              kv_norm_g, kv_ada_w, kv_ada_b, kv_w, cmp_pos, cmp_w1, cmp_w2, b_w_in, b_w_out):
    B = x.shape[0]
    D = x.shape[-1]
    n_a = DEPTH // 2
    kv_cmp = kv_slc = kv_win = None
    for layer in range(DEPTH):
        if layer == n_a:
            kv_cmp, kv_slc, kv_win = build_shared_kv(
                x, c, kv_norm_g, kv_ada_w, kv_ada_b, kv_w, cmp_pos, cmp_w1, cmp_w2)
        mod = (jax.nn.silu(c) @ ada_w[layer] + ada_b[layer]).reshape(B, 3, 3, D)
        g = norm_g[layer]
        h = modulate_pre(x, g[0, 0], mod[:, 0, 0], mod[:, 0, 1])
        y = swiglu_ffn(h, ffn_w_in[layer, 0], ffn_w_out[layer, 0])
        x = gated_post_add(x, y, g[0, 1], mod[:, 0, 2], 0.5)
        h = modulate_pre(x, g[1, 0], mod[:, 1, 0], mod[:, 1, 1])
        if layer < n_a:
            y = short_conv_mixer(h, a_w_in[layer], a_conv[layer], a_w_out[layer])
        else:
            y = nsa_mixer(h, kv_cmp, kv_slc, kv_win, b_w_in[layer - n_a], b_w_out[layer - n_a])
        x = gated_post_add(x, y, g[1, 1], mod[:, 1, 2], 1.0)
        h = modulate_pre(x, g[2, 0], mod[:, 2, 0], mod[:, 2, 1])
        y = swiglu_ffn(h, ffn_w_in[layer, 1], ffn_w_out[layer, 1])
        x = gated_post_add(x, y, g[2, 1], mod[:, 2, 2], 0.5)
    return x


CHUNK = 64
D_RWKV = D_MODEL // 2
RWKV_HEAD = 64
RWKV_HEADS = D_RWKV // RWKV_HEAD
LORA_W = 64
LORA_A = 64
LORA_V = 32
LORA_G = 160
RWKV_GN_EPS = 64e-5
D_MLSTM = D_MODEL // 2
MLSTM_HEADS = 4
MLSTM_HEAD = D_MLSTM // MLSTM_HEADS
CONV_W = 4
MLSTM_NORM_EPS = 1e-5
D_FF_2 = ((8 * D_MODEL // 3 + 255) // 256) * 256
NORM_EPS = 1e-6
HALF = 0.5

RW_SPLITS = (D_RWKV, D_RWKV, D_RWKV, LORA_W, LORA_A, LORA_G)
ML_SPLITS = (D_MLSTM, D_MLSTM, D_MLSTM, D_MLSTM, MLSTM_HEADS, MLSTM_HEADS)
N_RW_IN = 3 * D_RWKV + LORA_W + LORA_A + LORA_G
N_ML_IN = 4 * D_MLSTM + 2 * MLSTM_HEADS
N_GATE = 2 * D_MODEL
N_IN = N_RW_IN + N_ML_IN + N_GATE


def _rmsnorm(x, g):
    xf = x.astype(jnp.float32)
    y = xf * lax.rsqrt(jnp.mean(xf * xf, axis=-1, keepdims=True) + NORM_EPS)
    return (y * g.astype(jnp.float32)).astype(x.dtype)

def _swiglu(x, w_in, w_out):
    gate, up = jnp.split(x @ w_in, 2, axis=-1)
    return (jax.nn.silu(gate) * up) @ w_out

def _time_shift(z):
    return jnp.pad(z, ((0, 0), (1, 0), (0, 0)))[:, :-1]

def _causal_dwconv(z, w, b):
    K, T = w.shape[0], z.shape[1]
    zp = jnp.pad(z, ((0, 0), (K - 1, 0), (0, 0)))
    out = b
    for j in range(K):
        out = out + w[j] * zp[:, j:j + T]
    return out

def _split_cols(z, sizes):
    out, start = [], 0
    for s in sizes:
        out.append(z[..., start:start + s])
        start += s
    return out

def _head_standardize(y, eps):
    yf = y.astype(jnp.float32)
    mu = jnp.mean(yf, axis=-1, keepdims=True)
    var = jnp.mean(jnp.square(yf - mu), axis=-1, keepdims=True)
    yn = (yf - mu) * lax.rsqrt(var + eps)
    return yn.reshape(y.shape[0], y.shape[1], -1)

def _rwkv7_recurrence(r, w, k, v, kk, b):
    Bn, T, H, N = r.shape
    xs = tuple(jnp.moveaxis(t.astype(jnp.float32), 1, 0) for t in (r, w, k, v, kk, b))

    def step(S, inp):
        r_t, w_t, k_t, v_t, kk_t, b_t = inp
        sa = jnp.einsum('bhvk,bhk->bhv', S, kk_t)
        S = (S * w_t[:, :, None, :]
             - sa[..., :, None] * b_t[:, :, None, :]
             + v_t[..., :, None] * k_t[:, :, None, :])
        return S, jnp.einsum('bhvk,bhk->bhv', S, r_t)

    S0 = jnp.zeros((Bn, H, N, N), jnp.float32)
    _, ys = lax.scan(step, S0, xs)
    return jnp.moveaxis(ys, 0, 1)

def _rwkv7_mixer(r, k, v, xw, xa, xg, w0, w_up, a0, a_up, g_up, k_k, k_a, r_k, gn_w, gn_b):
    Bn, T, _ = r.shape
    heads = lambda t: t.reshape(Bn, T, RWKV_HEADS, RWKV_HEAD)
    w_log = -jax.nn.softplus(-(w0 + jnp.tanh(xw) @ w_up)) - 0.5
    decay = jnp.exp(-jnp.exp(w_log.astype(jnp.float32)))
    a = jax.nn.sigmoid(a0 + xa @ a_up)
    g = jax.nn.sigmoid(xg) @ g_up
    kk = heads(k * k_k).astype(jnp.float32)
    kk = kk / jnp.maximum(jnp.sqrt(jnp.sum(kk * kk, axis=-1, keepdims=True)), 1e-12)
    k = k * (1.0 + (a - 1.0) * k_a)
    rh, kh, vh, ah = heads(r), heads(k), heads(v), heads(a)
    y = _rwkv7_recurrence(rh, heads(decay), kh, vh, kk, kk * ah.astype(jnp.float32))
    y = _head_standardize(y, RWKV_GN_EPS) * gn_w + gn_b
    bonus = (jnp.sum(rh * kh * r_k, axis=-1, keepdims=True) * vh).reshape(Bn, T, -1)
    return ((y + bonus) * g).astype(r.dtype)

def _mlstm_chunkwise(q, k, v, i_pre, f_pre):
    Bn, T, H, d = q.shape
    nc = T // CHUNK
    to_chunks = lambda t: t.astype(jnp.float32).reshape(Bn, nc, CHUNK, H, -1).transpose(1, 0, 3, 2, 4)
    qc = to_chunks(q) * (d ** -0.5)
    kc, vc = to_chunks(k), to_chunks(v)
    lic = to_chunks(i_pre[..., None])[..., 0]
    lfc = jax.nn.log_sigmoid(to_chunks(f_pre[..., None])[..., 0])
    causal = jnp.tril(jnp.ones((CHUNK, CHUNK), bool))

    def step(carry, inp):
        C, n, m = carry
        q_, k_, v_, li, lf = inp
        bcum = jnp.cumsum(lf, axis=-1)
        Dm = jnp.where(causal, bcum[..., :, None] - bcum[..., None, :] + li[..., None, :], -jnp.inf)
        inter = bcum + m[..., None]
        m_t = jnp.maximum(inter, jnp.max(Dm, axis=-1))
        inter_w = jnp.exp(inter - m_t)
        s = jnp.einsum('bhtd,bhsd->bhts', q_, k_) * jnp.exp(Dm - m_t[..., None])
        num = inter_w[..., None] * jnp.einsum('bhvk,bhtk->bhtv', C, q_) + jnp.einsum('bhts,bhsv->bhtv', s, v_)
        den = inter_w * jnp.einsum('bhk,bhtk->bht', n, q_) + jnp.sum(s, axis=-1)
        h = num / jnp.maximum(jnp.abs(den), jnp.exp(-m_t))[..., None]
        bL = bcum[..., -1]
        ws_log = bL[..., None] - bcum + li
        m_new = jnp.maximum(bL + m, jnp.max(ws_log, axis=-1))
        sdec = jnp.exp(bL + m - m_new)
        ws = jnp.exp(ws_log - m_new[..., None])
        C_new = sdec[..., None, None] * C + jnp.einsum('bhs,bhsv,bhsk->bhvk', ws, v_, k_)
        n_new = sdec[..., None] * n + jnp.einsum('bhs,bhsk->bhk', ws, k_)
        return (C_new, n_new, m_new), h

    carry0 = (jnp.zeros((Bn, H, d, d), jnp.float32), jnp.zeros((Bn, H, d), jnp.float32),
              jnp.zeros((Bn, H), jnp.float32))
    _, hs = lax.scan(step, carry0, (qc, kc, vc, lic, lfc))
    return hs.transpose(1, 0, 3, 2, 4).reshape(Bn, T, H, d)

def _mlstm_mixer(mq, mk, mv, mo, mi, mf, conv_w, conv_b, i_bias, f_bias, norm_w):
    Bn, T, _ = mq.shape
    heads = lambda t: t.reshape(Bn, T, MLSTM_HEADS, MLSTM_HEAD)
    qk = jax.nn.silu(_causal_dwconv(jnp.concatenate([mq, mk], axis=-1), conv_w, conv_b))
    q, k = jnp.split(qk, 2, axis=-1)
    h = _mlstm_chunkwise(heads(q), heads(k), heads(mv), mi + i_bias, mf + f_bias)
    h = _head_standardize(h, MLSTM_NORM_EPS) * norm_w
    return (jax.nn.sigmoid(mo) * h).astype(mq.dtype)

def second_inputs(seed: int = 0) -> dict:
    key = jax.random.key(seed)
    ks = iter(jax.random.split(key, 48))
    f32 = jnp.float32
    L = DEPTH

    def nrm(shape, scale):
        return jax.random.normal(next(ks), shape, f32) * scale

    def gain(shape):
        return 1.0 + nrm(shape, 0.05)

    return {
        "x": nrm((BATCH, SEQ, D_MODEL), 1.0),
        "ffn1_norm": gain((L, D_MODEL)),
        "ffn1_w_in": nrm((L, D_MODEL, 2 * D_FF_2), D_MODEL ** -0.5),
        "ffn1_w_out": nrm((L, D_FF_2, D_MODEL), D_FF_2 ** -0.5),
        "mix_norm": gain((L, D_MODEL)),
        "w_in": nrm((L, D_MODEL, N_IN), D_MODEL ** -0.5),
        "shift_mu": jax.random.uniform(next(ks), (L, N_RW_IN), f32, 0.1, 0.9),
        "rw_w0": jnp.linspace(-6.0, -1.0, D_RWKV, dtype=f32)[None, :] + nrm((L, D_RWKV), 0.1),
        "rw_w_up": nrm((L, LORA_W, D_RWKV), 0.5 * LORA_W ** -0.5),
        "rw_a0": nrm((L, D_RWKV), 0.1),
        "rw_a_up": nrm((L, LORA_A, D_RWKV), 0.5 * LORA_A ** -0.5),
        "rw_g_up": nrm((L, LORA_G, D_RWKV), LORA_G ** -0.5),
        "rw_k_k": 0.85 + nrm((L, D_RWKV), 0.05),
        "rw_k_a": gain((L, D_RWKV)),
        "rw_r_k": nrm((L, RWKV_HEADS, RWKV_HEAD), 0.1),
        "rw_gn_w": gain((L, D_RWKV)),
        "rw_gn_b": nrm((L, D_RWKV), 0.02),
        "vres_down": nrm((L - 1, D_MODEL, LORA_V), D_MODEL ** -0.5),
        "vres_up": nrm((L - 1, LORA_V, D_RWKV), 0.5 * LORA_V ** -0.5),
        "vres_bias": 1.0 + nrm((L - 1, D_RWKV), 0.1),
        "ml_conv_w": nrm((L, CONV_W, 2 * D_MLSTM), CONV_W ** -0.5),
        "ml_conv_b": nrm((L, 2 * D_MLSTM), 0.02),
        "ml_i_bias": nrm((L, MLSTM_HEADS), 0.1),
        "ml_f_bias": jnp.linspace(3.0, 6.0, MLSTM_HEADS, dtype=f32)[None, :] + nrm((L, MLSTM_HEADS), 0.1),
        "ml_norm_w": gain((L, D_MLSTM)),
        "br_a": nrm((L, D_RWKV, D_MODEL), D_RWKV ** -0.5),
        "br_b": nrm((L, D_MLSTM, D_MODEL), D_MLSTM ** -0.5),
        "w_out": nrm((L, D_MODEL, D_MODEL), D_MODEL ** -0.5),
        "ffn2_norm": gain((L, D_MODEL)),
        "ffn2_w_in": nrm((L, D_MODEL, 2 * D_FF_2), D_MODEL ** -0.5),
        "ffn2_w_out": nrm((L, D_FF_2, D_MODEL), D_FF_2 ** -0.5),
        "final_norm": gain((D_MODEL,)),
    }

def second_block(x, ffn1_norm, ffn1_w_in, ffn1_w_out, mix_norm, w_in, shift_mu,
              rw_w0, rw_w_up, rw_a0, rw_a_up, rw_g_up, rw_k_k, rw_k_a, rw_r_k, rw_gn_w, rw_gn_b,
              vres_down, vres_up, vres_bias,
              ml_conv_w, ml_conv_b, ml_i_bias, ml_f_bias, ml_norm_w,
              br_a, br_b, w_out, ffn2_norm, ffn2_w_in, ffn2_w_out, final_norm):
    h = x
    v_first = None
    for l in range(DEPTH):
        h = h + HALF * _swiglu(_rmsnorm(h, ffn1_norm[l]), ffn1_w_in[l], ffn1_w_out[l])

        xn = _rmsnorm(h, mix_norm[l])
        z = xn @ w_in[l]
        z_rw = z[..., :N_RW_IN]
        z_ml = z[..., N_RW_IN:N_RW_IN + N_ML_IN]
        z_gate = z[..., N_RW_IN + N_ML_IN:]

        z_rw = z_rw + shift_mu[l] * (_time_shift(z_rw) - z_rw)
        r, k, v, xw, xa, xg = _split_cols(z_rw, RW_SPLITS)
        if l == 0:
            v_first = v
        else:
            vg = jax.nn.sigmoid(vres_bias[l - 1] + (xn @ vres_down[l - 1]) @ vres_up[l - 1])
            v = v + (v_first - v) * vg
        y_a = _rwkv7_mixer(r, k, v, xw, xa, xg, rw_w0[l], rw_w_up[l], rw_a0[l], rw_a_up[l],
                           rw_g_up[l], rw_k_k[l], rw_k_a[l], rw_r_k[l], rw_gn_w[l], rw_gn_b[l])

        mq, mk, mv, mo, mi, mf = _split_cols(z_ml, ML_SPLITS)
        y_b = _mlstm_mixer(mq, mk, mv, mo, mi, mf, ml_conv_w[l], ml_conv_b[l],
                           ml_i_bias[l], ml_f_bias[l], ml_norm_w[l])

        g_a, g_b = jnp.split(z_gate, 2, axis=-1)
        u = jax.nn.sigmoid(g_a) * (y_a @ br_a[l]) + jax.nn.sigmoid(g_b) * (y_b @ br_b[l])
        h = h + u @ w_out[l]

        h = h + HALF * _swiglu(_rmsnorm(h, ffn2_norm[l]), ffn2_w_in[l], ffn2_w_out[l])
    return _rmsnorm(h, final_norm)


def setup_inputs(seed=0):
    out = dict(first_inputs(seed))
    for name, value in second_inputs(seed + 1).items():
        if name != "x":
            out[name + "_2"] = value
    return out


def reference(
    x, c, ada_w, ada_b, norm_g, ffn_w_in, ffn_w_out, a_w_in, a_conv, a_w_out, kv_norm_g,
    kv_ada_w, kv_ada_b, kv_w, cmp_pos, cmp_w1, cmp_w2, b_w_in, b_w_out, ffn1_norm_2,
    ffn1_w_in_2, ffn1_w_out_2, mix_norm_2, w_in_2, shift_mu_2, rw_w0_2, rw_w_up_2, rw_a0_2,
    rw_a_up_2, rw_g_up_2, rw_k_k_2, rw_k_a_2, rw_r_k_2, rw_gn_w_2, rw_gn_b_2, vres_down_2,
    vres_up_2, vres_bias_2, ml_conv_w_2, ml_conv_b_2, ml_i_bias_2, ml_f_bias_2, ml_norm_w_2,
    br_a_2, br_b_2, w_out_2, ffn2_norm_2, ffn2_w_in_2, ffn2_w_out_2, final_norm_2,
):
    x = first_block(
        x, c, ada_w, ada_b, norm_g, ffn_w_in, ffn_w_out, a_w_in, a_conv, a_w_out, kv_norm_g,
        kv_ada_w, kv_ada_b, kv_w, cmp_pos, cmp_w1, cmp_w2, b_w_in, b_w_out,
    )
    return second_block(
        x, ffn1_norm_2, ffn1_w_in_2, ffn1_w_out_2, mix_norm_2, w_in_2, shift_mu_2, rw_w0_2,
        rw_w_up_2, rw_a0_2, rw_a_up_2, rw_g_up_2, rw_k_k_2, rw_k_a_2, rw_r_k_2, rw_gn_w_2,
        rw_gn_b_2, vres_down_2, vres_up_2, vres_bias_2, ml_conv_w_2, ml_conv_b_2, ml_i_bias_2,
        ml_f_bias_2, ml_norm_w_2, br_a_2, br_b_2, w_out_2, ffn2_norm_2, ffn2_w_in_2,
        ffn2_w_out_2, final_norm_2,
    )


_drawn_inputs = setup_inputs


def setup_inputs(seed=0):
    import zlib

    import numpy as np

    out = dict(_drawn_inputs(seed))
    spreads = {}
    factors = {'kv_ada_b': 7.822,
     'rw_w_up_2': 3.368,
     'rw_a0_2': 4.443,
     'rw_k_k_2': 2.786,
     'rw_gn_w_2': 4.45,
     'rw_gn_b_2': 8.0,
     'vres_bias_2': 64.0,
     'ml_conv_b_2': 8.0,
     'ml_i_bias_2': 64.0,
     'ml_norm_w_2': 4.163,
     'ffn2_norm_2': 2.909,
     'vres_down_2': 8.0,
     'vres_up_2': 8.0}
    for name, (base, spread) in spreads.items():
        noise = np.random.default_rng([zlib.crc32(name.encode()), seed]).standard_normal(out[name].shape)
        drawn = base * np.exp(spread * noise) if base else spread * noise
        out[name] = jnp.asarray(drawn.astype(out[name].dtype))
    for name, factor in factors.items():
        out[name] = (out[name] * factor).astype(out[name].dtype)
    return out
```

```python
from contextlib import ExitStack

import numpy as np
import concourse.bass as bass
from concourse import mybir

P = 128
TOK = 256
D = 1024
KC = D // P
TILE_COLS = 256
TILE = KC * TILE_COLS
RING = 6
D_FF = 2816
FFN_STEPS = D_FF // TILE_COLS
FFN_TILES = 3 * FFN_STEPS
HALVES = 2 * FFN_STEPS
NH, NG, DH = 16, 4, 64
N_CMP, CMP_LEN, CMP_STRIDE = 15, 32, 16
MOD_COLS = 72 + 72 + 16
CH = 64
PAD = 4
ZW = TOK + PAD
NZ = 15
RH, MH = 8, 4
LEVELS = 6
RMS_EPS = 1e-6
GN_EPS = 64e-5
ML_EPS = 1e-5
EXP_MINUS_HALF = 0.6065306597126334

F32 = mybir.dt.float32
ALU = mybir.AluOpType
ACT = mybir.ActivationFunctionType
AX_X = mybir.AxisListType.X


def columns(sizes):
    at, out = 0, {}
    for name, n in sizes:
        out[name] = (at, n)
        at += n
    return out, at


CONST, NCONST = columns(
    [("ident", P), ("ones", P), ("mean_d", P), ("mean_p", P), ("blk", P), ("blk_mean", P)]
    + [(f"level{i}", P) for i in range(LEVELS)] + [("level0_ts", P), ("strict", P), ("incl", P), ("causal", P)]
    + [(f"pick{h}", P) for h in range(MH)] + [("reset", TOK), ("dist", 2 * TOK),
       ("cmp_bias", 2 * NH * N_CMP), ("cmp_mask", 2 * N_CMP)])

_second = []
for _l in range(2):
    _second += [(f"ffn1{_l}", 8), (f"mix{_l}", 8), (f"ffn2{_l}", 8), (f"mu{_l}", NZ), (f"w0{_l}", 4), (f"a0{_l}", 4),
                (f"kk{_l}", 4), (f"ka{_l}", 4), (f"rk{_l}", 4), (f"gnw{_l}", 4), (f"gnb{_l}", 4), (f"vres{_l}", 4),
                (f"convw{_l}", 32), (f"convb{_l}", 8), (f"gbias{_l}", 1), (f"mlnorm{_l}", 4)]
VEC, NVEC = columns([("c", 8), ("mod_b", MOD_COLS), ("norm_g", 96), ("kv_norm", 8), ("conv", 24), ("pos", 32)]
                    + _second + [("final", 8)])


USES = {
    "ada": dict(tile=MOD_COLS * P // TILE_COLS), "norm": dict(norm=1, pre=1), "post": dict(norm=1, post=1, update=1),
    "half": dict(update=1), "ffn": dict(tile=FFN_TILES, front=HALVES, ffn=1),
    "conv": dict(tile=12, front=12), "lin4": dict(tile=4, front=4), "kv": dict(tile=15, front=10),
    "nsa": dict(tile=5, front=5), "mix": dict(tile=17, front=16), "gates": dict(tile=8, front=8),
    "branch": dict(tile=4, front=8, branch=1), "resid": dict(update=1), "final": dict(norm=1),
}


class Stage:

    def __init__(self, kind, at, mod=None, gain=None, source=None, rhs=None, layer=None):
        self.kind, self.mod, self.gain, self.source, self.rhs, self.layer = kind, mod, gain, source, rhs, layer
        self.tile, self.front, self.norm, self.pre = at["tile"], at["front"], at["norm"], at["pre"]
        self.post, self.update, self.ffn, self.branch = at["post"], at["update"], at["ffn"], at["branch"]


class Engines:

    def __init__(self, steps, mixer):
        self.pe, self.vec, self.act, self.pool = (steps(f"{mixer}_{e}") for e in ("pe", "vec", "act", "pool"))


def make_plan():
    at = dict(tile=0, front=0, norm=0, pre=0, post=0, update=0, ffn=0, branch=0)
    plan = []

    def add(kind, **kw):
        plan.append(Stage(kind, at, **kw))
        for k, n in USES[kind].items():
            at[k] += n

    add("ada")
    for layer in range(2):
        if layer == 1:
            add("norm", mod="kv")
            add("kv")
        for i in range(3):
            add("norm", mod=(layer, i))
            if i != 1:
                add("ffn")
                add("post", mod=(layer, i), source="ffn")
            else:
                add("nsa" if layer else "conv")
                add("lin4", rhs="o" if layer else "conv_y")
                add("post", mod=(layer, i), source="lin4")
    for layer in range(2):
        add("norm", mod=None, gain=f"ffn1{layer}")
        add("ffn")
        add("half")
        add("norm", mod=None, gain=f"mix{layer}")
        add("mix", layer=layer)
        add("gates")
        add("branch")
        add("lin4", rhs="u")
        add("resid")
        add("norm", mod=None, gain=f"ffn2{layer}")
        add("ffn")
        add("half")
    add("final", mod=None, gain="final")
    return plan, at


PLAN, TOTAL = make_plan()
N_TILES = TOTAL["tile"]


class Steps:

    def __init__(self, sem, names):
        self.sem, self.names, self.made = sem, names, 0
        self.value = {n: i + 1 for i, n in enumerate(names)}

    def step(self, name):
        assert self.names[self.made] == name, (name, self.names[self.made])
        self.made += 1
        return self.sem, 1

    def at(self, name):
        return self.sem, self.value[name]


STEPS = {
    "conv_vector": """
        v a0 a1 a2 a3 a4 a5 a6 a7 b0 b1 b2 b3 b4 b5 b6 b7 c0 c1 c2 c3 c4 c5 c6 c7 y0 y1 y2 y3 y4 y5 y6 y7""".split(),
    "conv_pool": """
        pad""".split(),
    "kv_vector": """
        blocks kcz0 kcz1 vcz0 vcz1""".split(),
    "kv_scalar": """
        gelu""".split(),
    "kv_pool": """
        zero zero_cmp""".split(),
    "attention_tensor": """
        cmp_scores0 cmp_scores1 scores0 scores1 cmp_turned0 cmp_turned1 cmp_turned2 cmp_turned3 cmp_turned4
        cmp_turned5 cmp_turned6 cmp_turned7 turned0 scores2 values0 turned1 scores3 values1 turned2 scores4 values2
        turned3 scores5 values3 turned4 scores6 values4 turned5 scores7 values5 turned6 scores8 values6 turned7
        scores9 values7 turned8 scores10 values8 turned9 scores11 values9 turned10 scores12 values10 turned11
        scores13 values11 turned12 scores14 values12 turned13 scores15 values13 turned14 scores16 values14 turned15
        scores17 values15 turned16 scores18 values16 turned17 scores19 values17 turned18 scores20 values18 turned19
        scores21 values19 turned20 scores22 values20 turned21 scores23 values21 turned22 scores24 values22 turned23
        scores25 values23 turned24 scores26 values24 turned25 scores27 values25 turned26 scores28 values26 turned27
        scores29 values27 turned28 scores30 values28 turned29 scores31 values29 turned30 values30 turned31 values31""".split(),
    "attention_vector": """
        q3 cmp_biased0 cmp_max0 cmp_centred0 cmp_masked0 cmp_sum0 cmp_floor0 cmp_inv0 cmp_gate0 pc0 cmp_biased1
        cmp_max1 cmp_centred1 cmp_masked1 cmp_sum1 cmp_floor1 cmp_inv1 cmp_gate1 pc1 pcT0 pcT1 pcT2 pcT3 pcT4 pcT5
        pcT6 pcT7 biased0 rawmax0 max0 biased1 rawmax1 max1 inv0 weight0 p0 biased2 rawmax2 max2 inv1 weight1 p1
        biased3 rawmax3 max3 inv2 weight2 p2 biased4 rawmax4 max4 inv3 weight3 p3 o0 biased5 rawmax5 max5 inv4
        weight4 p4 biased6 rawmax6 max6 inv5 weight5 p5 o1 biased7 rawmax7 max7 inv6 weight6 p6 biased8 rawmax8 max8
        inv7 weight7 p7 o2 biased9 rawmax9 max9 inv8 weight8 p8 biased10 rawmax10 max10 inv9 weight9 p9 o3 biased11
        rawmax11 max11 inv10 weight10 p10 biased12 rawmax12 max12 inv11 weight11 p11 o4 biased13 rawmax13 max13
        inv12 weight12 p12 biased14 rawmax14 max14 inv13 weight13 p13 o5 biased15 rawmax15 max15 inv14 weight14 p14
        biased16 rawmax16 max16 inv15 weight15 p15 o6 biased17 rawmax17 max17 inv16 weight16 p16 biased18 rawmax18
        max18 inv17 weight17 p17 o7 biased19 rawmax19 max19 inv18 weight18 p18 biased20 rawmax20 max20 inv19
        weight19 p19 o8 biased21 rawmax21 max21 inv20 weight20 p20 biased22 rawmax22 max22 inv21 weight21 p21 o9
        biased23 rawmax23 max23 inv22 weight22 p22 biased24 rawmax24 max24 inv23 weight23 p23 o10 biased25 rawmax25
        max25 inv24 weight24 p24 biased26 rawmax26 max26 inv25 weight25 p25 o11 biased27 rawmax27 max27 inv26
        weight26 p26 biased28 rawmax28 max28 inv27 weight27 p27 o12 biased29 rawmax29 max29 inv28 weight28 p28
        biased30 rawmax30 max30 inv29 weight29 p29 o13 biased31 rawmax31 max31 inv30 weight30 p30 inv31 weight31 p31
        o14 o15""".split(),
    "attention_scalar": """
        cmp_exp0 cmp_exp1 exp0_0 exp0_1 exp1_0 exp1_1 pt0 exp2_0 exp2_1 pt1 exp3_0 exp3_1 pt2 exp4_0 exp4_1 pt3
        exp5_0 exp5_1 pt4 exp6_0 exp6_1 pt5 exp7_0 exp7_1 pt6 exp8_0 exp8_1 pt7 exp9_0 exp9_1 pt8 exp10_0 exp10_1
        pt9 exp11_0 exp11_1 pt10 exp12_0 exp12_1 pt11 exp13_0 exp13_1 pt12 exp14_0 exp14_1 pt13 exp15_0 exp15_1 pt14
        exp16_0 exp16_1 pt15 exp17_0 exp17_1 pt16 exp18_0 exp18_1 pt17 exp19_0 exp19_1 pt18 exp20_0 exp20_1 pt19
        exp21_0 exp21_1 pt20 exp22_0 exp22_1 pt21 exp23_0 exp23_1 pt22 exp24_0 exp24_1 pt23 exp25_0 exp25_1 pt24
        exp26_0 exp26_1 pt25 exp27_0 exp27_1 pt26 exp28_0 exp28_1 pt27 exp29_0 exp29_1 pt28 exp30_0 exp30_1 pt29
        exp31_0 exp31_1 pt30 pt31""".split(),
    "mlstm0_pe": """
        g_turned M_spread em_spread scores0 scores1 scores2 scores3 sums0 scores4 scores5 sums1 scores6 scores7
        sums2 sums3 mean var""".split(),
    "mlstm0_vec": """
        m_o diff shifted li xf minus_abs lf F g_row M_row F_plus_M tap0_0 tap0_1 tap0_2 tap0_3 tap0_4 tap0_5 tap0_6
        tap0_7 tap1_0 tap1_1 tap1_2 tap1_3 tap1_4 tap1_5 tap1_6 tap1_7 tap2_0 tap2_1 tap2_2 tap2_3 tap2_4 tap2_5
        tap2_6 tap2_7 conv0 conv1 conv2 conv3 conv4 conv5 conv6 conv7 g_col gap0 gap1 gap2 sw0 masked0 gap3 sw1
        masked1 gap4 sw2 masked2 gap5 sw3 masked3 gap6 floor0 den0 inv0 h0 sw4 masked4 gap7 sw5 masked5 floor1 den1
        inv1 h1 sw6 masked6 sw7 masked7 floor2 den2 inv2 h2 floor3 den3 inv3 h3 centred0 centred1 rstd0 rstd1 normed
        y_b""".split(),
    "mlstm0_act": """
        exp_f ln_f em_row qk em_copy weight0 weight1 weight2 weight3 weight4 weight5 weight6 weight7 sig_o squares
        root0 root1""".split(),
    "mlstm0_pool": """
        pads rows_zero""".split(),
    "mlstm1_pe": """
        g_turned M_spread em_spread scores0 scores1 scores2 scores3 sums0 scores4 scores5 sums1 scores6 scores7
        sums2 sums3 mean var""".split(),
    "mlstm1_vec": """
        m_o diff shifted li xf minus_abs lf F g_row M_row F_plus_M tap0_0 tap0_1 tap0_2 tap0_3 tap0_4 tap0_5 tap0_6
        tap0_7 tap1_0 tap1_1 tap1_2 tap1_3 tap1_4 tap1_5 tap1_6 tap1_7 tap2_0 tap2_1 tap2_2 tap2_3 tap2_4 tap2_5
        tap2_6 tap2_7 conv0 conv1 conv2 conv3 conv4 conv5 conv6 conv7 g_col gap0 gap1 gap2 sw0 masked0 gap3 sw1
        masked1 gap4 sw2 masked2 gap5 sw3 masked3 gap6 floor0 den0 inv0 h0 sw4 masked4 gap7 sw5 masked5 floor1 den1
        inv1 h1 sw6 masked6 sw7 masked7 floor2 den2 inv2 h2 floor3 den3 inv3 h3 centred0 centred1 rstd0 rstd1 normed
        y_b""".split(),
    "mlstm1_act": """
        exp_f ln_f em_row qk em_copy weight0 weight1 weight2 weight3 weight4 weight5 weight6 weight7 sig_o squares
        root0 root1""".split(),
    "mlstm1_pool": """
        pads rows_zero""".split(),
    "rwkv0_pe": """
        w a kk_norm rk_sum turned0_0 turned1_0 turned2_0 A_t0_0 A_t1_0 A0_0 A1_0 A_kk0_0 A_kk1_0 A_rk0_0 A_rk1_0
        A_rb0_0 A_rb1_0 U1_0_0 U1_1_0 D1_0_0 D_t1_0_0 D1_1_0 D_t1_1_0 U2_0_0 U2_1_0 D2_0_0 D_t2_0_0 D2_1_0 D_t2_1_0
        U3_0_0 U3_1_0 D3_0_0 D_t3_0_0 D3_1_0 D_t3_1_0 U4_0_0 U4_1_0 D4_0_0 D_t4_0_0 D4_1_0 D_t4_1_0 U5_0_0 U5_1_0
        D_t5_0_0 D_t5_1_0 G0 SA0 dS0 y0 G1 SA1 dS1 y1 turned0_1 turned1_1 turned2_1 A_t0_1 A_t1_1 A0_1 A1_1 A_kk0_1
        A_kk1_1 A_rk0_1 A_rk1_1 A_rb0_1 A_rb1_1 U1_0_1 U1_1_1 D1_0_1 D_t1_0_1 D1_1_1 D_t1_1_1 U2_0_1 U2_1_1 D2_0_1
        D_t2_0_1 D2_1_1 D_t2_1_1 U3_0_1 U3_1_1 D3_0_1 D_t3_0_1 D3_1_1 D_t3_1_1 U4_0_1 U4_1_1 D4_0_1 D_t4_0_1 D4_1_1
        D_t4_1_1 U5_0_1 U5_1_1 D_t5_0_1 D_t5_1_1 G2 SA2 dS2 y2 G3 SA3 dS3 y3 gn_mean gn_var""".split(),
    "rwkv0_vec": """
        lora_zero lora_tail one_minus_ka kk_raw0 kk_raw1 kk_raw2 kk_raw3 lw L L_prev g_taken0 g_taken1 ka k_mixed rk
        rk0 rk1 rk2 rk3 v_mixed kk_floor0 kk_floor1 kk_rstd0 kk_rstd1 kk bonus0 bonus1 b kap rho P khat bhat k_z0
        k_z1 b_z0 b_z1 keep0 keep1 ktok0_0 ktok1_0 btok0_0 btok1_0 v_z0_0 v_z1_0 A_t0_0 A_t1_0 X_off0_0 X0_0_0
        Xt_off0_0 X_t0_0_0 X_off1_0 X0_1_0 Xt_off1_0 X_t0_1_0 A_kk0_0 A_kk1_0 A_rk0_0 A_rk1_0 A_rb0_0 A_rb1_0 X1_0_0
        X_t1_0_0 X1_1_0 X_t1_1_0 X2_0_0 X_t2_0_0 X2_1_0 X_t2_1_0 X3_0_0 X_t3_0_0 X3_1_0 X_t3_1_0 X4_0_0 X_t4_0_0
        X4_1_0 X_t4_1_0 X_t5_0_0 X_t5_1_0 S0_3 G0 SA0_0 SA0_1 S_sum0 S1_0 S1_1 S1_2 S1_3 y0 G1 SA1_0 SA1_1 S_sum1
        S2_0 S2_1 S2_2 S2_3 y1 ktok0_1 ktok1_1 btok0_1 btok1_1 v_z0_1 v_z1_1 A_t0_1 A_t1_1 X_off0_1 X0_0_1 Xt_off0_1
        X_t0_0_1 X_off1_1 X0_1_1 Xt_off1_1 X_t0_1_1 A_kk0_1 A_kk1_1 A_rk0_1 A_rk1_1 A_rb0_1 A_rb1_1 X1_0_1 X_t1_0_1
        X1_1_1 X_t1_1_1 X2_0_1 X_t2_0_1 X2_1_1 X_t2_1_1 X3_0_1 X_t3_0_1 X3_1_1 X_t3_1_1 X4_0_1 X_t4_0_1 X4_1_1
        X_t4_1_1 X_t5_0_1 X_t5_1_1 G2 SA2_0 SA2_1 S_sum2 S3_0 S3_1 S3_2 S3_3 y2 G3 SA3_0 SA3_1 S_sum3 S4_0 S4_1 S4_2
        S4_3 y3 gn_centred0 gn_centred1 gn_rstd0 gn_rstd1 gn0 gn1 gn2 gn3 with_bonus0 with_bonus1 with_bonus2
        with_bonus3 y_a0 y_a1 y_a2 y_a3""".split(),
    "rwkv0_act": """
        lora_mid lora_in sig_w a kk_sq kk_root0 kk_root1 E E_inv E_prev U1_0_0 U1_1_0 U2_0_0 U2_1_0 U3_0_0 U3_1_0
        U4_0_0 U4_1_0 U5_0_0 U5_1_0 U1_0_1 U1_1_1 U2_0_1 U2_1_1 U3_0_1 U3_1_1 U4_0_1 U4_1_1 U5_0_1 U5_1_1 gn_squares
        gn_root0 gn_root1""".split(),
    "rwkv0_pool": """
        z_zero tok_zero A_lv1_0 A_lv2_0 A_lv3_0 A_lv4_0 A_lv5_0 A_lv1_1 A_lv2_1 A_lv3_1 A_lv4_1 A_lv5_1""".split(),
    "rwkv1_pe": """
        w a g kk_norm rk_sum turned0_0 turned1_0 turned2_0 A_t0_0 A_t1_0 A0_0 A1_0 A_kk0_0 A_kk1_0 A_rk0_0 A_rk1_0
        A_rb0_0 A_rb1_0 U1_0_0 U1_1_0 D1_0_0 D_t1_0_0 D1_1_0 D_t1_1_0 U2_0_0 U2_1_0 D2_0_0 D_t2_0_0 D2_1_0 D_t2_1_0
        U3_0_0 U3_1_0 D3_0_0 D_t3_0_0 D3_1_0 D_t3_1_0 U4_0_0 U4_1_0 D4_0_0 D_t4_0_0 D4_1_0 D_t4_1_0 U5_0_0 U5_1_0
        D_t5_0_0 D_t5_1_0 G0 SA0 dS0 y0 G1 SA1 dS1 y1 turned0_1 turned1_1 turned2_1 A_t0_1 A_t1_1 A0_1 A1_1 A_kk0_1
        A_kk1_1 A_rk0_1 A_rk1_1 A_rb0_1 A_rb1_1 U1_0_1 U1_1_1 D1_0_1 D_t1_0_1 D1_1_1 D_t1_1_1 U2_0_1 U2_1_1 D2_0_1
        D_t2_0_1 D2_1_1 D_t2_1_1 U3_0_1 U3_1_1 D3_0_1 D_t3_0_1 D3_1_1 D_t3_1_1 U4_0_1 U4_1_1 D4_0_1 D_t4_0_1 D4_1_1
        D_t4_1_1 U5_0_1 U5_1_1 D_t5_0_1 D_t5_1_1 G2 SA2 dS2 y2 G3 SA3 dS3 y3 gn_mean gn_var""".split(),
    "rwkv1_vec": """
        lora_zero lora_tail one_minus_ka kk_raw0 kk_raw1 kk_raw2 kk_raw3 lw L L_prev g_taken0 g_taken1 ka k_mixed rk
        rk0 rk1 rk2 rk3 v_gap v_gated v_mixed kk_floor0 kk_floor1 kk_rstd0 kk_rstd1 kk bonus0 bonus1 b kap rho P
        khat bhat k_z0 k_z1 b_z0 b_z1 keep0 keep1 ktok0_0 ktok1_0 btok0_0 btok1_0 v_z0_0 v_z1_0 A_t0_0 A_t1_0
        X_off0_0 X0_0_0 Xt_off0_0 X_t0_0_0 X_off1_0 X0_1_0 Xt_off1_0 X_t0_1_0 A_kk0_0 A_kk1_0 A_rk0_0 A_rk1_0
        A_rb0_0 A_rb1_0 X1_0_0 X_t1_0_0 X1_1_0 X_t1_1_0 X2_0_0 X_t2_0_0 X2_1_0 X_t2_1_0 X3_0_0 X_t3_0_0 X3_1_0
        X_t3_1_0 X4_0_0 X_t4_0_0 X4_1_0 X_t4_1_0 X_t5_0_0 X_t5_1_0 S0_3 G0 SA0_0 SA0_1 S_sum0 S1_0 S1_1 S1_2 S1_3 y0
        G1 SA1_0 SA1_1 S_sum1 S2_0 S2_1 S2_2 S2_3 y1 ktok0_1 ktok1_1 btok0_1 btok1_1 v_z0_1 v_z1_1 A_t0_1 A_t1_1
        X_off0_1 X0_0_1 Xt_off0_1 X_t0_0_1 X_off1_1 X0_1_1 Xt_off1_1 X_t0_1_1 A_kk0_1 A_kk1_1 A_rk0_1 A_rk1_1
        A_rb0_1 A_rb1_1 X1_0_1 X_t1_0_1 X1_1_1 X_t1_1_1 X2_0_1 X_t2_0_1 X2_1_1 X_t2_1_1 X3_0_1 X_t3_0_1 X3_1_1
        X_t3_1_1 X4_0_1 X_t4_0_1 X4_1_1 X_t4_1_1 X_t5_0_1 X_t5_1_1 G2 SA2_0 SA2_1 S_sum2 S3_0 S3_1 S3_2 S3_3 y2 G3
        SA3_0 SA3_1 S_sum3 S4_0 S4_1 S4_2 S4_3 y3 gn_centred0 gn_centred1 gn_rstd0 gn_rstd1 gn0 gn1 gn2 gn3
        with_bonus0 with_bonus1 with_bonus2 with_bonus3 y_a0 y_a1 y_a2 y_a3""".split(),
    "rwkv1_act": """
        lora_mid lora_in sig_w a vg kk_sq kk_root0 kk_root1 E E_inv E_prev U1_0_0 U1_1_0 U2_0_0 U2_1_0 U3_0_0 U3_1_0
        U4_0_0 U4_1_0 U5_0_0 U5_1_0 U1_0_1 U1_1_1 U2_0_1 U2_1_1 U3_0_1 U3_1_1 U4_0_1 U4_1_1 U5_0_1 U5_1_1 gn_squares
        gn_root0 gn_root1""".split(),
    "rwkv1_pool": """
        z_zero tok_zero A_lv1_0 A_lv2_0 A_lv3_0 A_lv4_0 A_lv5_0 A_lv1_1 A_lv2_1 A_lv3_1 A_lv4_1 A_lv5_1""".split(),
}



def build(nc, consts_d, vecs_d, x_d, weights_d, out_d):
    with ExitStack() as ctx:
        def sb(name, cols):
            return ctx.enter_context(nc.sbuf_tensor(name, [P, cols], F32))

        def sem(name):
            return ctx.enter_context(nc.semaphore(name))

        consts, vecs = sb("const_sb", NCONST), sb("vec_sb", NVEC)
        ring = [sb(f"ring{i}", TILE) for i in range(RING)]
        x, h, y, sq = sb("x", KC * TOK), sb("h", KC * TOK), sb("y", KC * TOK), sb("sq", KC * TOK)
        act_t, silu_t, rstd = sb("act_t", 2 * TOK), sb("silu_t", 2 * TOK), sb("rstd", TOK)
        mods, pre_gain, post_gain, cond = sb("mods", MOD_COLS), sb("pre_gain", 56), sb("post_gain", 48), sb("cond", 8)
        v_first = sb("v_first", 4 * TOK)
        work = sb("work", 24500)
        bank = [ctx.enter_context(nc.psum_tensor(f"bank{i}", [P, 512], F32)) for i in range(8)]
        Y_BANK, FRONT, LOW = 0, (4, 5), 6

        def K(name):
            a, n = CONST[name]
            return consts[:, a:a + n]

        def V(name, i=0, n=1):
            a = VEC[name][0] + i
            return vecs[:, a:a + n]

        def tiles(t, n=KC, w=TOK):
            return t[:, :].rearrange("p (j t) -> p j t", j=n) if w is None else \
                t[:, 0:n * w].rearrange("p (j t) -> p j t", j=n)

        x3, h3, y3, sq3 = tiles(x), tiles(h), tiles(y), tiles(sq)
        rings = [r[:, :].rearrange("p (k c) -> p k c", k=KC) for r in ring]
        ring_out = [r[:, :].rearrange("p (k c) -> p k c", k=2) for r in ring]

        def carve(start, *dims):
            n = int(np.prod(dims))
            assert start + n <= 24500, (start, n)
            v = work[:, start:start + n]
            if len(dims) == 2:
                v = v.rearrange("p (a b) -> p a b", a=dims[0])
            if len(dims) == 3:
                v = v.rearrange("p (a b c) -> p a b c", a=dims[0], b=dims[1])
            if len(dims) == 4:
                v = v.rearrange("p (a b c d) -> p a b c d", a=dims[0], b=dims[1], c=dims[2])
            return v

        def half(b, i):
            return bank[b][:, i * TOK:(i + 1) * TOK]

        def pair(b):
            return bank[b][:, :].rearrange("p (a t) -> p a t", a=2)

        def quad(b):
            return bank[b][:, :].rearrange("p (a t) -> p a t", a=4)

        def mod_col(layer, sub, what):
            return 72 * layer + 24 * sub + 8 * what

        consts_landed, vecs_landed, x_landed = sem("consts_landed"), sem("vecs_landed"), sem("x_landed")
        tile_landed = [sem(f"tile_landed{i}") for i in range(RING)]
        tiles_used = sem("tiles_used")
        front_ready, front_taken, silu_ready = sem("front_ready"), sem("front_taken"), sem("silu_ready")
        squares_ready, meansq_ready = sem("squares_ready"), sem("meansq_ready")
        root_ready, rstd_ready = sem("root_ready"), sem("rstd_ready")
        h_scaled, h_ready = sem("h_scaled"), sem("h_ready")
        y_ready, delta_ready, x_ready = sem("y_ready"), sem("delta_ready"), sem("x_ready")
        cond_ready, mods_taken = sem("cond_ready"), sem("mods_taken")
        gains_ready, u_ready, br_product = sem("gains_ready"), sem("u_ready"), sem("br_product")
        first_columns = sem("first_columns")
        out_ready, out_stored = sem("out_ready"), sem("out_stored")

        def steps(name):
            return Steps(sem(name), STEPS.get(name, []))

        conv_vec, conv_pool = steps("conv_vector"), steps("conv_pool")
        kv_pe, kv_vec, kv_act, kv_pool = (steps(f"kv_{e}") for e in ("tensor", "vector", "scalar", "pool"))
        at_pe, at_vec, at_act, at_pool = (steps(f"attention_{e}") for e in ("tensor", "vector", "scalar", "pool"))
        ML = [Engines(steps, f"mlstm{l}") for l in range(2)]
        RW = [Engines(steps, f"rwkv{l}") for l in range(2)]

        conv_z = carve(0, 24, TOK)
        conv_v = carve(6144, 8, ZW)
        conv_y = carve(6144 + 8 * ZW, 8, TOK)

        kz = carve(0, 2, NG, 2, TOK)
        vz = carve(4096, 16, 2, P)
        blocks = carve(8192, 2, 16, NG * N_CMP)
        hid = carve(10112, 2, 2, NG * N_CMP)
        kcz = carve(10352, NG, 2, N_CMP)
        vcz = carve(10472, NG, 2, P)
        q_t = carve(11496, 8, TOK)
        o_t = carve(13544, 8, TOK)
        gate_tok = carve(15592, 2, 3 * NH)
        pc = carve(15688, 2, NH, N_CMP)
        pc_t = carve(16168, 2, NH, P)
        s_buf = carve(20264, 2, 2, TOK)
        pt_buf = carve(21288, 2, 4, P)
        at_small = carve(22312, 256)

        zp = carve(0, NZ, ZW)
        C0 = NZ * ZW
        y_b = carve(C0, 4, TOK)
        g_up = carve(C0 + 1024, 4, TOK)
        bonus = carve(C0 + 2048, 4, TOK)
        y_a = carve(C0 + 3072, 4, TOK)
        rho, kap = carve(C0 + 4096, 4, TOK), carve(C0 + 5120, 4, TOK)
        k_z, b_z = carve(C0 + 6144, 4, 2, TOK), carve(C0 + 8192, 4, 2, TOK)
        C1 = C0 + 10240
        mqk = carve(C0 + 4096, 8, ZW)
        m_o = carve(C0 + 6176, 4, TOK)
        v_tok = carve(C0 + 7200, 2, 512)
        diff = carve(C1, NZ, TOK)
        qk = carve(C1, 8, TOK)
        sw = carve(C1 + 2048, 8, TOK)
        h_b = carve(C1 + 4096, 4, TOK)
        rows = carve(C1 + 5120, 3, TOK)
        row_tmp = carve(C1 + 5888, 5, TOK)
        bc_e = carve(C1 + 7168, 4, TOK)
        w_buf = carve(C1 + 8192, 4, TOK)
        e1, e2, e3, e4, e5, e6, e7, e8 = (carve(C1 + 1024 * i, 4, TOK) for i in range(8))
        lora_in = carve(C1 + 8192, 4, TOK)
        A_t, A_kk, A_rk, A_rb = (carve(C1 + 1024 * i, RH, P) for i in range(4))
        X, X_t, U = (carve(C1 + 4096 + 1024 * i, RH, P) for i in range(3))
        A_lv = [carve(C1 + 7168, RH, P), carve(C1 + 8192, RH, P)]
        ktok = y[:, 0:1024].rearrange("p (c f) -> p c f", c=2)
        btok = y[:, 1024:2048].rearrange("p (c f) -> p c f", c=2)
        v_z = sq[:, 0:1024].rearrange("p (j r v) -> p j r v", j=4, r=2)
        sa_z = sq[:, 1024:2048].rearrange("p (j r v) -> p j r v", j=4, r=2)
        rw_small = C1 + 9216
        S = act_t[:, 0:512].rearrange("p (j v) -> p j v", j=4)
        gs = silu_t
        small = sb("small", 64)
        keep = [zp[:, 4 * s:4 * s + 4, PAD:PAD + P] for s in range(2)]
        sgate = carve(C1, 16, TOK)
        br_t = carve(C1 + 4096, 2, TOK)
        u = sq3

        block = ctx.enter_context(nc.Block())

        @block.sync
        def _(sp):
            sp.dma_start(vecs[:, :], vecs_d).then_inc(vecs_landed, 16)
            for n in range(RING):
                sp.dma_start(ring[n][:, :], weights_d[n]).then_inc(tile_landed[n], 16)
                if n == 0:
                    sp.dma_start(x[:, :], x_d).then_inc(x_landed, 16)
                    sp.dma_start(consts[:, :], consts_d).then_inc(consts_landed, 16)
            with sp.Fori(1, N_TILES // RING) as turn:
                for n in range(RING):
                    sp.wait_ge(tiles_used, turn * RING + (n + 1 - RING))
                    sp.dma_start(ring[n][:, :], weights_d[bass.ds(turn * RING + n, 1)].rearrange("a p c -> p (a c)")
                                 ).then_inc(tile_landed[n], 16)
            for m in range(N_TILES // RING * RING, N_TILES):
                sp.wait_ge(tiles_used, m + 1 - RING)
                sp.dma_start(ring[m % RING][:, :], weights_d[m]).then_inc(tile_landed[m % RING], 16)
            sp.wait_ge(out_ready, 8)
            sp.dma_start(out_d, y[:, :]).then_inc(out_stored, 16)
            sp.wait_ge(out_stored, 16)

        @block.tensor
        def _(pe):
            def tile_wait(n, turn=0):
                pe.wait_ge(tile_landed[n % RING], (turn + (n // RING + 1)) * 16)

            def front_wait(f, extra=0):
                if isinstance(extra, int) and f + extra < 2:
                    return
                pe.wait_ge(front_taken, extra + (f - 1))

            def mm(out, lhsT, rhs, start, stop, skip=False):
                return nc.tensor.matmul(out, lhsT, rhs, start=start, stop=stop, skip_group_check=skip)

            def ada(st):
                pe.wait_ge(cond_ready, 1)

                def one(t, col, turn):
                    n = st.tile + t
                    tile_wait(n, turn)
                    for c in range(2):
                        for k in range(KC):
                            ins = mm(bank[LOW][:, bass.ds(col + c, 1)] if not isinstance(col, int)
                                     else bank[LOW][:, col + c:col + c + 1],
                                     rings[n % RING][:, k, c * P:(c + 1) * P], cond[:, k:k + 1], k == 0, k == KC - 1)
                    ins.then_inc(tiles_used, 1)
                    return ins

                n_t = USES["ada"]["tile"]
                with pe.Fori(0, n_t // RING) as turn:
                    for t in range(RING):
                        one(t, turn * (2 * RING) + 2 * t, turn)
                for t in range(n_t // RING * RING, n_t):
                    one(t, 2 * t, 0)

            def meansq(st):
                for p in range(4):
                    pe.wait_ge(squares_ready, 4 * st.norm + p + 1)
                    if p == 0:
                        if st.norm == 0:
                            pe.wait_ge(mods_taken, 1)
                            pe.wait_ge(consts_landed, 16)
                        else:
                            pe.wait_ge(rstd_ready, st.norm)
                    for j in (2 * p, 2 * p + 1):
                        ins = mm(bank[LOW][:, 0:TOK], K("mean_d"), sq3[:, j, :], j == 0, j == KC - 1)
                ins.then_inc(meansq_ready, 1)

            def gate_up(st, hh, turn=0, extra=0, first=False):
                n = st.tile + 3 * (hh // 2)
                f = st.front + hh
                if hh % 2 == 0:
                    tile_wait(n, turn)
                    tile_wait(n + 1, turn)
                front_wait(f, extra)
                b, c = FRONT[f % 2], hh % 2
                for i in range(2):
                    for k in range(KC):
                        if first and i == 0:
                            pe.wait_ge(h_ready, 8 * st.pre - 8 + k + 1)
                        ins = mm(half(b, i), rings[(n + i) % RING][:, k, c * P:(c + 1) * P], h3[:, k, :],
                                 k == 0, k == KC - 1)
                        if k == KC - 1 and c == 1 and i == 0:
                            ins.then_inc(tiles_used, 1)
                ins.then_inc(front_ready, 1)

            def down(st, hh, turn=0, extra=0):
                n = st.tile + 3 * (hh // 2) + 2
                f = st.front + hh
                if hh % 2 == 0:
                    tile_wait(n, turn)
                pe.wait_ge(front_taken, extra + (f + 1))
                for j in range(KC):
                    ins = mm(half(Y_BANK + j // 2, j % 2), ring_out[n % RING][:, hh % 2, j * P:(j + 1) * P],
                             act_t[:, (f % 2) * TOK:(f % 2 + 1) * TOK], hh == 0 and j % 2 == 0, hh == HALVES - 1, True)
                    if (hh % 2 == 0 and j == 0) or (hh % 2 == 1 and j == KC - 1):
                        ins.then_inc(tiles_used, 1)

            def ffn(st):
                if st.ffn:
                    pe.wait_ge(y_ready, 4 * st.ffn)
                gate_up(st, 0, first=True)
                for hh in range(4):
                    gate_up(st, hh + 1)
                    down(st, hh)
                with pe.Fori(0, (HALVES - 6) // 4) as turn:
                    for hh in range(4, 8):
                        gate_up(st, hh + 1, turn, turn * 4)
                        down(st, hh, turn, turn * 4)
                gate_up(st, HALVES - 1)
                down(st, HALVES - 2)
                down(st, HALVES - 1)

            def linear(st, n_tiles, rhs, wait=None, tile=0, front=0):
                for t in range(n_tiles):
                    n, f = st.tile + tile + t, st.front + front + t
                    tile_wait(n)
                    front_wait(f)
                    for c in range(2):
                        for k in range(KC):
                            if t == 0 and c == 0 and wait:
                                wait(k)
                            ins = mm(half(FRONT[f % 2], c), rings[n % RING][:, k, c * P:(c + 1) * P], rhs[:, k, :],
                                     k == 0, k == KC - 1)
                    ins.then_inc(tiles_used, 1)

            def token_major(st, n_tiles, cols, tile, front):
                for t in range(n_tiles):
                    n, f = st.tile + tile + t, st.front + front + t
                    tile_wait(n)
                    front_wait(f)
                    for c in range(2):
                        for k in range(KC):
                            ins = mm(half(FRONT[f % 2], c)[:, 0:cols], h3[:, k, c * P:(c + 1) * P],
                                     rings[n % RING][:, k, 0:cols], k == 0, k == KC - 1)
                    ins.then_inc(tiles_used, 1)

            def wait_h(st):
                return lambda k: pe.wait_ge(h_ready, 8 * st.pre - 8 + k + 1)

            def kv(st):
                linear(st, 8, h3, wait_h(st))
                token_major(st, 2, TILE_COLS, 8, 8)
                pe.wait_ge(*kv_vec.at("blocks"))
                for s in range(2):
                    for a in range(2):
                        tile_wait(st.tile + 10 + 2 * s + a)
                    for ht in range(2):
                        for a in range(2):
                            for k in range(KC):
                                ins = mm(bank[7][:, (2 * s + ht) * 64:(2 * s + ht) * 64 + NG * N_CMP],
                                         rings[(st.tile + 10 + 2 * s + a) % RING][:, k, ht * P:(ht + 1) * P],
                                         blocks[:, s, 8 * a + k, :], a == 0 and k == 0, a == 1 and k == KC - 1)
                    ins.then_inc(tiles_used, 2)
                pe.wait_ge(*kv_act.at("gelu"))
                tile_wait(st.tile + 14)
                w2 = ring[(st.tile + 14) % RING]
                for ht in range(2):
                    ins = mm(bank[7][:, 0:NG * N_CMP], w2[:, ht * P:(ht + 1) * P], hid[:, 0, ht, :], ht == 0, ht == 1)
                for g in range(NG):
                    for ht in range(2):
                        ins = mm(bank[7][0:N_CMP, 64 + g * DH:64 + (g + 1) * DH],
                                 hid[:, 1, ht, g * N_CMP:(g + 1) * N_CMP], w2[:, 256 + ht * DH:256 + (ht + 1) * DH],
                                 ht == 0, ht == 1)
                ins.then_inc(tiles_used, 1)

            def nsa(st):
                linear(st, 4, h3, wait_h(st))
                token_major(st, 1, 3 * NH, 4, 4)
                pe.wait_ge(*at_vec.at("q3"))
                pe.wait_ge(*kv_vec.at("vcz1"))
                for qt in range(2):
                    for hd in range(NH):
                        ins = mm(bank[6 + qt][:, hd * 16:hd * 16 + N_CMP], q_t[:, hd // 2, qt * P:(qt + 1) * P],
                                 kcz[:, hd // 4, hd % 2, :], True, True)
                    ins.then_inc(*at_pe.step(f"cmp_scores{qt}"))

                def scores(u):
                    j, qt, r = u // 4, u // 2 % 2, u % 2
                    if u >= 2:
                        pe.wait_ge(*at_vec.at(f"biased{u - 2}"))
                    nk = (qt + 1) * P
                    for br in range(2):
                        ins = mm(bank[u % 2][:, br * TOK:br * TOK + nk], q_t[:, j, qt * P:(qt + 1) * P],
                                 kz[:, br, (2 * j + r) // 4, r, 0:nk], True, True)
                    ins.then_inc(*at_pe.step(f"scores{u}"))

                def turn(u):
                    qt = u // 2 % 2
                    pe.wait_ge(*at_vec.at(f"p{u}"))
                    if u >= 2:
                        pe.wait_ge(*at_act.at(f"pt{u - 2}"))
                    for br in range(2):
                        for kt in range(qt + 1):
                            ins = nc.tensor.transpose(quad(2 + u % 2)[:, 2 * br + kt, :],
                                                      s_buf[:, u % 2, br, kt * P:(kt + 1) * P], K("ident"))
                    ins.then_inc(*at_pe.step(f"turned{u}"))

                def values(u):
                    j, qt, r = u // 4, u // 2 % 2, u % 2
                    g = (2 * j + r) // 4
                    o = bank[4 + u // 2 % 2][:, 0:P]
                    if r == 0:
                        if u == 0:
                            pe.wait_ge(*at_vec.at("pcT7"))
                        if u >= 4:
                            pe.wait_ge(*at_vec.at(f"o{u // 2 - 2}"))
                    mm(o, vcz[0:N_CMP, g, r, :], pc_t[0:N_CMP, qt, 2 * j + r, :], r == 0, False)
                    pe.wait_ge(*at_act.at(f"pt{u}"))
                    for br in range(2):
                        for kt in range(qt + 1):
                            ins = mm(o, vz[:, (br * 2 + kt) * NG + g, r, :], pt_buf[:, u % 2, 2 * br + kt, :],
                                     False, r == 1 and br == 1 and kt == qt)
                    ins.then_inc(*at_pe.step(f"values{u}"))

                scores(0)
                scores(1)
                for i in range(8):
                    qt, q4 = i // 4, i % 4
                    if q4 == 0:
                        pe.wait_ge(*at_vec.at(f"pc{qt}"))
                    if i >= 2:
                        pe.wait_ge(*at_vec.at(f"pcT{i - 2}"))
                    for m in range(4):
                        ins = nc.tensor.transpose(quad(2 + i % 2)[0:N_CMP, m, :], pc[:, qt, 4 * q4 + m, :], K("ident"))
                    ins.then_inc(*at_pe.step(f"cmp_turned{i}"))
                pe.wait_ge(*at_vec.at("pcT7"))
                for u in range(32):
                    turn(u)
                    if u + 2 < 32:
                        scores(u + 2)
                    values(u)

            def mix(st):
                linear(st, 12, h3, wait_h(st))
                token_major(st, 2, TILE_COLS, 12, 12)
                linear(st, 2, h3, None, 14, 14)
                l, M, R = st.layer, ML[st.layer], RW[st.layer]
                pe.wait_ge(*M.vec.at("g_row"))
                for c in range(2):
                    ins = nc.tensor.transpose(bank[7][:, c * P:(c + 1) * P], rows[:, 0, c * P:(c + 1) * P], K("ident"))
                ins.then_inc(*M.pe.step("g_turned"))
                pe.wait_ge(*M.vec.at("M_row"))
                for hd in range(MH):
                    ins = mm(half(hd // 2, hd % 2), K(f"pick{hd}"), rows[:, 1, :], True, True)
                ins.then_inc(*M.pe.step("M_spread"))
                pe.wait_ge(*M.act.at("em_row"))
                for hd in range(MH):
                    ins = mm(half(2 + hd // 2, hd % 2), K(f"pick{hd}"), rows[:, 2, :], True, True)
                ins.then_inc(*M.pe.step("em_spread"))
                pe.wait_ge(*M.act.at("qk"))
                pe.wait_ge(*M.vec.at("g_col"))
                def m_scores(i):
                    hd, kt = i // 2, i % 2
                    if i >= 2:
                        pe.wait_ge(*M.vec.at(f"sw{i - 2}"))
                    mm(bank[6 + i % 2][:, kt * P:TOK], qk[:, 4 + hd, kt * P:(kt + 1) * P], qk[:, hd, kt * P:TOK],
                       True, True).then_inc(*M.pe.step(f"scores{i}"))

                m_scores(0)
                m_scores(1)
                for i in range(8):
                    if i + 2 < 8:
                        m_scores(i + 2)
                    hd = i // 2
                    if i % 2 == 0:
                        continue
                    pe.wait_ge(*M.vec.at(f"masked{i}"))
                    if hd >= 2:
                        pe.wait_ge(*M.vec.at(f"h{hd - 2}"))
                    b = FRONT[hd % 2]
                    for kt in range(2):
                        mm(bank[b][:, kt * P:TOK], v_tok[:, kt, hd * P:(hd + 1) * P], sw[:, 2 * hd + kt, kt * P:TOK],
                           kt == 0, kt == 1)
                    for kt in range(2):
                        ins = mm(bank[b][:, TOK + kt * P:2 * TOK], K("ones"), sw[:, 2 * hd + kt, kt * P:TOK],
                                 kt == 0, kt == 1)
                    ins.then_inc(*M.pe.step(f"sums{hd}"))
                pe.wait_ge(*M.vec.at("h3"))
                for hd in range(MH):
                    ins = mm(half(hd // 2, hd % 2), K("mean_p"), h_b[:, hd, :], True, True)
                ins.then_inc(*M.pe.step("mean"))
                pe.wait_ge(*M.act.at("squares"))
                for hd in range(MH):
                    ins = mm(half(2 + hd // 2, hd % 2), K("mean_p"), sw[:, hd, :], True, True)
                ins.then_inc(*M.pe.step("var"))

                n = st.tile + 16
                tile_wait(n)
                lora = ring[n % RING][:, :].rearrange("p (s c) -> p s c", s=4)
                pe.wait_ge(*M.vec.at("rstd1"))
                pe.wait_ge(*R.act.at("lora_in"))
                pe.wait_ge(*R.vec.at("lora_tail"))

                def low(b, slot, rhs, name):
                    for j in range(4):
                        ins = mm(half(b + j // 2, j % 2), lora[:, slot, j * P:(j + 1) * P], rhs, True, True)
                    return ins.then_inc(*R.pe.step(name))

                low(0, 0, lora_in[:, 0, :], "w")
                low(2, 1, zp[:, 12, PAD:ZW], "a")
                for j in range(4):
                    mm(half(4 + j // 2, j % 2), lora[:, 2, j * P:(j + 1) * P], lora_in[:, 1, :], True, False)
                    ins = mm(half(4 + j // 2, j % 2), lora[:, 3, j * P:(j + 1) * P], lora_in[:, 2, :], False, True)
                if l == 1:
                    ins.then_inc(*R.pe.step("g"))
                    for j in range(4):
                        ins = mm(half(6 + j // 2, j % 2), lora[:, 3, j * P:(j + 1) * P], lora_in[:, 3, :], True, True)
                ins.then_inc(tiles_used, 1)
                pe.wait_ge(*R.act.at("sig_w"))
                pe.wait_ge(*R.act.at("kk_sq"))
                for j in range(4):
                    ins = mm(half(j // 2, j % 2), K("blk"), e2[:, j, :], True, True)
                ins.then_inc(*R.pe.step("kk_norm"))
                pe.wait_ge(*R.act.at("a"))
                pe.wait_ge(*R.vec.at("rk3"))
                for j in range(4):
                    ins = mm(half(2 + j // 2, j % 2), K("blk"), e8[:, j, :], True, True)
                ins.then_inc(*R.pe.step("rk_sum"))
                pe.wait_ge(*R.vec.at("g_taken1"))
                if l == 1:
                    pe.wait_ge(*R.act.at("vg"))
                for T in range(2):
                    ts = slice(T * P, (T + 1) * P)
                    if T == 0:
                        pe.wait_ge(*R.vec.at("khat"))
                        pe.wait_ge(*R.vec.at("bhat"))
                        pe.wait_ge(*R.vec.at("v_mixed"))
                        pe.wait_ge(*R.vec.at("kk_rstd1"))
                        pe.wait_ge(*R.vec.at("bonus1"))
                    else:
                        pe.wait_ge(*R.vec.at("y1"))
                    for s, (src, b) in enumerate(((e5, 4), (e6, 5), (None, 6))):
                        for j in range(4):
                            a = zp[:, 8 + j, PAD + T * P:PAD + (T + 1) * P] if src is None else (
                                src[:, j, ts] if T == 0 else keep[s][:, j, :])
                            ins = nc.tensor.transpose(quad(b)[:, j, :], a, K("ident"))
                        ins.then_inc(*R.pe.step(f"turned{s}_{T}"))
                    pe.wait_ge(*R.vec.at("k_z1"))
                    pe.wait_ge(*R.vec.at("b_z1"))
                    pe.wait_ge(*R.vec.at("kap"))
                    pe.wait_ge(*R.vec.at("rho"))

                    def pairs(name, b, left, right):
                        for hf in range(2):
                            for m in range(4):
                                hd = 4 * hf + m
                                ins = mm(quad(b + hf)[:, m, :], left(hd), right(hd), True, True)
                            ins.then_inc(*R.pe.step(f"{name}{hf}_{T}"))

                    bzs = lambda hd: b_z[:, hd // 2, hd % 2, ts]
                    kzs = lambda hd: k_z[:, hd // 2, hd % 2, ts]
                    kaps = lambda hd: kap[:, hd // 2, ts]
                    rhos = lambda hd: rho[:, hd // 2, ts]
                    pairs("A_t", 0, bzs, kaps)
                    pairs("A", 2, kaps, bzs)
                    pe.wait_ge(*R.vec.at(f"btok1_{T}"))
                    pairs("A_kk", 4, kzs, kaps)
                    pe.wait_ge(*R.vec.at(f"v_z1_{T}"))
                    pairs("A_rk", 6, kzs, rhos)
                    pe.wait_ge(*R.vec.at(f"A_t1_{T}"))
                    pairs("A_rb", 0, bzs, rhos)
                    for lv in range(1, LEVELS):
                        for hf in range(2):
                            if lv == 1:
                                pe.wait_ge(*R.vec.at(f"X0_{hf}_{T}"))
                                pe.wait_ge(*R.vec.at(f"A_kk{hf}_{T}"))
                            else:
                                pe.wait_ge(*R.vec.at(f"X{lv - 1}_{hf}_{T}"))
                            pe.wait_ge(*R.pool.at(f"A_lv{lv}_{T}"))
                            for m in range(4):
                                ins = mm(quad(4 + hf)[:, m, :], A_lv[lv % 2][:, 4 * hf + m, :], X[:, 4 * hf + m, :],
                                         True, True)
                            ins.then_inc(*R.pe.step(f"U{lv}_{hf}_{T}"))
                        for hf in range(2):
                            pe.wait_ge(*R.act.at(f"U{lv}_{hf}_{T}"))
                            if lv == 1:
                                pe.wait_ge(*R.vec.at(f"X_t0_{hf}_{T}"))
                                pe.wait_ge(*R.vec.at(f"A_rk{hf}_{T}"))
                                pe.wait_ge(*R.vec.at(f"A_rb{hf}_{T}"))
                            else:
                                pe.wait_ge(*R.vec.at(f"X_t{lv - 1}_{hf}_{T}"))
                            if lv < LEVELS - 1:
                                for m in range(4):
                                    ins = mm(quad(2 + hf)[:, m, :], X_t[:, 4 * hf + m, :], U[:, 4 * hf + m, :], True, True)
                                ins.then_inc(*R.pe.step(f"D{lv}_{hf}_{T}"))
                            for m in range(4):
                                ins = mm(quad(6 + hf)[:, m, :], U[:, 4 * hf + m, :], X_t[:, 4 * hf + m, :], True, True)
                            ins.then_inc(*R.pe.step(f"D_t{lv}_{hf}_{T}"))
                    for cl in range(2):
                        c = 2 * T + cl
                        cs = slice(T * P + cl * CH, T * P + (cl + 1) * CH)
                        pe.wait_ge(*R.vec.at(f"S{c}_3"))
                        if cl == 0:
                            pe.wait_ge(*R.vec.at(f"X_t{LEVELS - 1}_1_{T}"))
                            pe.wait_ge(*R.vec.at(f"A_rb1_{T}"))
                        for j in range(4):
                            mm(bank[0][:, j * P:(j + 1) * P], kap[:, j, ts], S[:, j, :], True, False)
                            for r in range(2):
                                ins = mm(bank[0][:, j * P + r * CH:j * P + (r + 1) * CH], A_kk[:, 2 * j + r, :],
                                         v_z[:, j, r, r * CH:(r + 1) * CH], False, r == 1)
                        ins.then_inc(*R.pe.step(f"G{c}"))
                        if c:
                            pe.wait_ge(*R.vec.at(f"y{c - 1}"))
                        for j in range(4):
                            yb = bank[3][:, j * CH:(j + 1) * CH]
                            mm(yb, S[:, j, :], rho[:, j, cs], j == 0, False, True)
                            for r in range(2):
                                mm(yb, v_z[:, j, r, :], A_rk[:, 2 * j + r, cl * CH:(cl + 1) * CH], False, False, True)
                        pe.wait_ge(*R.vec.at(f"G{c}"))
                        for hd in range(RH):
                            ins = mm(bank[1][:, hd * CH:(hd + 1) * CH], X_t[:, hd, :], gs[:, hd * CH:(hd + 1) * CH],
                                     True, True)
                        ins.then_inc(*R.pe.step(f"SA{c}"))
                        pe.wait_ge(*R.vec.at(f"SA{c}_1"))
                        for hd in range(RH):
                            j, r = hd // 2, hd % 2
                            o = bank[2][:, hd * CH:(hd + 1) * CH]
                            mm(o, ktok[:, cl, j * P:(j + 1) * P], v_z[:, j, r, r * CH:(r + 1) * CH], True, False)
                            ins = mm(o, btok[:, cl, j * P:(j + 1) * P], sa_z[:, j, r, r * CH:(r + 1) * CH], False, True)
                        ins.then_inc(*R.pe.step(f"dS{c}"))
                        for j in range(4):
                            for r in range(2):
                                ins = mm(bank[3][:, j * CH:(j + 1) * CH], sa_z[:, j, r, :],
                                         A_rb[:, 2 * j + r, cl * CH:(cl + 1) * CH], False, j == 3 and r == 1, True)
                        ins.then_inc(*R.pe.step(f"y{c}"))
                pe.wait_ge(*R.vec.at("y3"))
                for j in range(4):
                    ins = mm(half(j // 2, j % 2), K("blk_mean"), y_a[:, j, :], True, True)
                ins.then_inc(*R.pe.step("gn_mean"))
                pe.wait_ge(*R.act.at("gn_squares"))
                pe.wait_ge(*R.vec.at("S4_3"))
                for j in range(4):
                    ins = mm(half(2 + j // 2, j % 2), K("blk_mean"), e2[:, j, :], True, True)
                ins.then_inc(*R.pe.step("gn_var"))

            def branch(st):
                for t in range(4):
                    n = st.tile + t
                    tile_wait(n)
                    for c in range(2):
                        f = st.front + 2 * t + c
                        front_wait(f)
                        for br, src in enumerate((y_a, y_b)):
                            for k in range(4):
                                ins = mm(half(FRONT[f % 2], br), rings[n % RING][:, 4 * br + k, c * P:(c + 1) * P],
                                         src[:, k, :], k == 0, k == 3)
                        ins.then_inc(tiles_used if c else first_columns, 1)

            for st in PLAN:
                if st.kind == "ada":
                    ada(st)
                elif st.kind in ("norm", "post", "final"):
                    meansq(st)
                elif st.kind == "ffn":
                    ffn(st)
                elif st.kind == "conv":
                    linear(st, 12, h3, wait_h(st))
                elif st.kind == "kv":
                    kv(st)
                elif st.kind == "nsa":
                    nsa(st)
                elif st.kind == "lin4":
                    if st.rhs == "conv_y":
                        linear(st, 4, conv_y, lambda k: pe.wait_ge(*conv_vec.at(f"y{k}")))
                    elif st.rhs == "o":
                        linear(st, 4, o_t, lambda k: pe.wait_ge(*at_vec.at("o15")))
                    else:
                        linear(st, 4, u, lambda k: pe.wait_ge(u_ready, 8 * st.branch - 8 + k + 1))
                elif st.kind == "mix":
                    mix(st)
                elif st.kind == "gates":
                    pe.wait_ge(*RW[last_mix].vec.at("y_a3"))
                    linear(st, 8, h3)
                elif st.kind == "branch":
                    branch(st)
                last_mix = st.layer if st.kind == "mix" else (0 if st.kind == "ada" else last_mix)

        @block.scalar
        def _(act):
            def fn(out, in_, f, bias=0.0, scale=1.0):
                return nc.scalar.activation(out, in_, f, bias=bias, scale=scale)

            def squares(st, src, ready):
                for p in range(4):
                    ready(p)
                    if p == 0 and st.norm:
                        act.wait_ge(meansq_ready, st.norm)
                        act.wait_ge(tiles_used, st.tile)
                    fn(sq[:, 2 * p * TOK:(2 * p + 2) * TOK], src[:, 2 * p * TOK:(2 * p + 2) * TOK], ACT.Square
                       ).then_inc(squares_ready, 1)
                act.wait_ge(meansq_ready, st.norm + 1)
                fn(rstd[:, :], bank[LOW][:, 0:TOK], ACT.Sqrt, bias=RMS_EPS).then_inc(root_ready, 1)

            def x_wait(st):
                def wait(p):
                    if st.update:
                        act.wait_ge(x_ready, 4 * st.update - 4 + p + 1)
                    else:
                        act.wait_ge(x_landed, 16)
                return wait

            def norm(st):
                squares(st, x, x_wait(st))
                if st.mod is None:
                    return
                shift = mod_col(*st.mod, 0) if st.mod != "kv" else 144
                for j in range(KC):
                    act.wait_ge(h_scaled, 8 * n_scaled[0] + j + 1)
                    fn(h3[:, j, :], h3[:, j, :], ACT.Identity, bias=mods[:, shift + j:shift + j + 1]
                       ).then_inc(h_ready, 1)
                n_scaled[0] += 1

            def ffn(st):
                def gate(hh, extra=0):
                    f = st.front + hh
                    act.wait_ge(front_ready, extra + (HALVES * st.ffn + hh + 1))
                    if not (isinstance(extra, int) and hh + extra < 2):
                        act.wait_ge(front_taken, extra + (f - 1))
                    fn(silu_t[:, (f % 2) * TOK:(f % 2 + 1) * TOK], half(FRONT[f % 2], 0), ACT.Silu
                       ).then_inc(silu_ready, 1)
                gate(0)
                gate(1)
                with act.Fori(1, HALVES // 2) as i:
                    gate(0, i * 2)
                    gate(1, i * 2)

            def nsa(st):
                act.wait_ge(tiles_used, st.tile + 5)
                act.wait_ge(front_taken, st.front + 4)
                fn(gate_tok[:, :, :], pair(FRONT[(st.front + 4) % 2])[:, :, 0:3 * NH], ACT.Sigmoid
                   ).then_inc(front_taken, 1)
                for qt in range(2):
                    act.wait_ge(*at_vec.at(f"cmp_centred{qt}"))
                    fn(pc[:, qt, :, :], pc[:, qt, :, :], ACT.Exp).then_inc(*at_act.step(f"cmp_exp{qt}"))

                def exps(u):
                    nk = (u // 2 % 2 + 1) * P
                    act.wait_ge(*at_vec.at(f"max{u}"))
                    for br in range(2):
                        nc.scalar.activation(s_buf[:, u % 2, br, 0:nk], s_buf[:, u % 2, br, 0:nk], ACT.Exp,
                                             bias=at_small[:, 2 * (u % 2) + br:2 * (u % 2) + br + 1], scale=1.0,
                                             accum_out=at_small[:, 8 + 2 * (u % 2) + br:8 + 2 * (u % 2) + br + 1]
                                             ).then_inc(*at_act.step(f"exp{u}_{br}"))

                def copy(u):
                    qt = u // 2 % 2
                    act.wait_ge(*at_pe.at(f"turned{u}"))
                    if u >= 2:
                        act.wait_ge(*at_pe.at(f"values{u - 2}"))
                    a = quad(2 + u % 2).rearrange("p (b k) t -> p b k t", b=2)[:, :, 0:qt + 1, :]
                    o = pt_buf[:, u % 2].rearrange("p (b k) t -> p b k t", b=2)[:, :, 0:qt + 1, :]
                    fn(o, a, ACT.Copy).then_inc(*at_act.step(f"pt{u}"))

                exps(0)
                for v in range(32):
                    if v + 1 < 32:
                        exps(v + 1)
                    copy(v)

            def mix(st):
                l, M, R = st.layer, ML[st.layer], RW[st.layer]
                rt = row_tmp[64:68]
                act.wait_ge(*M.vec.at("minus_abs"))
                fn(rt[:, 2, :], rt[:, 2, :], ACT.Exp).then_inc(*M.act.step("exp_f"))
                act.wait_ge(*M.act.at("exp_f"))
                fn(rt[:, 2, :], rt[:, 2, :], ACT.Ln, bias=1.0).then_inc(*M.act.step("ln_f"))
                act.wait_ge(*M.vec.at("F_plus_M"))
                act.wait_ge(*M.pool.at("rows_zero"))
                fn(rows[64:68, 2, :], rt[:, 4, :], ACT.Exp, scale=-1.0).then_inc(*M.act.step("em_row"))
                act.wait_ge(*M.vec.at("conv7"))
                fn(qk[:, :, :], qk[:, :, :], ACT.Silu).then_inc(*M.act.step("qk"))
                act.wait_ge(*M.pe.at("em_spread"))
                for i in range(2):
                    ins = fn(bc_e[:, 2 * i:2 * i + 2, :], pair(2 + i), ACT.Copy)
                ins.then_inc(*M.act.step("em_copy"))
                for i in range(8):
                    kt = i % 2
                    act.wait_ge(*M.vec.at(f"gap{i}"))
                    fn(w_buf[:, i % 4, kt * P:TOK], w_buf[:, i % 4, kt * P:TOK], ACT.Exp, scale=-1.0
                       ).then_inc(*M.act.step(f"weight{i}"))
                act.wait_ge(*M.vec.at("m_o"))
                fn(m_o[:, :, :], m_o[:, :, :], ACT.Sigmoid).then_inc(*M.act.step("sig_o"))
                act.wait_ge(*M.vec.at("centred1"))
                fn(sw[:, 0:4, :], h_b[:, :, :], ACT.Square).then_inc(*M.act.step("squares"))
                act.wait_ge(*M.pe.at("var"))
                for i in range(2):
                    fn(sw[:, 2 * i:2 * i + 2, :], pair(2 + i), ACT.Sqrt, bias=ML_EPS).then_inc(*M.act.step(f"root{i}"))
                act.wait_ge(*M.vec.at("y_b"))
                fn(lora_in[:, 0, :], zp[:, 12, PAD:ZW], ACT.Tanh)
                fn(lora_in[:, 1, :], zp[:, 13, PAD:ZW], ACT.Sigmoid).then_inc(*R.act.step("lora_mid"))
                act.wait_ge(*R.vec.at("lora_tail"))
                fn(lora_in[0:32, 2, :], zp[0:32, 14, PAD:ZW], ACT.Sigmoid).then_inc(*R.act.step("lora_in"))
                act.wait_ge(*R.pe.at("w"))
                for j in range(4):
                    ins = fn(e1[:, j, :], half(j // 2, j % 2), ACT.Sigmoid, bias=V(f"w0{l}", j))
                ins.then_inc(*R.act.step("sig_w"))
                act.wait_ge(*R.pe.at("a"))
                for j in range(4):
                    ins = fn(e4[:, j, :], half(2 + j // 2, j % 2), ACT.Sigmoid, bias=V(f"a0{l}", j))
                ins.then_inc(*R.act.step("a"))
                if l == 1:
                    act.wait_ge(tiles_used, st.tile + 17)
                    for j in range(4):
                        ins = fn(e7[:, j, :], half(6 + j // 2, j % 2), ACT.Sigmoid, bias=V(f"vres{l}", j))
                    ins.then_inc(*R.act.step("vg"))
                act.wait_ge(*R.vec.at("kk_raw3"))
                fn(e2[:, :, :], e3[:, :, :], ACT.Square).then_inc(*R.act.step("kk_sq"))
                for i in range(2):
                    act.wait_ge(*R.vec.at(f"kk_floor{i}"))
                    fn(e2[:, 2 * i:2 * i + 2, :], e2[:, 2 * i:2 * i + 2, :], ACT.Sqrt).then_inc(*R.act.step(f"kk_root{i}"))
                act.wait_ge(*R.vec.at("L_prev"))
                act.wait_ge(*R.vec.at("v_mixed"))
                act.wait_ge(*R.vec.at("bonus1"))
                fn(e8[:, :, :], e5[:, :, :], ACT.Exp).then_inc(*R.act.step("E"))
                act.wait_ge(*R.vec.at("v_mixed"))
                fn(e7[:, :, :], e5[:, :, :], ACT.Exp, scale=-1.0).then_inc(*R.act.step("E_inv"))
                fn(e6[:, :, :], e6[:, :, :], ACT.Exp).then_inc(*R.act.step("E_prev"))
                for T in range(2):
                    for lv in range(1, LEVELS):
                        for hf in range(2):
                            act.wait_ge(*R.pe.at(f"U{lv}_{hf}_{T}"))
                            if lv > 1:
                                act.wait_ge(*R.pe.at(f"D_t{lv - 1}_{hf}_{T}"))
                            fn(U[:, 4 * hf:4 * hf + 4, :], quad(4 + hf), ACT.Copy
                               ).then_inc(*R.act.step(f"U{lv}_{hf}_{T}"))
                act.wait_ge(*R.vec.at("gn_centred1"))
                fn(e2[:, :, :], y_a[:, :, :], ACT.Square).then_inc(*R.act.step("gn_squares"))
                act.wait_ge(*R.pe.at("gn_var"))
                for i in range(2):
                    fn(e3[:, 2 * i:2 * i + 2, :], pair(2 + i), ACT.Sqrt, bias=GN_EPS).then_inc(*R.act.step(f"gn_root{i}"))

            def gates(st):
                for t in range(8):
                    f = st.front + t
                    act.wait_ge(tiles_used, st.tile + t + 1)
                    fn(sgate[:, 2 * t:2 * t + 2, :], pair(FRONT[f % 2]), ACT.Sigmoid).then_inc(front_taken, 1)

            n_scaled = [0]
            act.wait_ge(vecs_landed, 16)
            fn(cond[:, :], V("c", 0, 8), ACT.Silu).then_inc(cond_ready, 1)
            for st in PLAN:
                if st.kind == "norm":
                    norm(st)
                elif st.kind == "final":
                    squares(st, x, x_wait(st))
                elif st.kind == "post":
                    if st.source == "ffn":
                        squares(st, y, lambda p: act.wait_ge(y_ready, 4 * st.ffn - 4 + p + 1))
                    else:
                        squares(st, y, lambda p: act.wait_ge(front_taken, st.front - 4 + p + 1))
                elif st.kind == "ffn":
                    ffn(st)
                elif st.kind == "kv":
                    act.wait_ge(tiles_used, st.tile + 14)
                    src = bank[7][:, 0:256].rearrange("p (s c) -> p s c", s=4)[:, :, 0:NG * N_CMP]
                    fn(hid.rearrange("p a b c -> p (a b) c"), src, ACT.Gelu_apprx_tanh).then_inc(*kv_act.step("gelu"))
                elif st.kind == "nsa":
                    nsa(st)
                elif st.kind == "mix":
                    mix(st)
                elif st.kind == "gates":
                    gates(st)

        @block.gpsimd
        def _(pool):
            for st in PLAN:
                if st.kind in ("post", "half", "resid"):
                    for p in range(4):
                        if st.kind == "post":
                            pool.wait_ge(delta_ready, 8 * st.post + 2 * p + 2)
                        elif st.kind == "half":
                            pool.wait_ge(y_ready, 4 * st.ffn - 4 + p + 1)
                        else:
                            pool.wait_ge(front_taken, st.front - 4 + p + 1)
                        c = slice(2 * p * TOK, (2 * p + 2) * TOK)
                        nc.gpsimd.tensor_tensor(x[:, c], x[:, c], y[:, c], ALU.add).then_inc(x_ready, 1)
                elif st.kind == "conv":
                    nc.gpsimd.memset(conv_v[:, :, 0:PAD], 0.0).then_inc(*conv_pool.step("pad"))
                elif st.kind == "kv":
                    nc.gpsimd.memset(carve(0, 8192), 0.0).then_inc(*kv_pool.step("zero"))
                    nc.gpsimd.memset(carve(10352, 1144), 0.0).then_inc(*kv_pool.step("zero_cmp"))
                elif st.kind == "mix":
                    l, M, R = st.layer, ML[st.layer], RW[st.layer]
                    if l == 1:
                        pool.wait_ge(u_ready, 8)
                    nc.gpsimd.memset(zp[:, :, 0:PAD], 0.0)
                    nc.gpsimd.memset(mqk[:, :, 0:PAD], 0.0).then_inc(*M.pool.step("pads"))
                    pool.wait_ge(*M.vec.at("shifted"))
                    nc.gpsimd.memset(rows[:, :, :], 0.0).then_inc(*M.pool.step("rows_zero"))
                    pool.wait_ge(*M.vec.at("y_b"))
                    nc.gpsimd.memset(k_z[:, :, :, :], 0.0)
                    nc.gpsimd.memset(b_z[:, :, :, :], 0.0).then_inc(*R.pool.step("z_zero"))
                    nc.gpsimd.memset(y[:, :], 0.0)
                    nc.gpsimd.memset(sq[:, :], 0.0)
                    nc.gpsimd.memset(S[:, :, :], 0.0).then_inc(*R.pool.step("tok_zero"))
                    for T in range(2):
                        for lv in range(1, LEVELS):
                            if lv <= 2:
                                pool.wait_ge(*R.vec.at(f"A_t1_{T}"))
                                if T == 0:
                                    pool.wait_ge(*R.vec.at("b_z1"))
                                    pool.wait_ge(*R.act.at("E_prev"))
                                    pool.wait_ge(*R.vec.at("ktok1_0"))
                            if lv > 2:
                                pool.wait_ge(*R.pe.at(f"U{lv - 2}_1_{T}"))
                            nc.gpsimd.tensor_tensor(A_lv[lv % 2][:, :, :], A_t[:, :, :],
                                                    K(f"level{lv}").unsqueeze(1).to_broadcast([P, RH, P]), ALU.mult
                                                    ).then_inc(*R.pool.step(f"A_lv{lv}_{T}"))

        @block.vector
        def _(dve):
            tt, ts_, stt = nc.vector.tensor_tensor, nc.vector.tensor_scalar, nc.vector.scalar_tensor_tensor
            cp = nc.vector.tensor_copy

            def norm(st, out, ready, gain, src, add=None, extra_wait=None):
                dve.wait_ge(root_ready, st.norm + 1)
                nc.vector.reciprocal(rstd[:, :], rstd[:, :]).then_inc(rstd_ready, 1)
                dve.wait_ge(rstd_ready, st.norm + 1)
                for j in range(KC):
                    stt(out=out[:, j, :], in0=src[:, j, :], scalar=gain(j), in1=rstd[:, :], op0=ALU.mult,
                        op1=ALU.mult).then_inc(ready, 1)

            def take(st, t, out, n=2):
                f = st.front + t
                dve.wait_ge(tiles_used, st.tile + t + 1)
                cp(out, pair(FRONT[f % 2])[:, 0:n, :]).then_inc(front_taken, 1)

            def ffn(st):
                def gated(hh, extra=0):
                    f = st.front + hh
                    dve.wait_ge(silu_ready, extra + (HALVES * st.ffn + hh + 1))
                    tt(act_t[:, (f % 2) * TOK:(f % 2 + 1) * TOK], silu_t[:, (f % 2) * TOK:(f % 2 + 1) * TOK],
                       half(FRONT[f % 2], 1), ALU.mult).then_inc(front_taken, 1)
                with dve.Fori(0, HALVES // 2) as i:
                    gated(0, i * 2)
                    gated(1, i * 2)

            def ffn_out(st, scale):
                for p in range(4):
                    if p == 0:
                        dve.wait_ge(tiles_used, st.tile)
                    ts_(y3[:, 2 * p:2 * p + 2, :], pair(Y_BANK + p), scale, None, ALU.mult).then_inc(y_ready, 1)

            def mods_out():
                dve.wait_ge(tiles_used, USES["ada"]["tile"])
                tt(mods[:, :], bank[LOW][:, 0:MOD_COLS], V("mod_b", 0, MOD_COLS), ALU.add).then_inc(mods_taken, 1)
                dve.wait_ge(mods_taken, 1)
                for layer in range(2):
                    for i in range(3):
                        q = 3 * layer + i
                        sc, gt = mod_col(layer, i, 1), mod_col(layer, i, 2)
                        stt(out=pre_gain[:, 8 * q:8 * q + 8], in0=mods[:, sc:sc + 8], scalar=1.0,
                            in1=V("norm_g", 16 * q, 8), op0=ALU.add, op1=ALU.mult)
                        stt(out=post_gain[:, 8 * q:8 * q + 8], in0=mods[:, gt:gt + 8], scalar=1.0 if i == 1 else 0.5,
                            in1=V("norm_g", 16 * q + 8, 8), op0=ALU.mult, op1=ALU.mult)
                stt(out=pre_gain[:, 48:56], in0=mods[:, 152:160], scalar=1.0, in1=V("kv_norm", 0, 8),
                    op0=ALU.add, op1=ALU.mult).then_inc(gains_ready, 1)
                dve.wait_ge(gains_ready, 1)

            def conv(st):
                for t in range(12):
                    take(st, t, conv_z[:, 2 * t:2 * t + 2, :])
                dve.wait_ge(front_taken, st.front + 12)
                dve.wait_ge(*conv_pool.at("pad"))
                tt(conv_v[:, :, PAD:ZW], conv_z[:, 8:16, :], conv_z[:, 16:24, :], ALU.mult
                   ).then_inc(*conv_vec.step("v"))
                dve.wait_ge(*conv_vec.at("v"))
                for j in range(8):
                    ts_(conv_y[:, j, :], conv_v[:, j, PAD:ZW], V("conv", 16 + j), None, ALU.mult
                        ).then_inc(*conv_vec.step(f"a{j}"))
                for s in (1, 0):
                    for j in range(8):
                        dve.wait_ge(*conv_vec.at(f"a{j}" if s else f"b{j}"))
                        o = PAD - 2 + s
                        stt(out=conv_y[:, j, :], in0=conv_v[:, j, o:o + TOK], scalar=V("conv", 8 * s + j),
                            in1=conv_y[:, j, :], op0=ALU.mult, op1=ALU.add
                            ).then_inc(*conv_vec.step(f"b{j}" if s else f"c{j}"))
                for j in range(8):
                    dve.wait_ge(*conv_vec.at(f"c{j}"))
                    tt(conv_y[:, j, :], conv_y[:, j, :], conv_z[:, j, :], ALU.mult).then_inc(*conv_vec.step(f"y{j}"))

            def kv(st):
                for t in range(4):
                    f, s = st.front + t, t // 2
                    dve.wait_ge(tiles_used, st.tile + t + 1)
                    for gi in range(2):
                        g = 2 * (t % 2) + gi
                        for r in range(2):
                            rows_ = slice(r * DH, (r + 1) * DH)
                            src = half(FRONT[f % 2], gi).rearrange("p (m b r) -> p r b m", b=8, r=2)
                            for a in range(2):
                                kc = slice(8 * a, 8 * a + 8)
                                a0 = VEC["pos"][0] + 16 * s + 8 * a
                                ins = tt(blocks[rows_, s, kc, g * N_CMP:(g + 1) * N_CMP],
                                         src[rows_, r, :, a:a + N_CMP],
                                         vecs[rows_, a0:a0 + 8].unsqueeze(2).to_broadcast([DH, 8, N_CMP]), ALU.add)
                    ins.then_inc(front_taken, 1)
                dve.wait_ge(front_taken, st.front + 4)
                cp(small[:, 0:1], V("c")).then_inc(*kv_vec.step("blocks"))
                dve.wait_ge(*kv_pool.at("zero"))
                for t in range(4):
                    f, br = st.front + 4 + t, t // 2
                    dve.wait_ge(tiles_used, st.tile + 4 + t + 1)
                    for r in range(2):
                        rows_ = slice(r * DH, (r + 1) * DH)
                        g = 2 * (t % 2)
                        ins = cp(kz[rows_, br, g:g + 2, r, :], pair(FRONT[f % 2])[rows_, :, :])
                    ins.then_inc(front_taken, 1)
                for br in range(2):
                    f = st.front + 8 + br
                    dve.wait_ge(tiles_used, st.tile + 8 + br + 1)
                    for c in range(2):
                        src = half(FRONT[f % 2], c).rearrange("p (g d) -> p g d", g=NG)
                        for r in range(2):
                            i = (br * 2 + c) * NG
                            ins = cp(vz[:, i:i + NG, r, r * DH:(r + 1) * DH], src)
                    ins.then_inc(front_taken, 1)
                dve.wait_ge(*kv_pool.at("zero_cmp"))
                dve.wait_ge(tiles_used, st.tile + 15)
                for r in range(2):
                    rows_ = slice(r * DH, (r + 1) * DH)
                    cp(kcz[rows_, :, r, :], bank[7][rows_, 0:NG * N_CMP].rearrange("p (g n) -> p g n", g=NG)
                       ).then_inc(*kv_vec.step(f"kcz{r}"))
                for r in range(2):
                    cp(vcz[0:N_CMP, :, r, r * DH:(r + 1) * DH],
                       bank[7][0:N_CMP, 64:64 + NG * DH].rearrange("p (g n) -> p g n", g=NG)
                       ).then_inc(*kv_vec.step(f"vcz{r}"))

            def nsa(st):
                for t in range(4):
                    f = st.front + t
                    dve.wait_ge(tiles_used, st.tile + t + 1)
                    ts_(q_t[:, 2 * t:2 * t + 2, :], pair(FRONT[f % 2]), DH ** -0.5, None, ALU.mult
                        ).then_inc(front_taken, 1)
                dve.wait_ge(front_taken, st.front + 4)
                cp(small[:, 1:2], q_t[:, 7, 0:1]).then_inc(*at_vec.step("q3"))
                dve.wait_ge(front_taken, st.front + 5)
                for qt in range(2):
                    p = pc[:, qt, :, :]
                    bias = K("cmp_bias").rearrange("p (q h n) -> p q h n", q=2, h=NH)[:, qt]
                    mask = K("cmp_mask").rearrange("p (q n) -> p q n", q=2)[:, qt:qt + 1, :].to_broadcast([P, NH, N_CMP])
                    src = bank[6 + qt][:, 0:256].rearrange("p (h n) -> p h n", h=NH)[:, :, 0:N_CMP]
                    m = at_small[:, 16 + 64 * qt:32 + 64 * qt]
                    z = at_small[:, 32 + 64 * qt:48 + 64 * qt]
                    dve.wait_ge(*at_pe.at(f"cmp_scores{qt}"))
                    tt(p, src, bias, ALU.add).then_inc(*at_vec.step(f"cmp_biased{qt}"))
                    dve.wait_ge(*at_vec.at(f"cmp_biased{qt}"))
                    nc.vector.tensor_reduce(m, p, AX_X, ALU.max).then_inc(*at_vec.step(f"cmp_max{qt}"))
                    dve.wait_ge(*at_vec.at(f"cmp_max{qt}"))
                    tt(p, p, m.unsqueeze(2).to_broadcast([P, NH, N_CMP]), ALU.subtract
                       ).then_inc(*at_vec.step(f"cmp_centred{qt}"))
                    dve.wait_ge(*at_act.at(f"cmp_exp{qt}"))
                    tt(p, p, mask, ALU.mult).then_inc(*at_vec.step(f"cmp_masked{qt}"))
                    dve.wait_ge(*at_vec.at(f"cmp_masked{qt}"))
                    nc.vector.tensor_reduce(z, p, AX_X, ALU.add).then_inc(*at_vec.step(f"cmp_sum{qt}"))
                    dve.wait_ge(*at_vec.at(f"cmp_sum{qt}"))
                    ts_(z, z, 1e-30, None, ALU.max).then_inc(*at_vec.step(f"cmp_floor{qt}"))
                    dve.wait_ge(*at_vec.at(f"cmp_floor{qt}"))
                    nc.vector.reciprocal(m, z).then_inc(*at_vec.step(f"cmp_inv{qt}"))
                    dve.wait_ge(*at_vec.at(f"cmp_inv{qt}"))
                    tt(z, m, gate_tok[:, qt, 0:NH], ALU.mult).then_inc(*at_vec.step(f"cmp_gate{qt}"))
                    dve.wait_ge(*at_vec.at(f"cmp_gate{qt}"))
                    tt(p, p, z.unsqueeze(2).to_broadcast([P, NH, N_CMP]), ALU.mult).then_inc(*at_vec.step(f"pc{qt}"))
                for i in range(8):
                    dve.wait_ge(*at_pe.at(f"cmp_turned{i}"))
                    cp(pc_t[0:N_CMP, i // 4, 4 * (i % 4):4 * (i % 4) + 4, :], quad(2 + i % 2)[0:N_CMP, :, :]
                       ).then_inc(*at_vec.step(f"pcT{i}"))

                def first(u):
                    j, qt, r = u // 4, u // 2 % 2, u % 2
                    hd, nk = 2 * j + r, (qt + 1) * P
                    dist = K("dist")[:, qt * TOK:qt * TOK + nk].unsqueeze(1).to_broadcast([P, 2, nk])
                    s = s_buf[:, u % 2, :, 0:nk]
                    dve.wait_ge(*at_pe.at(f"scores{u}"))
                    if u >= 2:
                        dve.wait_ge(*at_pe.at(f"turned{u - 2}"))
                    stt(out=s, in0=dist, scalar=-(2.0 ** (-8.0 * (hd + 1) / NH)), in1=pair(u % 2)[:, :, 0:nk],
                        op0=ALU.mult, op1=ALU.add).then_inc(*at_vec.step(f"biased{u}"))
                    dve.wait_ge(*at_vec.at(f"biased{u}"))
                    m = at_small[:, 4 + 2 * (u % 2):6 + 2 * (u % 2)]
                    nc.vector.tensor_reduce(m, s, AX_X, ALU.max).then_inc(*at_vec.step(f"rawmax{u}"))
                    dve.wait_ge(*at_vec.at(f"rawmax{u}"))
                    ts_(at_small[:, 2 * (u % 2):2 * (u % 2) + 2], m, -1.0, None, ALU.mult
                        ).then_inc(*at_vec.step(f"max{u}"))

                def second(u):
                    j, qt, r = u // 4, u // 2 % 2, u % 2
                    hd, nk = 2 * j + r, (qt + 1) * P
                    z = at_small[:, 8 + 2 * (u % 2):10 + 2 * (u % 2)]
                    w = at_small[:, 12 + 2 * (u % 2):14 + 2 * (u % 2)]
                    dve.wait_ge(*at_act.at(f"exp{u}_1"))
                    nc.vector.reciprocal(w, z).then_inc(*at_vec.step(f"inv{u}"))
                    dve.wait_ge(*at_vec.at(f"inv{u}"))
                    gate = gate_tok[:, qt, :].rearrange("p (b h) -> p b h", b=3)[:, 1:3, hd]
                    tt(w, w, gate, ALU.mult).then_inc(*at_vec.step(f"weight{u}"))
                    dve.wait_ge(*at_vec.at(f"weight{u}"))
                    for br in range(2):
                        ins = ts_(s_buf[:, u % 2, br, 0:nk], s_buf[:, u % 2, br, 0:nk], w[:, br:br + 1], None, ALU.mult)
                    ins.then_inc(*at_vec.step(f"p{u}"))

                def out(i):
                    dve.wait_ge(*at_pe.at(f"values{2 * i + 1}"))
                    cp(o_t[:, i // 2, (i % 2) * P:(i % 2 + 1) * P], bank[4 + i % 2][:, 0:P]
                       ).then_inc(*at_vec.step(f"o{i}"))

                first(0)
                for v in range(32):
                    if v + 1 < 32:
                        first(v + 1)
                    second(v)
                    if v % 2 == 1 and v > 2:
                        out(v // 2 - 1)
                out(15)

            def mix(st):
                l, M, R = st.layer, ML[st.layer], RW[st.layer]
                Mv, Rv = M.vec, R.vec
                dve.wait_ge(*M.pool.at("pads"))
                for t in range(16):
                    f = st.front + t
                    if t < 7:
                        take(st, t, zp[:, 2 * t:2 * t + 2, PAD:ZW])
                    elif t == 7:
                        take(st, t, zp[:, 14:15, PAD:ZW], 1)
                    elif t < 12:
                        take(st, t, mqk[:, 2 * t - 16:2 * t - 14, PAD:ZW])
                    elif t < 14:
                        take(st, t, v_tok[:, :, (t - 12) * TOK:(t - 11) * TOK])
                    else:
                        take(st, t, m_o[:, 2 * t - 28:2 * t - 26, :])
                dve.wait_ge(front_taken, st.front + 16)
                cp(small[:, 0:1], m_o[:, 3, 0:1]).then_inc(*Mv.step("m_o"))
                tt(diff[:, :, :], zp[:, :, PAD - 1:ZW - 1], zp[:, :, PAD:ZW], ALU.subtract).then_inc(*Mv.step("diff"))
                dve.wait_ge(*Mv.at("diff"))
                for i in range(NZ):
                    ins = stt(out=zp[:, i, PAD:ZW], in0=diff[:, i, :], scalar=V(f"mu{l}", i), in1=zp[:, i, PAD:ZW],
                              op0=ALU.mult, op1=ALU.add)
                ins.then_inc(*Mv.step("shifted"))
                dve.wait_ge(*Mv.at("shifted"))
                rt = row_tmp[64:68]
                gb = V(f"gbias{l}")
                ts_(rt[:, 0, :], zp[64:68, 14, PAD:ZW], gb[64:68], None, ALU.add).then_inc(*Mv.step("li"))
                ts_(rt[:, 1, :], zp[96:100, 14, PAD:ZW], gb[96:100], None, ALU.add).then_inc(*Mv.step("xf"))
                dve.wait_ge(*Mv.at("xf"))
                stt(out=rt[:, 2, :], in0=rt[:, 1, :], scalar=-1.0, in1=rt[:, 1, :], op0=ALU.mult, op1=ALU.min
                    ).then_inc(*Mv.step("minus_abs"))
                dve.wait_ge(*M.act.at("ln_f"))
                stt(out=rt[:, 1, :], in0=rt[:, 1, :], scalar=0.0, in1=rt[:, 2, :], op0=ALU.min, op1=ALU.subtract
                    ).then_inc(*Mv.step("lf"))
                dve.wait_ge(*Mv.at("lf"))
                nc.vector.tensor_tensor_scan(rt[:, 3, :], K("ones")[64:68, 0:1].to_broadcast([4, TOK]), rt[:, 1, :],
                                             0.0, ALU.mult, ALU.add).then_inc(*Mv.step("F"))
                dve.wait_ge(*Mv.at("F"))
                dve.wait_ge(*M.pool.at("rows_zero"))
                tt(rows[64:68, 0, :], rt[:, 0, :], rt[:, 3, :], ALU.subtract).then_inc(*Mv.step("g_row"))
                dve.wait_ge(*Mv.at("g_row"))
                nc.vector.tensor_tensor_scan(rows[64:68, 1, :], rows[64:68, 0, :], rows[64:68, 0, :], 0.0,
                                             ALU.max, ALU.max).then_inc(*Mv.step("M_row"))
                dve.wait_ge(*Mv.at("M_row"))
                tt(rt[:, 4, :], rt[:, 3, :], rows[64:68, 1, :], ALU.add).then_inc(*Mv.step("F_plus_M"))
                for j in range(8):
                    ts_(qk[:, j, :], mqk[:, j, 1:1 + TOK], V(f"convw{l}", j), V(f"convb{l}", j), ALU.mult, ALU.add
                        ).then_inc(*Mv.step(f"tap0_{j}"))
                for i in range(1, 4):
                    for j in range(8):
                        dve.wait_ge(*Mv.at(f"tap{i - 1}_{j}"))
                        stt(out=qk[:, j, :], in0=mqk[:, j, 1 + i:1 + i + TOK], scalar=V(f"convw{l}", 8 * i + j),
                            in1=qk[:, j, :], op0=ALU.mult, op1=ALU.add
                            ).then_inc(*Mv.step(f"tap{i}_{j}" if i < 3 else f"conv{j}"))
                dve.wait_ge(*M.pe.at("g_turned"))
                g_col = small[:, 8:16].rearrange("p (c h) -> p c h", c=2)
                cp(g_col, bank[7][:, 0:TOK].rearrange("p (c r) -> p c r", c=2)[:, :, 64:68]).then_inc(*Mv.step("g_col"))
                dve.wait_ge(*Mv.at("g_col"))
                dve.wait_ge(*M.pe.at("M_spread"))

                def gap(i):
                    hd, kt = i // 2, i % 2
                    ts_(w_buf[:, i % 4, kt * P:TOK], half(hd // 2, hd % 2)[:, kt * P:TOK], g_col[:, kt, hd:hd + 1], 0.0,
                        ALU.subtract, ALU.max).then_inc(*Mv.step(f"gap{i}"))

                def finish(hd):
                    b = FRONT[hd % 2]
                    dve.wait_ge(*M.pe.at(f"sums{hd}"))
                    if hd == 0:
                        dve.wait_ge(*M.act.at("em_copy"))
                    e = bc_e[:, hd, :]
                    stt(out=e, in0=half(b, 1), scalar=-1.0, in1=e, op0=ALU.mult, op1=ALU.max
                        ).then_inc(*Mv.step(f"floor{hd}"))
                    dve.wait_ge(*Mv.at(f"floor{hd}"))
                    tt(e, half(b, 1), e, ALU.max).then_inc(*Mv.step(f"den{hd}"))
                    dve.wait_ge(*Mv.at(f"den{hd}"))
                    nc.vector.reciprocal(e, e).then_inc(*Mv.step(f"inv{hd}"))
                    dve.wait_ge(*Mv.at(f"inv{hd}"))
                    tt(h_b[:, hd, :], half(b, 0), e, ALU.mult).then_inc(*Mv.step(f"h{hd}"))

                for i in range(3):
                    gap(i)
                for i in range(8):
                    hd, kt = i // 2, i % 2
                    dve.wait_ge(*M.pe.at(f"scores{i}"))
                    dve.wait_ge(*M.act.at(f"weight{i}"))
                    stt(out=sw[:, i, kt * P:TOK], in0=w_buf[:, i % 4, kt * P:TOK], scalar=float(P) ** -0.5,
                        in1=bank[6 + i % 2][:, kt * P:TOK], op0=ALU.mult, op1=ALU.mult).then_inc(*Mv.step(f"sw{i}"))
                    dve.wait_ge(*Mv.at(f"sw{i}"))
                    dg = sw[:, i, kt * P:(kt + 1) * P]
                    tt(dg, dg, K("causal"), ALU.mult).then_inc(*Mv.step(f"masked{i}"))
                    if i + 3 < 8:
                        gap(i + 3)
                    if i % 2 == 1 and i > 2:
                        finish(hd - 1)
                finish(3)
                dve.wait_ge(*M.pe.at("mean"))
                for i in range(2):
                    tt(h_b[:, 2 * i:2 * i + 2, :], h_b[:, 2 * i:2 * i + 2, :], pair(i), ALU.subtract
                       ).then_inc(*Mv.step(f"centred{i}"))
                for i in range(2):
                    dve.wait_ge(*M.act.at(f"root{i}"))
                    nc.vector.reciprocal(sw[:, 2 * i:2 * i + 2, :], sw[:, 2 * i:2 * i + 2, :]
                                         ).then_inc(*Mv.step(f"rstd{i}"))
                dve.wait_ge(*Mv.at("rstd1"))
                for j in range(4):
                    ins = stt(out=h_b[:, j, :], in0=h_b[:, j, :], scalar=V(f"mlnorm{l}", j), in1=sw[:, j, :],
                              op0=ALU.mult, op1=ALU.mult)
                ins.then_inc(*Mv.step("normed"))
                dve.wait_ge(*Mv.at("normed"))
                dve.wait_ge(*M.act.at("sig_o"))
                tt(y_b[:, :, :], h_b[:, :, :], m_o[:, :, :], ALU.mult).then_inc(*Mv.step("y_b"))
                dve.wait_ge(*Mv.at("y_b"))

                zr, zk, zv = zp[:, 0:4, PAD:ZW], zp[:, 4:8, PAD:ZW], zp[:, 8:12, PAD:ZW]
                nc.vector.memset(lora_in[:, 2:4, :], 0.0).then_inc(*Rv.step("lora_zero"))
                dve.wait_ge(*Rv.at("lora_zero"))
                cp(lora_in[32:64, 3, :], zp[32:64, 14, PAD:ZW]).then_inc(*Rv.step("lora_tail"))
                ts_(small[:, 16:20], V(f"ka{l}", 0, 4), -1.0, 1.0, ALU.mult, ALU.add).then_inc(*Rv.step("one_minus_ka"))
                for j in range(4):
                    ts_(e3[:, j, :], zp[:, 4 + j, PAD:ZW], V(f"kk{l}", j), None, ALU.mult
                        ).then_inc(*Rv.step(f"kk_raw{j}"))
                dve.wait_ge(*R.act.at("sig_w"))
                ts_(e1[:, :, :], e1[:, :, :], -EXP_MINUS_HALF, None, ALU.mult).then_inc(*Rv.step("lw"))
                dve.wait_ge(*Rv.at("lw"))
                for j in range(4):
                    ins = nc.vector.tensor_tensor_scan(e5[:, j, :], K("reset"), e1[:, j, :], 0.0, ALU.mult, ALU.add)
                ins.then_inc(*Rv.step("L"))
                dve.wait_ge(*Rv.at("L"))
                tt(e6[:, :, :], e5[:, :, :], e1[:, :, :], ALU.subtract).then_inc(*Rv.step("L_prev"))
                if l == 0:
                    dve.wait_ge(tiles_used, st.tile + 17)
                else:
                    dve.wait_ge(*R.pe.at("g"))
                for i in range(2):
                    cp(g_up[:, 2 * i:2 * i + 2, :], pair(4 + i)).then_inc(*Rv.step(f"g_taken{i}"))
                dve.wait_ge(*R.act.at("a"))
                dve.wait_ge(*Rv.at("one_minus_ka"))
                for j in range(4):
                    ins = ts_(e8[:, j, :], e4[:, j, :], V(f"ka{l}", j), small[:, 16 + j:17 + j], ALU.mult, ALU.add)
                ins.then_inc(*Rv.step("ka"))
                dve.wait_ge(*Rv.at("ka"))
                dve.wait_ge(*Rv.at("kk_raw3"))
                tt(zk, zk, e8[:, :, :], ALU.mult).then_inc(*Rv.step("k_mixed"))
                dve.wait_ge(*Rv.at("k_mixed"))
                tt(e8[:, :, :], zr, zk, ALU.mult).then_inc(*Rv.step("rk"))
                dve.wait_ge(*Rv.at("rk"))
                for j in range(4):
                    ts_(e8[:, j, :], e8[:, j, :], V(f"rk{l}", j), None, ALU.mult).then_inc(*Rv.step(f"rk{j}"))
                vf = tiles(v_first, 4)
                if l == 0:
                    cp(vf, zv).then_inc(*Rv.step("v_mixed"))
                else:
                    dve.wait_ge(*R.act.at("vg"))
                    tt(e1[:, :, :], vf, zv, ALU.subtract).then_inc(*Rv.step("v_gap"))
                    dve.wait_ge(*Rv.at("v_gap"))
                    tt(e1[:, :, :], e1[:, :, :], e7[:, :, :], ALU.mult).then_inc(*Rv.step("v_gated"))
                    dve.wait_ge(*Rv.at("v_gated"))
                    tt(zv, zv, e1[:, :, :], ALU.add).then_inc(*Rv.step("v_mixed"))
                dve.wait_ge(*Rv.at("v_mixed"))
                dve.wait_ge(*R.pe.at("kk_norm"))
                for i in range(2):
                    ts_(e2[:, 2 * i:2 * i + 2, :], pair(i), 1e-24, None, ALU.max).then_inc(*Rv.step(f"kk_floor{i}"))
                for i in range(2):
                    dve.wait_ge(*R.act.at(f"kk_root{i}"))
                    nc.vector.reciprocal(e2[:, 2 * i:2 * i + 2, :], e2[:, 2 * i:2 * i + 2, :]
                                         ).then_inc(*Rv.step(f"kk_rstd{i}"))
                dve.wait_ge(*Rv.at("kk_rstd1"))
                tt(e3[:, :, :], e3[:, :, :], e2[:, :, :], ALU.mult).then_inc(*Rv.step("kk"))
                dve.wait_ge(*Rv.at("kk"))
                dve.wait_ge(*R.pe.at("rk_sum"))
                for i in range(2):
                    tt(bonus[:, 2 * i:2 * i + 2, :], pair(2 + i), zp[:, 8 + 2 * i:10 + 2 * i, PAD:ZW], ALU.mult
                       ).then_inc(*Rv.step(f"bonus{i}"))
                tt(e4[:, :, :], e4[:, :, :], e3[:, :, :], ALU.mult).then_inc(*Rv.step("b"))
                dve.wait_ge(*R.act.at("E_prev"))
                tt(kap[:, :, :], e3[:, :, :], e6[:, :, :], ALU.mult).then_inc(*Rv.step("kap"))
                tt(rho[:, :, :], zr, e8[:, :, :], ALU.mult).then_inc(*Rv.step("rho"))
                pcol = small[:, 20:36].rearrange("p (j c) -> p j c", j=4)
                cp(pcol, e8.rearrange("p j (c t) -> p j c t", t=CH)[:, :, :, CH - 1]).then_inc(*Rv.step("P"))
                dve.wait_ge(*Rv.at("b"))
                dve.wait_ge(*Rv.at("kap"))
                tt(e5[:, :, :], zk, e7[:, :, :], ALU.mult).then_inc(*Rv.step("khat"))
                tt(e6[:, :, :], e4[:, :, :], e7[:, :, :], ALU.mult).then_inc(*Rv.step("bhat"))
                dve.wait_ge(*Rv.at("bhat"))
                dve.wait_ge(*R.pool.at("z_zero"))
                for name, z, src in (("k_z", k_z, e5), ("b_z", b_z, e6)):
                    for r in range(2):
                        rows_ = slice(r * CH, (r + 1) * CH)
                        cp(z[rows_, :, r, :], src[rows_, :, :]).then_inc(*Rv.step(f"{name}{r}"))
                dve.wait_ge(*Rv.at("khat"))
                for s, src in enumerate((e5, e6)):
                    cp(keep[s], src[:, :, P:TOK]).then_inc(*Rv.step(f"keep{s}"))
                dve.wait_ge(*Rv.at("keep1"))
                dve.wait_ge(*R.pool.at("tok_zero"))

                def masked(name, hf, T, dst, b, mask, sign=None):
                    mk = K(mask).unsqueeze(1).to_broadcast([P, 4, P])
                    dve.wait_ge(*R.pe.at(f"{name}{hf}_{T}"))
                    d = dst[:, 4 * hf:4 * hf + 4, :]
                    if sign is None:
                        ins = tt(d, quad(b + hf), mk, ALU.mult)
                    else:
                        ins = stt(out=d, in0=quad(b + hf), scalar=sign, in1=mk, op0=ALU.mult, op1=ALU.mult)
                    return ins

                for T in range(2):
                    for s, (dst, b) in enumerate(((ktok, 4), (btok, 5))):
                        dve.wait_ge(*R.pe.at(f"turned{s}_{T}"))
                        for cl in range(2):
                            rows_ = slice(cl * CH, (cl + 1) * CH)
                            ts_(dst[rows_, cl, :], bank[b][rows_, :], -1.0 if s else 1.0, None, ALU.mult
                                ).then_inc(*Rv.step(f"{'btok' if s else 'ktok'}{cl}_{T}"))
                    dve.wait_ge(*R.pe.at(f"turned2_{T}"))
                    for r in range(2):
                        cp(v_z[:, :, r, r * CH:(r + 1) * CH], quad(6)[:, :, r * CH:(r + 1) * CH]
                           ).then_inc(*Rv.step(f"v_z{r}_{T}"))
                    idn = K("ident").unsqueeze(1).to_broadcast([P, 4, P])
                    for hf in range(2):
                        masked("A_t", hf, T, A_t, 0, "strict").then_inc(*Rv.step(f"A_t{hf}_{T}"))
                    for hf in range(2):
                        d = X[:, 4 * hf:4 * hf + 4, :]
                        masked("A", hf, T, X, 2, "level0_ts").then_inc(*Rv.step(f"X_off{hf}_{T}"))
                        dve.wait_ge(*Rv.at(f"X_off{hf}_{T}"))
                        tt(d, idn, d, ALU.subtract).then_inc(*Rv.step(f"X0_{hf}_{T}"))
                        d, a = X_t[:, 4 * hf:4 * hf + 4, :], A_t[:, 4 * hf:4 * hf + 4, :]
                        dve.wait_ge(*Rv.at(f"A_t{hf}_{T}"))
                        tt(d, a, K("level0").unsqueeze(1).to_broadcast([P, 4, P]), ALU.mult
                           ).then_inc(*Rv.step(f"Xt_off{hf}_{T}"))
                        dve.wait_ge(*Rv.at(f"Xt_off{hf}_{T}"))
                        tt(d, idn, d, ALU.subtract).then_inc(*Rv.step(f"X_t0_{hf}_{T}"))
                    for hf in range(2):
                        masked("A_kk", hf, T, A_kk, 4, "strict").then_inc(*Rv.step(f"A_kk{hf}_{T}"))
                    for hf in range(2):
                        masked("A_rk", hf, T, A_rk, 6, "incl").then_inc(*Rv.step(f"A_rk{hf}_{T}"))
                    for hf in range(2):
                        masked("A_rb", hf, T, A_rb, 0, "incl", -1.0).then_inc(*Rv.step(f"A_rb{hf}_{T}"))
                    for lv in range(1, LEVELS):
                        for hf in range(2):
                            for nm, dst, b in (("", X, 2), ("_t", X_t, 6)):
                                if nm == "" and lv == LEVELS - 1:
                                    continue
                                dve.wait_ge(*R.pe.at(f"D{nm}{lv}_{hf}_{T}"))
                                d = dst[:, 4 * hf:4 * hf + 4, :]
                                tt(d, d, quad(b + hf), ALU.subtract).then_inc(*Rv.step(f"X{nm}{lv}_{hf}_{T}"))
                    for cl in range(2):
                        c = 2 * T + cl
                        if c == 0:
                            cp(small[:, 40:44], small[:, 16:20]).then_inc(*Rv.step("S0_3"))
                        dve.wait_ge(*R.pe.at(f"G{c}"))
                        cp(gs[:, :], bank[0][:, :]).then_inc(*Rv.step(f"G{c}"))
                        dve.wait_ge(*R.pe.at(f"SA{c}"))
                        rows_ = slice(cl * CH, (cl + 1) * CH)
                        for r in range(2):
                            cp(sa_z[rows_, :, r, r * CH:(r + 1) * CH], quad(1)[rows_, :, r * CH:(r + 1) * CH]
                               ).then_inc(*Rv.step(f"SA{c}_{r}"))
                        dve.wait_ge(*R.pe.at(f"dS{c}"))
                        tt(S, S, quad(2), ALU.add).then_inc(*Rv.step(f"S_sum{c}"))
                        dve.wait_ge(*Rv.at(f"S_sum{c}"))
                        for j in range(4):
                            stt(out=S[:, j, :], in0=S[:, j, :], scalar=pcol[:, j, c:c + 1], in1=K("blk"), op0=ALU.mult,
                                op1=ALU.mult).then_inc(*Rv.step(f"S{c + 1}_{j}"))
                        dve.wait_ge(*Rv.at(f"S{c + 1}_3"))
                        dve.wait_ge(*R.pe.at(f"y{c}"))
                        cp(y_a[:, :, c * CH:(c + 1) * CH], bank[3][:, 0:TOK].rearrange("p (j t) -> p j t", j=4)
                           ).then_inc(*Rv.step(f"y{c}"))
                dve.wait_ge(*R.pe.at("gn_mean"))
                for i in range(2):
                    tt(y_a[:, 2 * i:2 * i + 2, :], y_a[:, 2 * i:2 * i + 2, :], pair(i), ALU.subtract
                       ).then_inc(*Rv.step(f"gn_centred{i}"))
                for i in range(2):
                    dve.wait_ge(*R.act.at(f"gn_root{i}"))
                    nc.vector.reciprocal(e3[:, 2 * i:2 * i + 2, :], e3[:, 2 * i:2 * i + 2, :]
                                         ).then_inc(*Rv.step(f"gn_rstd{i}"))
                dve.wait_ge(*Rv.at("gn_rstd1"))
                for j in range(4):
                    stt(out=y_a[:, j, :], in0=y_a[:, j, :], scalar=V(f"gnw{l}", j), in1=e3[:, j, :], op0=ALU.mult,
                        op1=ALU.mult).then_inc(*Rv.step(f"gn{j}"))
                for j in range(4):
                    dve.wait_ge(*Rv.at(f"gn{j}"))
                    stt(out=y_a[:, j, :], in0=y_a[:, j, :], scalar=V(f"gnb{l}", j), in1=bonus[:, j, :], op0=ALU.add,
                        op1=ALU.add).then_inc(*Rv.step(f"with_bonus{j}"))
                for j in range(4):
                    dve.wait_ge(*Rv.at(f"with_bonus{j}"))
                    tt(y_a[:, j, :], y_a[:, j, :], g_up[:, j, :], ALU.mult).then_inc(*Rv.step(f"y_a{j}"))

            def branch(st):
                for ct in range(8):
                    f = st.front + ct
                    q = 8 * st.branch + ct
                    if ct % 2 == 0:
                        dve.wait_ge(first_columns, q // 2 + 1)
                    else:
                        dve.wait_ge(tiles_used, st.tile + ct // 2 + 1)
                    if ct == 0:
                        dve.wait_ge(front_taken, st.front)
                    tt(br_t[:, 0, :], sgate[:, ct, :], half(FRONT[f % 2], 0), ALU.mult).then_inc(br_product, 1)
                    tt(br_t[:, 1, :], sgate[:, 8 + ct, :], half(FRONT[f % 2], 1), ALU.mult).then_inc(front_taken, 1)
                    dve.wait_ge(br_product, q + 1)
                    dve.wait_ge(front_taken, f + 1)
                    tt(u[:, ct, :], br_t[:, 0, :], br_t[:, 1, :], ALU.add).then_inc(u_ready, 1)
                    dve.wait_ge(u_ready, q + 1)

            dve.wait_ge(vecs_landed, 16)
            for st in PLAN:
                if st.kind == "ada":
                    mods_out()
                elif st.kind == "norm":
                    if st.mod is None:
                        norm(st, h3, h_ready, lambda j: V(st.gain, j), x3)
                    else:
                        q = 6 if st.mod == "kv" else 3 * st.mod[0] + st.mod[1]
                        norm(st, h3, h_scaled, lambda j: pre_gain[:, 8 * q + j:8 * q + j + 1], x3)
                elif st.kind == "final":
                    norm(st, y3, out_ready, lambda j: V(st.gain, j), x3)
                elif st.kind == "post":
                    if st.source == "ffn":
                        ffn_out(st, 1.0)
                    q = 3 * st.mod[0] + st.mod[1]
                    norm(st, y3, delta_ready, lambda j: post_gain[:, 8 * q + j:8 * q + j + 1], y3)
                elif st.kind == "ffn":
                    ffn(st)
                elif st.kind == "half":
                    ffn_out(st, 0.5)
                elif st.kind == "conv":
                    conv(st)
                elif st.kind == "kv":
                    kv(st)
                elif st.kind == "nsa":
                    nsa(st)
                elif st.kind == "mix":
                    mix(st)
                elif st.kind == "branch":
                    branch(st)
                elif st.kind == "lin4":
                    for t in range(4):
                        take(st, t, y3[:, 2 * t:2 * t + 2, :])


def constant_array():
    out = np.zeros((P, NCONST), np.float32)

    def put(name, a):
        s, n = CONST[name]
        out[:, s:s + n] = np.asarray(a, np.float32).reshape(a.shape[0], -1)

    i = np.arange(P)
    s, t = i[:, None], i[None, :]
    put("ident", np.eye(P))
    put("ones", np.ones((P, P)))
    put("mean_d", np.full((P, P), 1.0 / D))
    put("mean_p", np.full((P, P), 1.0 / P))
    same = s // CH == t // CH
    put("blk", same)
    put("blk_mean", same / CH)
    for lv in range(LEVELS):
        b = 1 << lv
        m = (s // (2 * b) == t // (2 * b)) & (s // b % 2 == 0) & (t // b % 2 == 1)
        put(f"level{lv}", m)
        if lv == 0:
            put("level0_ts", m.T)
    put("strict", same & (s < t))
    put("incl", same & (s <= t))
    put("causal", s <= t)
    for hd in range(MH):
        m = np.zeros((P, P))
        m[64 + hd] = 1
        put(f"pick{hd}", m)
    put("reset", np.broadcast_to(np.arange(TOK) % CH != 0, (P, TOK)))
    q = np.arange(TOK).reshape(2, P).T
    d = q[:, :, None] - np.arange(TOK)
    put("dist", np.where(d >= 0, d, 1e30))
    dc = q[:, :, None] - (np.arange(N_CMP) * CMP_STRIDE + CMP_LEN - 1)
    slope = 2.0 ** (-8.0 * np.arange(1, NH + 1) / NH)
    put("cmp_bias", np.where(dc[:, :, None] >= 0, -slope[:, None] * dc[:, :, None], -1e30))
    put("cmp_mask", dc >= 0)
    return out


def vector_array(a):
    out = np.zeros((P, NVEC), np.float32)

    def put(name, v):
        s, n = VEC[name]
        v = np.asarray(v).reshape(-1, P).T
        out[:, s:s + v.shape[1]] = v

    put("c", a["c"])
    put("mod_b", np.concatenate([a["ada_b"].reshape(-1), a["kv_ada_b"]]))
    put("norm_g", a["norm_g"])
    put("kv_norm", a["kv_norm_g"])
    put("conv", a["a_conv"])
    put("pos", a["cmp_pos"])
    for l in range(2):
        put(f"ffn1{l}", a["ffn1_norm_2"][l])
        put(f"mix{l}", a["mix_norm_2"][l])
        put(f"ffn2{l}", a["ffn2_norm_2"][l])
        put(f"mu{l}", np.concatenate([a["shift_mu_2"][l], np.zeros(96, np.float32)]))
        for name, key in (("w0", "rw_w0_2"), ("a0", "rw_a0_2"), ("kk", "rw_k_k_2"), ("ka", "rw_k_a_2"),
                          ("rk", "rw_r_k_2"), ("gnw", "rw_gn_w_2"), ("gnb", "rw_gn_b_2"), ("convw", "ml_conv_w_2"),
                          ("convb", "ml_conv_b_2"), ("mlnorm", "ml_norm_w_2")):
            put(f"{name}{l}", a[key][l])
        if l:
            put(f"vres{l}", a["vres_bias_2"][l - 1])
        g = VEC[f"gbias{l}"][0]
        out[64:68, g] = a["ml_i_bias_2"][l]
        out[96:100, g] = a["ml_f_bias_2"][l]
    put("final", a["final_norm_2"])
    return out


def weight_tiles(a):
    out = np.zeros((N_TILES, P, KC, TILE_COLS), np.float32)
    n = 0

    def put(w):
        nonlocal n
        t = -(-w.shape[1] // TILE_COLS)
        for i in range(t):
            v = w[:, i * TILE_COLS:(i + 1) * TILE_COLS]
            out[n, :, :, :v.shape[1]] = v.reshape(KC, P, -1).transpose(1, 0, 2)
            n += 1

    def put_flat(v):
        nonlocal n
        out[n].reshape(P, TILE)[:, :v.shape[1]] = v
        n += 1

    def put_ffn(w_in, w_out):
        for s in range(FFN_STEPS):
            c = slice(s * TILE_COLS, (s + 1) * TILE_COLS)
            put(w_in[:, c])
            put(w_in[:, D_FF:][:, c])
            put_flat(w_out[c].reshape(2, P, D).transpose(1, 0, 2).reshape(P, 2 * D))

    def twice(w):
        return np.repeat(w.reshape(w.shape[0], -1, 1, DH), 2, axis=2).reshape(w.shape[0], -1)

    put(a["ada_w"][0])
    put(a["ada_w"][1])
    put(a["kv_ada_w"])
    put_ffn(a["ffn_w_in"][0, 0], a["ffn_w_out"][0, 0])
    put(a["a_w_in"][0])
    put(a["a_w_out"][0])
    put_ffn(a["ffn_w_in"][0, 1], a["ffn_w_out"][0, 1])
    kv = a["kv_w"].reshape(D, 3, 2, NG * DH)
    for br, s in ((0, 0), (0, 1), (1, 0), (2, 0)):
        put(twice(kv[:, br, s]))
    put(kv[:, 1, 1])
    put(kv[:, 2, 1])
    for s in range(2):
        w1 = a["cmp_w1"][s].reshape(2, KC, P, 256)
        for i in range(2):
            put_flat(w1[i].transpose(1, 0, 2).reshape(P, TILE))
    w2 = a["cmp_w2"].reshape(2, 2, P, DH)
    put_flat(np.concatenate([w2[0, 0], w2[0, 0], w2[0, 1], w2[0, 1], w2[1, 0], w2[1, 1]], axis=1))
    put_ffn(a["ffn_w_in"][1, 0], a["ffn_w_out"][1, 0])
    put(a["b_w_in"][0])
    put(a["b_w_out"][0])
    put_ffn(a["ffn_w_in"][1, 1], a["ffn_w_out"][1, 1])
    for l in range(2):
        put_ffn(a["ffn1_w_in_2"][l], a["ffn1_w_out_2"][l])
        w = a["w_in_2"][l]
        put(w[:, 0:1792])
        tail = np.zeros((D, TILE_COLS), np.float32)
        tail[:, 0:32] = w[:, 1792:1824]
        if l:
            tail[:, 32:64] = a["vres_down_2"][l - 1]
        tail[:, 64:68] = w[:, 3872:3876]
        tail[:, 96:100] = w[:, 3876:3880]
        put(tail)
        put(w[:, 1824:3872])
        lora = np.zeros((P, 4, 512), np.float32)
        lora[0:64, 0] = a["rw_w_up_2"][l]
        lora[64:128, 1] = a["rw_a_up_2"][l]
        lora[:, 2] = a["rw_g_up_2"][l][0:P]
        lora[0:32, 3] = a["rw_g_up_2"][l][P:]
        if l:
            lora[32:64, 3] = a["vres_up_2"][l - 1]
        put_flat(lora.reshape(P, TILE))
        put(w[:, 3880:])
        put(np.concatenate([a["br_a_2"][l], a["br_b_2"][l]], axis=0))
        put(a["w_out_2"][l])
        put_ffn(a["ffn2_w_in_2"][l], a["ffn2_w_out_2"][l])
    assert n == N_TILES, (n, N_TILES)
    return out.reshape(N_TILES, P, TILE)


def kernel(**inputs):
    import concourse.bacc as bacc
    from concourse.bass_utils import run_bass_kernel_spmd

    a = {k: np.asarray(v) for k, v in inputs.items()}
    x = a["x"].reshape(TOK, KC, P).transpose(2, 1, 0).reshape(P, KC * TOK)
    arrays = {"consts": constant_array(), "vecs": vector_array(a), "x_in": np.ascontiguousarray(x),
              "weights": weight_tiles(a)}
    nc = bacc.Bacc("TRN2", target_bir_lowering=False, num_devices=1)
    args = [nc.dram_tensor(k, v.shape, F32, kind="ExternalInput").ap() for k, v in arrays.items()]
    out = nc.dram_tensor("out", (P, KC * TOK), F32, kind="ExternalOutput").ap()
    build(nc, *args, out)
    got = run_bass_kernel_spmd(nc, [arrays], core_ids=[0]).results[0]["out"]
    return np.ascontiguousarray(got.reshape(P, KC, TOK).transpose(2, 1, 0).reshape(1, TOK, D))
```

```python
from contextlib import ExitStack

import numpy as np
import concourse.bass as bass
from concourse import mybir

P = 128
TOK = 256
D = 1024
KC = D // P
TILE_COLS = 256
TILE = KC * TILE_COLS
RING = 3
SLOTS = 3
HALF = TILE // 2
D_FF = 2816
FFN_STEPS = D_FF // TILE_COLS
FFN_TILES = 3 * FFN_STEPS
HALVES = 2 * FFN_STEPS
NH, NG, DH = 16, 4, 64
N_CMP, CMP_LEN, CMP_STRIDE = 15, 32, 16
MOD_COLS = 72 + 72 + 16
ADA_FFN = 3 * FFN_STEPS - 1
ADA_FIRST = MOD_COLS * P // TILE_COLS - 2 * ADA_FFN
CH = 64
PAD = 4
ZW = TOK + PAD
NZ = 15
RH, MH = 8, 4
LEVELS = 6
RMS_EPS = 1e-6
GN_EPS = 64e-5
ML_EPS = 1e-5
EXP_MINUS_HALF = 0.6065306597126334

F32 = mybir.dt.float32
F32R = mybir.dt.float32r
ALU = mybir.AluOpType
ACT = mybir.ActivationFunctionType
AX_X = mybir.AxisListType.X


def columns(sizes):
    at, out = 0, {}
    for name, n in sizes:
        out[name] = (at, n)
        at += n
    return out, at


CONST, NCONST = columns(
    [("ident", P), ("ones", P), ("blk", P)]
    + [(f"level{i}", P) for i in range(LEVELS)] + [("level0_ts", P), ("strict", P), ("incl", P), ("causal", P)]
    + [("reset", TOK), ("dist", TOK), ("cmp_dist", 2 * N_CMP), ("cmp_mask", 2 * N_CMP)])

_second = []
for _l in range(2):
    _second += [(f"ffn1{_l}", 8), (f"mix{_l}", 8), (f"ffn2{_l}", 8), (f"mu{_l}", NZ), (f"w0{_l}", 4), (f"a0{_l}", 4),
                (f"kk{_l}", 4), (f"ka{_l}", 4), (f"rk{_l}", 4), (f"gnw{_l}", 4), (f"gnb{_l}", 4), (f"vres{_l}", 4),
                (f"convw{_l}", 32), (f"convb{_l}", 8), (f"gbias{_l}", 1), (f"mlnorm{_l}", 4)]
VEC, NVEC = columns([("c", 8), ("mod_b", MOD_COLS), ("norm_g", 96), ("kv_norm", 8), ("conv", 24), ("pos", 32)]
                    + _second + [("final", 8)])


USES = {
    "ada": dict(tile=ADA_FIRST, ada=ADA_FIRST), "norm": dict(norm=1, pre=1, scaled=1), "post": dict(norm=1, post=1, update=1),
    "half": dict(update=1), "ffn": dict(tile=FFN_TILES, half=2 * FFN_TILES, front=HALVES, ffn=1),
    "ffn_ada": dict(tile=FFN_TILES + ADA_FFN, half=2 * FFN_TILES, front=HALVES, ffn=1, ada=ADA_FFN),
    "conv": dict(tile=12, half=24, front=12), "lin4": dict(tile=4, half=8, front=4, pre=1),
    "kv": dict(tile=15, half=20, front=10), "nsa": dict(tile=5, half=10, front=5),
    "mix": dict(tile=17, half=32, front=16), "gates": dict(tile=8, half=16, front=8),
    "branch": dict(tile=4, half=8, front=8, branch=1, pre=1), "resid": dict(update=1), "final": dict(norm=1),
}


class Stage:

    def __init__(self, kind, at, mod=None, gain=None, source=None, rhs=None, layer=None):
        self.kind, self.mod, self.gain, self.source, self.rhs, self.layer = kind, mod, gain, source, rhs, layer
        self.ada = at["ada"]
        self.tile, self.half, self.front = at["tile"], at["half"], at["front"]
        self.norm, self.pre, self.scaled = at["norm"], at["pre"], at["scaled"]
        self.post, self.update, self.ffn, self.branch = at["post"], at["update"], at["ffn"], at["branch"]


class Engines:

    def __init__(self, steps, mixer):
        self.pe, self.vec, self.act, self.pool = (steps(f"{mixer}_{e}") for e in ("pe", "vec", "act", "pool"))


def make_plan():
    at = dict(tile=0, half=0, ada=0, scaled=0, front=0, norm=0, pre=0, post=0, update=0, ffn=0, branch=0)
    plan = []

    def add(kind, **kw):
        plan.append(Stage(kind, at, **kw))
        for k, n in USES[kind].items():
            at[k] += n

    add("ada")
    for layer in range(2):
        if layer == 1:
            add("norm", mod="kv")
            add("kv")
        for i in range(3):
            add("norm", mod=(layer, i))
            if i != 1:
                add("ffn" if layer else "ffn_ada")
                add("post", mod=(layer, i), source="ffn")
            else:
                add("nsa" if layer else "conv")
                add("lin4", rhs="o" if layer else "conv_y")
                add("post", mod=(layer, i), source="lin4")
    for layer in range(2):
        add("norm", mod=None, gain=f"ffn1{layer}")
        add("ffn")
        add("half")
        add("norm", mod=None, gain=f"mix{layer}")
        add("mix", layer=layer)
        add("gates")
        add("branch")
        add("lin4", rhs="u")
        add("resid")
        add("norm", mod=None, gain=f"ffn2{layer}")
        add("ffn")
        add("half")
    add("final", mod=None, gain="final")
    return plan, at


PLAN, TOTAL = make_plan()
N_TILES = TOTAL["tile"]
N_HALVES = TOTAL["half"]


def slope(head):
    return 2.0 ** (-8.0 * (head + 1) / NH)


def split_halves():
    out, run = [], 0
    for st in PLAN:
        n, tiles = USES[st.kind].get("half", 0), USES[st.kind].get("tile", 0)
        at = range(tiles)
        if st.kind == "ffn_ada":
            at = [t for t in at if t == 0 or t % 2]
        out += [(st.tile + at[i // 2], i % 2, run) for i in range(n)]
        run += st.kind in ("kv", "mix")
    return out


SPLIT = split_halves()


class Steps:

    def __init__(self, sem, names):
        self.sem, self.names, self.made = sem, names, 0
        self.value = {n: i + 1 for i, n in enumerate(names)}

    def step(self, name):
        assert self.names[self.made] == name, (name, self.names[self.made])
        self.made += 1
        return self.sem, 1

    def at(self, name):
        return self.sem, self.value[name]


STEPS = {
    "conv_vector": """
        v a0 a1 a2 a3 a4 a5 a6 a7 b0 b1 b2 b3 b4 b5 b6 b7 c0 c1 c2 c3 c4 c5 c6 c7 y0 y1 y2 y3 y4 y5 y6 y7""".split(),
    "conv_pool": """
        pad""".split(),
    "kv_vector": """
        blocks kcz0 kcz1 vcz0 vcz1""".split(),
    "kv_scalar": """
        gelu""".split(),
    "kv_pool": """
        zero zero_cmp""".split(),
    "attention_tensor": """
        cmp_scores0 cmp_scores1 scores0 scores1 cmp_turned0 cmp_turned1 cmp_turned2 cmp_turned3 cmp_turned4
        cmp_turned5 cmp_turned6 cmp_turned7 turned0 scores2 values0 turned1 scores3 values1 turned2 scores4 values2
        turned3 scores5 values3 turned4 scores6 values4 turned5 scores7 values5 turned6 scores8 values6 turned7
        scores9 values7 turned8 scores10 values8 turned9 scores11 values9 turned10 scores12 values10 turned11
        scores13 values11 turned12 scores14 values12 turned13 scores15 values13 turned14 scores16 values14 turned15
        scores17 values15 turned16 scores18 values16 turned17 scores19 values17 turned18 scores20 values18 turned19
        scores21 values19 turned20 scores22 values20 turned21 scores23 values21 turned22 scores24 values22 turned23
        scores25 values23 turned24 scores26 values24 turned25 scores27 values25 turned26 scores28 values26 turned27
        scores29 values27 turned28 scores30 values28 turned29 scores31 values29 turned30 values30 turned31 values31""".split(),
    "attention_vector": """
        q3 cmp_biased0 cmp_max0 cmp_centred0 cmp_masked0 cmp_sum0 cmp_floor0 cmp_inv0 cmp_gate0 pc0 cmp_biased1
        cmp_max1 cmp_centred1 cmp_masked1 cmp_sum1 cmp_floor1 cmp_inv1 cmp_gate1 pc1 pcT0 pcT1 pcT2 pcT3 pcT4 pcT5
        pcT6 pcT7 biased0 rawmax0 max0 biased1 rawmax1 max1 inv0 weight0 p0 biased2 rawmax2 max2 inv1 weight1 p1
        biased3 rawmax3 max3 inv2 weight2 p2 biased4 rawmax4 max4 inv3 weight3 p3 o0 biased5 rawmax5 max5 inv4
        weight4 p4 biased6 rawmax6 max6 inv5 weight5 p5 o1 biased7 rawmax7 max7 inv6 weight6 p6 biased8 rawmax8 max8
        inv7 weight7 p7 o2 biased9 rawmax9 max9 inv8 weight8 p8 biased10 rawmax10 max10 inv9 weight9 p9 o3 biased11
        rawmax11 max11 inv10 weight10 p10 biased12 rawmax12 max12 inv11 weight11 p11 o4 biased13 rawmax13 max13
        inv12 weight12 p12 biased14 rawmax14 max14 inv13 weight13 p13 o5 biased15 rawmax15 max15 inv14 weight14 p14
        biased16 rawmax16 max16 inv15 weight15 p15 o6 biased17 rawmax17 max17 inv16 weight16 p16 biased18 rawmax18
        max18 inv17 weight17 p17 o7 biased19 rawmax19 max19 inv18 weight18 p18 biased20 rawmax20 max20 inv19
        weight19 p19 o8 biased21 rawmax21 max21 inv20 weight20 p20 biased22 rawmax22 max22 inv21 weight21 p21 o9
        biased23 rawmax23 max23 inv22 weight22 p22 biased24 rawmax24 max24 inv23 weight23 p23 o10 biased25 rawmax25
        max25 inv24 weight24 p24 biased26 rawmax26 max26 inv25 weight25 p25 o11 biased27 rawmax27 max27 inv26
        weight26 p26 biased28 rawmax28 max28 inv27 weight27 p27 o12 biased29 rawmax29 max29 inv28 weight28 p28
        biased30 rawmax30 max30 inv29 weight29 p29 o13 biased31 rawmax31 max31 inv30 weight30 p30 inv31 weight31 p31
        o14 o15""".split(),
    "attention_scalar": """
        cmp_exp0 cmp_exp1 exp0_0 exp0_1 exp1_0 exp1_1 pt0 exp2_0 exp2_1 pt1 exp3_0 exp3_1 pt2 exp4_0 exp4_1 pt3
        exp5_0 exp5_1 pt4 exp6_0 exp6_1 pt5 exp7_0 exp7_1 pt6 exp8_0 exp8_1 pt7 exp9_0 exp9_1 pt8 exp10_0 exp10_1
        pt9 exp11_0 exp11_1 pt10 exp12_0 exp12_1 pt11 exp13_0 exp13_1 pt12 exp14_0 exp14_1 pt13 exp15_0 exp15_1 pt14
        exp16_0 exp16_1 pt15 exp17_0 exp17_1 pt16 exp18_0 exp18_1 pt17 exp19_0 exp19_1 pt18 exp20_0 exp20_1 pt19
        exp21_0 exp21_1 pt20 exp22_0 exp22_1 pt21 exp23_0 exp23_1 pt22 exp24_0 exp24_1 pt23 exp25_0 exp25_1 pt24
        exp26_0 exp26_1 pt25 exp27_0 exp27_1 pt26 exp28_0 exp28_1 pt27 exp29_0 exp29_1 pt28 exp30_0 exp30_1 pt29
        exp31_0 exp31_1 pt30 pt31""".split(),
    "mlstm0_pe": """
        g_turned M_spread em_spread scores0 scores1 scores2 scores3 sums0 scores4 scores5 sums1 scores6 scores7
        sums2 sums3 mean var""".split(),
    "mlstm0_vec": """
        m_o diff shifted li xf minus_abs lf F g_row M_row F_plus_M tap0_0 tap0_1 tap0_2 tap0_3 tap0_4 tap0_5 tap0_6
        tap0_7 tap1_0 tap1_1 tap1_2 tap1_3 tap1_4 tap1_5 tap1_6 tap1_7 tap2_0 tap2_1 tap2_2 tap2_3 tap2_4 tap2_5
        tap2_6 tap2_7 conv0 conv1 conv2 conv3 conv4 conv5 conv6 conv7 g_col gap0 gap1 gap2 sw0 masked0 gap3 sw1
        masked1 gap4 sw2 masked2 gap5 sw3 masked3 gap6 floor0 den0 inv0 h0 sw4 masked4 gap7 sw5 masked5 floor1 den1
        inv1 h1 sw6 masked6 sw7 masked7 floor2 den2 inv2 h2 floor3 den3 inv3 h3 centred0 centred1 rstd0 rstd1 normed
        y_b""".split(),
    "mlstm0_act": """
        exp_f ln_f em_row qk em_copy weight0 weight1 weight2 weight3 weight4 weight5 weight6 weight7 sig_o squares
        root0 root1""".split(),
    "mlstm0_pool": """
        pads rows_zero""".split(),
    "mlstm1_pe": """
        g_turned M_spread em_spread scores0 scores1 scores2 scores3 sums0 scores4 scores5 sums1 scores6 scores7
        sums2 sums3 mean var""".split(),
    "mlstm1_vec": """
        m_o diff shifted li xf minus_abs lf F g_row M_row F_plus_M tap0_0 tap0_1 tap0_2 tap0_3 tap0_4 tap0_5 tap0_6
        tap0_7 tap1_0 tap1_1 tap1_2 tap1_3 tap1_4 tap1_5 tap1_6 tap1_7 tap2_0 tap2_1 tap2_2 tap2_3 tap2_4 tap2_5
        tap2_6 tap2_7 conv0 conv1 conv2 conv3 conv4 conv5 conv6 conv7 g_col gap0 gap1 gap2 sw0 masked0 gap3 sw1
        masked1 gap4 sw2 masked2 gap5 sw3 masked3 gap6 floor0 den0 inv0 h0 sw4 masked4 gap7 sw5 masked5 floor1 den1
        inv1 h1 sw6 masked6 sw7 masked7 floor2 den2 inv2 h2 floor3 den3 inv3 h3 centred0 centred1 rstd0 rstd1 normed
        y_b""".split(),
    "mlstm1_act": """
        exp_f ln_f em_row qk em_copy weight0 weight1 weight2 weight3 weight4 weight5 weight6 weight7 sig_o squares
        root0 root1""".split(),
    "mlstm1_pool": """
        pads rows_zero""".split(),
    "rwkv0_pe": """
        w a kk_norm rk_sum turned0_0 turned1_0 turned2_0 A_t0_0 A_t1_0 A0_0 A1_0 A_kk0_0 A_kk1_0 A_rk0_0 A_rk1_0
        A_rb0_0 A_rb1_0 U1_0_0 U1_1_0 D1_0_0 D_t1_0_0 D1_1_0 D_t1_1_0 U2_0_0 U2_1_0 D2_0_0 D_t2_0_0 D2_1_0 D_t2_1_0
        U3_0_0 U3_1_0 D3_0_0 D_t3_0_0 D3_1_0 D_t3_1_0 U4_0_0 U4_1_0 D4_0_0 D_t4_0_0 D4_1_0 D_t4_1_0 U5_0_0 U5_1_0
        D_t5_0_0 D_t5_1_0 G0 SA0 dS0 y0 G1 SA1 dS1 y1 turned0_1 turned1_1 turned2_1 A_t0_1 A_t1_1 A0_1 A1_1 A_kk0_1
        A_kk1_1 A_rk0_1 A_rk1_1 A_rb0_1 A_rb1_1 U1_0_1 U1_1_1 D1_0_1 D_t1_0_1 D1_1_1 D_t1_1_1 U2_0_1 U2_1_1 D2_0_1
        D_t2_0_1 D2_1_1 D_t2_1_1 U3_0_1 U3_1_1 D3_0_1 D_t3_0_1 D3_1_1 D_t3_1_1 U4_0_1 U4_1_1 D4_0_1 D_t4_0_1 D4_1_1
        D_t4_1_1 U5_0_1 U5_1_1 D_t5_0_1 D_t5_1_1 G2 SA2 dS2 y2 G3 SA3 dS3 y3 gn_mean gn_var""".split(),
    "rwkv0_vec": """
        lora_zero lora_tail one_minus_ka kk_raw0 kk_raw1 kk_raw2 kk_raw3 lw L L_prev g_taken0 g_taken1 ka k_mixed rk
        rk0 rk1 rk2 rk3 v_mixed kk_floor0 kk_floor1 kk_rstd0 kk_rstd1 kk bonus0 bonus1 b kap rho P khat bhat k_z0
        k_z1 b_z0 b_z1 keep0 keep1 ktok0_0 ktok1_0 btok0_0 btok1_0 v_z0_0 v_z1_0 A_t0_0 A_t1_0 X_off0_0 X0_0_0
        Xt_off0_0 X_t0_0_0 X_off1_0 X0_1_0 Xt_off1_0 X_t0_1_0 A_kk0_0 A_kk1_0 A_rk0_0 A_rk1_0 A_rb0_0 A_rb1_0 X1_0_0
        X_t1_0_0 X1_1_0 X_t1_1_0 X2_0_0 X_t2_0_0 X2_1_0 X_t2_1_0 X3_0_0 X_t3_0_0 X3_1_0 X_t3_1_0 X4_0_0 X_t4_0_0
        X4_1_0 X_t4_1_0 X_t5_0_0 X_t5_1_0 S0_3 G0 SA0_0 SA0_1 S_sum0 S1_0 S1_1 S1_2 S1_3 y0 G1 SA1_0 SA1_1 S_sum1
        S2_0 S2_1 S2_2 S2_3 y1 ktok0_1 ktok1_1 btok0_1 btok1_1 v_z0_1 v_z1_1 A_t0_1 A_t1_1 X_off0_1 X0_0_1 Xt_off0_1
        X_t0_0_1 X_off1_1 X0_1_1 Xt_off1_1 X_t0_1_1 A_kk0_1 A_kk1_1 A_rk0_1 A_rk1_1 A_rb0_1 A_rb1_1 X1_0_1 X_t1_0_1
        X1_1_1 X_t1_1_1 X2_0_1 X_t2_0_1 X2_1_1 X_t2_1_1 X3_0_1 X_t3_0_1 X3_1_1 X_t3_1_1 X4_0_1 X_t4_0_1 X4_1_1
        X_t4_1_1 X_t5_0_1 X_t5_1_1 G2 SA2_0 SA2_1 S_sum2 S3_0 S3_1 S3_2 S3_3 y2 G3 SA3_0 SA3_1 S_sum3 S4_0 S4_1 S4_2
        S4_3 y3 gn_centred0 gn_centred1 gn_rstd0 gn_rstd1 gn0 gn1 gn2 gn3 with_bonus0 with_bonus1 with_bonus2
        with_bonus3 y_a0 y_a1 y_a2 y_a3""".split(),
    "rwkv0_act": """
        lora_mid lora_in sig_w a kk_sq kk_root0 kk_root1 E E_inv E_prev U1_0_0 U1_1_0 U2_0_0 U2_1_0 U3_0_0 U3_1_0
        U4_0_0 U4_1_0 U5_0_0 U5_1_0 U1_0_1 U1_1_1 U2_0_1 U2_1_1 U3_0_1 U3_1_1 U4_0_1 U4_1_1 U5_0_1 U5_1_1 gn_squares
        gn_root0 gn_root1""".split(),
    "rwkv0_pool": """
        z_zero tok_zero A_lv1_0 A_lv2_0 A_lv3_0 A_lv4_0 A_lv5_0 A_lv1_1 A_lv2_1 A_lv3_1 A_lv4_1 A_lv5_1""".split(),
    "rwkv1_pe": """
        w a g kk_norm rk_sum turned0_0 turned1_0 turned2_0 A_t0_0 A_t1_0 A0_0 A1_0 A_kk0_0 A_kk1_0 A_rk0_0 A_rk1_0
        A_rb0_0 A_rb1_0 U1_0_0 U1_1_0 D1_0_0 D_t1_0_0 D1_1_0 D_t1_1_0 U2_0_0 U2_1_0 D2_0_0 D_t2_0_0 D2_1_0 D_t2_1_0
        U3_0_0 U3_1_0 D3_0_0 D_t3_0_0 D3_1_0 D_t3_1_0 U4_0_0 U4_1_0 D4_0_0 D_t4_0_0 D4_1_0 D_t4_1_0 U5_0_0 U5_1_0
        D_t5_0_0 D_t5_1_0 G0 SA0 dS0 y0 G1 SA1 dS1 y1 turned0_1 turned1_1 turned2_1 A_t0_1 A_t1_1 A0_1 A1_1 A_kk0_1
        A_kk1_1 A_rk0_1 A_rk1_1 A_rb0_1 A_rb1_1 U1_0_1 U1_1_1 D1_0_1 D_t1_0_1 D1_1_1 D_t1_1_1 U2_0_1 U2_1_1 D2_0_1
        D_t2_0_1 D2_1_1 D_t2_1_1 U3_0_1 U3_1_1 D3_0_1 D_t3_0_1 D3_1_1 D_t3_1_1 U4_0_1 U4_1_1 D4_0_1 D_t4_0_1 D4_1_1
        D_t4_1_1 U5_0_1 U5_1_1 D_t5_0_1 D_t5_1_1 G2 SA2 dS2 y2 G3 SA3 dS3 y3 gn_mean gn_var""".split(),
    "rwkv1_vec": """
        lora_zero lora_tail one_minus_ka kk_raw0 kk_raw1 kk_raw2 kk_raw3 lw L L_prev g_taken0 g_taken1 ka k_mixed rk
        rk0 rk1 rk2 rk3 v_gap v_gated v_mixed kk_floor0 kk_floor1 kk_rstd0 kk_rstd1 kk bonus0 bonus1 b kap rho P
        khat bhat k_z0 k_z1 b_z0 b_z1 keep0 keep1 ktok0_0 ktok1_0 btok0_0 btok1_0 v_z0_0 v_z1_0 A_t0_0 A_t1_0
        X_off0_0 X0_0_0 Xt_off0_0 X_t0_0_0 X_off1_0 X0_1_0 Xt_off1_0 X_t0_1_0 A_kk0_0 A_kk1_0 A_rk0_0 A_rk1_0
        A_rb0_0 A_rb1_0 X1_0_0 X_t1_0_0 X1_1_0 X_t1_1_0 X2_0_0 X_t2_0_0 X2_1_0 X_t2_1_0 X3_0_0 X_t3_0_0 X3_1_0
        X_t3_1_0 X4_0_0 X_t4_0_0 X4_1_0 X_t4_1_0 X_t5_0_0 X_t5_1_0 S0_3 G0 SA0_0 SA0_1 S_sum0 S1_0 S1_1 S1_2 S1_3 y0
        G1 SA1_0 SA1_1 S_sum1 S2_0 S2_1 S2_2 S2_3 y1 ktok0_1 ktok1_1 btok0_1 btok1_1 v_z0_1 v_z1_1 A_t0_1 A_t1_1
        X_off0_1 X0_0_1 Xt_off0_1 X_t0_0_1 X_off1_1 X0_1_1 Xt_off1_1 X_t0_1_1 A_kk0_1 A_kk1_1 A_rk0_1 A_rk1_1
        A_rb0_1 A_rb1_1 X1_0_1 X_t1_0_1 X1_1_1 X_t1_1_1 X2_0_1 X_t2_0_1 X2_1_1 X_t2_1_1 X3_0_1 X_t3_0_1 X3_1_1
        X_t3_1_1 X4_0_1 X_t4_0_1 X4_1_1 X_t4_1_1 X_t5_0_1 X_t5_1_1 G2 SA2_0 SA2_1 S_sum2 S3_0 S3_1 S3_2 S3_3 y2 G3
        SA3_0 SA3_1 S_sum3 S4_0 S4_1 S4_2 S4_3 y3 gn_centred0 gn_centred1 gn_rstd0 gn_rstd1 gn0 gn1 gn2 gn3
        with_bonus0 with_bonus1 with_bonus2 with_bonus3 y_a0 y_a1 y_a2 y_a3""".split(),
    "rwkv1_act": """
        lora_mid lora_in sig_w a vg kk_sq kk_root0 kk_root1 E E_inv E_prev U1_0_0 U1_1_0 U2_0_0 U2_1_0 U3_0_0 U3_1_0
        U4_0_0 U4_1_0 U5_0_0 U5_1_0 U1_0_1 U1_1_1 U2_0_1 U2_1_1 U3_0_1 U3_1_1 U4_0_1 U4_1_1 U5_0_1 U5_1_1 gn_squares
        gn_root0 gn_root1""".split(),
    "rwkv1_pool": """
        z_zero tok_zero A_lv1_0 A_lv2_0 A_lv3_0 A_lv4_0 A_lv5_0 A_lv1_1 A_lv2_1 A_lv3_1 A_lv4_1 A_lv5_1""".split(),
}



def build(nc, consts_d, vecs_d, x_d, weights_d, out_d):
    with ExitStack() as ctx:
        def sb(name, cols, dtype=F32):
            return ctx.enter_context(nc.sbuf_tensor(name, [P, cols], dtype))

        def sem(name):
            return ctx.enter_context(nc.semaphore(name))

        consts, vecs = sb("const_sb", NCONST), sb("vec_sb", NVEC)
        ring = [sb(f"ring{i}", TILE) for i in range(RING)]
        w_hi, w_lo = ([sb(f"w_{e}{i}", HALF, F32R) for i in range(SLOTS)] for e in ("hi", "lo"))
        h_hi, h_lo = sb("h_hi", KC * TOK, F32R), sb("h_lo", KC * TOK, F32R)
        x, y, sq = sb("x", KC * TOK), sb("y", KC * TOK), sb("sq", KC * TOK)
        act_t, silu_t, rstd = sb("act_t", 2 * TOK), sb("silu_t", 2 * TOK), sb("rstd", TOK)
        act_hi, act_lo = sb("act_hi", 2 * TOK, F32R), sb("act_lo", 2 * TOK, F32R)
        mods, pre_gain, post_gain, cond = sb("mods", MOD_COLS), sb("pre_gain", 56), sb("post_gain", 48), sb("cond", 8)
        v_first = sb("v_first", 4 * TOK)
        work = sb("work", 23360)
        bank = [ctx.enter_context(nc.psum_tensor(f"bank{i}", [P, 512], F32)) for i in range(8)]
        Y_BANK, FRONT, LOW, MOD_BANK = 0, (4, 5), 6, 7

        def K(name):
            a, n = CONST[name]
            return consts[:, a:a + n]

        def V(name, i=0, n=1):
            a = VEC[name][0] + i
            return vecs[:, a:a + n]

        def tiles(t, n=KC, w=TOK):
            return t[:, :].rearrange("p (j t) -> p j t", j=n) if w is None else \
                t[:, 0:n * w].rearrange("p (j t) -> p j t", j=n)

        x3, hi3, lo3, y3, sq3 = tiles(x), tiles(h_hi), tiles(h_lo), tiles(y), tiles(sq)
        ada_acc = tiles(y, 3)
        rings = [r[:, :].rearrange("p (h k c) -> p h k c", h=2, k=KC) for r in ring]
        whi3, wlo3 = ([r[:, :].rearrange("p (k c) -> p k c", k=KC) for r in w] for w in (w_hi, w_lo))

        def carve(start, *dims):
            n = int(np.prod(dims))
            assert start + n <= 23360, (start, n)
            v = work[:, start:start + n]
            if len(dims) == 2:
                v = v.rearrange("p (a b) -> p a b", a=dims[0])
            if len(dims) == 3:
                v = v.rearrange("p (a b c) -> p a b c", a=dims[0], b=dims[1])
            if len(dims) == 4:
                v = v.rearrange("p (a b c d) -> p a b c d", a=dims[0], b=dims[1], c=dims[2])
            return v

        def half(b, i):
            return bank[b][:, i * TOK:(i + 1) * TOK]

        def pair(b):
            return bank[b][:, :].rearrange("p (a t) -> p a t", a=2)

        def quad(b):
            return bank[b][:, :].rearrange("p (a t) -> p a t", a=4)

        def mod_col(layer, sub, what):
            return 72 * layer + 24 * sub + 8 * what

        consts_landed, vecs_landed, x_landed = sem("consts_landed"), sem("vecs_landed"), sem("x_landed")
        tile_landed = [sem(f"tile_landed{i}") for i in range(RING)]
        halves_left = sem("halves_left")
        hi_ready, half_used = sem("hi_ready"), sem("half_used")
        front_taken, silu_ready = sem("front_taken"), sem("silu_ready")
        hidden_hi, hidden_ready = sem("hidden_hi"), sem("hidden_ready")
        squares_ready, meansq_ready = sem("squares_ready"), sem("meansq_ready")
        root_ready, rstd_ready = sem("root_ready"), sem("rstd_ready")
        h_scaled, h_hi_ready, h_ready = sem("h_scaled"), sem("h_hi_ready"), sem("h_ready")
        y_ready, delta_ready, x_ready = sem("y_ready"), sem("delta_ready"), sem("x_ready")
        cond_ready, mods_taken = sem("cond_ready"), sem("mods_taken")
        ada_partial, ada_summed = sem("ada_partial"), sem("ada_summed")
        gains_ready, u_ready, br_product = sem("gains_ready"), sem("u_ready"), sem("br_product")
        out_ready, out_stored = sem("out_ready"), sem("out_stored")

        def steps(name):
            return Steps(sem(name), STEPS.get(name, []))

        conv_vec, conv_pool = steps("conv_vector"), steps("conv_pool")
        kv_pe, kv_vec, kv_act, kv_pool = (steps(f"kv_{e}") for e in ("tensor", "vector", "scalar", "pool"))
        at_pe, at_vec, at_act, at_pool = (steps(f"attention_{e}") for e in ("tensor", "vector", "scalar", "pool"))
        ML = [Engines(steps, f"mlstm{l}") for l in range(2)]
        RW = [Engines(steps, f"rwkv{l}") for l in range(2)]

        conv_z = carve(0, 24, TOK)
        conv_v = carve(6144, 8, ZW)
        conv_y = carve(6144 + 8 * ZW, 8, TOK)

        kz = carve(0, 2, NG, 2, TOK)
        vz = carve(4096, 16, 2, P)
        blocks = carve(8192, 2, 16, NG * N_CMP)
        hid = carve(10112, 2, 2, NG * N_CMP)
        kcz = carve(10352, NG, 2, N_CMP)
        vcz = carve(10472, NG, 2, P)
        q_t = carve(11496, 8, TOK)
        o_t = carve(13544, 8, TOK)
        gate_tok = carve(15592, 2, 3 * NH)
        pc = carve(15688, 2, NH, N_CMP)
        pc_t = carve(16168, 2, NH, P)
        s_buf = carve(20264, 2, 2, TOK)
        pt_buf = carve(21288, 2, 4, P)
        at_small = carve(22312, 256)

        zp = carve(0, NZ, ZW)
        C0 = NZ * ZW
        y_b = carve(C0, 4, TOK)
        g_up = carve(C0 + 1024, 4, TOK)
        bonus = carve(C0 + 2048, 4, TOK)
        y_a = carve(C0 + 3072, 4, TOK)
        rho, kap = carve(C0 + 4096, 4, TOK), carve(C0 + 5120, 4, TOK)
        k_z, b_z = carve(C0 + 6144, 4, 2, TOK), carve(C0 + 8192, 4, 2, TOK)
        C1 = C0 + 10240
        mqk = carve(C0 + 4096, 8, ZW)
        m_o = carve(C0 + 6176, 4, TOK)
        v_tok = carve(C0 + 7200, 2, 512)
        diff = carve(C1, NZ, TOK)
        qk = carve(C1, 8, TOK)
        sw = carve(C1 + 2048, 8, TOK)
        h_b = carve(C1 + 4096, 4, TOK)
        rows = carve(C1 + 5120, 3, TOK)
        row_tmp = carve(C1 + 5888, 5, TOK)
        bc_e = carve(C1 + 7168, 4, TOK)
        w_buf = carve(C1 + 8192, 4, TOK)
        e1, e2, e3, e4, e5, e6, e7, e8 = (carve(C1 + 1024 * i, 4, TOK) for i in range(8))
        lora_in = carve(C1 + 8192, 4, TOK)
        A_t, A_kk, A_rk, A_rb = (carve(C1 + 1024 * i, RH, P) for i in range(4))
        X, X_t, U = (carve(C1 + 4096 + 1024 * i, RH, P) for i in range(3))
        A_lv = [carve(C1 + 7168, RH, P), carve(C1 + 8192, RH, P)]
        ktok = y[:, 0:1024].rearrange("p (c f) -> p c f", c=2)
        btok = y[:, 1024:2048].rearrange("p (c f) -> p c f", c=2)
        v_z = sq[:, 0:1024].rearrange("p (j r v) -> p j r v", j=4, r=2)
        sa_z = sq[:, 1024:2048].rearrange("p (j r v) -> p j r v", j=4, r=2)
        rw_small = C1 + 9216
        S = act_t[:, 0:512].rearrange("p (j v) -> p j v", j=4)
        gs = silu_t
        small = sb("small", 64)
        keep = [zp[:, 4 * s:4 * s + 4, PAD:PAD + P] for s in range(2)]
        sgate = carve(C1, 16, TOK)
        br_t = carve(C1 + 4096, 2, TOK)
        u = sq3

        block = ctx.enter_context(nc.Block())

        @block.sync
        def _(sp):
            sp.dma_start(vecs[:, :], vecs_d).then_inc(vecs_landed, 16)
            for n in range(RING):
                sp.dma_start(ring[n][:, :], weights_d[n]).then_inc(tile_landed[n], 16)
                if n == 0:
                    sp.dma_start(x[:, :], x_d).then_inc(x_landed, 16)
                    sp.dma_start(consts[:, :], consts_d).then_inc(consts_landed, 16)
            with sp.Fori(1, N_TILES // RING) as turn:
                for n in range(RING):
                    sp.wait_ge(halves_left, turn * (2 * RING) + 2 * (n + 1 - RING))
                    sp.dma_start(ring[n][:, :], weights_d[bass.ds(turn * RING + n, 1)].rearrange("a p c -> p (a c)")
                                 ).then_inc(tile_landed[n], 16)
            for m in range(N_TILES // RING * RING, N_TILES):
                sp.wait_ge(halves_left, 2 * (m + 1 - RING))
                sp.dma_start(ring[m % RING][:, :], weights_d[m]).then_inc(tile_landed[m % RING], 16)
            sp.wait_ge(out_ready, 8)
            sp.dma_start(out_d, y[:, :]).then_inc(out_stored, 16)
            sp.wait_ge(out_stored, 16)

        @block.tensor
        def _(pe):
            def tile_wait(n, turn=0):
                pe.wait_ge(tile_landed[n % RING], (turn + (n // RING + 1)) * 16)

            def front_wait(f, extra=0):
                if isinstance(extra, int) and f + extra < 2:
                    return
                pe.wait_ge(front_taken, extra + (f - 1))

            def mm(out, lhsT, rhs, start, stop, skip=False):
                return nc.tensor.matmul(out, lhsT, rhs, start=start, stop=stop, skip_group_check=skip)

            def mm3(out, w_hi_, w_lo_, a_hi, a_lo, start, stop, skip=False):
                mm(out, w_hi_, a_hi, start, False, skip)
                mm(out, w_hi_, a_lo, False, False, skip)
                return mm(out, w_lo_, a_hi, False, stop, skip)

            def half_wait(q, extra=0):
                n, c, _ = SPLIT[q]
                pe.wait_ge(halves_left, extra + (2 * n + c + 1))

            def column_sums(a, n, turn=0, per_turn=RING):
                pe.wait_ge(halves_left, turn * (2 * per_turn) + (2 * n + 2))
                for c in range(2):
                    o = bank[MOD_BANK][:, 2 * a + c:2 * a + c + 1] if isinstance(turn, int) else \
                        bank[MOD_BANK][:, bass.ds(turn * 6 + (2 * a + c), 1)]
                    ins = mm(o, ada_acc[:, a % 3, c * P:(c + 1) * P], K("ones")[:, 0:1], True, True)
                ins.then_inc(ada_summed, 1)

            def ada(st):
                pe.wait_ge(consts_landed, 16)
                with pe.Fori(0, ADA_FIRST // 3) as turn:
                    for a in range(3):
                        column_sums(a, a, turn)
                for a in range(ADA_FIRST // 3 * 3, ADA_FIRST):
                    column_sums(a, a)

            def meansq(st):
                for p in range(4):
                    pe.wait_ge(squares_ready, 4 * st.norm + p + 1)
                    if p == 0:
                        if st.norm == 0:
                            pe.wait_ge(consts_landed, 16)
                        else:
                            pe.wait_ge(rstd_ready, st.norm)
                    for j in (2 * p, 2 * p + 1):
                        ins = mm(bank[LOW][:, 0:TOK], K("ones"), sq3[:, j, :], j == 0, j == KC - 1)
                ins.then_inc(meansq_ready, 1)

            def gate_up(st, q, hh, turn=0, first=False, left=6):
                f = st.front + hh
                front_wait(f, turn * 2)
                for i in range(2):
                    half_wait(q + i, turn * left)
                    w = (q + i) % SLOTS
                    for k in range(KC):
                        if first and i == 0:
                            pe.wait_ge(h_ready, 8 * st.pre - 8 + k + 1)
                        ins = mm3(half(FRONT[f % 2], i), whi3[w][:, k, :], wlo3[w][:, k, :], hi3[:, k, :], lo3[:, k, :],
                                  k == 0, k == KC - 1)
                    ins.then_inc(half_used, 1)

            def down(st, q, hh, turn=0, left=6):
                half_wait(q, turn * left)
                pe.wait_ge(hidden_ready, turn * 2 + (HALVES * st.ffn + hh + 1))
                w, a = q % SLOTS, slice(hh % 2 * TOK, (hh % 2 + 1) * TOK)
                for j in range(KC):
                    ins = mm3(half(Y_BANK + j // 2, j % 2), whi3[w][:, j, :], wlo3[w][:, j, :], act_hi[:, a], act_lo[:, a],
                              hh == 0 and j % 2 == 0, hh == HALVES - 1, True)
                ins.then_inc(half_used, 1)

            def ffn(st):
                if st.ffn:
                    pe.wait_ge(y_ready, 4 * st.ffn)
                q = st.half
                gate_up(st, q, 0, first=True)

                with_ada = st.kind == "ffn_ada"
                left = 12 if with_ada else 6

                def rider(q_, i, turn=0):
                    if with_ada:
                        column_sums(st.ada + i, SPLIT[q_][0] + 1, turn, 6)

                def pattern(s, turn=0):
                    gate_up(st, q + 6 * s + 2, 2 * s + 1, turn, left=left)
                    rider(q + 6 * s + 2, 3 * s, turn)
                    gate_up(st, q + 6 * s + 4, 2 * s + 2, turn, left=left)
                    rider(q + 6 * s + 4, 3 * s + 1, turn)
                    down(st, q + 6 * s + 6, 2 * s, turn, left)
                    down(st, q + 6 * s + 7, 2 * s + 1, turn, left)
                    rider(q + 6 * s + 6, 3 * s + 2, turn)

                pattern(0)
                with pe.Fori(0, FFN_STEPS - 2) as turn:
                    pattern(1, turn)
                gate_up(st, q + 6 * FFN_STEPS - 4, HALVES - 1)
                rider(q + 6 * FFN_STEPS - 4, ADA_FFN - 2)
                down(st, q + 6 * FFN_STEPS - 2, HALVES - 2)
                down(st, q + 6 * FFN_STEPS - 1, HALVES - 1)
                rider(q + 6 * FFN_STEPS - 2, ADA_FFN - 1)

            def linear(st, n_tiles, wait=None, first=0):
                for t in range(first, first + n_tiles):
                    f = st.front + t
                    front_wait(f)
                    for c in range(2):
                        q = st.half + 2 * t + c
                        half_wait(q)
                        w = q % SLOTS
                        for k in range(KC):
                            if t == first and c == 0 and wait:
                                wait(k)
                            if (st.kind, t, k) == ("mix", 7, KC - 1):
                                half_wait(q + 1)
                            ins = mm3(half(FRONT[f % 2], c), whi3[w][:, k, :], wlo3[w][:, k, :], hi3[:, k, :],
                                      lo3[:, k, :], k == 0, k == KC - 1)
                        if (st.kind, t) == ("mix", 7):
                            break
                        ins.then_inc(half_used, 1)
                    if c == 0:
                        ins.then_inc(half_used, 2)

            def token_major(st, n_tiles, cols, first):
                for t in range(first, first + n_tiles):
                    f = st.front + t
                    front_wait(f)
                    for i in range(-(-cols // P)):
                        q = st.half + 2 * t + i
                        half_wait(q)
                        w, n = q % SLOTS, min(cols, P)
                        for c in range(2):
                            ts = slice(c * P, (c + 1) * P)
                            for k in range(KC):
                                if cols < P and c == 1 and k == KC - 1:
                                    half_wait(q + 1)
                                ins = mm3(half(FRONT[f % 2], c)[:, i * P:i * P + n], hi3[:, k, ts], lo3[:, k, ts],
                                          whi3[w][:, k, 0:n], wlo3[w][:, k, 0:n], k == 0, k == KC - 1)
                        ins.then_inc(half_used, 1 if cols > P else 2)

            def wait_h(st):
                return lambda k: pe.wait_ge(h_ready, 8 * st.pre - 8 + k + 1)

            def kv(st):
                linear(st, 8, wait_h(st))
                token_major(st, 2, TILE_COLS, 8)
                pe.wait_ge(*kv_vec.at("blocks"))
                for s in range(2):
                    for a in range(2):
                        tile_wait(st.tile + 10 + 2 * s + a)
                    for ht in range(2):
                        for a in range(2):
                            for k in range(KC):
                                ins = mm(bank[7][:, (2 * s + ht) * 64:(2 * s + ht) * 64 + NG * N_CMP],
                                         rings[(st.tile + 10 + 2 * s + a) % RING][:, ht, k, :],
                                         blocks[:, s, 8 * a + k, :], a == 0 and k == 0, a == 1 and k == KC - 1)
                    ins.then_inc(halves_left, 4)
                pe.wait_ge(*kv_act.at("gelu"))
                tile_wait(st.tile + 14)
                w2 = ring[(st.tile + 14) % RING]
                for ht in range(2):
                    ins = mm(bank[7][:, 0:NG * N_CMP], w2[:, ht * P:(ht + 1) * P], hid[:, 0, ht, :], ht == 0, ht == 1)
                for g in range(NG):
                    for ht in range(2):
                        ins = mm(bank[7][0:N_CMP, 64 + g * DH:64 + (g + 1) * DH],
                                 hid[:, 1, ht, g * N_CMP:(g + 1) * N_CMP], w2[:, 256 + ht * DH:256 + (ht + 1) * DH],
                                 ht == 0, ht == 1)
                ins.then_inc(halves_left, 2)

            def nsa(st):
                linear(st, 4, wait_h(st))
                token_major(st, 1, 3 * NH, 4)
                pe.wait_ge(*at_vec.at("q3"))
                pe.wait_ge(*kv_vec.at("vcz1"))
                for qt in range(2):
                    for hd in range(NH):
                        ins = mm(bank[6 + qt][:, hd * 16:hd * 16 + N_CMP], q_t[:, hd // 2, qt * P:(qt + 1) * P],
                                 kcz[:, hd // 4, hd % 2, :], True, True)
                    ins.then_inc(*at_pe.step(f"cmp_scores{qt}"))

                def scores(u):
                    j, qt, r = u // 4, u // 2 % 2, u % 2
                    if u >= 2:
                        pe.wait_ge(*at_vec.at(f"biased{u - 2}"))
                    nk = (qt + 1) * P
                    for br in range(2):
                        ins = mm(bank[u % 2][:, br * TOK:br * TOK + nk], q_t[:, j, qt * P:(qt + 1) * P],
                                 kz[:, br, (2 * j + r) // 4, r, 0:nk], True, True)
                    ins.then_inc(*at_pe.step(f"scores{u}"))

                def turn(u):
                    qt = u // 2 % 2
                    pe.wait_ge(*at_vec.at(f"p{u}"))
                    if u >= 2:
                        pe.wait_ge(*at_act.at(f"pt{u - 2}"))
                    for br in range(2):
                        for kt in range(qt + 1):
                            ins = nc.tensor.transpose(quad(2 + u % 2)[:, 2 * br + kt, :],
                                                      s_buf[:, u % 2, br, kt * P:(kt + 1) * P], K("ident"))
                    ins.then_inc(*at_pe.step(f"turned{u}"))

                def values(u):
                    j, qt, r = u // 4, u // 2 % 2, u % 2
                    g = (2 * j + r) // 4
                    o = bank[4 + u // 2 % 2][:, 0:P]
                    if r == 0:
                        if u == 0:
                            pe.wait_ge(*at_vec.at("pcT7"))
                        if u >= 4:
                            pe.wait_ge(*at_vec.at(f"o{u // 2 - 2}"))
                    mm(o, vcz[0:N_CMP, g, r, :], pc_t[0:N_CMP, qt, 2 * j + r, :], r == 0, False)
                    pe.wait_ge(*at_act.at(f"pt{u}"))
                    for br in range(2):
                        for kt in range(qt + 1):
                            ins = mm(o, vz[:, (br * 2 + kt) * NG + g, r, :], pt_buf[:, u % 2, 2 * br + kt, :],
                                     False, r == 1 and br == 1 and kt == qt)
                    ins.then_inc(*at_pe.step(f"values{u}"))

                scores(0)
                scores(1)
                for i in range(8):
                    qt, q4 = i // 4, i % 4
                    if q4 == 0:
                        pe.wait_ge(*at_vec.at(f"pc{qt}"))
                    if i >= 2:
                        pe.wait_ge(*at_vec.at(f"pcT{i - 2}"))
                    for m in range(4):
                        ins = nc.tensor.transpose(quad(2 + i % 2)[0:N_CMP, m, :], pc[:, qt, 4 * q4 + m, :], K("ident"))
                    ins.then_inc(*at_pe.step(f"cmp_turned{i}"))
                pe.wait_ge(*at_vec.at("pcT7"))
                for u in range(32):
                    turn(u)
                    if u + 2 < 32:
                        scores(u + 2)
                    values(u)

            def mix(st):
                linear(st, 12, wait_h(st))
                token_major(st, 2, TILE_COLS, 12)
                linear(st, 2, None, 14)
                l, M, R = st.layer, ML[st.layer], RW[st.layer]
                pe.wait_ge(*M.vec.at("g_row"))
                for c in range(2):
                    ins = nc.tensor.transpose(bank[7][:, c * P:(c + 1) * P], rows[:, 0, c * P:(c + 1) * P], K("ident"))
                ins.then_inc(*M.pe.step("g_turned"))
                pe.wait_ge(*M.vec.at("M_row"))
                for hd in range(MH):
                    ins = mm(half(hd // 2, hd % 2), K("ident")[:, 64 + hd:65 + hd].to_broadcast([P, P]), rows[:, 1, :], True, True)
                ins.then_inc(*M.pe.step("M_spread"))
                pe.wait_ge(*M.act.at("em_row"))
                for hd in range(MH):
                    ins = mm(half(2 + hd // 2, hd % 2), K("ident")[:, 64 + hd:65 + hd].to_broadcast([P, P]), rows[:, 2, :], True, True)
                ins.then_inc(*M.pe.step("em_spread"))
                pe.wait_ge(*M.act.at("qk"))
                pe.wait_ge(*M.vec.at("g_col"))
                def m_scores(i):
                    hd, kt = i // 2, i % 2
                    if i >= 2:
                        pe.wait_ge(*M.vec.at(f"sw{i - 2}"))
                    mm(bank[6 + i % 2][:, kt * P:TOK], qk[:, 4 + hd, kt * P:(kt + 1) * P], qk[:, hd, kt * P:TOK],
                       True, True).then_inc(*M.pe.step(f"scores{i}"))

                m_scores(0)
                m_scores(1)
                for i in range(8):
                    if i + 2 < 8:
                        m_scores(i + 2)
                    hd = i // 2
                    if i % 2 == 0:
                        continue
                    pe.wait_ge(*M.vec.at(f"masked{i}"))
                    if hd >= 2:
                        pe.wait_ge(*M.vec.at(f"h{hd - 2}"))
                    b = FRONT[hd % 2]
                    for kt in range(2):
                        mm(bank[b][:, kt * P:TOK], v_tok[:, kt, hd * P:(hd + 1) * P], sw[:, 2 * hd + kt, kt * P:TOK],
                           kt == 0, kt == 1)
                    for kt in range(2):
                        ins = mm(bank[b][:, TOK + kt * P:2 * TOK], K("ones"), sw[:, 2 * hd + kt, kt * P:TOK],
                                 kt == 0, kt == 1)
                    ins.then_inc(*M.pe.step(f"sums{hd}"))
                pe.wait_ge(*M.vec.at("h3"))
                for hd in range(MH):
                    ins = mm(half(hd // 2, hd % 2), K("ones"), h_b[:, hd, :], True, True)
                ins.then_inc(*M.pe.step("mean"))
                pe.wait_ge(*M.act.at("squares"))
                for hd in range(MH):
                    ins = mm(half(2 + hd // 2, hd % 2), K("ones"), sw[:, hd, :], True, True)
                ins.then_inc(*M.pe.step("var"))

                n = st.tile + 16
                tile_wait(n)
                lora = ring[n % RING][:, :].rearrange("p (s c) -> p s c", s=4)
                pe.wait_ge(*M.vec.at("rstd1"))
                pe.wait_ge(*R.act.at("lora_in"))
                pe.wait_ge(*R.vec.at("lora_tail"))

                def low(b, slot, rhs, name):
                    for j in range(4):
                        ins = mm(half(b + j // 2, j % 2), lora[:, slot, j * P:(j + 1) * P], rhs, True, True)
                    return ins.then_inc(*R.pe.step(name))

                low(0, 0, lora_in[:, 0, :], "w")
                low(2, 1, zp[:, 12, PAD:ZW], "a")
                for j in range(4):
                    mm(half(4 + j // 2, j % 2), lora[:, 2, j * P:(j + 1) * P], lora_in[:, 1, :], True, False)
                    ins = mm(half(4 + j // 2, j % 2), lora[:, 3, j * P:(j + 1) * P], lora_in[:, 2, :], False, True)
                if l == 1:
                    ins.then_inc(*R.pe.step("g"))
                    for j in range(4):
                        ins = mm(half(6 + j // 2, j % 2), lora[:, 3, j * P:(j + 1) * P], lora_in[:, 3, :], True, True)
                ins.then_inc(halves_left, 2)
                pe.wait_ge(*R.act.at("sig_w"))
                pe.wait_ge(*R.act.at("kk_sq"))
                for j in range(4):
                    ins = mm(half(j // 2, j % 2), K("blk"), e2[:, j, :], True, True)
                ins.then_inc(*R.pe.step("kk_norm"))
                pe.wait_ge(*R.act.at("a"))
                pe.wait_ge(*R.vec.at("rk3"))
                for j in range(4):
                    ins = mm(half(2 + j // 2, j % 2), K("blk"), e8[:, j, :], True, True)
                ins.then_inc(*R.pe.step("rk_sum"))
                pe.wait_ge(*R.vec.at("g_taken1"))
                if l == 1:
                    pe.wait_ge(*R.act.at("vg"))
                for T in range(2):
                    ts = slice(T * P, (T + 1) * P)
                    if T == 0:
                        pe.wait_ge(*R.vec.at("khat"))
                        pe.wait_ge(*R.vec.at("bhat"))
                        pe.wait_ge(*R.vec.at("v_mixed"))
                        pe.wait_ge(*R.vec.at("kk_rstd1"))
                        pe.wait_ge(*R.vec.at("bonus1"))
                    else:
                        pe.wait_ge(*R.vec.at("y1"))
                    for s, (src, b) in enumerate(((e5, 4), (e6, 5), (None, 6))):
                        for j in range(4):
                            a = zp[:, 8 + j, PAD + T * P:PAD + (T + 1) * P] if src is None else (
                                src[:, j, ts] if T == 0 else keep[s][:, j, :])
                            ins = nc.tensor.transpose(quad(b)[:, j, :], a, K("ident"))
                        ins.then_inc(*R.pe.step(f"turned{s}_{T}"))
                    pe.wait_ge(*R.vec.at("k_z1"))
                    pe.wait_ge(*R.vec.at("b_z1"))
                    pe.wait_ge(*R.vec.at("kap"))
                    pe.wait_ge(*R.vec.at("rho"))

                    def pairs(name, b, left, right):
                        for hf in range(2):
                            for m in range(4):
                                hd = 4 * hf + m
                                ins = mm(quad(b + hf)[:, m, :], left(hd), right(hd), True, True)
                            ins.then_inc(*R.pe.step(f"{name}{hf}_{T}"))

                    bzs = lambda hd: b_z[:, hd // 2, hd % 2, ts]
                    kzs = lambda hd: k_z[:, hd // 2, hd % 2, ts]
                    kaps = lambda hd: kap[:, hd // 2, ts]
                    rhos = lambda hd: rho[:, hd // 2, ts]
                    pairs("A_t", 0, bzs, kaps)
                    pairs("A", 2, kaps, bzs)
                    pe.wait_ge(*R.vec.at(f"btok1_{T}"))
                    pairs("A_kk", 4, kzs, kaps)
                    pe.wait_ge(*R.vec.at(f"v_z1_{T}"))
                    pairs("A_rk", 6, kzs, rhos)
                    pe.wait_ge(*R.vec.at(f"A_t1_{T}"))
                    pairs("A_rb", 0, bzs, rhos)
                    for lv in range(1, LEVELS):
                        for hf in range(2):
                            if lv == 1:
                                pe.wait_ge(*R.vec.at(f"X0_{hf}_{T}"))
                                pe.wait_ge(*R.vec.at(f"A_kk{hf}_{T}"))
                            else:
                                pe.wait_ge(*R.vec.at(f"X{lv - 1}_{hf}_{T}"))
                            pe.wait_ge(*R.pool.at(f"A_lv{lv}_{T}"))
                            for m in range(4):
                                ins = mm(quad(4 + hf)[:, m, :], A_lv[lv % 2][:, 4 * hf + m, :], X[:, 4 * hf + m, :],
                                         True, True)
                            ins.then_inc(*R.pe.step(f"U{lv}_{hf}_{T}"))
                        for hf in range(2):
                            pe.wait_ge(*R.act.at(f"U{lv}_{hf}_{T}"))
                            if lv == 1:
                                pe.wait_ge(*R.vec.at(f"X_t0_{hf}_{T}"))
                                pe.wait_ge(*R.vec.at(f"A_rk{hf}_{T}"))
                                pe.wait_ge(*R.vec.at(f"A_rb{hf}_{T}"))
                            else:
                                pe.wait_ge(*R.vec.at(f"X_t{lv - 1}_{hf}_{T}"))
                            if lv < LEVELS - 1:
                                for m in range(4):
                                    ins = mm(quad(2 + hf)[:, m, :], X_t[:, 4 * hf + m, :], U[:, 4 * hf + m, :], True, True)
                                ins.then_inc(*R.pe.step(f"D{lv}_{hf}_{T}"))
                            for m in range(4):
                                ins = mm(quad(6 + hf)[:, m, :], U[:, 4 * hf + m, :], X_t[:, 4 * hf + m, :], True, True)
                            ins.then_inc(*R.pe.step(f"D_t{lv}_{hf}_{T}"))
                    for cl in range(2):
                        c = 2 * T + cl
                        cs = slice(T * P + cl * CH, T * P + (cl + 1) * CH)
                        pe.wait_ge(*R.vec.at(f"S{c}_3"))
                        if cl == 0:
                            pe.wait_ge(*R.vec.at(f"X_t{LEVELS - 1}_1_{T}"))
                            pe.wait_ge(*R.vec.at(f"A_rb1_{T}"))
                        for j in range(4):
                            mm(bank[0][:, j * P:(j + 1) * P], kap[:, j, ts], S[:, j, :], True, False)
                            for r in range(2):
                                ins = mm(bank[0][:, j * P + r * CH:j * P + (r + 1) * CH], A_kk[:, 2 * j + r, :],
                                         v_z[:, j, r, r * CH:(r + 1) * CH], False, r == 1)
                        ins.then_inc(*R.pe.step(f"G{c}"))
                        if c:
                            pe.wait_ge(*R.vec.at(f"y{c - 1}"))
                        for j in range(4):
                            yb = bank[3][:, j * CH:(j + 1) * CH]
                            mm(yb, S[:, j, :], rho[:, j, cs], j == 0, False, True)
                            for r in range(2):
                                mm(yb, v_z[:, j, r, :], A_rk[:, 2 * j + r, cl * CH:(cl + 1) * CH], False, False, True)
                        pe.wait_ge(*R.vec.at(f"G{c}"))
                        for hd in range(RH):
                            ins = mm(bank[1][:, hd * CH:(hd + 1) * CH], X_t[:, hd, :], gs[:, hd * CH:(hd + 1) * CH],
                                     True, True)
                        ins.then_inc(*R.pe.step(f"SA{c}"))
                        pe.wait_ge(*R.vec.at(f"SA{c}_1"))
                        for hd in range(RH):
                            j, r = hd // 2, hd % 2
                            o = bank[2][:, hd * CH:(hd + 1) * CH]
                            mm(o, ktok[:, cl, j * P:(j + 1) * P], v_z[:, j, r, r * CH:(r + 1) * CH], True, False)
                            ins = mm(o, btok[:, cl, j * P:(j + 1) * P], sa_z[:, j, r, r * CH:(r + 1) * CH], False, True)
                        ins.then_inc(*R.pe.step(f"dS{c}"))
                        for j in range(4):
                            for r in range(2):
                                ins = mm(bank[3][:, j * CH:(j + 1) * CH], sa_z[:, j, r, :],
                                         A_rb[:, 2 * j + r, cl * CH:(cl + 1) * CH], False, j == 3 and r == 1, True)
                        ins.then_inc(*R.pe.step(f"y{c}"))
                pe.wait_ge(*R.vec.at("y3"))
                for j in range(4):
                    ins = mm(half(j // 2, j % 2), K("blk"), y_a[:, j, :], True, True)
                ins.then_inc(*R.pe.step("gn_mean"))
                pe.wait_ge(*R.act.at("gn_squares"))
                pe.wait_ge(*R.vec.at("S4_3"))
                for j in range(4):
                    ins = mm(half(2 + j // 2, j % 2), K("blk"), e2[:, j, :], True, True)
                ins.then_inc(*R.pe.step("gn_var"))

            def branch(st):
                for t in range(8):
                    f = st.front + t
                    q = st.half + t
                    front_wait(f)
                    half_wait(q)
                    w = q % SLOTS
                    for br in range(2):
                        for k in range(4 * br, 4 * br + 4):
                            if t == 0:
                                pe.wait_ge(h_ready, 8 * st.pre + k + 1)
                            ins = mm3(half(FRONT[f % 2], br), whi3[w][:, k, :], wlo3[w][:, k, :], hi3[:, k, :],
                                      lo3[:, k, :], k % 4 == 0, k % 4 == 3)
                    ins.then_inc(half_used, 1)

            for st in PLAN:
                if st.kind == "ada":
                    ada(st)
                elif st.kind in ("norm", "post", "final"):
                    meansq(st)
                elif st.kind in ("ffn", "ffn_ada"):
                    ffn(st)
                elif st.kind == "conv":
                    linear(st, 12, wait_h(st))
                elif st.kind == "kv":
                    kv(st)
                elif st.kind == "nsa":
                    nsa(st)
                elif st.kind == "lin4":
                    linear(st, 4, lambda k: pe.wait_ge(h_ready, 8 * st.pre + k + 1))
                elif st.kind == "mix":
                    mix(st)
                elif st.kind == "gates":
                    pe.wait_ge(*RW[last_mix].vec.at("y_a3"))
                    linear(st, 8)
                elif st.kind == "branch":
                    branch(st)
                last_mix = st.layer if st.kind == "mix" else (0 if st.kind == "ada" else last_mix)

        @block.scalar
        def _(act):
            def fn(out, in_, f, bias=0.0, scale=1.0):
                return nc.scalar.activation(out, in_, f, bias=bias, scale=scale)

            at_half = [0, 0]

            def hi(q, turn=0, landed=16):
                n, c, _ = SPLIT[q]
                act.wait_ge(tile_landed[n % RING], turn * landed + (n // RING + 1) * 16)
                if not (isinstance(turn, int) and q < SLOTS):
                    act.wait_ge(half_used, turn * 6 + (q + 1 - SLOTS))
                fn(w_hi[q % SLOTS][:, :], ring[n % RING][:, c * HALF:(c + 1) * HALF], ACT.Copy).then_inc(hi_ready, 1)

            def advance(to):
                while at_half[0] <= to and at_half[0] < N_HALVES and SPLIT[at_half[0]][2] == at_half[1]:
                    hi(at_half[0])
                    at_half[0] += 1

            def open_run():
                if at_half[0] < N_HALVES and SPLIT[at_half[0]][2] != at_half[1]:
                    act.wait_ge(halves_left, 2 * SPLIT[at_half[0]][0])
                    at_half[1] = SPLIT[at_half[0]][2]

            def squares(st, src, ready):
                for p in range(4):
                    ready(p)
                    if p == 0 and st.norm:
                        act.wait_ge(meansq_ready, st.norm)
                    fn(sq[:, 2 * p * TOK:(2 * p + 2) * TOK], src[:, 2 * p * TOK:(2 * p + 2) * TOK], ACT.Square
                       ).then_inc(squares_ready, 1)
                open_run()
                advance(st.half + 2)
                act.wait_ge(meansq_ready, st.norm + 1)
                fn(rstd[:, :], bank[LOW][:, 0:TOK], ACT.Sqrt, bias=RMS_EPS, scale=1.0 / D).then_inc(root_ready, 1)

            def x_wait(st):
                def wait(p):
                    if st.update:
                        act.wait_ge(x_ready, 4 * st.update - 4 + p + 1)
                    else:
                        act.wait_ge(x_landed, 16)
                return wait

            def norm(st):
                squares(st, x, x_wait(st))
                shift = None if st.mod is None else (mod_col(*st.mod, 0) if st.mod != "kv" else 144)
                for j in range(KC):
                    act.wait_ge(h_scaled, 8 * st.scaled + j + 1)
                    if shift is None:
                        ins = fn(hi3[:, j, :], y3[:, j, :], ACT.Copy)
                    else:
                        ins = fn(hi3[:, j, :], y3[:, j, :], ACT.Identity, bias=mods[:, shift + j:shift + j + 1])
                    ins.then_inc(h_hi_ready, 1)

            def parts(st, src, wait):
                for j in range(KC):
                    wait(j)
                    fn(hi3[:, j, :], src(j), ACT.Copy).then_inc(h_hi_ready, 1)

            def ffn(st):
                q = st.half

                def gate(hh, j, turn=0):
                    f = st.front + hh
                    act.wait_ge(half_used, turn * 6 + (q + j + 1))
                    if not (isinstance(turn, int) and f < 2):
                        act.wait_ge(front_taken, turn * 2 + (f - 1))
                    fn(silu_t[:, (f % 2) * TOK:(f % 2 + 1) * TOK], half(FRONT[f % 2], 0), ACT.Silu
                       ).then_inc(silu_ready, 1)

                landed = 32 if st.kind == "ffn_ada" else 16
                advance(q + 3)
                gate(0, 1)
                advance(q + 5)
                with act.Fori(0, FFN_STEPS - 1) as turn:
                    gate(1, 3, turn)
                    hi(q + 6, turn, landed)
                    hi(q + 7, turn, landed)
                    gate(2, 5, turn)
                    for i in range(8, 12):
                        hi(q + i, turn, landed)
                at_half[0] = q + 6 * FFN_STEPS
                gate(HALVES - 1, 6 * FFN_STEPS - 3)

            def nsa(st):
                advance(st.half + 9)
                act.wait_ge(half_used, st.half + 10)
                act.wait_ge(front_taken, st.front + 4)
                fn(gate_tok[:, :, :], pair(FRONT[(st.front + 4) % 2])[:, :, 0:3 * NH], ACT.Sigmoid
                   ).then_inc(front_taken, 1)
                for qt in range(2):
                    act.wait_ge(*at_vec.at(f"cmp_centred{qt}"))
                    fn(pc[:, qt, :, :], pc[:, qt, :, :], ACT.Exp).then_inc(*at_act.step(f"cmp_exp{qt}"))

                def exps(u):
                    nk = (u // 2 % 2 + 1) * P
                    act.wait_ge(*at_vec.at(f"max{u}"))
                    for br in range(2):
                        nc.scalar.activation(s_buf[:, u % 2, br, 0:nk], s_buf[:, u % 2, br, 0:nk], ACT.Exp,
                                             bias=at_small[:, 2 * (u % 2) + br:2 * (u % 2) + br + 1], scale=1.0,
                                             accum_out=at_small[:, 8 + 2 * (u % 2) + br:8 + 2 * (u % 2) + br + 1]
                                             ).then_inc(*at_act.step(f"exp{u}_{br}"))

                def copy(u):
                    qt = u // 2 % 2
                    act.wait_ge(*at_pe.at(f"turned{u}"))
                    if u >= 2:
                        act.wait_ge(*at_pe.at(f"values{u - 2}"))
                    a = quad(2 + u % 2).rearrange("p (b k) t -> p b k t", b=2)[:, :, 0:qt + 1, :]
                    o = pt_buf[:, u % 2].rearrange("p (b k) t -> p b k t", b=2)[:, :, 0:qt + 1, :]
                    fn(o, a, ACT.Copy).then_inc(*at_act.step(f"pt{u}"))

                exps(0)
                for v in range(32):
                    if v + 1 < 32:
                        exps(v + 1)
                    copy(v)

            def mix(st):
                l, M, R = st.layer, ML[st.layer], RW[st.layer]
                advance(st.half + 31)
                rt = row_tmp[64:68]
                act.wait_ge(*M.vec.at("minus_abs"))
                fn(rt[:, 2, :], rt[:, 2, :], ACT.Exp).then_inc(*M.act.step("exp_f"))
                act.wait_ge(*M.act.at("exp_f"))
                fn(rt[:, 2, :], rt[:, 2, :], ACT.Ln, bias=1.0).then_inc(*M.act.step("ln_f"))
                act.wait_ge(*M.vec.at("F_plus_M"))
                act.wait_ge(*M.pool.at("rows_zero"))
                fn(rows[64:68, 2, :], rt[:, 4, :], ACT.Exp, scale=-1.0).then_inc(*M.act.step("em_row"))
                act.wait_ge(*M.vec.at("conv7"))
                fn(qk[:, :, :], qk[:, :, :], ACT.Silu).then_inc(*M.act.step("qk"))
                act.wait_ge(*M.pe.at("em_spread"))
                for i in range(2):
                    ins = fn(bc_e[:, 2 * i:2 * i + 2, :], pair(2 + i), ACT.Copy)
                ins.then_inc(*M.act.step("em_copy"))
                for i in range(8):
                    kt = i % 2
                    act.wait_ge(*M.vec.at(f"gap{i}"))
                    fn(w_buf[:, i % 4, kt * P:TOK], w_buf[:, i % 4, kt * P:TOK], ACT.Exp, scale=-1.0
                       ).then_inc(*M.act.step(f"weight{i}"))
                act.wait_ge(*M.vec.at("m_o"))
                fn(m_o[:, :, :], m_o[:, :, :], ACT.Sigmoid).then_inc(*M.act.step("sig_o"))
                act.wait_ge(*M.vec.at("centred1"))
                fn(sw[:, 0:4, :], h_b[:, :, :], ACT.Square).then_inc(*M.act.step("squares"))
                act.wait_ge(*M.pe.at("var"))
                for i in range(2):
                    fn(sw[:, 2 * i:2 * i + 2, :], pair(2 + i), ACT.Sqrt, bias=ML_EPS, scale=1.0 / P).then_inc(*M.act.step(f"root{i}"))
                act.wait_ge(*M.vec.at("y_b"))
                fn(lora_in[:, 0, :], zp[:, 12, PAD:ZW], ACT.Tanh)
                fn(lora_in[:, 1, :], zp[:, 13, PAD:ZW], ACT.Sigmoid).then_inc(*R.act.step("lora_mid"))
                act.wait_ge(*R.vec.at("lora_tail"))
                fn(lora_in[0:32, 2, :], zp[0:32, 14, PAD:ZW], ACT.Sigmoid).then_inc(*R.act.step("lora_in"))
                act.wait_ge(*R.pe.at("w"))
                for j in range(4):
                    ins = fn(e1[:, j, :], half(j // 2, j % 2), ACT.Sigmoid, bias=V(f"w0{l}", j))
                ins.then_inc(*R.act.step("sig_w"))
                act.wait_ge(*R.pe.at("a"))
                for j in range(4):
                    ins = fn(e4[:, j, :], half(2 + j // 2, j % 2), ACT.Sigmoid, bias=V(f"a0{l}", j))
                ins.then_inc(*R.act.step("a"))
                if l == 1:
                    act.wait_ge(halves_left, 2 * (st.tile + 17))
                    for j in range(4):
                        ins = fn(e7[:, j, :], half(6 + j // 2, j % 2), ACT.Sigmoid, bias=V(f"vres{l}", j))
                    ins.then_inc(*R.act.step("vg"))
                act.wait_ge(*R.vec.at("kk_raw3"))
                fn(e2[:, :, :], e3[:, :, :], ACT.Square).then_inc(*R.act.step("kk_sq"))
                for i in range(2):
                    act.wait_ge(*R.vec.at(f"kk_floor{i}"))
                    fn(e2[:, 2 * i:2 * i + 2, :], e2[:, 2 * i:2 * i + 2, :], ACT.Sqrt).then_inc(*R.act.step(f"kk_root{i}"))
                act.wait_ge(*R.vec.at("L_prev"))
                act.wait_ge(*R.vec.at("v_mixed"))
                act.wait_ge(*R.vec.at("bonus1"))
                fn(e8[:, :, :], e5[:, :, :], ACT.Exp).then_inc(*R.act.step("E"))
                act.wait_ge(*R.vec.at("v_mixed"))
                fn(e7[:, :, :], e5[:, :, :], ACT.Exp, scale=-1.0).then_inc(*R.act.step("E_inv"))
                fn(e6[:, :, :], e6[:, :, :], ACT.Exp).then_inc(*R.act.step("E_prev"))
                for T in range(2):
                    for lv in range(1, LEVELS):
                        for hf in range(2):
                            act.wait_ge(*R.pe.at(f"U{lv}_{hf}_{T}"))
                            if lv > 1:
                                act.wait_ge(*R.pe.at(f"D_t{lv - 1}_{hf}_{T}"))
                            fn(U[:, 4 * hf:4 * hf + 4, :], quad(4 + hf), ACT.Copy
                               ).then_inc(*R.act.step(f"U{lv}_{hf}_{T}"))
                act.wait_ge(*R.vec.at("gn_centred1"))
                fn(e2[:, :, :], y_a[:, :, :], ACT.Square).then_inc(*R.act.step("gn_squares"))
                act.wait_ge(*R.pe.at("gn_var"))
                for i in range(2):
                    fn(e3[:, 2 * i:2 * i + 2, :], pair(2 + i), ACT.Sqrt, bias=GN_EPS, scale=1.0 / CH).then_inc(*R.act.step(f"gn_root{i}"))

            def gates(st):
                open_run()
                for t in range(8):
                    f = st.front + t
                    advance(st.half + 2 * t + 3)
                    act.wait_ge(half_used, st.half + 2 * t + 2)
                    fn(sgate[:, 2 * t:2 * t + 2, :], pair(FRONT[f % 2]), ACT.Sigmoid).then_inc(front_taken, 1)

            act.wait_ge(vecs_landed, 16)
            fn(cond[:, :], V("c", 0, 8), ACT.Silu).then_inc(cond_ready, 1)
            for st in PLAN:
                if st.kind == "norm":
                    norm(st)
                elif st.kind == "final":
                    squares(st, x, x_wait(st))
                elif st.kind == "post":
                    if st.source == "ffn":
                        squares(st, y, lambda p: act.wait_ge(y_ready, 4 * st.ffn - 4 + p + 1))
                    else:
                        squares(st, y, lambda p: act.wait_ge(front_taken, st.front - 4 + p + 1))
                elif st.kind in ("ffn", "ffn_ada"):
                    ffn(st)
                elif st.kind == "conv":
                    advance(st.half + 25)
                elif st.kind == "lin4":
                    if st.rhs == "conv_y":
                        parts(st, lambda j: conv_y[:, j, :], lambda j: act.wait_ge(*conv_vec.at(f"y{j}")))
                    elif st.rhs == "o":
                        parts(st, lambda j: o_t[:, j, :], lambda j: act.wait_ge(*at_vec.at(f"o{2 * j + 1}")))
                    else:
                        act.wait_ge(half_used, st.half)
                        parts(st, lambda j: u[:, j, :], lambda j: act.wait_ge(u_ready, 8 * st.branch - 8 + j + 1))
                    advance(st.half + 9)
                elif st.kind == "branch":
                    act.wait_ge(half_used, st.half)
                    parts(st, lambda j: (y_a, y_b)[j // 4][:, j % 4, :], lambda j: None)
                    advance(st.half + 9)
                elif st.kind == "kv":
                    advance(st.half + 19)
                    act.wait_ge(halves_left, 2 * (st.tile + 14))
                    src = bank[7][:, 0:256].rearrange("p (s c) -> p s c", s=4)[:, :, 0:NG * N_CMP]
                    fn(hid.rearrange("p a b c -> p (a b) c"), src, ACT.Gelu_apprx_tanh).then_inc(*kv_act.step("gelu"))
                elif st.kind == "nsa":
                    nsa(st)
                elif st.kind == "mix":
                    mix(st)
                elif st.kind == "gates":
                    gates(st)

        @block.gpsimd
        def _(pool):
            for st in PLAN:
                if st.kind in ("post", "half", "resid"):
                    for p in range(4):
                        if st.kind == "post":
                            pool.wait_ge(delta_ready, 8 * st.post + 2 * p + 2)
                        elif st.kind == "half":
                            pool.wait_ge(y_ready, 4 * st.ffn - 4 + p + 1)
                        else:
                            pool.wait_ge(front_taken, st.front - 4 + p + 1)
                        c = slice(2 * p * TOK, (2 * p + 2) * TOK)
                        nc.gpsimd.tensor_tensor(x[:, c], x[:, c], y[:, c], ALU.add).then_inc(x_ready, 1)
                elif st.kind == "conv":
                    nc.gpsimd.memset(conv_v[:, :, 0:PAD], 0.0).then_inc(*conv_pool.step("pad"))
                elif st.kind == "kv":
                    nc.gpsimd.memset(carve(0, 8192), 0.0).then_inc(*kv_pool.step("zero"))
                    nc.gpsimd.memset(carve(10352, 1144), 0.0).then_inc(*kv_pool.step("zero_cmp"))
                elif st.kind == "mix":
                    l, M, R = st.layer, ML[st.layer], RW[st.layer]
                    if l == 1:
                        pool.wait_ge(u_ready, 8)
                    nc.gpsimd.memset(zp[:, :, 0:PAD], 0.0)
                    nc.gpsimd.memset(mqk[:, :, 0:PAD], 0.0).then_inc(*M.pool.step("pads"))
                    pool.wait_ge(*M.vec.at("shifted"))
                    nc.gpsimd.memset(rows[:, :, :], 0.0).then_inc(*M.pool.step("rows_zero"))
                    pool.wait_ge(*M.vec.at("y_b"))
                    nc.gpsimd.memset(k_z[:, :, :, :], 0.0)
                    nc.gpsimd.memset(b_z[:, :, :, :], 0.0).then_inc(*R.pool.step("z_zero"))
                    nc.gpsimd.memset(y[:, :], 0.0)
                    nc.gpsimd.memset(sq[:, :], 0.0)
                    nc.gpsimd.memset(S[:, :, :], 0.0).then_inc(*R.pool.step("tok_zero"))
                    for T in range(2):
                        for lv in range(1, LEVELS):
                            if lv <= 2:
                                pool.wait_ge(*R.vec.at(f"A_t1_{T}"))
                                if T == 0:
                                    pool.wait_ge(*R.vec.at("b_z1"))
                                    pool.wait_ge(*R.act.at("E_prev"))
                                    pool.wait_ge(*R.vec.at("ktok1_0"))
                            if lv > 2:
                                pool.wait_ge(*R.pe.at(f"U{lv - 2}_1_{T}"))
                            nc.gpsimd.tensor_tensor(A_lv[lv % 2][:, :, :], A_t[:, :, :],
                                                    K(f"level{lv}").unsqueeze(1).to_broadcast([P, RH, P]), ALU.mult
                                                    ).then_inc(*R.pool.step(f"A_lv{lv}_{T}"))

        @block.vector
        def _(dve):
            tt, ts_, stt = nc.vector.tensor_tensor, nc.vector.tensor_scalar, nc.vector.scalar_tensor_tensor
            cp = nc.vector.tensor_copy

            at_half = [0, SPLIT[0][2]]

            def lo(q, turn=0):
                n, c, _ = SPLIT[q]
                dve.wait_ge(hi_ready, turn * 6 + (q + 1))
                tt(w_lo[q % SLOTS][:, :], ring[n % RING][:, c * HALF:(c + 1) * HALF], w_hi[q % SLOTS][:, :].bitcast(F32),
                   ALU.subtract).then_inc(halves_left, 1)

            def advance(to):
                while at_half[0] <= to and at_half[0] < N_HALVES and SPLIT[at_half[0]][2] == at_half[1]:
                    lo(at_half[0])
                    at_half[0] += 1

            def modulate(a, n, turn=0, per_turn=RING):
                acc = ada_acc[:, a % 3, :]
                w = ring[n % RING][:, :].rearrange("p (k c) -> p k c", k=KC)
                dve.wait_ge(tile_landed[n % RING], turn * (16 * per_turn // RING) + (n // RING + 1) * 16)
                if a >= 3:
                    dve.wait_ge(ada_summed, turn * 3 + (a - 2))
                for k in range(KC):
                    if k == 0:
                        ins = ts_(acc, w[:, 0, :], cond[:, 0:1], None, ALU.mult)
                    else:
                        dve.wait_ge(ada_partial, turn * 21 + (7 * a + k))
                        ins = stt(out=acc, in0=w[:, k, :], scalar=cond[:, k:k + 1], in1=acc, op0=ALU.mult, op1=ALU.add)
                    if k < KC - 1:
                        ins.then_inc(ada_partial, 1)
                ins.then_inc(halves_left, 2)

            def ada(st):
                dve.wait_ge(cond_ready, 1)
                for a in range(3):
                    modulate(a, a)
                with dve.Fori(0, ADA_FIRST // 3 - 1) as turn:
                    for a in range(3, 6):
                        modulate(a, a, turn)
                for a in range(ADA_FIRST // 3 * 3, ADA_FIRST):
                    modulate(a, a)
                mods_out(0)

            def open_run():
                if at_half[0] < N_HALVES:
                    at_half[1] = SPLIT[at_half[0]][2]

            def norm(st, out, ready, gain, src, shift=None):
                open_run()
                advance(st.half + 2)
                dve.wait_ge(root_ready, st.norm + 1)
                nc.vector.reciprocal(rstd[:, :], rstd[:, :]).then_inc(rstd_ready, 1)
                dve.wait_ge(rstd_ready, st.norm + 1)

                def scaled(j):
                    stt(out=out[:, j, :], in0=src[:, j, :], scalar=gain(j), in1=rstd[:, :], op0=ALU.mult,
                        op1=ALU.mult).then_inc(ready, 1)

                if ready is not h_scaled:
                    for j in range(KC):
                        scaled(j)
                    return
                for j in range(KC + 2):
                    if j < KC:
                        scaled(j)
                    if j >= 2:
                        dve.wait_ge(h_hi_ready, 8 * st.pre + j - 1)
                        stt(out=lo3[:, j - 2, :], in0=out[:, j - 2, :], scalar=0.0 if shift is None else shift(j - 2),
                            in1=hi3[:, j - 2, :].bitcast(F32), op0=ALU.add, op1=ALU.subtract).then_inc(h_ready, 1)

            def parts(st, src):
                for j in range(KC):
                    dve.wait_ge(h_hi_ready, 8 * st.pre + j + 1)
                    tt(lo3[:, j, :], src(j), hi3[:, j, :].bitcast(F32), ALU.subtract).then_inc(h_ready, 1)

            def take(st, t, out, n=2):
                f = st.front + t
                advance(st.half + 2 * t + 3)
                dve.wait_ge(half_used, st.half + 2 * t + 2)
                cp(out, pair(FRONT[f % 2])[:, 0:n, :]).then_inc(front_taken, 1)

            def ffn(st):
                q = st.half

                def gated(hh, turn=0, slot_free=None):
                    f, h = st.front + hh, HALVES * st.ffn + hh
                    a = slice(hh % 2 * TOK, (hh % 2 + 1) * TOK)
                    dve.wait_ge(silu_ready, turn * 2 + (h + 1))
                    tt(act_t[:, a], silu_t[:, (f % 2) * TOK:(f % 2 + 1) * TOK], half(FRONT[f % 2], 1), ALU.mult
                       ).then_inc(front_taken, 1)
                    if slot_free is not None:
                        dve.wait_ge(half_used, turn * 6 + slot_free)
                    dve.wait_ge(front_taken, turn * 2 + (f + 1))
                    cp(act_hi[:, a], act_t[:, a]).then_inc(hidden_hi, 1)
                    dve.wait_ge(hidden_hi, turn * 2 + (h + 1))
                    tt(act_lo[:, a], act_t[:, a], act_hi[:, a].bitcast(F32), ALU.subtract).then_inc(hidden_ready, 1)

                with_ada = st.kind == "ffn_ada"

                def rider(q_, i, turn=0):
                    if with_ada:
                        modulate(st.ada + i, SPLIT[q_][0] + 1, turn, 6)

                advance(q + 3)
                rider(q + 3, 0)
                gated(0)
                advance(q + 5)
                rider(q + 5, 1)
                with dve.Fori(0, FFN_STEPS - 1) as turn:
                    gated(1, turn, q + 2)
                    lo(q + 6, turn)
                    lo(q + 7, turn)
                    rider(q + 7, 2, turn)
                    lo(q + 8, turn)
                    gated(2, turn, q + 7)
                    lo(q + 9, turn)
                    rider(q + 9, 3, turn)
                    lo(q + 10, turn)
                    lo(q + 11, turn)
                    rider(q + 11, 4, turn)
                at_half[0] = q + 6 * FFN_STEPS
                gated(HALVES - 1, 0, q + 6 * FFN_STEPS - 4)

            def ffn_out(st, scale):
                dve.wait_ge(half_used, st.half)
                for p in range(4):
                    ts_(y3[:, 2 * p:2 * p + 2, :], pair(Y_BANK + p), scale, None, ALU.mult).then_inc(y_ready, 1)

            def mods_out(part):
                c0, c1, tiles, norms = ((0, 24, ADA_FIRST, [0]), (24, 72, ADA_FIRST + ADA_FFN, [1, 2]),
                                          (72, MOD_COLS, ADA_FIRST + 2 * ADA_FFN, [3, 4, 5, 6]))[part]
                dve.wait_ge(ada_summed, tiles)
                tt(mods[:, c0:c1], bank[MOD_BANK][:, c0:c1], V("mod_b", c0, c1 - c0), ALU.add).then_inc(mods_taken, 1)
                dve.wait_ge(mods_taken, part + 1)
                for q in norms:
                    sc, g = (152, V("kv_norm", 0, 8)) if q == 6 else (mod_col(q // 3, q % 3, 1), V("norm_g", 16 * q, 8))
                    ins = stt(out=pre_gain[:, 8 * q:8 * q + 8], in0=mods[:, sc:sc + 8], scalar=1.0, in1=g,
                              op0=ALU.add, op1=ALU.mult)
                    if q < 6:
                        gt = mod_col(q // 3, q % 3, 2)
                        ins = stt(out=post_gain[:, 8 * q:8 * q + 8], in0=mods[:, gt:gt + 8],
                                  scalar=1.0 if q % 3 == 1 else 0.5, in1=V("norm_g", 16 * q + 8, 8),
                                  op0=ALU.mult, op1=ALU.mult)
                ins.then_inc(gains_ready, 1)
                dve.wait_ge(gains_ready, part + 1)

            def conv(st):
                for t in range(12):
                    take(st, t, conv_z[:, 2 * t:2 * t + 2, :])
                dve.wait_ge(front_taken, st.front + 12)
                dve.wait_ge(*conv_pool.at("pad"))
                tt(conv_v[:, :, PAD:ZW], conv_z[:, 8:16, :], conv_z[:, 16:24, :], ALU.mult
                   ).then_inc(*conv_vec.step("v"))
                dve.wait_ge(*conv_vec.at("v"))
                for j in range(8):
                    ts_(conv_y[:, j, :], conv_v[:, j, PAD:ZW], V("conv", 16 + j), None, ALU.mult
                        ).then_inc(*conv_vec.step(f"a{j}"))
                for s in (1, 0):
                    for j in range(8):
                        dve.wait_ge(*conv_vec.at(f"a{j}" if s else f"b{j}"))
                        o = PAD - 2 + s
                        stt(out=conv_y[:, j, :], in0=conv_v[:, j, o:o + TOK], scalar=V("conv", 8 * s + j),
                            in1=conv_y[:, j, :], op0=ALU.mult, op1=ALU.add
                            ).then_inc(*conv_vec.step(f"b{j}" if s else f"c{j}"))
                for j in range(8):
                    dve.wait_ge(*conv_vec.at(f"c{j}"))
                    tt(conv_y[:, j, :], conv_y[:, j, :], conv_z[:, j, :], ALU.mult).then_inc(*conv_vec.step(f"y{j}"))

            def kv(st):
                for t in range(4):
                    f, s = st.front + t, t // 2
                    advance(st.half + 2 * t + 3)
                    dve.wait_ge(half_used, st.half + 2 * t + 2)
                    for gi in range(2):
                        g = 2 * (t % 2) + gi
                        for r in range(2):
                            rows_ = slice(r * DH, (r + 1) * DH)
                            src = half(FRONT[f % 2], gi).rearrange("p (m b r) -> p r b m", b=8, r=2)
                            for a in range(2):
                                kc = slice(8 * a, 8 * a + 8)
                                a0 = VEC["pos"][0] + 16 * s + 8 * a
                                ins = tt(blocks[rows_, s, kc, g * N_CMP:(g + 1) * N_CMP],
                                         src[rows_, r, :, a:a + N_CMP],
                                         vecs[rows_, a0:a0 + 8].unsqueeze(2).to_broadcast([DH, 8, N_CMP]), ALU.add)
                    ins.then_inc(front_taken, 1)
                dve.wait_ge(front_taken, st.front + 4)
                cp(small[:, 0:1], V("c")).then_inc(*kv_vec.step("blocks"))
                dve.wait_ge(*kv_pool.at("zero"))
                for t in range(4):
                    f, br = st.front + 4 + t, t // 2
                    advance(st.half + 2 * (4 + t) + 3)
                    dve.wait_ge(half_used, st.half + 2 * (4 + t) + 2)
                    for r in range(2):
                        rows_ = slice(r * DH, (r + 1) * DH)
                        g = 2 * (t % 2)
                        ins = cp(kz[rows_, br, g:g + 2, r, :], pair(FRONT[f % 2])[rows_, :, :])
                    ins.then_inc(front_taken, 1)
                for br in range(2):
                    f = st.front + 8 + br
                    advance(st.half + 2 * (8 + br) + 3)
                    dve.wait_ge(half_used, st.half + 2 * (8 + br) + 2)
                    for c in range(2):
                        src = half(FRONT[f % 2], c).rearrange("p (g d) -> p g d", g=NG)
                        for r in range(2):
                            i = (br * 2 + c) * NG
                            ins = cp(vz[:, i:i + NG, r, r * DH:(r + 1) * DH], src)
                    ins.then_inc(front_taken, 1)
                dve.wait_ge(*kv_pool.at("zero_cmp"))
                dve.wait_ge(halves_left, 2 * (st.tile + 15))
                for r in range(2):
                    rows_ = slice(r * DH, (r + 1) * DH)
                    cp(kcz[rows_, :, r, :], bank[7][rows_, 0:NG * N_CMP].rearrange("p (g n) -> p g n", g=NG)
                       ).then_inc(*kv_vec.step(f"kcz{r}"))
                for r in range(2):
                    cp(vcz[0:N_CMP, :, r, r * DH:(r + 1) * DH],
                       bank[7][0:N_CMP, 64:64 + NG * DH].rearrange("p (g n) -> p g n", g=NG)
                       ).then_inc(*kv_vec.step(f"vcz{r}"))

            def nsa(st):
                for t in range(4):
                    f = st.front + t
                    advance(st.half + 2 * t + 3)
                    dve.wait_ge(half_used, st.half + 2 * t + 2)
                    ts_(q_t[:, 2 * t:2 * t + 2, :], pair(FRONT[f % 2]), DH ** -0.5, None, ALU.mult
                        ).then_inc(front_taken, 1)
                dve.wait_ge(front_taken, st.front + 4)
                cp(small[:, 1:2], q_t[:, 7, 0:1]).then_inc(*at_vec.step("q3"))
                dve.wait_ge(front_taken, st.front + 5)
                for qt in range(2):
                    p = pc[:, qt, :, :]
                    dist = K("cmp_dist")[:, qt * N_CMP:(qt + 1) * N_CMP]
                    mask = K("cmp_mask").rearrange("p (q n) -> p q n", q=2)[:, qt:qt + 1, :].to_broadcast([P, NH, N_CMP])
                    src = bank[6 + qt][:, 0:256].rearrange("p (h n) -> p h n", h=NH)[:, :, 0:N_CMP]
                    m = at_small[:, 16 + 64 * qt:32 + 64 * qt]
                    z = at_small[:, 32 + 64 * qt:48 + 64 * qt]
                    dve.wait_ge(*at_pe.at(f"cmp_scores{qt}"))
                    for hd in range(NH):
                        ins = stt(out=p[:, hd, :], in0=dist, scalar=-slope(hd), in1=src[:, hd, :], op0=ALU.mult,
                                  op1=ALU.add)
                    ins.then_inc(*at_vec.step(f"cmp_biased{qt}"))
                    dve.wait_ge(*at_vec.at(f"cmp_biased{qt}"))
                    nc.vector.tensor_reduce(m, p, AX_X, ALU.max).then_inc(*at_vec.step(f"cmp_max{qt}"))
                    dve.wait_ge(*at_vec.at(f"cmp_max{qt}"))
                    tt(p, p, m.unsqueeze(2).to_broadcast([P, NH, N_CMP]), ALU.subtract
                       ).then_inc(*at_vec.step(f"cmp_centred{qt}"))
                    dve.wait_ge(*at_act.at(f"cmp_exp{qt}"))
                    tt(p, p, mask, ALU.mult).then_inc(*at_vec.step(f"cmp_masked{qt}"))
                    dve.wait_ge(*at_vec.at(f"cmp_masked{qt}"))
                    nc.vector.tensor_reduce(z, p, AX_X, ALU.add).then_inc(*at_vec.step(f"cmp_sum{qt}"))
                    dve.wait_ge(*at_vec.at(f"cmp_sum{qt}"))
                    ts_(z, z, 1e-30, None, ALU.max).then_inc(*at_vec.step(f"cmp_floor{qt}"))
                    dve.wait_ge(*at_vec.at(f"cmp_floor{qt}"))
                    nc.vector.reciprocal(m, z).then_inc(*at_vec.step(f"cmp_inv{qt}"))
                    dve.wait_ge(*at_vec.at(f"cmp_inv{qt}"))
                    tt(z, m, gate_tok[:, qt, 0:NH], ALU.mult).then_inc(*at_vec.step(f"cmp_gate{qt}"))
                    dve.wait_ge(*at_vec.at(f"cmp_gate{qt}"))
                    tt(p, p, z.unsqueeze(2).to_broadcast([P, NH, N_CMP]), ALU.mult).then_inc(*at_vec.step(f"pc{qt}"))
                for i in range(8):
                    dve.wait_ge(*at_pe.at(f"cmp_turned{i}"))
                    cp(pc_t[0:N_CMP, i // 4, 4 * (i % 4):4 * (i % 4) + 4, :], quad(2 + i % 2)[0:N_CMP, :, :]
                       ).then_inc(*at_vec.step(f"pcT{i}"))

                def first(u):
                    j, qt, r = u // 4, u // 2 % 2, u % 2
                    hd, nk = 2 * j + r, (qt + 1) * P
                    dist = K("dist")[:, TOK - nk:TOK].unsqueeze(1).to_broadcast([P, 2, nk])
                    s = s_buf[:, u % 2, :, 0:nk]
                    dve.wait_ge(*at_pe.at(f"scores{u}"))
                    if u >= 2:
                        dve.wait_ge(*at_pe.at(f"turned{u - 2}"))
                    stt(out=s, in0=dist, scalar=-slope(hd), in1=pair(u % 2)[:, :, 0:nk],
                        op0=ALU.mult, op1=ALU.add).then_inc(*at_vec.step(f"biased{u}"))
                    dve.wait_ge(*at_vec.at(f"biased{u}"))
                    m = at_small[:, 4 + 2 * (u % 2):6 + 2 * (u % 2)]
                    nc.vector.tensor_reduce(m, s, AX_X, ALU.max).then_inc(*at_vec.step(f"rawmax{u}"))
                    dve.wait_ge(*at_vec.at(f"rawmax{u}"))
                    ts_(at_small[:, 2 * (u % 2):2 * (u % 2) + 2], m, -1.0, None, ALU.mult
                        ).then_inc(*at_vec.step(f"max{u}"))

                def second(u):
                    j, qt, r = u // 4, u // 2 % 2, u % 2
                    hd, nk = 2 * j + r, (qt + 1) * P
                    z = at_small[:, 8 + 2 * (u % 2):10 + 2 * (u % 2)]
                    w = at_small[:, 12 + 2 * (u % 2):14 + 2 * (u % 2)]
                    dve.wait_ge(*at_act.at(f"exp{u}_1"))
                    nc.vector.reciprocal(w, z).then_inc(*at_vec.step(f"inv{u}"))
                    dve.wait_ge(*at_vec.at(f"inv{u}"))
                    gate = gate_tok[:, qt, :].rearrange("p (b h) -> p b h", b=3)[:, 1:3, hd]
                    tt(w, w, gate, ALU.mult).then_inc(*at_vec.step(f"weight{u}"))
                    dve.wait_ge(*at_vec.at(f"weight{u}"))
                    for br in range(2):
                        ins = ts_(s_buf[:, u % 2, br, 0:nk], s_buf[:, u % 2, br, 0:nk], w[:, br:br + 1], None, ALU.mult)
                    ins.then_inc(*at_vec.step(f"p{u}"))

                def out(i):
                    dve.wait_ge(*at_pe.at(f"values{2 * i + 1}"))
                    cp(o_t[:, i // 2, (i % 2) * P:(i % 2 + 1) * P], bank[4 + i % 2][:, 0:P]
                       ).then_inc(*at_vec.step(f"o{i}"))

                first(0)
                for v in range(32):
                    if v + 1 < 32:
                        first(v + 1)
                    second(v)
                    if v % 2 == 1 and v > 2:
                        out(v // 2 - 1)
                out(15)

            def mix(st):
                l, M, R = st.layer, ML[st.layer], RW[st.layer]
                Mv, Rv = M.vec, R.vec
                dve.wait_ge(*M.pool.at("pads"))
                for t in range(16):
                    f = st.front + t
                    if t < 7:
                        take(st, t, zp[:, 2 * t:2 * t + 2, PAD:ZW])
                    elif t == 7:
                        take(st, t, zp[:, 14:15, PAD:ZW], 1)
                    elif t < 12:
                        take(st, t, mqk[:, 2 * t - 16:2 * t - 14, PAD:ZW])
                    elif t < 14:
                        take(st, t, v_tok[:, :, (t - 12) * TOK:(t - 11) * TOK])
                    else:
                        take(st, t, m_o[:, 2 * t - 28:2 * t - 26, :])
                dve.wait_ge(front_taken, st.front + 16)
                cp(small[:, 0:1], m_o[:, 3, 0:1]).then_inc(*Mv.step("m_o"))
                tt(diff[:, :, :], zp[:, :, PAD - 1:ZW - 1], zp[:, :, PAD:ZW], ALU.subtract).then_inc(*Mv.step("diff"))
                dve.wait_ge(*Mv.at("diff"))
                for i in range(NZ):
                    ins = stt(out=zp[:, i, PAD:ZW], in0=diff[:, i, :], scalar=V(f"mu{l}", i), in1=zp[:, i, PAD:ZW],
                              op0=ALU.mult, op1=ALU.add)
                ins.then_inc(*Mv.step("shifted"))
                dve.wait_ge(*Mv.at("shifted"))
                rt = row_tmp[64:68]
                gb = V(f"gbias{l}")
                ts_(rt[:, 0, :], zp[64:68, 14, PAD:ZW], gb[64:68], None, ALU.add).then_inc(*Mv.step("li"))
                ts_(rt[:, 1, :], zp[96:100, 14, PAD:ZW], gb[96:100], None, ALU.add).then_inc(*Mv.step("xf"))
                dve.wait_ge(*Mv.at("xf"))
                stt(out=rt[:, 2, :], in0=rt[:, 1, :], scalar=-1.0, in1=rt[:, 1, :], op0=ALU.mult, op1=ALU.min
                    ).then_inc(*Mv.step("minus_abs"))
                dve.wait_ge(*M.act.at("ln_f"))
                stt(out=rt[:, 1, :], in0=rt[:, 1, :], scalar=0.0, in1=rt[:, 2, :], op0=ALU.min, op1=ALU.subtract
                    ).then_inc(*Mv.step("lf"))
                dve.wait_ge(*Mv.at("lf"))
                nc.vector.tensor_tensor_scan(rt[:, 3, :], K("ones")[64:68, 0:1].to_broadcast([4, TOK]), rt[:, 1, :],
                                             0.0, ALU.mult, ALU.add).then_inc(*Mv.step("F"))
                dve.wait_ge(*Mv.at("F"))
                dve.wait_ge(*M.pool.at("rows_zero"))
                tt(rows[64:68, 0, :], rt[:, 0, :], rt[:, 3, :], ALU.subtract).then_inc(*Mv.step("g_row"))
                dve.wait_ge(*Mv.at("g_row"))
                nc.vector.tensor_tensor_scan(rows[64:68, 1, :], rows[64:68, 0, :], rows[64:68, 0, :], 0.0,
                                             ALU.max, ALU.max).then_inc(*Mv.step("M_row"))
                dve.wait_ge(*Mv.at("M_row"))
                tt(rt[:, 4, :], rt[:, 3, :], rows[64:68, 1, :], ALU.add).then_inc(*Mv.step("F_plus_M"))
                for j in range(8):
                    ts_(qk[:, j, :], mqk[:, j, 1:1 + TOK], V(f"convw{l}", j), V(f"convb{l}", j), ALU.mult, ALU.add
                        ).then_inc(*Mv.step(f"tap0_{j}"))
                for i in range(1, 4):
                    for j in range(8):
                        dve.wait_ge(*Mv.at(f"tap{i - 1}_{j}"))
                        stt(out=qk[:, j, :], in0=mqk[:, j, 1 + i:1 + i + TOK], scalar=V(f"convw{l}", 8 * i + j),
                            in1=qk[:, j, :], op0=ALU.mult, op1=ALU.add
                            ).then_inc(*Mv.step(f"tap{i}_{j}" if i < 3 else f"conv{j}"))
                dve.wait_ge(*M.pe.at("g_turned"))
                g_col = small[:, 8:16].rearrange("p (c h) -> p c h", c=2)
                cp(g_col, bank[7][:, 0:TOK].rearrange("p (c r) -> p c r", c=2)[:, :, 64:68]).then_inc(*Mv.step("g_col"))
                dve.wait_ge(*Mv.at("g_col"))
                dve.wait_ge(*M.pe.at("M_spread"))

                def gap(i):
                    hd, kt = i // 2, i % 2
                    ts_(w_buf[:, i % 4, kt * P:TOK], half(hd // 2, hd % 2)[:, kt * P:TOK], g_col[:, kt, hd:hd + 1], 0.0,
                        ALU.subtract, ALU.max).then_inc(*Mv.step(f"gap{i}"))

                def finish(hd):
                    b = FRONT[hd % 2]
                    dve.wait_ge(*M.pe.at(f"sums{hd}"))
                    if hd == 0:
                        dve.wait_ge(*M.act.at("em_copy"))
                    e = bc_e[:, hd, :]
                    stt(out=e, in0=half(b, 1), scalar=-1.0, in1=e, op0=ALU.mult, op1=ALU.max
                        ).then_inc(*Mv.step(f"floor{hd}"))
                    dve.wait_ge(*Mv.at(f"floor{hd}"))
                    tt(e, half(b, 1), e, ALU.max).then_inc(*Mv.step(f"den{hd}"))
                    dve.wait_ge(*Mv.at(f"den{hd}"))
                    nc.vector.reciprocal(e, e).then_inc(*Mv.step(f"inv{hd}"))
                    dve.wait_ge(*Mv.at(f"inv{hd}"))
                    tt(h_b[:, hd, :], half(b, 0), e, ALU.mult).then_inc(*Mv.step(f"h{hd}"))

                for i in range(3):
                    gap(i)
                for i in range(8):
                    hd, kt = i // 2, i % 2
                    dve.wait_ge(*M.pe.at(f"scores{i}"))
                    dve.wait_ge(*M.act.at(f"weight{i}"))
                    stt(out=sw[:, i, kt * P:TOK], in0=w_buf[:, i % 4, kt * P:TOK], scalar=float(P) ** -0.5,
                        in1=bank[6 + i % 2][:, kt * P:TOK], op0=ALU.mult, op1=ALU.mult).then_inc(*Mv.step(f"sw{i}"))
                    dve.wait_ge(*Mv.at(f"sw{i}"))
                    dg = sw[:, i, kt * P:(kt + 1) * P]
                    tt(dg, dg, K("causal"), ALU.mult).then_inc(*Mv.step(f"masked{i}"))
                    if i + 3 < 8:
                        gap(i + 3)
                    if i % 2 == 1 and i > 2:
                        finish(hd - 1)
                finish(3)
                dve.wait_ge(*M.pe.at("mean"))
                for i in range(2):
                    d = h_b[:, 2 * i:2 * i + 2, :]
                    stt(out=d, in0=pair(i), scalar=-1.0 / P, in1=d, op0=ALU.mult, op1=ALU.add
                        ).then_inc(*Mv.step(f"centred{i}"))
                for i in range(2):
                    dve.wait_ge(*M.act.at(f"root{i}"))
                    nc.vector.reciprocal(sw[:, 2 * i:2 * i + 2, :], sw[:, 2 * i:2 * i + 2, :]
                                         ).then_inc(*Mv.step(f"rstd{i}"))
                dve.wait_ge(*Mv.at("rstd1"))
                for j in range(4):
                    ins = stt(out=h_b[:, j, :], in0=h_b[:, j, :], scalar=V(f"mlnorm{l}", j), in1=sw[:, j, :],
                              op0=ALU.mult, op1=ALU.mult)
                ins.then_inc(*Mv.step("normed"))
                dve.wait_ge(*Mv.at("normed"))
                dve.wait_ge(*M.act.at("sig_o"))
                tt(y_b[:, :, :], h_b[:, :, :], m_o[:, :, :], ALU.mult).then_inc(*Mv.step("y_b"))
                dve.wait_ge(*Mv.at("y_b"))

                zr, zk, zv = zp[:, 0:4, PAD:ZW], zp[:, 4:8, PAD:ZW], zp[:, 8:12, PAD:ZW]
                nc.vector.memset(lora_in[:, 2:4, :], 0.0).then_inc(*Rv.step("lora_zero"))
                dve.wait_ge(*Rv.at("lora_zero"))
                cp(lora_in[32:64, 3, :], zp[32:64, 14, PAD:ZW]).then_inc(*Rv.step("lora_tail"))
                ts_(small[:, 16:20], V(f"ka{l}", 0, 4), -1.0, 1.0, ALU.mult, ALU.add).then_inc(*Rv.step("one_minus_ka"))
                for j in range(4):
                    ts_(e3[:, j, :], zp[:, 4 + j, PAD:ZW], V(f"kk{l}", j), None, ALU.mult
                        ).then_inc(*Rv.step(f"kk_raw{j}"))
                dve.wait_ge(*R.act.at("sig_w"))
                ts_(e1[:, :, :], e1[:, :, :], -EXP_MINUS_HALF, None, ALU.mult).then_inc(*Rv.step("lw"))
                dve.wait_ge(*Rv.at("lw"))
                for j in range(4):
                    ins = nc.vector.tensor_tensor_scan(e5[:, j, :], K("reset"), e1[:, j, :], 0.0, ALU.mult, ALU.add)
                ins.then_inc(*Rv.step("L"))
                dve.wait_ge(*Rv.at("L"))
                tt(e6[:, :, :], e5[:, :, :], e1[:, :, :], ALU.subtract).then_inc(*Rv.step("L_prev"))
                if l == 0:
                    dve.wait_ge(halves_left, 2 * (st.tile + 17))
                else:
                    dve.wait_ge(*R.pe.at("g"))
                for i in range(2):
                    cp(g_up[:, 2 * i:2 * i + 2, :], pair(4 + i)).then_inc(*Rv.step(f"g_taken{i}"))
                dve.wait_ge(*R.act.at("a"))
                dve.wait_ge(*Rv.at("one_minus_ka"))
                for j in range(4):
                    ins = ts_(e8[:, j, :], e4[:, j, :], V(f"ka{l}", j), small[:, 16 + j:17 + j], ALU.mult, ALU.add)
                ins.then_inc(*Rv.step("ka"))
                dve.wait_ge(*Rv.at("ka"))
                dve.wait_ge(*Rv.at("kk_raw3"))
                tt(zk, zk, e8[:, :, :], ALU.mult).then_inc(*Rv.step("k_mixed"))
                dve.wait_ge(*Rv.at("k_mixed"))
                tt(e8[:, :, :], zr, zk, ALU.mult).then_inc(*Rv.step("rk"))
                dve.wait_ge(*Rv.at("rk"))
                for j in range(4):
                    ts_(e8[:, j, :], e8[:, j, :], V(f"rk{l}", j), None, ALU.mult).then_inc(*Rv.step(f"rk{j}"))
                vf = tiles(v_first, 4)
                if l == 0:
                    cp(vf, zv).then_inc(*Rv.step("v_mixed"))
                else:
                    dve.wait_ge(*R.act.at("vg"))
                    tt(e1[:, :, :], vf, zv, ALU.subtract).then_inc(*Rv.step("v_gap"))
                    dve.wait_ge(*Rv.at("v_gap"))
                    tt(e1[:, :, :], e1[:, :, :], e7[:, :, :], ALU.mult).then_inc(*Rv.step("v_gated"))
                    dve.wait_ge(*Rv.at("v_gated"))
                    tt(zv, zv, e1[:, :, :], ALU.add).then_inc(*Rv.step("v_mixed"))
                dve.wait_ge(*Rv.at("v_mixed"))
                dve.wait_ge(*R.pe.at("kk_norm"))
                for i in range(2):
                    ts_(e2[:, 2 * i:2 * i + 2, :], pair(i), 1e-24, None, ALU.max).then_inc(*Rv.step(f"kk_floor{i}"))
                for i in range(2):
                    dve.wait_ge(*R.act.at(f"kk_root{i}"))
                    nc.vector.reciprocal(e2[:, 2 * i:2 * i + 2, :], e2[:, 2 * i:2 * i + 2, :]
                                         ).then_inc(*Rv.step(f"kk_rstd{i}"))
                dve.wait_ge(*Rv.at("kk_rstd1"))
                tt(e3[:, :, :], e3[:, :, :], e2[:, :, :], ALU.mult).then_inc(*Rv.step("kk"))
                dve.wait_ge(*Rv.at("kk"))
                dve.wait_ge(*R.pe.at("rk_sum"))
                for i in range(2):
                    tt(bonus[:, 2 * i:2 * i + 2, :], pair(2 + i), zp[:, 8 + 2 * i:10 + 2 * i, PAD:ZW], ALU.mult
                       ).then_inc(*Rv.step(f"bonus{i}"))
                tt(e4[:, :, :], e4[:, :, :], e3[:, :, :], ALU.mult).then_inc(*Rv.step("b"))
                dve.wait_ge(*R.act.at("E_prev"))
                tt(kap[:, :, :], e3[:, :, :], e6[:, :, :], ALU.mult).then_inc(*Rv.step("kap"))
                tt(rho[:, :, :], zr, e8[:, :, :], ALU.mult).then_inc(*Rv.step("rho"))
                pcol = small[:, 20:36].rearrange("p (j c) -> p j c", j=4)
                cp(pcol, e8.rearrange("p j (c t) -> p j c t", t=CH)[:, :, :, CH - 1]).then_inc(*Rv.step("P"))
                dve.wait_ge(*Rv.at("b"))
                dve.wait_ge(*Rv.at("kap"))
                tt(e5[:, :, :], zk, e7[:, :, :], ALU.mult).then_inc(*Rv.step("khat"))
                tt(e6[:, :, :], e4[:, :, :], e7[:, :, :], ALU.mult).then_inc(*Rv.step("bhat"))
                dve.wait_ge(*Rv.at("bhat"))
                dve.wait_ge(*R.pool.at("z_zero"))
                for name, z, src in (("k_z", k_z, e5), ("b_z", b_z, e6)):
                    for r in range(2):
                        rows_ = slice(r * CH, (r + 1) * CH)
                        cp(z[rows_, :, r, :], src[rows_, :, :]).then_inc(*Rv.step(f"{name}{r}"))
                dve.wait_ge(*Rv.at("khat"))
                for s, src in enumerate((e5, e6)):
                    cp(keep[s], src[:, :, P:TOK]).then_inc(*Rv.step(f"keep{s}"))
                dve.wait_ge(*Rv.at("keep1"))
                dve.wait_ge(*R.pool.at("tok_zero"))

                def masked(name, hf, T, dst, b, mask, sign=None):
                    mk = K(mask).unsqueeze(1).to_broadcast([P, 4, P])
                    dve.wait_ge(*R.pe.at(f"{name}{hf}_{T}"))
                    d = dst[:, 4 * hf:4 * hf + 4, :]
                    if sign is None:
                        ins = tt(d, quad(b + hf), mk, ALU.mult)
                    else:
                        ins = stt(out=d, in0=quad(b + hf), scalar=sign, in1=mk, op0=ALU.mult, op1=ALU.mult)
                    return ins

                for T in range(2):
                    for s, (dst, b) in enumerate(((ktok, 4), (btok, 5))):
                        dve.wait_ge(*R.pe.at(f"turned{s}_{T}"))
                        for cl in range(2):
                            rows_ = slice(cl * CH, (cl + 1) * CH)
                            ts_(dst[rows_, cl, :], bank[b][rows_, :], -1.0 if s else 1.0, None, ALU.mult
                                ).then_inc(*Rv.step(f"{'btok' if s else 'ktok'}{cl}_{T}"))
                    dve.wait_ge(*R.pe.at(f"turned2_{T}"))
                    for r in range(2):
                        cp(v_z[:, :, r, r * CH:(r + 1) * CH], quad(6)[:, :, r * CH:(r + 1) * CH]
                           ).then_inc(*Rv.step(f"v_z{r}_{T}"))
                    idn = K("ident").unsqueeze(1).to_broadcast([P, 4, P])
                    for hf in range(2):
                        masked("A_t", hf, T, A_t, 0, "strict").then_inc(*Rv.step(f"A_t{hf}_{T}"))
                    for hf in range(2):
                        d = X[:, 4 * hf:4 * hf + 4, :]
                        masked("A", hf, T, X, 2, "level0_ts").then_inc(*Rv.step(f"X_off{hf}_{T}"))
                        dve.wait_ge(*Rv.at(f"X_off{hf}_{T}"))
                        tt(d, idn, d, ALU.subtract).then_inc(*Rv.step(f"X0_{hf}_{T}"))
                        d, a = X_t[:, 4 * hf:4 * hf + 4, :], A_t[:, 4 * hf:4 * hf + 4, :]
                        dve.wait_ge(*Rv.at(f"A_t{hf}_{T}"))
                        tt(d, a, K("level0").unsqueeze(1).to_broadcast([P, 4, P]), ALU.mult
                           ).then_inc(*Rv.step(f"Xt_off{hf}_{T}"))
                        dve.wait_ge(*Rv.at(f"Xt_off{hf}_{T}"))
                        tt(d, idn, d, ALU.subtract).then_inc(*Rv.step(f"X_t0_{hf}_{T}"))
                    for hf in range(2):
                        masked("A_kk", hf, T, A_kk, 4, "strict").then_inc(*Rv.step(f"A_kk{hf}_{T}"))
                    for hf in range(2):
                        masked("A_rk", hf, T, A_rk, 6, "incl").then_inc(*Rv.step(f"A_rk{hf}_{T}"))
                    for hf in range(2):
                        masked("A_rb", hf, T, A_rb, 0, "incl", -1.0).then_inc(*Rv.step(f"A_rb{hf}_{T}"))
                    for lv in range(1, LEVELS):
                        for hf in range(2):
                            for nm, dst, b in (("", X, 2), ("_t", X_t, 6)):
                                if nm == "" and lv == LEVELS - 1:
                                    continue
                                dve.wait_ge(*R.pe.at(f"D{nm}{lv}_{hf}_{T}"))
                                d = dst[:, 4 * hf:4 * hf + 4, :]
                                tt(d, d, quad(b + hf), ALU.subtract).then_inc(*Rv.step(f"X{nm}{lv}_{hf}_{T}"))
                    for cl in range(2):
                        c = 2 * T + cl
                        if c == 0:
                            cp(small[:, 40:44], small[:, 16:20]).then_inc(*Rv.step("S0_3"))
                        dve.wait_ge(*R.pe.at(f"G{c}"))
                        cp(gs[:, :], bank[0][:, :]).then_inc(*Rv.step(f"G{c}"))
                        dve.wait_ge(*R.pe.at(f"SA{c}"))
                        rows_ = slice(cl * CH, (cl + 1) * CH)
                        for r in range(2):
                            cp(sa_z[rows_, :, r, r * CH:(r + 1) * CH], quad(1)[rows_, :, r * CH:(r + 1) * CH]
                               ).then_inc(*Rv.step(f"SA{c}_{r}"))
                        dve.wait_ge(*R.pe.at(f"dS{c}"))
                        tt(S, S, quad(2), ALU.add).then_inc(*Rv.step(f"S_sum{c}"))
                        dve.wait_ge(*Rv.at(f"S_sum{c}"))
                        for j in range(4):
                            stt(out=S[:, j, :], in0=S[:, j, :], scalar=pcol[:, j, c:c + 1], in1=K("blk"), op0=ALU.mult,
                                op1=ALU.mult).then_inc(*Rv.step(f"S{c + 1}_{j}"))
                        dve.wait_ge(*Rv.at(f"S{c + 1}_3"))
                        dve.wait_ge(*R.pe.at(f"y{c}"))
                        cp(y_a[:, :, c * CH:(c + 1) * CH], bank[3][:, 0:TOK].rearrange("p (j t) -> p j t", j=4)
                           ).then_inc(*Rv.step(f"y{c}"))
                dve.wait_ge(*R.pe.at("gn_mean"))
                for i in range(2):
                    d = y_a[:, 2 * i:2 * i + 2, :]
                    stt(out=d, in0=pair(i), scalar=-1.0 / CH, in1=d, op0=ALU.mult, op1=ALU.add
                        ).then_inc(*Rv.step(f"gn_centred{i}"))
                for i in range(2):
                    dve.wait_ge(*R.act.at(f"gn_root{i}"))
                    nc.vector.reciprocal(e3[:, 2 * i:2 * i + 2, :], e3[:, 2 * i:2 * i + 2, :]
                                         ).then_inc(*Rv.step(f"gn_rstd{i}"))
                dve.wait_ge(*Rv.at("gn_rstd1"))
                for j in range(4):
                    stt(out=y_a[:, j, :], in0=y_a[:, j, :], scalar=V(f"gnw{l}", j), in1=e3[:, j, :], op0=ALU.mult,
                        op1=ALU.mult).then_inc(*Rv.step(f"gn{j}"))
                for j in range(4):
                    dve.wait_ge(*Rv.at(f"gn{j}"))
                    stt(out=y_a[:, j, :], in0=y_a[:, j, :], scalar=V(f"gnb{l}", j), in1=bonus[:, j, :], op0=ALU.add,
                        op1=ALU.add).then_inc(*Rv.step(f"with_bonus{j}"))
                for j in range(4):
                    dve.wait_ge(*Rv.at(f"with_bonus{j}"))
                    tt(y_a[:, j, :], y_a[:, j, :], g_up[:, j, :], ALU.mult).then_inc(*Rv.step(f"y_a{j}"))

            def branch(st):
                parts(st, lambda j: (y_a, y_b)[j // 4][:, j % 4, :])
                for ct in range(8):
                    f = st.front + ct
                    q = 8 * st.branch + ct
                    advance(st.half + ct + 2)
                    dve.wait_ge(half_used, st.half + ct + 1)
                    if ct == 0:
                        dve.wait_ge(front_taken, st.front)
                    tt(br_t[:, 0, :], sgate[:, ct, :], half(FRONT[f % 2], 0), ALU.mult).then_inc(br_product, 1)
                    tt(br_t[:, 1, :], sgate[:, 8 + ct, :], half(FRONT[f % 2], 1), ALU.mult).then_inc(front_taken, 1)
                    dve.wait_ge(br_product, q + 1)
                    dve.wait_ge(front_taken, f + 1)
                    tt(u[:, ct, :], br_t[:, 0, :], br_t[:, 1, :], ALU.add).then_inc(u_ready, 1)
                    dve.wait_ge(u_ready, q + 1)

            dve.wait_ge(vecs_landed, 16)
            for st in PLAN:
                if st.kind == "ada":
                    ada(st)
                elif st.kind == "norm":
                    if st.mod is None:
                        norm(st, y3, h_scaled, lambda j: V(st.gain, j), x3)
                    else:
                        q = 6 if st.mod == "kv" else 3 * st.mod[0] + st.mod[1]
                        sh = mod_col(*st.mod, 0) if st.mod != "kv" else 144
                        norm(st, y3, h_scaled, lambda j: pre_gain[:, 8 * q + j:8 * q + j + 1], x3,
                             lambda j: mods[:, sh + j:sh + j + 1])
                elif st.kind == "final":
                    norm(st, y3, out_ready, lambda j: V(st.gain, j), x3)
                elif st.kind == "post":
                    if st.source == "ffn":
                        if st.ffn <= 2:
                            mods_out(st.ffn)
                        ffn_out(st, 1.0)
                    q = 3 * st.mod[0] + st.mod[1]
                    norm(st, y3, delta_ready, lambda j: post_gain[:, 8 * q + j:8 * q + j + 1], y3)
                elif st.kind in ("ffn", "ffn_ada"):
                    ffn(st)
                elif st.kind == "half":
                    ffn_out(st, 0.5)
                elif st.kind == "conv":
                    conv(st)
                elif st.kind == "kv":
                    kv(st)
                elif st.kind == "nsa":
                    nsa(st)
                elif st.kind == "mix":
                    mix(st)
                elif st.kind == "branch":
                    branch(st)
                elif st.kind == "gates":
                    open_run()
                    advance(st.half + 15)
                elif st.kind == "lin4":
                    src = conv_y if st.rhs == "conv_y" else o_t if st.rhs == "o" else u
                    parts(st, lambda j: src[:, j, :])
                    for t in range(4):
                        take(st, t, y3[:, 2 * t:2 * t + 2, :])


def constant_array():
    out = np.zeros((P, NCONST), np.float32)

    def put(name, a):
        s, n = CONST[name]
        out[:, s:s + n] = np.asarray(a, np.float32).reshape(a.shape[0], -1)

    i = np.arange(P)
    s, t = i[:, None], i[None, :]
    put("ident", np.eye(P))
    put("ones", np.ones((P, P)))
    same = s // CH == t // CH
    put("blk", same)
    for lv in range(LEVELS):
        b = 1 << lv
        m = (s // (2 * b) == t // (2 * b)) & (s // b % 2 == 0) & (t // b % 2 == 1)
        put(f"level{lv}", m)
        if lv == 0:
            put("level0_ts", m.T)
    put("strict", same & (s < t))
    put("incl", same & (s <= t))
    put("causal", s <= t)
    put("reset", np.broadcast_to(np.arange(TOK) % CH != 0, (P, TOK)))
    put("dist", np.concatenate([s - t + P, np.where(s >= t, s - t, 1e30)], axis=1))
    q = np.arange(TOK).reshape(2, P).T
    dc = q[:, :, None] - (np.arange(N_CMP) * CMP_STRIDE + CMP_LEN - 1)
    put("cmp_dist", np.where(dc >= 0, dc, 1e30))
    put("cmp_mask", dc >= 0)
    return out


def vector_array(a):
    out = np.zeros((P, NVEC), np.float32)

    def put(name, v):
        s, n = VEC[name]
        v = np.asarray(v).reshape(-1, P).T
        out[:, s:s + v.shape[1]] = v

    put("c", a["c"])
    put("mod_b", np.concatenate([a["ada_b"].reshape(-1), a["kv_ada_b"]]))
    put("norm_g", a["norm_g"])
    put("kv_norm", a["kv_norm_g"])
    put("conv", a["a_conv"])
    put("pos", a["cmp_pos"])
    for l in range(2):
        put(f"ffn1{l}", a["ffn1_norm_2"][l])
        put(f"mix{l}", a["mix_norm_2"][l])
        put(f"ffn2{l}", a["ffn2_norm_2"][l])
        put(f"mu{l}", np.concatenate([a["shift_mu_2"][l], np.zeros(96, np.float32)]))
        for name, key in (("w0", "rw_w0_2"), ("a0", "rw_a0_2"), ("kk", "rw_k_k_2"), ("ka", "rw_k_a_2"),
                          ("rk", "rw_r_k_2"), ("gnw", "rw_gn_w_2"), ("gnb", "rw_gn_b_2"), ("convw", "ml_conv_w_2"),
                          ("convb", "ml_conv_b_2"), ("mlnorm", "ml_norm_w_2")):
            put(f"{name}{l}", a[key][l])
        if l:
            put(f"vres{l}", a["vres_bias_2"][l - 1])
        g = VEC[f"gbias{l}"][0]
        out[64:68, g] = a["ml_i_bias_2"][l]
        out[96:100, g] = a["ml_f_bias_2"][l]
    put("final", a["final_norm_2"])
    return out


def weight_tiles(a):
    out = np.zeros((N_TILES, P, 2, KC, P), np.float32)
    n = 0

    def put(w):
        nonlocal n
        t = -(-w.shape[1] // TILE_COLS)
        for i in range(t):
            for c in range(2):
                v = w[:, (2 * i + c) * P:(2 * i + c + 1) * P]
                out[n, :, c, :, :v.shape[1]] = v.reshape(KC, P, -1).transpose(1, 0, 2)
            n += 1

    def put_flat(v):
        nonlocal n
        out[n].reshape(P, TILE)[:, :v.shape[1]] = v
        n += 1

    def put_ffn(w_in, w_out, riders=None):
        for hh in range(HALVES):
            c = slice(hh * P, (hh + 1) * P)
            put(np.concatenate([w_in[:, c], w_in[:, D_FF:][:, c]], axis=1))
            if riders is not None and hh:
                put_flat(riders.pop(0))
            if hh and (hh % 2 == 0 or hh == HALVES - 1):
                s = (hh - 1) // 2
                if hh == HALVES - 1:
                    s = FFN_STEPS - 1
                put_flat(w_out[s * TILE_COLS:(s + 1) * TILE_COLS].reshape(2, P, D).transpose(1, 0, 2).reshape(P, 2 * D))
                if riders is not None:
                    put_flat(riders.pop(0))

    def twice(w):
        return np.repeat(w.reshape(w.shape[0], -1, 1, DH), 2, axis=2).reshape(w.shape[0], -1)

    ada_w = np.concatenate([a["ada_w"][0], a["ada_w"][1], a["kv_ada_w"]], axis=1)
    ada = [ada_w[:, i:i + TILE_COLS].reshape(KC, P, TILE_COLS).transpose(1, 0, 2).reshape(P, TILE)
           for i in range(0, MOD_COLS * P, TILE_COLS)]
    for _ in range(ADA_FIRST):
        put_flat(ada.pop(0))
    put_ffn(a["ffn_w_in"][0, 0], a["ffn_w_out"][0, 0], ada)
    put(a["a_w_in"][0])
    put(a["a_w_out"][0])
    put_ffn(a["ffn_w_in"][0, 1], a["ffn_w_out"][0, 1], ada)
    kv = a["kv_w"].reshape(D, 3, 2, NG * DH)
    for br, s in ((0, 0), (0, 1), (1, 0), (2, 0)):
        put(twice(kv[:, br, s]))
    put(kv[:, 1, 1])
    put(kv[:, 2, 1])
    for s in range(2):
        w1 = a["cmp_w1"][s].reshape(2, KC, P, 256)
        for i in range(2):
            put_flat(w1[i].reshape(KC, P, 2, P).transpose(1, 2, 0, 3).reshape(P, TILE))
    w2 = a["cmp_w2"].reshape(2, 2, P, DH)
    put_flat(np.concatenate([w2[0, 0], w2[0, 0], w2[0, 1], w2[0, 1], w2[1, 0], w2[1, 1]], axis=1))
    put_ffn(a["ffn_w_in"][1, 0], a["ffn_w_out"][1, 0])
    put(a["b_w_in"][0])
    put(a["b_w_out"][0])
    put_ffn(a["ffn_w_in"][1, 1], a["ffn_w_out"][1, 1])
    for l in range(2):
        put_ffn(a["ffn1_w_in_2"][l], a["ffn1_w_out_2"][l])
        w = a["w_in_2"][l]
        put(w[:, 0:1792])
        tail = np.zeros((D, TILE_COLS), np.float32)
        tail[:, 0:32] = w[:, 1792:1824]
        if l:
            tail[:, 32:64] = a["vres_down_2"][l - 1]
        tail[:, 64:68] = w[:, 3872:3876]
        tail[:, 96:100] = w[:, 3876:3880]
        put(tail)
        put(w[:, 1824:3872])
        lora = np.zeros((P, 4, 512), np.float32)
        lora[0:64, 0] = a["rw_w_up_2"][l]
        lora[64:128, 1] = a["rw_a_up_2"][l]
        lora[:, 2] = a["rw_g_up_2"][l][0:P]
        lora[0:32, 3] = a["rw_g_up_2"][l][P:]
        if l:
            lora[32:64, 3] = a["vres_up_2"][l - 1]
        put_flat(lora.reshape(P, TILE))
        put(w[:, 3880:])
        put(np.concatenate([a["br_a_2"][l], a["br_b_2"][l]], axis=0))
        put(a["w_out_2"][l])
        put_ffn(a["ffn2_w_in_2"][l], a["ffn2_w_out_2"][l])
    assert n == N_TILES, (n, N_TILES)
    return out.reshape(N_TILES, P, TILE)


def kernel(**inputs):
    import concourse.bacc as bacc
    from concourse.bass_utils import run_bass_kernel_spmd

    a = {k: np.asarray(v) for k, v in inputs.items()}
    x = a["x"].reshape(TOK, KC, P).transpose(2, 1, 0).reshape(P, KC * TOK)
    arrays = {"consts": constant_array(), "vecs": vector_array(a), "x_in": np.ascontiguousarray(x),
              "weights": weight_tiles(a)}
    nc = bacc.Bacc("TRN2", target_bir_lowering=False, num_devices=1)
    args = [nc.dram_tensor(k, v.shape, F32, kind="ExternalInput").ap() for k, v in arrays.items()]
    out = nc.dram_tensor("out", (P, KC * TOK), F32, kind="ExternalOutput").ap()
    build(nc, *args, out)
    got = run_bass_kernel_spmd(nc, [arrays], core_ids=[0]).results[0]["out"]
    return np.ascontiguousarray(got.reshape(P, KC, TOK).transpose(2, 1, 0).reshape(1, TOK, D))
```

```python
from contextlib import ExitStack

import numpy as np
import concourse.bass as bass
from concourse import mybir

P = 128
TOK = 256
D = 1024
KC = D // P
TILE_COLS = 256
TILE = KC * TILE_COLS
RING = 3
SLOTS = 3
HALF = TILE // 2
D_FF = 2816
FFN_STEPS = D_FF // TILE_COLS
FFN_TILES = 3 * FFN_STEPS
HALVES = 2 * FFN_STEPS
NH, NG, DH = 16, 4, 64
N_CMP, CMP_LEN, CMP_STRIDE = 15, 32, 16
MOD_COLS = 72 + 72 + 16
ADA_POOL = 3
ADA_DVE = KC - ADA_POOL + 1
ADA_FFN = 3 * FFN_STEPS - 1
ADA_FIRST = MOD_COLS * P // TILE_COLS - 2 * ADA_FFN
CH = 64
PAD = 4
ZW = TOK + PAD
NZ = 15
RH, MH = 8, 4
LEVELS = 6
RMS_EPS = 1e-6
GN_EPS = 64e-5
ML_EPS = 1e-5
EXP_MINUS_HALF = 0.6065306597126334

F32 = mybir.dt.float32
F32R = mybir.dt.float32r
ALU = mybir.AluOpType
ACT = mybir.ActivationFunctionType
AX_X = mybir.AxisListType.X


def columns(sizes):
    at, out = 0, {}
    for name, n in sizes:
        out[name] = (at, n)
        at += n
    return out, at


CONST, NCONST = columns(
    [("ident", P), ("ones", P), ("blk", P)]
    + [(f"level{i}", P) for i in range(LEVELS)] + [("level0_ts", P), ("strict", P), ("incl", P), ("causal", P)]
    + [("reset", TOK), ("dist", TOK), ("cmp_dist", 2 * N_CMP), ("cmp_mask", 2 * N_CMP)])

_second = []
for _l in range(2):
    _second += [(f"ffn1{_l}", 8), (f"mix{_l}", 8), (f"ffn2{_l}", 8), (f"mu{_l}", NZ), (f"w0{_l}", 4), (f"a0{_l}", 4),
                (f"kk{_l}", 4), (f"ka{_l}", 4), (f"rk{_l}", 4), (f"gnw{_l}", 4), (f"gnb{_l}", 4), (f"vres{_l}", 4),
                (f"convw{_l}", 32), (f"convb{_l}", 8), (f"gbias{_l}", 1), (f"mlnorm{_l}", 4)]
VEC, NVEC = columns([("c", 8), ("mod_b", MOD_COLS), ("norm_g", 96), ("kv_norm", 8), ("conv", 24), ("pos", 32)]
                    + _second + [("final", 8)])


USES = {
    "ada": dict(tile=ADA_FIRST, ada=ADA_FIRST), "norm": dict(norm=1, pre=1, scaled=1), "post": dict(norm=1, post=1, update=2),
    "half": dict(update=4), "ffn": dict(tile=FFN_TILES, half=2 * FFN_TILES, front=HALVES, ffn=1),
    "ffn_ada": dict(tile=FFN_TILES + ADA_FFN, half=2 * FFN_TILES, front=HALVES, ffn=1, ada=ADA_FFN),
    "conv": dict(tile=12, half=24, front=12), "lin4": dict(tile=4, half=8, front=4, pre=1),
    "kv": dict(tile=15, half=20, front=10), "nsa": dict(tile=5, half=10, front=5),
    "mix": dict(tile=17, half=32, front=16), "gates": dict(tile=8, half=16, front=8),
    "branch": dict(tile=4, half=8, front=8, branch=1, pre=1), "resid": dict(), "final": dict(norm=1),
}


KEEP_BEFORE = {"ffn": 18, "ffn_ada": 18, "half": 12, "lin4": 8, "resid": 8}
KEEP_AFTER = {"post": 28, "norm": 14}


class Stage:

    def __init__(self, kind, at, mod=None, gain=None, source=None, rhs=None, layer=None):
        self.kind, self.mod, self.gain, self.source, self.rhs, self.layer = kind, mod, gain, source, rhs, layer
        self.ada = at["ada"]
        self.tile, self.half, self.front = at["tile"], at["half"], at["front"]
        self.norm, self.pre, self.scaled = at["norm"], at["pre"], at["scaled"]
        self.post, self.update, self.ffn, self.branch = at["post"], at["update"], at["ffn"], at["branch"]


class Engines:

    def __init__(self, steps, mixer):
        self.pe, self.vec, self.act, self.pool = (steps(f"{mixer}_{e}") for e in ("pe", "vec", "act", "pool"))


def make_plan():
    at = dict(tile=0, half=0, ada=0, scaled=0, front=0, norm=0, pre=0, post=0, update=0, ffn=0, branch=0)
    plan = []

    def add(kind, **kw):
        plan.append(Stage(kind, at, **kw))
        plan[-1].after = plan[-2].kind if len(plan) > 1 else None
        if plan[-1].after == "post" and plan[-2].source == "ffn":
            plan[-1].after = "post_ffn"
        writers = [st.kind for st in plan[:-1] if st.kind in ("post", "half", "resid")]
        plan[-1].x_from = writers[-1] if writers else None
        for k, n in USES[kind].items():
            at[k] += n

    add("ada")
    for layer in range(2):
        if layer == 1:
            add("norm", mod="kv")
            add("kv")
        for i in range(3):
            add("norm", mod=(layer, i))
            if i != 1:
                add("ffn" if layer else "ffn_ada")
                add("post", mod=(layer, i), source="ffn")
            else:
                add("nsa" if layer else "conv")
                add("lin4", rhs="o" if layer else "conv_y")
                add("post", mod=(layer, i), source="lin4")
    for layer in range(2):
        add("norm", mod=None, gain=f"ffn1{layer}")
        add("ffn")
        add("half")
        add("norm", mod=None, gain=f"mix{layer}")
        add("mix", layer=layer)
        add("gates", layer=layer)
        add("branch")
        add("lin4", rhs="u")
        add("resid")
        add("norm", mod=None, gain=f"ffn2{layer}")
        add("ffn")
        add("half")
    add("final", mod=None, gain="final")
    return plan, at


PLAN, TOTAL = make_plan()
N_POST_FFN = sum(st.kind == "post" and st.source == "ffn" for st in PLAN)
N_TILES = TOTAL["tile"]
N_HALVES = TOTAL["half"]


def slope(head):
    return 2.0 ** (-8.0 * (head + 1) / NH)


def split_halves():
    out, run = [], 0
    for st in PLAN:
        n, tiles = USES[st.kind].get("half", 0), USES[st.kind].get("tile", 0)
        at = range(tiles)
        if st.kind == "ffn_ada":
            at = [t for t in at if t == 0 or t % 2]
        out += [(st.tile + at[i // 2], i % 2, run) for i in range(n)]
        run += st.kind in ("kv", "mix")
    return out


SPLIT = split_halves()


class Steps:

    def __init__(self, sem, names):
        self.sem, self.names, self.made = sem, names, 0
        self.value = {n: i + 1 for i, n in enumerate(names)}

    def step(self, name):
        assert self.names[self.made] == name, (name, self.names[self.made])
        self.made += 1
        return self.sem, 1

    def at(self, name):
        return self.sem, self.value[name]


STEPS = {
    "conv_vector": """
        v0 a0 a1 b0 b1 c0 c1 y0 y1 v1 a2 a3 b2 b3 c2 c3 y2 y3 v2 a4 a5 b4 b5 c4 c5 y4 y5 v3 a6 a7 b6 b7 c6 c7 y6 y7""".split(),
    "conv_pool": """
        pad""".split(),
    "kv_vector": """
        blocks kcz0 kcz1 vcz0 vcz1""".split(),
    "kv_scalar": """
        gelu""".split(),
    "kv_pool": """
        zero zero_cmp""".split(),
    "attention_tensor": """
        cmp_scores0 cmp_scores1 scores0 scores1 cmp_turned0 cmp_turned1 cmp_turned2 cmp_turned3 cmp_turned4
        cmp_turned5 cmp_turned6 cmp_turned7 scores2 turned0 values0 scores3 turned1 values1 scores4 turned2 values2
        scores5 turned3 values3 scores6 turned4 values4 scores7 turned5 values5 scores8 turned6 values6 scores9
        turned7 values7 scores10 turned8 values8 scores11 turned9 values9 scores12 turned10 values10 scores13
        turned11 values11 scores14 turned12 values12 scores15 turned13 values13 scores16 turned14 values14 scores17
        turned15 values15 scores18 turned16 values16 scores19 turned17 values17 scores20 turned18 values18 scores21
        turned19 values19 scores22 turned20 values20 scores23 turned21 values21 scores24 turned22 values22 scores25
        turned23 values23 scores26 turned24 values24 scores27 turned25 values25 scores28 turned26 values26 scores29
        turned27 values27 scores30 turned28 values28 scores31 turned29 values29 turned30 values30 turned31 values31""".split(),
    "attention_vector": """
        q3 cmp_biased0 cmp_max0 cmp_centred0 cmp_masked0 cmp_sum0 cmp_floor0 cmp_inv0 cmp_gate0 pc0 cmp_biased1
        cmp_max1 cmp_centred1 cmp_masked1 cmp_sum1 cmp_floor1 cmp_inv1 cmp_gate1 pc1 pcT0 pcT1 pcT2 pcT3 pcT4 pcT5
        pcT6 pcT7 biased0 rawmax0 max0 biased1 rawmax1 max1 inv0 weight0 p0 biased2 rawmax2 max2 inv1 weight1 p1
        biased3 rawmax3 max3 inv2 weight2 p2 biased4 rawmax4 max4 inv3 weight3 p3 o0 biased5 rawmax5 max5 inv4
        weight4 p4 biased6 rawmax6 max6 inv5 weight5 p5 o1 biased7 rawmax7 max7 inv6 weight6 p6 biased8 rawmax8 max8
        inv7 weight7 p7 o2 biased9 rawmax9 max9 inv8 weight8 p8 biased10 rawmax10 max10 inv9 weight9 p9 o3 biased11
        rawmax11 max11 inv10 weight10 p10 biased12 rawmax12 max12 inv11 weight11 p11 o4 biased13 rawmax13 max13
        inv12 weight12 p12 biased14 rawmax14 max14 inv13 weight13 p13 o5 biased15 rawmax15 max15 inv14 weight14 p14
        biased16 rawmax16 max16 inv15 weight15 p15 o6 biased17 rawmax17 max17 inv16 weight16 p16 biased18 rawmax18
        max18 inv17 weight17 p17 o7 biased19 rawmax19 max19 inv18 weight18 p18 biased20 rawmax20 max20 inv19
        weight19 p19 o8 biased21 rawmax21 max21 inv20 weight20 p20 biased22 rawmax22 max22 inv21 weight21 p21 o9
        biased23 rawmax23 max23 inv22 weight22 p22 biased24 rawmax24 max24 inv23 weight23 p23 o10 biased25 rawmax25
        max25 inv24 weight24 p24 biased26 rawmax26 max26 inv25 weight25 p25 o11 biased27 rawmax27 max27 inv26
        weight26 p26 biased28 rawmax28 max28 inv27 weight27 p27 o12 biased29 rawmax29 max29 inv28 weight28 p28
        biased30 rawmax30 max30 inv29 weight29 p29 o13 biased31 rawmax31 max31 inv30 weight30 p30 inv31 weight31 p31
        o14 o15""".split(),
    "attention_scalar": """
        cmp_exp0 cmp_exp1 exp0_0 exp0_1 exp1_0 exp1_1 pt0 exp2_0 exp2_1 pt1 exp3_0 exp3_1 pt2 exp4_0 exp4_1 pt3
        exp5_0 exp5_1 pt4 exp6_0 exp6_1 pt5 exp7_0 exp7_1 pt6 exp8_0 exp8_1 pt7 exp9_0 exp9_1 pt8 exp10_0 exp10_1
        pt9 exp11_0 exp11_1 pt10 exp12_0 exp12_1 pt11 exp13_0 exp13_1 pt12 exp14_0 exp14_1 pt13 exp15_0 exp15_1 pt14
        exp16_0 exp16_1 pt15 exp17_0 exp17_1 pt16 exp18_0 exp18_1 pt17 exp19_0 exp19_1 pt18 exp20_0 exp20_1 pt19
        exp21_0 exp21_1 pt20 exp22_0 exp22_1 pt21 exp23_0 exp23_1 pt22 exp24_0 exp24_1 pt23 exp25_0 exp25_1 pt24
        exp26_0 exp26_1 pt25 exp27_0 exp27_1 pt26 exp28_0 exp28_1 pt27 exp29_0 exp29_1 pt28 exp30_0 exp30_1 pt29
        exp31_0 exp31_1 pt30 pt31""".split(),
    "mlstm0_pe": """
        g_turned M_spread em_spread scores0 scores1 scores2 scores3 sums0 scores4 scores5 sums1 scores6 scores7
        sums2 sums3 mean var""".split(),
    "mlstm0_vec": """
        diff0 shifted0 diff1 shifted1 diff2 shifted2 diff3 shifted3 diff4 shifted4 diff5 shifted5 diff6 shifted6
        diff7 shifted7 li xf minus_abs lf F g_row M_row F_plus_M tap0_0 tap0_1 tap1_0 tap1_1 tap2_0 tap2_1 conv0
        conv1 tap0_2 tap0_3 tap1_2 tap1_3 tap2_2 tap2_3 conv2 conv3 tap0_4 tap0_5 tap1_4 tap1_5 tap2_4 tap2_5 conv4
        conv5 tap0_6 tap0_7 tap1_6 tap1_7 tap2_6 tap2_7 conv6 conv7 m_o g_col gap0 gap1 gap2 sw0 masked0 gap3 sw1
        masked1 gap4 sw2 masked2 gap5 sw3 masked3 gap6 floor0 den0 inv0 h0 sw4 masked4 gap7 sw5 masked5 floor1 den1
        inv1 h1 sw6 masked6 sw7 masked7 floor2 den2 inv2 h2 floor3 den3 inv3 h3 centred0 centred1 rstd0 rstd1 normed
        y_b""".split(),
    "mlstm0_act": """
        exp_f ln_f em_row qk em_copy weight0 weight1 weight2 weight3 weight4 weight5 weight6 weight7 sig_o squares
        root0 root1""".split(),
    "mlstm0_pool": """
        pads rows_zero""".split(),
    "mlstm1_pe": """
        g_turned M_spread em_spread scores0 scores1 scores2 scores3 sums0 scores4 scores5 sums1 scores6 scores7
        sums2 sums3 mean var""".split(),
    "mlstm1_vec": """
        diff0 shifted0 diff1 shifted1 diff2 shifted2 diff3 shifted3 diff4 shifted4 diff5 shifted5 diff6 shifted6
        diff7 shifted7 li xf minus_abs lf F g_row M_row F_plus_M tap0_0 tap0_1 tap1_0 tap1_1 tap2_0 tap2_1 conv0
        conv1 tap0_2 tap0_3 tap1_2 tap1_3 tap2_2 tap2_3 conv2 conv3 tap0_4 tap0_5 tap1_4 tap1_5 tap2_4 tap2_5 conv4
        conv5 tap0_6 tap0_7 tap1_6 tap1_7 tap2_6 tap2_7 conv6 conv7 m_o g_col gap0 gap1 gap2 sw0 masked0 gap3 sw1
        masked1 gap4 sw2 masked2 gap5 sw3 masked3 gap6 floor0 den0 inv0 h0 sw4 masked4 gap7 sw5 masked5 floor1 den1
        inv1 h1 sw6 masked6 sw7 masked7 floor2 den2 inv2 h2 floor3 den3 inv3 h3 centred0 centred1 rstd0 rstd1 normed
        y_b""".split(),
    "mlstm1_act": """
        exp_f ln_f em_row qk em_copy weight0 weight1 weight2 weight3 weight4 weight5 weight6 weight7 sig_o squares
        root0 root1""".split(),
    "mlstm1_pool": """
        pads rows_zero""".split(),
    "rwkv0_pe": """
        w a kk_norm rk_sum turned0_0 turned1_0 turned2_0 A_t0_0 A_t1_0 A0_0 A1_0 A_kk0_0 A_kk1_0 A_rk0_0 A_rk1_0
        A_rb0_0 A_rb1_0 U1_0_0 U1_1_0 D1_0_0 D_t1_0_0 D1_1_0 D_t1_1_0 U2_0_0 U2_1_0 D2_0_0 D_t2_0_0 D2_1_0 D_t2_1_0
        U3_0_0 U3_1_0 D3_0_0 D_t3_0_0 D3_1_0 D_t3_1_0 U4_0_0 U4_1_0 D4_0_0 D_t4_0_0 D4_1_0 D_t4_1_0 U5_0_0 U5_1_0
        D_t5_0_0 D_t5_1_0 G0 SA0 dS0 y0 G1 SA1 dS1 y1 turned0_1 turned1_1 turned2_1 A_t0_1 A_t1_1 A0_1 A1_1 A_kk0_1
        A_kk1_1 A_rk0_1 A_rk1_1 A_rb0_1 A_rb1_1 U1_0_1 U1_1_1 D1_0_1 D_t1_0_1 D1_1_1 D_t1_1_1 U2_0_1 U2_1_1 D2_0_1
        D_t2_0_1 D2_1_1 D_t2_1_1 U3_0_1 U3_1_1 D3_0_1 D_t3_0_1 D3_1_1 D_t3_1_1 U4_0_1 U4_1_1 D4_0_1 D_t4_0_1 D4_1_1
        D_t4_1_1 U5_0_1 U5_1_1 D_t5_0_1 D_t5_1_1 G2 SA2 dS2 y2 G3 SA3 dS3 y3 gn_mean gn_var""".split(),
    "rwkv0_vec": """
        lora_zero lora_tail one_minus_ka kk_raw0 kk_raw1 kk_raw2 kk_raw3 lw L L_prev ka k_mixed rk rk0 rk1 rk2 rk3
        v_mixed kk_floor0 kk_floor1 kk_rstd0 kk_rstd1 kk bonus0 bonus1 b kap rho P khat bhat k_z0 k_z1 keep0 keep1
        ktok0_0 ktok1_0 A_t0_0 A_t1_0 X_off0_0 X0_0_0 Xt_off0_0 X_t0_0_0 X_off1_0 X0_1_0 Xt_off1_0 X_t0_1_0 A_kk0_0
        A_kk1_0 A_rk0_0 A_rk1_0 A_rb0_0 A_rb1_0 X1_0_0 X_t1_0_0 X1_1_0 X_t1_1_0 X2_0_0 X_t2_0_0 X2_1_0 X_t2_1_0
        X3_0_0 X_t3_0_0 X3_1_0 X_t3_1_0 X4_0_0 X_t4_0_0 X4_1_0 X_t4_1_0 X_t5_0_0 X_t5_1_0 S0_3 G0 SA0_0 SA0_1 S_sum0
        S1_0 S1_1 S1_2 S1_3 y0 G1 SA1_0 SA1_1 S_sum1 S2_0 S2_1 S2_2 S2_3 y1 ktok0_1 ktok1_1 A_t0_1 A_t1_1 X_off0_1
        X0_0_1 Xt_off0_1 X_t0_0_1 X_off1_1 X0_1_1 Xt_off1_1 X_t0_1_1 A_kk0_1 A_kk1_1 A_rk0_1 A_rk1_1 A_rb0_1 A_rb1_1
        X1_0_1 X_t1_0_1 X1_1_1 X_t1_1_1 X2_0_1 X_t2_0_1 X2_1_1 X_t2_1_1 X3_0_1 X_t3_0_1 X3_1_1 X_t3_1_1 X4_0_1
        X_t4_0_1 X4_1_1 X_t4_1_1 X_t5_0_1 X_t5_1_1 G2 SA2_0 SA2_1 S_sum2 S3_0 S3_1 S3_2 S3_3 y2 G3 SA3_0 SA3_1
        S_sum3 S4_0 S4_1 S4_2 S4_3 y3 gn_centred0 gn_centred1 gn_rstd0 gn_rstd1 gn0 gn1 gn2 gn3 with_bonus0
        with_bonus1 with_bonus2 with_bonus3 y_a0 y_a1 y_a2 y_a3""".split(),
    "rwkv0_act": """
        lora_mid lora_in kk_sq sig_w a g_taken0 g_taken1 kk_root0 kk_root1 E_prev E_inv E b_z0 b_z1 btok0_0 btok1_0
        v_z0_0 v_z1_0 U1_0_0 U1_1_0 U2_0_0 U2_1_0 U3_0_0 U3_1_0 U4_0_0 U4_1_0 U5_0_0 U5_1_0 btok0_1 btok1_1 v_z0_1
        v_z1_1 U1_0_1 U1_1_1 U2_0_1 U2_1_1 U3_0_1 U3_1_1 U4_0_1 U4_1_1 U5_0_1 U5_1_1 gn_squares gn_root0 gn_root1""".split(),
    "rwkv0_pool": """
        z_zero tok_zero A_lv1_0 A_lv2_0 A_lv3_0 A_lv4_0 A_lv5_0 A_lv1_1 A_lv2_1 A_lv3_1 A_lv4_1 A_lv5_1""".split(),
    "rwkv1_pe": """
        w a g kk_norm rk_sum turned0_0 turned1_0 turned2_0 A_t0_0 A_t1_0 A0_0 A1_0 A_kk0_0 A_kk1_0 A_rk0_0 A_rk1_0
        A_rb0_0 A_rb1_0 U1_0_0 U1_1_0 D1_0_0 D_t1_0_0 D1_1_0 D_t1_1_0 U2_0_0 U2_1_0 D2_0_0 D_t2_0_0 D2_1_0 D_t2_1_0
        U3_0_0 U3_1_0 D3_0_0 D_t3_0_0 D3_1_0 D_t3_1_0 U4_0_0 U4_1_0 D4_0_0 D_t4_0_0 D4_1_0 D_t4_1_0 U5_0_0 U5_1_0
        D_t5_0_0 D_t5_1_0 G0 SA0 dS0 y0 G1 SA1 dS1 y1 turned0_1 turned1_1 turned2_1 A_t0_1 A_t1_1 A0_1 A1_1 A_kk0_1
        A_kk1_1 A_rk0_1 A_rk1_1 A_rb0_1 A_rb1_1 U1_0_1 U1_1_1 D1_0_1 D_t1_0_1 D1_1_1 D_t1_1_1 U2_0_1 U2_1_1 D2_0_1
        D_t2_0_1 D2_1_1 D_t2_1_1 U3_0_1 U3_1_1 D3_0_1 D_t3_0_1 D3_1_1 D_t3_1_1 U4_0_1 U4_1_1 D4_0_1 D_t4_0_1 D4_1_1
        D_t4_1_1 U5_0_1 U5_1_1 D_t5_0_1 D_t5_1_1 G2 SA2 dS2 y2 G3 SA3 dS3 y3 gn_mean gn_var""".split(),
    "rwkv1_vec": """
        lora_zero lora_tail one_minus_ka kk_raw0 kk_raw1 kk_raw2 kk_raw3 lw L L_prev ka k_mixed rk rk0 rk1 rk2 rk3
        v_gap v_gated v_mixed kk_floor0 kk_floor1 kk_rstd0 kk_rstd1 kk bonus0 bonus1 b kap rho P khat bhat k_z0 k_z1
        keep0 keep1 ktok0_0 ktok1_0 A_t0_0 A_t1_0 X_off0_0 X0_0_0 Xt_off0_0 X_t0_0_0 X_off1_0 X0_1_0 Xt_off1_0
        X_t0_1_0 A_kk0_0 A_kk1_0 A_rk0_0 A_rk1_0 A_rb0_0 A_rb1_0 X1_0_0 X_t1_0_0 X1_1_0 X_t1_1_0 X2_0_0 X_t2_0_0
        X2_1_0 X_t2_1_0 X3_0_0 X_t3_0_0 X3_1_0 X_t3_1_0 X4_0_0 X_t4_0_0 X4_1_0 X_t4_1_0 X_t5_0_0 X_t5_1_0 S0_3 G0
        SA0_0 SA0_1 S_sum0 S1_0 S1_1 S1_2 S1_3 y0 G1 SA1_0 SA1_1 S_sum1 S2_0 S2_1 S2_2 S2_3 y1 ktok0_1 ktok1_1
        A_t0_1 A_t1_1 X_off0_1 X0_0_1 Xt_off0_1 X_t0_0_1 X_off1_1 X0_1_1 Xt_off1_1 X_t0_1_1 A_kk0_1 A_kk1_1 A_rk0_1
        A_rk1_1 A_rb0_1 A_rb1_1 X1_0_1 X_t1_0_1 X1_1_1 X_t1_1_1 X2_0_1 X_t2_0_1 X2_1_1 X_t2_1_1 X3_0_1 X_t3_0_1
        X3_1_1 X_t3_1_1 X4_0_1 X_t4_0_1 X4_1_1 X_t4_1_1 X_t5_0_1 X_t5_1_1 G2 SA2_0 SA2_1 S_sum2 S3_0 S3_1 S3_2 S3_3
        y2 G3 SA3_0 SA3_1 S_sum3 S4_0 S4_1 S4_2 S4_3 y3 gn_centred0 gn_centred1 gn_rstd0 gn_rstd1 gn0 gn1 gn2 gn3
        with_bonus0 with_bonus1 with_bonus2 with_bonus3 y_a0 y_a1 y_a2 y_a3""".split(),
    "rwkv1_act": """
        lora_mid lora_in kk_sq sig_w a vg g_taken0 g_taken1 kk_root0 kk_root1 E_prev E_inv E b_z0 b_z1 btok0_0
        btok1_0 v_z0_0 v_z1_0 U1_0_0 U1_1_0 U2_0_0 U2_1_0 U3_0_0 U3_1_0 U4_0_0 U4_1_0 U5_0_0 U5_1_0 btok0_1 btok1_1
        v_z0_1 v_z1_1 U1_0_1 U1_1_1 U2_0_1 U2_1_1 U3_0_1 U3_1_1 U4_0_1 U4_1_1 U5_0_1 U5_1_1 gn_squares gn_root0
        gn_root1""".split(),
    "rwkv1_pool": """
        z_zero tok_zero A_lv1_0 A_lv2_0 A_lv3_0 A_lv4_0 A_lv5_0 A_lv1_1 A_lv2_1 A_lv3_1 A_lv4_1 A_lv5_1""".split(),
}



def build(nc, consts_d, vecs_d, x_d, weights_d, out_d):
    with ExitStack() as ctx:
        def sb(name, cols, dtype=F32):
            return ctx.enter_context(nc.sbuf_tensor(name, [P, cols], dtype))

        def sem(name):
            return ctx.enter_context(nc.semaphore(name))

        consts, vecs = sb("const_sb", NCONST), sb("vec_sb", NVEC)
        ring = [sb(f"ring{i}", TILE) for i in range(RING)]
        w_hi, w_lo = ([sb(f"w_{e}{i}", HALF, F32R) for i in range(SLOTS)] for e in ("hi", "lo"))
        h_hi, h_lo = sb("h_hi", KC * TOK, F32R), sb("h_lo", KC * TOK, F32R)
        x, y, sq = sb("x", KC * TOK), sb("y", KC * TOK), sb("sq", KC * TOK)
        act_t, silu_t, rstd = sb("act_t", 2 * TOK), sb("silu_t", 2 * TOK), sb("rstd", TOK)
        act_hi, act_lo = sb("act_hi", 2 * TOK, F32R), sb("act_lo", 2 * TOK, F32R)
        mods, pre_gain, post_gain, cond = sb("mods", MOD_COLS), sb("pre_gain", 56), sb("post_gain", 48), sb("cond", 8)
        v_first = sb("v_first", 4 * TOK)
        work = sb("work", 23360)
        bank = [ctx.enter_context(nc.psum_tensor(f"bank{i}", [P, 512], F32)) for i in range(8)]
        Y_BANK, FRONT, LOW, MOD_BANK = 0, (4, 5), 6, 7

        def K(name):
            a, n = CONST[name]
            return consts[:, a:a + n]

        def V(name, i=0, n=1):
            a = VEC[name][0] + i
            return vecs[:, a:a + n]

        def tiles(t, n=KC, w=TOK):
            return t[:, :].rearrange("p (j t) -> p j t", j=n) if w is None else \
                t[:, 0:n * w].rearrange("p (j t) -> p j t", j=n)

        x3, hi3, lo3, y3, sq3 = tiles(x), tiles(h_hi), tiles(h_lo), tiles(y), tiles(sq)
        ada_acc = tiles(y, 3)
        rings = [r[:, :].rearrange("p (h k c) -> p h k c", h=2, k=KC) for r in ring]
        whi3, wlo3 = ([r[:, :].rearrange("p (k c) -> p k c", k=KC) for r in w] for w in (w_hi, w_lo))

        def carve(start, *dims):
            n = int(np.prod(dims))
            assert start + n <= 23360, (start, n)
            v = work[:, start:start + n]
            if len(dims) == 2:
                v = v.rearrange("p (a b) -> p a b", a=dims[0])
            if len(dims) == 3:
                v = v.rearrange("p (a b c) -> p a b c", a=dims[0], b=dims[1])
            if len(dims) == 4:
                v = v.rearrange("p (a b c d) -> p a b c d", a=dims[0], b=dims[1], c=dims[2])
            return v

        def half(b, i):
            return bank[b][:, i * TOK:(i + 1) * TOK]

        def pair(b):
            return bank[b][:, :].rearrange("p (a t) -> p a t", a=2)

        def quad(b):
            return bank[b][:, :].rearrange("p (a t) -> p a t", a=4)

        def mod_col(layer, sub, what):
            return 72 * layer + 24 * sub + 8 * what

        consts_landed, vecs_landed, x_landed = sem("consts_landed"), sem("vecs_landed"), sem("x_landed")
        tile_landed = [sem(f"tile_landed{i}") for i in range(RING)]
        halves_left = sem("halves_left")
        hi_ready, half_used = sem("hi_ready"), sem("half_used")
        front_taken, silu_ready = sem("front_taken"), sem("silu_ready")
        hidden_hi, hidden_ready = sem("hidden_hi"), sem("hidden_ready")
        squares_ready, meansq_ready = sem("squares_ready"), sem("meansq_ready")
        x_pool_ready = sem("x_pool_ready")
        squares_folded = sem("squares_folded")
        root_ready, rstd_ready = sem("root_ready"), sem("rstd_ready")
        h_scaled, h_hi_ready, h_ready = sem("h_scaled"), sem("h_hi_ready"), sem("h_ready")
        y_sums, y_ready, delta_ready, x_ready = sem("y_sums"), sem("y_ready"), sem("delta_ready"), sem("x_ready")
        cond_ready, mods_taken = sem("cond_ready"), sem("mods_taken")
        ada_partial, ada_summed = sem("ada_partial"), sem("ada_summed")
        ada_pool_partial = sem("ada_pool_partial")
        gains_ready, u_ready, br_product = sem("gains_ready"), sem("u_ready"), sem("br_product")
        out_ready, out_stored = sem("out_ready"), sem("out_stored")

        def steps(name):
            return Steps(sem(name), STEPS.get(name, []))

        conv_vec, conv_pool = steps("conv_vector"), steps("conv_pool")
        kv_pe, kv_vec, kv_act, kv_pool = (steps(f"kv_{e}") for e in ("tensor", "vector", "scalar", "pool"))
        at_pe, at_vec, at_act, at_pool = (steps(f"attention_{e}") for e in ("tensor", "vector", "scalar", "pool"))
        ML = [Engines(steps, f"mlstm{l}") for l in range(2)]
        RW = [Engines(steps, f"rwkv{l}") for l in range(2)]

        ada_pool = carve(0, 3, ADA_POOL, TILE_COLS)

        conv_z = carve(0, 24, TOK)
        conv_v = carve(6144, 8, ZW)
        conv_y = carve(6144 + 8 * ZW, 8, TOK)

        kz = carve(0, 2, NG, 2, TOK)
        vz = carve(4096, 16, 2, P)
        blocks = carve(8192, 2, 16, NG * N_CMP)
        hid = carve(10112, 2, 2, NG * N_CMP)
        kcz = carve(10352, NG, 2, N_CMP)
        vcz = carve(10472, NG, 2, P)
        q_t = carve(11496, 8, TOK)
        o_t = carve(13544, 8, TOK)
        gate_tok = carve(15592, 2, 3 * NH)
        pc = carve(15688, 2, NH, N_CMP)
        pc_t = carve(16168, 2, NH, P)
        s_buf = [carve(20264, 2, TOK), carve(20776, 2, TOK), carve(22568, 2, TOK)]
        pt_buf = carve(21288, 2, 4, P)
        at_small = carve(22312, 256)

        zp = carve(0, NZ, ZW)
        C0 = NZ * ZW
        y_b = carve(C0, 4, TOK)
        g_up = carve(C0 + 1024, 4, TOK)
        bonus = carve(C0 + 2048, 4, TOK)
        y_a = carve(C0 + 3072, 4, TOK)
        rho, kap = carve(C0 + 4096, 4, TOK), carve(C0 + 5120, 4, TOK)
        k_z, b_z = carve(C0 + 6144, 4, 2, TOK), carve(C0 + 8192, 4, 2, TOK)
        C1 = C0 + 10240
        mqk = carve(C0 + 4096, 8, ZW)
        m_o = carve(C0 + 6176, 4, TOK)
        v_tok = carve(C0 + 7200, 2, 512)
        diff = carve(C1, NZ, TOK)
        qk = carve(C1, 8, TOK)
        sw = carve(C1 + 2048, 8, TOK)
        h_b = carve(C1 + 4096, 4, TOK)
        rows = carve(C1 + 5120, 3, TOK)
        row_tmp = carve(C1 + 5888, 5, TOK)
        bc_e = carve(C1 + 7168, 4, TOK)
        w_buf = carve(C1 + 8192, 4, TOK)
        e1, e2, e3, e4, e5, e6, e7, e8 = (carve(C1 + 1024 * i, 4, TOK) for i in range(8))
        lora_in = carve(C1 + 8192, 4, TOK)
        A_t, A_kk, A_rk, A_rb = (carve(C1 + 1024 * i, RH, P) for i in range(4))
        X, X_t, U = (carve(C1 + 4096 + 1024 * i, RH, P) for i in range(3))
        A_lv = [carve(C1 + 7168, RH, P), carve(C1 + 8192, RH, P)]
        ktok = y[:, 0:1024].rearrange("p (c f) -> p c f", c=2)
        btok = y[:, 1024:2048].rearrange("p (c f) -> p c f", c=2)
        v_z = sq[:, 0:1024].rearrange("p (j r v) -> p j r v", j=4, r=2)
        sa_z = sq[:, 1024:2048].rearrange("p (j r v) -> p j r v", j=4, r=2)
        rw_small = C1 + 9216
        S = act_t[:, 0:512].rearrange("p (j v) -> p j v", j=4)
        gs = silu_t
        small = sb("small", 64)
        keep = [zp[:, 4 * s:4 * s + 4, PAD:PAD + P] for s in range(2)]
        sgate = carve(C1, 16, TOK)
        br_t = carve(C1 + 4096, 2, TOK)
        u = sq3

        block = ctx.enter_context(nc.Block())

        @block.sync
        def _(sp):
            sp.dma_start(vecs[:, :], vecs_d).then_inc(vecs_landed, 16)
            for n in range(RING):
                sp.dma_start(ring[n][:, :], weights_d[n]).then_inc(tile_landed[n], 16)
                if n == 0:
                    sp.dma_start(x[:, :], x_d).then_inc(x_landed, 16)
                    sp.dma_start(consts[:, :], consts_d).then_inc(consts_landed, 16)
            with sp.Fori(1, N_TILES // RING) as turn:
                for n in range(RING):
                    sp.wait_ge(halves_left, turn * (2 * RING) + 2 * (n + 1 - RING))
                    sp.dma_start(ring[n][:, :], weights_d[bass.ds(turn * RING + n, 1)].rearrange("a p c -> p (a c)")
                                 ).then_inc(tile_landed[n], 16)
            for m in range(N_TILES // RING * RING, N_TILES):
                sp.wait_ge(halves_left, 2 * (m + 1 - RING))
                sp.dma_start(ring[m % RING][:, :], weights_d[m]).then_inc(tile_landed[m % RING], 16)
            for i in range(2):
                c = slice(i * KC // 2 * TOK, (i + 1) * KC // 2 * TOK)
                sp.wait_ge(out_ready, (i + 1) * KC // 2)
                sp.dma_start(out_d[:, c], y[:, c]).then_inc(out_stored, 16)
            sp.wait_ge(out_stored, 32)

        @block.tensor
        def _(pe):
            def tile_wait(n, turn=0):
                pe.wait_ge(tile_landed[n % RING], (turn + (n // RING + 1)) * 16)

            def front_wait(f, extra=0):
                if isinstance(extra, int) and f + extra < 2:
                    return
                pe.wait_ge(front_taken, extra + (f - 1))

            def mm(out, lhsT, rhs, start, stop, skip=False):
                return nc.tensor.matmul(out, lhsT, rhs, start=start, stop=stop, skip_group_check=skip)

            def mm3(out, w_hi_, w_lo_, a_hi, a_lo, start, stop, skip=False):
                mm(out, w_hi_, a_hi, start, False, skip)
                mm(out, w_hi_, a_lo, False, False, skip)
                return mm(out, w_lo_, a_hi, False, stop, skip)

            def half_wait(q, extra=0):
                n, c, _ = SPLIT[q]
                pe.wait_ge(halves_left, extra + (2 * n + c + 1))

            def column_sums(a, n, turn=0, per_turn=RING):
                pe.wait_ge(halves_left, turn * (2 * per_turn) + (2 * n + 2))
                for c in range(2):
                    o = bank[MOD_BANK][:, 2 * a + c:2 * a + c + 1] if isinstance(turn, int) else \
                        bank[MOD_BANK][:, bass.ds(turn * 6 + (2 * a + c), 1)]
                    ins = mm(o, ada_acc[:, a % 3, c * P:(c + 1) * P], K("ones")[:, 0:1], True, True)
                ins.then_inc(ada_summed, 1)

            def ada(st):
                pe.wait_ge(consts_landed, 16)
                with pe.Fori(0, ADA_FIRST // 3) as turn:
                    for a in range(3):
                        column_sums(a, a, turn)
                for a in range(ADA_FIRST // 3 * 3, ADA_FIRST):
                    column_sums(a, a)

            def keep_clock(b, n):
                for _ in range(n):
                    mm(bank[b][:, 0:P], K("ones"), K("ident"), True, True)

            def meansq(st):
                free = FRONT[0] if st.after in ("ffn", "ffn_ada", "half", "post_ffn") else 0
                keep_clock(free, KEEP_BEFORE.get(st.after, 0))
                for p in range(2):
                    pe.wait_ge(squares_folded, 2 * st.norm + p + 1)
                    if p == 0:
                        if st.norm == 0:
                            pe.wait_ge(consts_landed, 16)
                        else:
                            pe.wait_ge(rstd_ready, st.norm)
                    for j in (4 * p, 4 * p + 1):
                        ins = mm(bank[LOW][:, 0:TOK], K("ones"), sq3[:, j, :], j == 0, j == 5)
                ins.then_inc(meansq_ready, 1)
                keep_clock(free, KEEP_AFTER.get(st.kind, 0))

            def gate_up(st, q, hh, turn=0, first=False, left=6):
                f = st.front + hh
                front_wait(f, turn * 2)
                if first:
                    half_wait(q + 1)
                    for k in range(KC):
                        pe.wait_ge(h_ready, 8 * st.pre - 8 + k + 1)
                        for i in range(2):
                            w = (q + i) % SLOTS
                            ins = mm3(half(FRONT[f % 2], i), whi3[w][:, k, :], wlo3[w][:, k, :], hi3[:, k, :],
                                      lo3[:, k, :], k == 0 and i == 0, k == KC - 1, True)
                    ins.then_inc(half_used, 2)
                    return
                for i in range(2):
                    half_wait(q + i, turn * left)
                    w = (q + i) % SLOTS
                    for k in range(KC):
                        ins = mm3(half(FRONT[f % 2], i), whi3[w][:, k, :], wlo3[w][:, k, :], hi3[:, k, :], lo3[:, k, :],
                                  k == 0, k == KC - 1)
                    ins.then_inc(half_used, 1)

            def down(st, q, hh, turn=0, left=6):
                half_wait(q, turn * left)
                pe.wait_ge(hidden_ready, turn * 2 + (HALVES * st.ffn + hh + 1))
                w, a = q % SLOTS, slice(hh % 2 * TOK, (hh % 2 + 1) * TOK)
                for j in range(KC):
                    ins = mm3(half(Y_BANK + j // 2, j % 2), whi3[w][:, j, :], wlo3[w][:, j, :], act_hi[:, a], act_lo[:, a],
                              hh == 0 and j % 2 == 0, hh == HALVES - 1, True)
                    if hh == HALVES - 1 and j in (1, 3, 5):
                        ins.then_inc(y_sums, 1)
                ins.then_inc(half_used, 1)

            def ffn(st):
                if st.ffn:
                    pe.wait_ge(*((y_ready, 4 * st.ffn) if st.ffn <= N_POST_FFN else (x_ready, st.update)))
                q = st.half
                gate_up(st, q, 0, first=True)

                with_ada = st.kind == "ffn_ada"
                left = 12 if with_ada else 6

                def rider(q_, i, turn=0):
                    if with_ada:
                        column_sums(st.ada + i, SPLIT[q_][0] + 1, turn, 6)

                def pattern(s, turn=0):
                    gate_up(st, q + 6 * s + 2, 2 * s + 1, turn, left=left)
                    rider(q + 6 * s + 2, 3 * s, turn)
                    gate_up(st, q + 6 * s + 4, 2 * s + 2, turn, left=left)
                    rider(q + 6 * s + 4, 3 * s + 1, turn)
                    down(st, q + 6 * s + 6, 2 * s, turn, left)
                    down(st, q + 6 * s + 7, 2 * s + 1, turn, left)
                    rider(q + 6 * s + 6, 3 * s + 2, turn)

                pattern(0)
                with pe.Fori(0, FFN_STEPS - 2) as turn:
                    pattern(1, turn)
                gate_up(st, q + 6 * FFN_STEPS - 4, HALVES - 1)
                rider(q + 6 * FFN_STEPS - 4, ADA_FFN - 2)
                down(st, q + 6 * FFN_STEPS - 2, HALVES - 2)
                down(st, q + 6 * FFN_STEPS - 1, HALVES - 1)
                rider(q + 6 * FFN_STEPS - 2, ADA_FFN - 1)

            def linear(st, n_tiles, wait=None, first=0):
                for t in range(first, first + n_tiles):
                    f = st.front + t
                    front_wait(f)
                    for c in range(2):
                        q = st.half + 2 * t + c
                        half_wait(q)
                        w = q % SLOTS
                        for k in range(KC):
                            if t == first and c == 0 and wait:
                                wait(k)
                            if (st.kind, t, k) == ("mix", 7, KC - 1):
                                half_wait(q + 1)
                            ins = mm3(half(FRONT[f % 2], c), whi3[w][:, k, :], wlo3[w][:, k, :], hi3[:, k, :],
                                      lo3[:, k, :], k == 0, k == KC - 1)
                        if (st.kind, t) == ("mix", 7):
                            break
                        ins.then_inc(half_used, 1)
                    if c == 0:
                        ins.then_inc(half_used, 2)

            def token_major(st, n_tiles, cols, first):
                for t in range(first, first + n_tiles):
                    f = st.front + t
                    front_wait(f)
                    for i in range(-(-cols // P)):
                        q = st.half + 2 * t + i
                        half_wait(q)
                        w, n = q % SLOTS, min(cols, P)
                        for c in range(2):
                            ts = slice(c * P, (c + 1) * P)
                            for k in range(KC):
                                if cols < P and c == 1 and k == KC - 1:
                                    half_wait(q + 1)
                                ins = mm3(half(FRONT[f % 2], c)[:, i * P:i * P + n], hi3[:, k, ts], lo3[:, k, ts],
                                          whi3[w][:, k, 0:n], wlo3[w][:, k, 0:n], k == 0, k == KC - 1)
                        ins.then_inc(half_used, 1 if cols > P else 2)

            def wait_h(st):
                return lambda k: pe.wait_ge(h_ready, 8 * st.pre - 8 + k + 1)

            def kv(st):
                linear(st, 8, wait_h(st))
                token_major(st, 2, TILE_COLS, 8)
                pe.wait_ge(*kv_vec.at("blocks"))
                for s in range(2):
                    for a in range(2):
                        tile_wait(st.tile + 10 + 2 * s + a)
                    for ht in range(2):
                        for a in range(2):
                            for k in range(KC):
                                ins = mm(bank[7][:, (2 * s + ht) * 64:(2 * s + ht) * 64 + NG * N_CMP],
                                         rings[(st.tile + 10 + 2 * s + a) % RING][:, ht, k, :],
                                         blocks[:, s, 8 * a + k, :], a == 0 and k == 0, a == 1 and k == KC - 1)
                    ins.then_inc(halves_left, 4)
                pe.wait_ge(*kv_act.at("gelu"))
                tile_wait(st.tile + 14)
                w2 = ring[(st.tile + 14) % RING]
                for ht in range(2):
                    ins = mm(bank[7][:, 0:NG * N_CMP], w2[:, ht * P:(ht + 1) * P], hid[:, 0, ht, :], ht == 0, ht == 1)
                for g in range(NG):
                    for ht in range(2):
                        ins = mm(bank[7][0:N_CMP, 64 + g * DH:64 + (g + 1) * DH],
                                 hid[:, 1, ht, g * N_CMP:(g + 1) * N_CMP], w2[:, 256 + ht * DH:256 + (ht + 1) * DH],
                                 ht == 0, ht == 1)
                ins.then_inc(halves_left, 2)

            def nsa(st):
                linear(st, 4, wait_h(st))
                token_major(st, 1, 3 * NH, 4)
                pe.wait_ge(*at_vec.at("q3"))
                pe.wait_ge(*kv_vec.at("vcz1"))
                for qt in range(2):
                    for hd in range(NH):
                        ins = mm(bank[6 + qt][:, hd * 16:hd * 16 + N_CMP], q_t[:, hd // 2, qt * P:(qt + 1) * P],
                                 kcz[:, hd // 4, hd % 2, :], True, True)
                    ins.then_inc(*at_pe.step(f"cmp_scores{qt}"))

                def scores(u):
                    j, qt, r = u // 4, u // 2 % 2, u % 2
                    if u >= 2:
                        pe.wait_ge(*at_vec.at(f"biased{u - 2}"))
                    nk = (qt + 1) * P
                    for br in range(2):
                        ins = mm(bank[u % 2][:, br * TOK:br * TOK + nk], q_t[:, j, qt * P:(qt + 1) * P],
                                 kz[:, br, (2 * j + r) // 4, r, 0:nk], True, True)
                    ins.then_inc(*at_pe.step(f"scores{u}"))

                def turn(u):
                    qt = u // 2 % 2
                    pe.wait_ge(*at_vec.at(f"p{u}"))
                    if u >= 2:
                        pe.wait_ge(*at_act.at(f"pt{u - 2}"))
                    for br in range(2):
                        for kt in range(qt + 1):
                            ins = nc.tensor.transpose(quad(2 + u % 2)[:, 2 * br + kt, :],
                                                      s_buf[u % 3][:, br, kt * P:(kt + 1) * P], K("ident"))
                    ins.then_inc(*at_pe.step(f"turned{u}"))

                def values(u):
                    j, qt, r = u // 4, u // 2 % 2, u % 2
                    g = (2 * j + r) // 4
                    o = bank[4 + u // 2 % 2][:, 0:P]
                    if r == 0:
                        if u == 0:
                            pe.wait_ge(*at_vec.at("pcT7"))
                        if u >= 4:
                            pe.wait_ge(*at_vec.at(f"o{u // 2 - 2}"))
                    mm(o, vcz[0:N_CMP, g, r, :], pc_t[0:N_CMP, qt, 2 * j + r, :], r == 0, False)
                    pe.wait_ge(*at_act.at(f"pt{u}"))
                    for br in range(2):
                        for kt in range(qt + 1):
                            ins = mm(o, vz[:, (br * 2 + kt) * NG + g, r, :], pt_buf[:, u % 2, 2 * br + kt, :],
                                     False, r == 1 and br == 1 and kt == qt)
                    ins.then_inc(*at_pe.step(f"values{u}"))

                scores(0)
                scores(1)
                for i in range(8):
                    qt, q4 = i // 4, i % 4
                    if q4 == 0:
                        pe.wait_ge(*at_vec.at(f"pc{qt}"))
                    if i >= 2:
                        pe.wait_ge(*at_vec.at(f"pcT{i - 2}"))
                    for m in range(4):
                        ins = nc.tensor.transpose(quad(2 + i % 2)[0:N_CMP, m, :], pc[:, qt, 4 * q4 + m, :], K("ident"))
                    ins.then_inc(*at_pe.step(f"cmp_turned{i}"))
                pe.wait_ge(*at_vec.at("pcT7"))
                for u in range(32):
                    if u + 2 < 32:
                        scores(u + 2)
                    turn(u)
                    values(u)

            def mix(st):
                linear(st, 12, wait_h(st))
                token_major(st, 2, TILE_COLS, 12)
                linear(st, 2, None, 14)
                l, M, R = st.layer, ML[st.layer], RW[st.layer]
                pe.wait_ge(*M.vec.at("g_row"))
                for c in range(2):
                    ins = nc.tensor.transpose(bank[7][:, c * P:(c + 1) * P], rows[:, 0, c * P:(c + 1) * P], K("ident"))
                ins.then_inc(*M.pe.step("g_turned"))
                pe.wait_ge(*M.vec.at("M_row"))
                for hd in range(MH):
                    ins = mm(half(hd // 2, hd % 2), K("ident")[:, 64 + hd:65 + hd].to_broadcast([P, P]), rows[:, 1, :], True, True)
                ins.then_inc(*M.pe.step("M_spread"))
                pe.wait_ge(*M.act.at("em_row"))
                for hd in range(MH):
                    ins = mm(half(2 + hd // 2, hd % 2), K("ident")[:, 64 + hd:65 + hd].to_broadcast([P, P]), rows[:, 2, :], True, True)
                ins.then_inc(*M.pe.step("em_spread"))
                pe.wait_ge(*M.act.at("qk"))
                pe.wait_ge(*M.vec.at("g_col"))
                def m_scores(i):
                    hd, kt = i // 2, i % 2
                    if i >= 2:
                        pe.wait_ge(*M.vec.at(f"sw{i - 2}"))
                    mm(bank[6 + i % 2][:, kt * P:TOK], qk[:, 4 + hd, kt * P:(kt + 1) * P], qk[:, hd, kt * P:TOK],
                       True, True).then_inc(*M.pe.step(f"scores{i}"))

                m_scores(0)
                m_scores(1)
                for i in range(8):
                    if i + 2 < 8:
                        m_scores(i + 2)
                    hd = i // 2
                    if i % 2 == 0:
                        continue
                    pe.wait_ge(*M.vec.at(f"masked{i}"))
                    if hd >= 2:
                        pe.wait_ge(*M.vec.at(f"h{hd - 2}"))
                    b = FRONT[hd % 2]
                    for kt in range(2):
                        mm(bank[b][:, kt * P:TOK], v_tok[:, kt, hd * P:(hd + 1) * P], sw[:, 2 * hd + kt, kt * P:TOK],
                           kt == 0, kt == 1)
                    for kt in range(2):
                        ins = mm(bank[b][:, TOK + kt * P:2 * TOK], K("ones"), sw[:, 2 * hd + kt, kt * P:TOK],
                                 kt == 0, kt == 1)
                    ins.then_inc(*M.pe.step(f"sums{hd}"))
                keep_clock(7, 6)
                pe.wait_ge(*M.vec.at("h3"))
                for hd in range(MH):
                    ins = mm(half(hd // 2, hd % 2), K("ones"), h_b[:, hd, :], True, True)
                ins.then_inc(*M.pe.step("mean"))
                keep_clock(7, 10)
                pe.wait_ge(*M.act.at("squares"))
                for hd in range(MH):
                    ins = mm(half(2 + hd // 2, hd % 2), K("ones"), sw[:, hd, :], True, True)
                ins.then_inc(*M.pe.step("var"))

                keep_clock(7, 12)
                n = st.tile + 16
                tile_wait(n)
                lora = ring[n % RING][:, :].rearrange("p (s c) -> p s c", s=4)
                pe.wait_ge(*M.act.at("root1"))
                pe.wait_ge(*R.act.at("lora_in"))
                pe.wait_ge(*R.vec.at("lora_tail"))

                def low(b, slot, rhs, name):
                    for j in range(4):
                        ins = mm(half(b + j // 2, j % 2), lora[:, slot, j * P:(j + 1) * P], rhs, True, True)
                    return ins.then_inc(*R.pe.step(name))

                low(0, 0, lora_in[:, 0, :], "w")
                low(2, 1, zp[:, 12, PAD:ZW], "a")
                for j in range(4):
                    mm(half(4 + j // 2, j % 2), lora[:, 2, j * P:(j + 1) * P], lora_in[:, 1, :], True, False)
                    ins = mm(half(4 + j // 2, j % 2), lora[:, 3, j * P:(j + 1) * P], lora_in[:, 2, :], False, True)
                if l == 1:
                    ins.then_inc(*R.pe.step("g"))
                    for j in range(4):
                        ins = mm(half(6 + j // 2, j % 2), lora[:, 3, j * P:(j + 1) * P], lora_in[:, 3, :], True, True)
                ins.then_inc(halves_left, 2)
                if l == 0:
                    keep_clock(7, 16)
                pe.wait_ge(*R.act.at("sig_w"))
                pe.wait_ge(*R.act.at("kk_sq"))
                for j in range(4):
                    ins = mm(half(j // 2, j % 2), K("blk"), e2[:, j, :], True, True)
                ins.then_inc(*R.pe.step("kk_norm"))
                pe.wait_ge(*R.act.at("a"))
                pe.wait_ge(*R.vec.at("rk3"))
                for j in range(4):
                    ins = mm(half(2 + j // 2, j % 2), K("blk"), e8[:, j, :], True, True)
                ins.then_inc(*R.pe.step("rk_sum"))
                pe.wait_ge(*R.act.at("g_taken1"))
                if l == 1:
                    pe.wait_ge(*R.act.at("vg"))
                keep_clock(7, 55)
                for T in range(2):
                    ts = slice(T * P, (T + 1) * P)
                    if T == 0:
                        pe.wait_ge(*R.vec.at("khat"))
                        pe.wait_ge(*R.vec.at("bhat"))
                        pe.wait_ge(*R.vec.at("v_mixed"))
                        pe.wait_ge(*R.vec.at("kk_rstd1"))
                        pe.wait_ge(*R.vec.at("bonus1"))
                    else:
                        pe.wait_ge(*R.vec.at("y1"))
                    for s, (src, b) in enumerate(((e5, 4), (e6, 5), (None, 6))):
                        for j in range(4):
                            a = zp[:, 8 + j, PAD + T * P:PAD + (T + 1) * P] if src is None else (
                                src[:, j, ts] if T == 0 else keep[s][:, j, :])
                            ins = nc.tensor.transpose(quad(b)[:, j, :], a, K("ident"))
                        ins.then_inc(*R.pe.step(f"turned{s}_{T}"))
                    pe.wait_ge(*R.vec.at("k_z1"))
                    pe.wait_ge(*R.vec.at("k_z1"))
                    pe.wait_ge(*R.act.at("b_z1"))
                    pe.wait_ge(*R.vec.at("kap"))
                    pe.wait_ge(*R.vec.at("rho"))

                    def pairs(name, b, left, right):
                        for hf in range(2):
                            for m in range(4):
                                hd = 4 * hf + m
                                ins = mm(quad(b + hf)[:, m, :], left(hd), right(hd), True, True)
                            ins.then_inc(*R.pe.step(f"{name}{hf}_{T}"))

                    bzs = lambda hd: b_z[:, hd // 2, hd % 2, ts]
                    kzs = lambda hd: k_z[:, hd // 2, hd % 2, ts]
                    kaps = lambda hd: kap[:, hd // 2, ts]
                    rhos = lambda hd: rho[:, hd // 2, ts]
                    pairs("A_t", 0, bzs, kaps)
                    pairs("A", 2, kaps, bzs)
                    pe.wait_ge(*R.vec.at(f"ktok1_{T}"))
                    pe.wait_ge(*R.act.at(f"btok1_{T}"))
                    pairs("A_kk", 4, kzs, kaps)
                    pe.wait_ge(*R.act.at(f"v_z1_{T}"))
                    pairs("A_rk", 6, kzs, rhos)
                    pe.wait_ge(*R.vec.at(f"A_t1_{T}"))
                    pairs("A_rb", 0, bzs, rhos)
                    for lv in range(1, LEVELS):
                        for hf in range(2):
                            if lv == 1:
                                pe.wait_ge(*R.vec.at(f"X0_{hf}_{T}"))
                                pe.wait_ge(*R.vec.at(f"A_kk{hf}_{T}"))
                            else:
                                pe.wait_ge(*R.vec.at(f"X{lv - 1}_{hf}_{T}"))
                            pe.wait_ge(*R.pool.at(f"A_lv{lv}_{T}"))
                            for m in range(4):
                                ins = mm(quad(4 + hf)[:, m, :], A_lv[lv % 2][:, 4 * hf + m, :], X[:, 4 * hf + m, :],
                                         True, True)
                            ins.then_inc(*R.pe.step(f"U{lv}_{hf}_{T}"))
                        for hf in range(2):
                            pe.wait_ge(*R.act.at(f"U{lv}_{hf}_{T}"))
                            if lv == 1:
                                pe.wait_ge(*R.vec.at(f"X_t0_{hf}_{T}"))
                                pe.wait_ge(*R.vec.at(f"A_rk{hf}_{T}"))
                                pe.wait_ge(*R.vec.at(f"A_rb{hf}_{T}"))
                            else:
                                pe.wait_ge(*R.vec.at(f"X_t{lv - 1}_{hf}_{T}"))
                            if lv < LEVELS - 1:
                                for m in range(4):
                                    ins = mm(quad(2 + hf)[:, m, :], X_t[:, 4 * hf + m, :], U[:, 4 * hf + m, :], True, True)
                                ins.then_inc(*R.pe.step(f"D{lv}_{hf}_{T}"))
                            for m in range(4):
                                ins = mm(quad(6 + hf)[:, m, :], U[:, 4 * hf + m, :], X_t[:, 4 * hf + m, :], True, True)
                            ins.then_inc(*R.pe.step(f"D_t{lv}_{hf}_{T}"))
                    for cl in range(2):
                        c = 2 * T + cl
                        cs = slice(T * P + cl * CH, T * P + (cl + 1) * CH)
                        if c % 2:
                            keep_clock(7, 4)
                        pe.wait_ge(*R.vec.at(f"S{c}_3"))
                        if cl == 0:
                            pe.wait_ge(*R.vec.at(f"X_t{LEVELS - 1}_1_{T}"))
                            pe.wait_ge(*R.vec.at(f"A_rb1_{T}"))
                        for j in range(4):
                            mm(bank[0][:, j * P:(j + 1) * P], kap[:, j, ts], S[:, j, :], True, False)
                            for r in range(2):
                                ins = mm(bank[0][:, j * P + r * CH:j * P + (r + 1) * CH], A_kk[:, 2 * j + r, :],
                                         v_z[:, j, r, r * CH:(r + 1) * CH], False, r == 1)
                        ins.then_inc(*R.pe.step(f"G{c}"))
                        if c:
                            pe.wait_ge(*R.vec.at(f"y{c - 1}"))
                        for j in range(4):
                            yb = bank[3][:, j * CH:(j + 1) * CH]
                            mm(yb, S[:, j, :], rho[:, j, cs], j == 0, False, True)
                            for r in range(2):
                                mm(yb, v_z[:, j, r, :], A_rk[:, 2 * j + r, cl * CH:(cl + 1) * CH], False, False, True)
                        pe.wait_ge(*R.vec.at(f"G{c}"))
                        for hd in range(RH):
                            ins = mm(bank[1][:, hd * CH:(hd + 1) * CH], X_t[:, hd, :], gs[:, hd * CH:(hd + 1) * CH],
                                     True, True)
                        ins.then_inc(*R.pe.step(f"SA{c}"))
                        keep_clock(7, 4)
                        pe.wait_ge(*R.vec.at(f"SA{c}_1"))
                        for hd in range(RH):
                            j, r = hd // 2, hd % 2
                            o = bank[2][:, hd * CH:(hd + 1) * CH]
                            mm(o, ktok[:, cl, j * P:(j + 1) * P], v_z[:, j, r, r * CH:(r + 1) * CH], True, False)
                            ins = mm(o, btok[:, cl, j * P:(j + 1) * P], sa_z[:, j, r, r * CH:(r + 1) * CH], False, True)
                        ins.then_inc(*R.pe.step(f"dS{c}"))
                        for j in range(4):
                            for r in range(2):
                                ins = mm(bank[3][:, j * CH:(j + 1) * CH], sa_z[:, j, r, :],
                                         A_rb[:, 2 * j + r, cl * CH:(cl + 1) * CH], False, j == 3 and r == 1, True)
                        ins.then_inc(*R.pe.step(f"y{c}"))
                keep_clock(7, 4)
                pe.wait_ge(*R.vec.at("y3"))
                for j in range(4):
                    ins = mm(half(j // 2, j % 2), K("blk"), y_a[:, j, :], True, True)
                ins.then_inc(*R.pe.step("gn_mean"))
                keep_clock(7, 10)
                pe.wait_ge(*R.act.at("gn_squares"))
                pe.wait_ge(*R.vec.at("S4_3"))
                for j in range(4):
                    ins = mm(half(2 + j // 2, j % 2), K("blk"), e2[:, j, :], True, True)
                ins.then_inc(*R.pe.step("gn_var"))

            def branch(st):
                for t in range(8):
                    f = st.front + t
                    q = st.half + t
                    front_wait(f)
                    half_wait(q)
                    w = q % SLOTS
                    for br in range(2):
                        for k in range(4 * br, 4 * br + 4):
                            if t == 0:
                                pe.wait_ge(h_ready, 8 * st.pre + k + 1)
                            ins = mm3(half(FRONT[f % 2], br), whi3[w][:, k, :], wlo3[w][:, k, :], hi3[:, k, :],
                                      lo3[:, k, :], k % 4 == 0, k % 4 == 3)
                    ins.then_inc(half_used, 1)

            for st in PLAN:
                if st.kind == "ada":
                    ada(st)
                elif st.kind in ("norm", "post", "final"):
                    meansq(st)
                elif st.kind in ("ffn", "ffn_ada"):
                    ffn(st)
                elif st.kind == "conv":
                    linear(st, 12, wait_h(st))
                elif st.kind == "kv":
                    kv(st)
                elif st.kind == "nsa":
                    nsa(st)
                elif st.kind == "lin4":
                    linear(st, 4, lambda k: pe.wait_ge(h_ready, 8 * st.pre + k + 1))
                elif st.kind == "mix":
                    mix(st)
                elif st.kind == "gates":
                    linear(st, 8)
                elif st.kind == "branch":
                    branch(st)

        @block.scalar
        def _(act):
            def fn(out, in_, f, bias=0.0, scale=1.0):
                return nc.scalar.activation(out, in_, f, bias=bias, scale=scale)

            at_half = [0, 0]

            def hi(q, turn=0, landed=16):
                n, c, _ = SPLIT[q]
                act.wait_ge(tile_landed[n % RING], turn * landed + (n // RING + 1) * 16)
                if not (isinstance(turn, int) and q < SLOTS):
                    act.wait_ge(half_used, turn * 6 + (q + 1 - SLOTS))
                fn(w_hi[q % SLOTS][:, :], ring[n % RING][:, c * HALF:(c + 1) * HALF], ACT.Copy).then_inc(hi_ready, 1)

            def advance(to):
                while at_half[0] <= to and at_half[0] < N_HALVES and SPLIT[at_half[0]][2] == at_half[1]:
                    hi(at_half[0])
                    at_half[0] += 1

            def open_run():
                if at_half[0] < N_HALVES and SPLIT[at_half[0]][2] != at_half[1]:
                    act.wait_ge(halves_left, 2 * SPLIT[at_half[0]][0])
                    at_half[1] = SPLIT[at_half[0]][2]

            def squares(st, src, ready):
                for p in range(4):
                    ready(p)
                    if p == 0 and st.norm:
                        act.wait_ge(meansq_ready, st.norm)
                    fn(sq[:, 2 * p * TOK:(2 * p + 2) * TOK], src[:, 2 * p * TOK:(2 * p + 2) * TOK], ACT.Square
                       ).then_inc(squares_ready, 1)
                open_run()
                advance(st.half + 2)
                act.wait_ge(meansq_ready, st.norm + 1)
                fn(rstd[:, :], bank[LOW][:, 0:TOK], ACT.Sqrt, bias=RMS_EPS, scale=1.0 / D).then_inc(root_ready, 1)

            def x_wait(st):
                def wait(p):
                    if st.x_from == "resid":
                        act.wait_ge(front_taken, st.front - 4 + p + 1)
                    elif st.x_from == "half":
                        act.wait_ge(x_ready, st.update - 4 + p + 1)
                    elif st.x_from == "post" and p < 2:
                        act.wait_ge(x_pool_ready, 2 * st.post - 2 + p + 1)
                    elif st.x_from == "post":
                        act.wait_ge(x_ready, st.update - 4 + p + 1)
                    else:
                        act.wait_ge(x_landed, 16)
                return wait

            def norm(st):
                squares(st, x, x_wait(st))
                shift = None if st.mod is None else (mod_col(*st.mod, 0) if st.mod != "kv" else 144)
                for j in range(KC):
                    act.wait_ge(h_scaled, 8 * st.scaled + j + 1)
                    if shift is None:
                        ins = fn(hi3[:, j, :], y3[:, j, :], ACT.Copy)
                    else:
                        ins = fn(hi3[:, j, :], y3[:, j, :], ACT.Identity, bias=mods[:, shift + j:shift + j + 1])
                    ins.then_inc(h_hi_ready, 1)

            def parts(st, src, wait):
                for j in range(KC):
                    wait(j)
                    fn(hi3[:, j, :], src(j), ACT.Copy).then_inc(h_hi_ready, 1)

            def ffn(st):
                q = st.half

                def gate(hh, j, turn=0):
                    f = st.front + hh
                    act.wait_ge(half_used, turn * 6 + (q + j + 1))
                    if not (isinstance(turn, int) and f < 2):
                        act.wait_ge(front_taken, turn * 2 + (f - 1))
                    fn(silu_t[:, (f % 2) * TOK:(f % 2 + 1) * TOK], half(FRONT[f % 2], 0), ACT.Silu
                       ).then_inc(silu_ready, 1)

                landed = 32 if st.kind == "ffn_ada" else 16
                advance(q + 3)
                gate(0, 1)
                advance(q + 5)
                with act.Fori(0, FFN_STEPS - 1) as turn:
                    gate(1, 3, turn)
                    hi(q + 6, turn, landed)
                    hi(q + 7, turn, landed)
                    gate(2, 5, turn)
                    for i in range(8, 12):
                        hi(q + i, turn, landed)
                at_half[0] = q + 6 * FFN_STEPS
                gate(HALVES - 1, 6 * FFN_STEPS - 3)
                advance(q + 6 * FFN_STEPS + 0)

            def nsa(st):
                advance(st.half + 9)
                act.wait_ge(half_used, st.half + 10)
                act.wait_ge(front_taken, st.front + 4)
                fn(gate_tok[:, :, :], pair(FRONT[(st.front + 4) % 2])[:, :, 0:3 * NH], ACT.Sigmoid
                   ).then_inc(front_taken, 1)
                for qt in range(2):
                    act.wait_ge(*at_vec.at(f"cmp_centred{qt}"))
                    fn(pc[:, qt, :, :], pc[:, qt, :, :], ACT.Exp).then_inc(*at_act.step(f"cmp_exp{qt}"))

                def exps(u):
                    nk = (u // 2 % 2 + 1) * P
                    act.wait_ge(*at_vec.at(f"max{u}"))
                    for br in range(2):
                        nc.scalar.activation(s_buf[u % 3][:, br, 0:nk], s_buf[u % 3][:, br, 0:nk], ACT.Exp,
                                             bias=at_small[:, 2 * (u % 2) + br:2 * (u % 2) + br + 1], scale=1.0,
                                             accum_out=at_small[:, 8 + 2 * (u % 2) + br:8 + 2 * (u % 2) + br + 1]
                                             ).then_inc(*at_act.step(f"exp{u}_{br}"))

                def copy(u):
                    qt = u // 2 % 2
                    act.wait_ge(*at_pe.at(f"turned{u}"))
                    if u >= 2:
                        act.wait_ge(*at_pe.at(f"values{u - 2}"))
                    a = quad(2 + u % 2).rearrange("p (b k) t -> p b k t", b=2)[:, :, 0:qt + 1, :]
                    o = pt_buf[:, u % 2].rearrange("p (b k) t -> p b k t", b=2)[:, :, 0:qt + 1, :]
                    fn(o, a, ACT.Copy).then_inc(*at_act.step(f"pt{u}"))

                exps(0)
                for v in range(32):
                    if v + 1 < 32:
                        exps(v + 1)
                    copy(v)

            def mix(st):
                l, M, R = st.layer, ML[st.layer], RW[st.layer]
                advance(st.half + 21)
                rt = row_tmp[64:68]
                act.wait_ge(*M.vec.at("minus_abs"))
                fn(rt[:, 2, :], rt[:, 2, :], ACT.Exp).then_inc(*M.act.step("exp_f"))
                act.wait_ge(*M.act.at("exp_f"))
                fn(rt[:, 2, :], rt[:, 2, :], ACT.Ln, bias=1.0).then_inc(*M.act.step("ln_f"))
                advance(st.half + 23)
                act.wait_ge(*M.vec.at("F_plus_M"))
                act.wait_ge(*M.pool.at("rows_zero"))
                fn(rows[64:68, 2, :], rt[:, 4, :], ACT.Exp, scale=-1.0).then_inc(*M.act.step("em_row"))
                advance(st.half + 31)
                act.wait_ge(*M.vec.at("conv7"))
                fn(qk[:, :, :], qk[:, :, :], ACT.Silu).then_inc(*M.act.step("qk"))
                act.wait_ge(*M.pe.at("em_spread"))
                for i in range(2):
                    ins = fn(bc_e[:, 2 * i:2 * i + 2, :], pair(2 + i), ACT.Copy)
                ins.then_inc(*M.act.step("em_copy"))
                for i in range(8):
                    kt = i % 2
                    act.wait_ge(*M.vec.at(f"gap{i}"))
                    fn(w_buf[:, i % 4, kt * P:TOK], w_buf[:, i % 4, kt * P:TOK], ACT.Exp, scale=-1.0
                       ).then_inc(*M.act.step(f"weight{i}"))
                act.wait_ge(*M.vec.at("m_o"))
                fn(m_o[:, :, :], m_o[:, :, :], ACT.Sigmoid).then_inc(*M.act.step("sig_o"))
                act.wait_ge(*M.vec.at("centred1"))
                fn(sw[:, 0:4, :], h_b[:, :, :], ACT.Square).then_inc(*M.act.step("squares"))
                act.wait_ge(*M.pe.at("var"))
                for i in range(2):
                    fn(sw[:, 2 * i:2 * i + 2, :], pair(2 + i), ACT.Sqrt, bias=ML_EPS, scale=1.0 / P).then_inc(*M.act.step(f"root{i}"))
                act.wait_ge(*R.vec.at("lora_zero"))
                fn(lora_in[:, 0, :], zp[:, 12, PAD:ZW], ACT.Tanh)
                fn(lora_in[:, 1, :], zp[:, 13, PAD:ZW], ACT.Sigmoid).then_inc(*R.act.step("lora_mid"))
                act.wait_ge(*R.vec.at("lora_tail"))
                fn(lora_in[0:32, 2, :], zp[0:32, 14, PAD:ZW], ACT.Sigmoid).then_inc(*R.act.step("lora_in"))
                for j in range(4):
                    ins = fn(e2[:, j, :], zp[:, 4 + j, PAD:ZW], ACT.Square, scale=V(f"kk{l}", j))
                ins.then_inc(*R.act.step("kk_sq"))
                act.wait_ge(*R.pe.at("w"))
                for j in range(4):
                    ins = fn(e1[:, j, :], half(j // 2, j % 2), ACT.Sigmoid, bias=V(f"w0{l}", j))
                ins.then_inc(*R.act.step("sig_w"))
                act.wait_ge(*R.pe.at("a"))
                for j in range(4):
                    ins = fn(e4[:, j, :], half(2 + j // 2, j % 2), ACT.Sigmoid, bias=V(f"a0{l}", j))
                ins.then_inc(*R.act.step("a"))
                if l == 1:
                    act.wait_ge(halves_left, 2 * (st.tile + 17))
                    for j in range(4):
                        ins = fn(e7[:, j, :], half(6 + j // 2, j % 2), ACT.Sigmoid, bias=V(f"vres{l}", j))
                    ins.then_inc(*R.act.step("vg"))
                if l == 0:
                    act.wait_ge(halves_left, 2 * (st.tile + 17))
                for i in range(2):
                    fn(g_up[:, 2 * i:2 * i + 2, :], pair(4 + i), ACT.Copy).then_inc(*R.act.step(f"g_taken{i}"))
                for i in range(2):
                    act.wait_ge(*R.vec.at(f"kk_floor{i}"))
                    fn(e2[:, 2 * i:2 * i + 2, :], e2[:, 2 * i:2 * i + 2, :], ACT.Sqrt).then_inc(*R.act.step(f"kk_root{i}"))
                act.wait_ge(*R.vec.at("L_prev"))
                fn(e6[:, :, :], e6[:, :, :], ACT.Exp).then_inc(*R.act.step("E_prev"))
                act.wait_ge(*R.vec.at("v_mixed"))
                fn(e7[:, :, :], e5[:, :, :], ACT.Exp, scale=-1.0).then_inc(*R.act.step("E_inv"))
                act.wait_ge(*R.pe.at("rk_sum"))
                fn(e8[:, :, :], e5[:, :, :], ACT.Exp).then_inc(*R.act.step("E"))
                act.wait_ge(*R.vec.at("bhat"))
                act.wait_ge(*R.pool.at("z_zero"))
                for r in range(2):
                    rows_ = slice(r * CH, (r + 1) * CH)
                    fn(b_z[rows_, :, r, :], e6[rows_, :, :], ACT.Copy).then_inc(*R.act.step(f"b_z{r}"))
                act.wait_ge(*R.pool.at("tok_zero"))
                for T in range(2):
                    act.wait_ge(*R.pe.at(f"turned1_{T}"))
                    for cl in range(2):
                        rows_ = slice(cl * CH, (cl + 1) * CH)
                        fn(btok[rows_, cl, :], bank[5][rows_, :], ACT.Copy, scale=-1.0
                           ).then_inc(*R.act.step(f"btok{cl}_{T}"))
                    act.wait_ge(*R.pe.at(f"turned2_{T}"))
                    for r in range(2):
                        fn(v_z[:, :, r, r * CH:(r + 1) * CH], quad(6)[:, :, r * CH:(r + 1) * CH], ACT.Copy
                           ).then_inc(*R.act.step(f"v_z{r}_{T}"))
                    for lv in range(1, LEVELS):
                        for hf in range(2):
                            act.wait_ge(*R.pe.at(f"U{lv}_{hf}_{T}"))
                            if lv > 1:
                                act.wait_ge(*R.pe.at(f"D_t{lv - 1}_{hf}_{T}"))
                            fn(U[:, 4 * hf:4 * hf + 4, :], quad(4 + hf), ACT.Copy
                               ).then_inc(*R.act.step(f"U{lv}_{hf}_{T}"))
                open_run()
                advance(st.half + 34)
                act.wait_ge(*R.vec.at("gn_centred1"))
                fn(e2[:, :, :], y_a[:, :, :], ACT.Square).then_inc(*R.act.step("gn_squares"))
                act.wait_ge(*R.pe.at("gn_var"))
                for i in range(2):
                    fn(e3[:, 2 * i:2 * i + 2, :], pair(2 + i), ACT.Sqrt, bias=GN_EPS, scale=1.0 / CH).then_inc(*R.act.step(f"gn_root{i}"))

            def gates(st, R):
                for t in range(8):
                    f = st.front + t
                    if t:
                        advance(st.half + 2 * t + 3)
                    else:
                        advance(st.half + 3)
                        act.wait_ge(*R.vec.at("y_a3"))
                    act.wait_ge(half_used, st.half + 2 * t + 2)
                    fn(sgate[:, 2 * t:2 * t + 2, :], pair(FRONT[f % 2]), ACT.Sigmoid).then_inc(front_taken, 1)

            act.wait_ge(vecs_landed, 16)
            fn(cond[:, :], V("c", 0, 8), ACT.Silu).then_inc(cond_ready, 1)
            for st in PLAN:
                if st.kind == "norm":
                    norm(st)
                elif st.kind == "final":
                    squares(st, x, x_wait(st))
                elif st.kind == "post":
                    if st.source == "ffn":
                        squares(st, y, lambda p: act.wait_ge(y_ready, 4 * st.ffn - 4 + p + 1))
                    else:
                        squares(st, y, lambda p: act.wait_ge(front_taken, st.front - 4 + p + 1))
                elif st.kind in ("ffn", "ffn_ada"):
                    ffn(st)
                elif st.kind == "conv":
                    advance(st.half + 25)
                elif st.kind == "lin4":
                    if st.rhs == "conv_y":
                        act.wait_ge(half_used, st.half)
                        parts(st, lambda j: conv_y[:, j, :], lambda j: act.wait_ge(*conv_vec.at(f"y{j}")))
                    elif st.rhs == "o":
                        parts(st, lambda j: o_t[:, j, :], lambda j: act.wait_ge(*at_vec.at(f"o{2 * j + 1}")))
                    else:
                        act.wait_ge(half_used, st.half)
                        parts(st, lambda j: u[:, j, :], lambda j: act.wait_ge(u_ready, 8 * st.branch - 8 + j + 1))
                    advance(st.half + 9)
                elif st.kind == "branch":
                    act.wait_ge(half_used, st.half)
                    parts(st, lambda j: (y_a, y_b)[j // 4][:, j % 4, :], lambda j: None)
                    advance(st.half + 9)
                elif st.kind == "kv":
                    advance(st.half + 19)
                    act.wait_ge(halves_left, 2 * (st.tile + 14))
                    src = bank[7][:, 0:256].rearrange("p (s c) -> p s c", s=4)[:, :, 0:NG * N_CMP]
                    fn(hid.rearrange("p a b c -> p (a b) c"), src, ACT.Gelu_apprx_tanh).then_inc(*kv_act.step("gelu"))
                elif st.kind == "nsa":
                    nsa(st)
                elif st.kind == "mix":
                    mix(st)
                elif st.kind == "gates":
                    gates(st, RW[st.layer])

        @block.gpsimd
        def _(pool):
            def modulate(a, n, turn=0, per_turn=RING):
                w = ring[n % RING][:, :].rearrange("p (k c) -> p k c", k=KC)
                pool.wait_ge(tile_landed[n % RING], turn * (16 * per_turn // RING) + (n // RING + 1) * 16)
                if a >= 3:
                    pool.wait_ge(ada_partial, turn * (3 * (ADA_DVE - 1)) + ((ADA_DVE - 1) * (a - 2) + 1))
                prod = ada_pool[:, a % 3]
                by_row = cond[:, 0:ADA_POOL].unsqueeze(2).to_broadcast([P, ADA_POOL, TILE_COLS])
                nc.gpsimd.tensor_tensor(prod, w[:, 0:ADA_POOL, :], by_row, ALU.mult).then_inc(ada_pool_partial, 1)
                for k in range(1, ADA_POOL):
                    pool.wait_ge(ada_pool_partial, turn * (3 * ADA_POOL) + (ADA_POOL * a + k))
                    nc.gpsimd.tensor_tensor(prod[:, 0, :], prod[:, 0, :], prod[:, k, :], ALU.add
                                            ).then_inc(ada_pool_partial, 1)

            def ada(st):
                pool.wait_ge(cond_ready, 1)
                for a in range(3):
                    modulate(a, a)
                with pool.Fori(0, ADA_FIRST // 3 - 1) as turn:
                    for a in range(3, 6):
                        modulate(a, a, turn)
                for a in range(ADA_FIRST // 3 * 3, ADA_FIRST):
                    modulate(a, a)

            def ffn(st):
                q = st.half
                pool.wait_ge(h_ready, 8 * st.pre)
                modulate(st.ada, SPLIT[q + 3][0] + 1)
                modulate(st.ada + 1, SPLIT[q + 5][0] + 1)
                with pool.Fori(0, FFN_STEPS - 1) as turn:
                    for i, behind in ((2, 7), (3, 9), (4, 11)):
                        modulate(st.ada + i, SPLIT[q + behind][0] + 1, turn, 6)

            for st in PLAN:
                if st.kind == "ada":
                    ada(st)
                elif st.kind == "ffn_ada":
                    ffn(st)
                if st.kind == "post":
                    for p in range(2):
                        pool.wait_ge(delta_ready, 8 * st.post + 2 * p + 2)
                        c = slice(2 * p * TOK, (2 * p + 2) * TOK)
                        nc.gpsimd.tensor_tensor(x[:, c], x[:, c], y[:, c], ALU.add).then_inc(x_pool_ready, 1)
                elif st.kind == "conv":
                    nc.gpsimd.memset(conv_v[:, :, 0:PAD], 0.0).then_inc(*conv_pool.step("pad"))
                elif st.kind == "kv":
                    nc.gpsimd.memset(carve(0, 8192), 0.0).then_inc(*kv_pool.step("zero"))
                    nc.gpsimd.memset(carve(10352, 1144), 0.0).then_inc(*kv_pool.step("zero_cmp"))
                elif st.kind == "mix":
                    l, M, R = st.layer, ML[st.layer], RW[st.layer]
                    if l == 1:
                        pool.wait_ge(u_ready, 8)
                    nc.gpsimd.memset(zp[:, :, 0:PAD], 0.0)
                    nc.gpsimd.memset(mqk[:, :, 0:PAD], 0.0).then_inc(*M.pool.step("pads"))
                    pool.wait_ge(*M.vec.at("shifted0"))
                    nc.gpsimd.memset(rows[:, :, :], 0.0).then_inc(*M.pool.step("rows_zero"))
                    pool.wait_ge(*M.vec.at("y_b"))
                    nc.gpsimd.memset(k_z[:, :, :, :], 0.0)
                    nc.gpsimd.memset(b_z[:, :, :, :], 0.0).then_inc(*R.pool.step("z_zero"))
                    nc.gpsimd.memset(y[:, :], 0.0)
                    nc.gpsimd.memset(sq[:, :], 0.0)
                    nc.gpsimd.memset(S[:, :, :], 0.0).then_inc(*R.pool.step("tok_zero"))
                    for T in range(2):
                        for lv in range(1, LEVELS):
                            if lv <= 2:
                                pool.wait_ge(*R.vec.at(f"A_t1_{T}"))
                                if T == 0:
                                    pool.wait_ge(*R.vec.at("keep1"))
                                    pool.wait_ge(*R.act.at("E"))
                                    pool.wait_ge(*R.vec.at("ktok1_0"))
                            if lv > 2:
                                pool.wait_ge(*R.pe.at(f"U{lv - 2}_1_{T}"))
                            nc.gpsimd.tensor_tensor(A_lv[lv % 2][:, :, :], A_t[:, :, :],
                                                    K(f"level{lv}").unsqueeze(1).to_broadcast([P, RH, P]), ALU.mult
                                                    ).then_inc(*R.pool.step(f"A_lv{lv}_{T}"))

        @block.vector
        def _(dve):
            tt, ts_, stt = nc.vector.tensor_tensor, nc.vector.tensor_scalar, nc.vector.scalar_tensor_tensor
            cp = nc.vector.tensor_copy

            at_half = [0, SPLIT[0][2]]

            def lo(q, turn=0):
                n, c, _ = SPLIT[q]
                dve.wait_ge(hi_ready, turn * 6 + (q + 1))
                tt(w_lo[q % SLOTS][:, :], ring[n % RING][:, c * HALF:(c + 1) * HALF], w_hi[q % SLOTS][:, :].bitcast(F32),
                   ALU.subtract).then_inc(halves_left, 1)

            def advance(to):
                while at_half[0] <= to and at_half[0] < N_HALVES and SPLIT[at_half[0]][2] == at_half[1]:
                    lo(at_half[0])
                    at_half[0] += 1

            def modulate(a, n, turn=0, per_turn=RING):
                acc = ada_acc[:, a % 3, :]
                w = ring[n % RING][:, :].rearrange("p (k c) -> p k c", k=KC)
                dve.wait_ge(tile_landed[n % RING], turn * (16 * per_turn // RING) + (n // RING + 1) * 16)
                if a >= 3:
                    dve.wait_ge(ada_summed, turn * 3 + (a - 2))
                for k in range(ADA_DVE):
                    if k:
                        dve.wait_ge(ada_partial, turn * (3 * (ADA_DVE - 1)) + ((ADA_DVE - 1) * a + k))
                    chunk = ADA_POOL + k
                    if k == 0:
                        ins = ts_(acc, w[:, chunk, :], cond[:, chunk:chunk + 1], None, ALU.mult)
                    elif k < ADA_DVE - 1:
                        ins = stt(out=acc, in0=w[:, chunk, :], scalar=cond[:, chunk:chunk + 1], in1=acc, op0=ALU.mult,
                                  op1=ALU.add)
                    else:
                        dve.wait_ge(ada_pool_partial, turn * (3 * ADA_POOL) + ADA_POOL * (a + 1))
                        ins = tt(acc, acc, ada_pool[:, a % 3, 0, :], ALU.add)
                    if k < ADA_DVE - 1:
                        ins.then_inc(ada_partial, 1)
                ins.then_inc(halves_left, 2)

            def ada(st):
                dve.wait_ge(cond_ready, 1)
                for a in range(3):
                    modulate(a, a)
                with dve.Fori(0, ADA_FIRST // 3 - 1) as turn:
                    for a in range(3, 6):
                        modulate(a, a, turn)
                for a in range(ADA_FIRST // 3 * 3, ADA_FIRST):
                    modulate(a, a)
                mods_out(0)

            def open_run():
                if at_half[0] < N_HALVES:
                    at_half[1] = SPLIT[at_half[0]][2]

            def norm(st, out, ready, gain, src, shift=None):
                fold(st)
                open_run()
                advance(st.half + 2)
                dve.wait_ge(root_ready, st.norm + 1)
                nc.vector.reciprocal(rstd[:, :], rstd[:, :]).then_inc(rstd_ready, 1)
                dve.wait_ge(rstd_ready, st.norm + 1)

                def scaled(j):
                    stt(out=out[:, j, :], in0=src[:, j, :], scalar=gain(j), in1=rstd[:, :], op0=ALU.mult,
                        op1=ALU.mult).then_inc(ready, 1)

                if ready is not h_scaled:
                    for j in range(KC):
                        scaled(j)
                        if st.kind == "post" and j in (5, 7):
                            dve.wait_ge(delta_ready, 8 * st.post + j + 1)
                            xp = x3[:, j - 1:j + 1, :]
                            tt(xp, xp, y3[:, j - 1:j + 1, :], ALU.add).then_inc(x_ready, 1)
                    return
                for j in range(KC + 2):
                    if j < KC:
                        scaled(j)
                    if j >= 2:
                        dve.wait_ge(h_hi_ready, 8 * st.pre + j - 1)
                        stt(out=lo3[:, j - 2, :], in0=out[:, j - 2, :], scalar=0.0 if shift is None else shift(j - 2),
                            in1=hi3[:, j - 2, :].bitcast(F32), op0=ALU.add, op1=ALU.subtract).then_inc(h_ready, 1)

            def parts(st, src, first=0, last=KC):
                for j in range(first, last):
                    dve.wait_ge(h_hi_ready, 8 * st.pre + j + 1)
                    tt(lo3[:, j, :], src(j), hi3[:, j, :].bitcast(F32), ALU.subtract).then_inc(h_ready, 1)

            def take(st, t, out, n=2):
                f = st.front + t
                advance(st.half + 2 * t + 3)
                dve.wait_ge(half_used, st.half + 2 * t + 2)
                cp(out, pair(FRONT[f % 2])[:, 0:n, :]).then_inc(front_taken, 1)

            def ffn(st):
                q = st.half

                def gated(hh, turn=0, slot_free=None):
                    f, h = st.front + hh, HALVES * st.ffn + hh
                    a = slice(hh % 2 * TOK, (hh % 2 + 1) * TOK)
                    dve.wait_ge(silu_ready, turn * 2 + (h + 1))
                    tt(act_t[:, a], silu_t[:, (f % 2) * TOK:(f % 2 + 1) * TOK], half(FRONT[f % 2], 1), ALU.mult
                       ).then_inc(front_taken, 1)
                    if slot_free is not None:
                        dve.wait_ge(half_used, turn * 6 + slot_free)
                    dve.wait_ge(front_taken, turn * 2 + (f + 1))
                    cp(act_hi[:, a], act_t[:, a]).then_inc(hidden_hi, 1)
                    dve.wait_ge(hidden_hi, turn * 2 + (h + 1))
                    tt(act_lo[:, a], act_t[:, a], act_hi[:, a].bitcast(F32), ALU.subtract).then_inc(hidden_ready, 1)

                with_ada = st.kind == "ffn_ada"

                def rider(q_, i, turn=0):
                    if with_ada:
                        modulate(st.ada + i, SPLIT[q_][0] + 1, turn, 6)

                advance(q + 3)
                rider(q + 3, 0)
                gated(0)
                advance(q + 5)
                rider(q + 5, 1)
                with dve.Fori(0, FFN_STEPS - 1) as turn:
                    gated(1, turn, q + 2)
                    lo(q + 6, turn)
                    lo(q + 7, turn)
                    rider(q + 7, 2, turn)
                    lo(q + 8, turn)
                    gated(2, turn, q + 7)
                    lo(q + 9, turn)
                    rider(q + 9, 3, turn)
                    lo(q + 10, turn)
                    lo(q + 11, turn)
                    rider(q + 11, 4, turn)
                at_half[0] = q + 6 * FFN_STEPS
                gated(HALVES - 1, 0, q + 6 * FFN_STEPS - 4)
                advance(q + 6 * FFN_STEPS + 0)

            def bank_wait(st, p):
                if p < 3:
                    dve.wait_ge(y_sums, 3 * st.ffn - 3 + p + 1)
                else:
                    dve.wait_ge(half_used, st.half)

            def ffn_out(st):
                for p in range(4):
                    bank_wait(st, p)
                    cp(y3[:, 2 * p:2 * p + 2, :], pair(Y_BANK + p)).then_inc(y_ready, 1)

            def half_add(st):
                for p in range(4):
                    bank_wait(st, p)
                    xp = x3[:, 2 * p:2 * p + 2, :]
                    stt(out=xp, in0=pair(Y_BANK + p), scalar=0.5, in1=xp, op0=ALU.mult, op1=ALU.add
                        ).then_inc(x_ready, 1)

            def fold(st):
                for p in range(2):
                    dve.wait_ge(squares_ready, 4 * st.norm + 2 * p + 2)
                    d = sq3[:, 4 * p:4 * p + 2, :]
                    tt(d, d, sq3[:, 4 * p + 2:4 * p + 4, :], ALU.add).then_inc(squares_folded, 1)

            def mods_out(part):
                c0, c1, tiles, norms = ((0, 24, ADA_FIRST, [0]), (24, 72, ADA_FIRST + ADA_FFN, [1, 2]),
                                          (72, MOD_COLS, ADA_FIRST + 2 * ADA_FFN, [3, 4, 5, 6]))[part]
                dve.wait_ge(ada_summed, tiles)
                tt(mods[:, c0:c1], bank[MOD_BANK][:, c0:c1], V("mod_b", c0, c1 - c0), ALU.add).then_inc(mods_taken, 1)
                dve.wait_ge(mods_taken, part + 1)
                for q in norms:
                    sc, g = (152, V("kv_norm", 0, 8)) if q == 6 else (mod_col(q // 3, q % 3, 1), V("norm_g", 16 * q, 8))
                    ins = stt(out=pre_gain[:, 8 * q:8 * q + 8], in0=mods[:, sc:sc + 8], scalar=1.0, in1=g,
                              op0=ALU.add, op1=ALU.mult)
                    if q < 6:
                        gt = mod_col(q // 3, q % 3, 2)
                        ins = stt(out=post_gain[:, 8 * q:8 * q + 8], in0=mods[:, gt:gt + 8],
                                  scalar=1.0 if q % 3 == 1 else 0.5, in1=V("norm_g", 16 * q + 8, 8),
                                  op0=ALU.mult, op1=ALU.mult)
                ins.then_inc(gains_ready, 1)
                dve.wait_ge(gains_ready, part + 1)

            def conv_rows(p):
                pair_ = slice(2 * p, 2 * p + 2)
                tt(conv_v[:, pair_, PAD:ZW], conv_z[:, 8 + 2 * p:10 + 2 * p, :], conv_z[:, 16 + 2 * p:18 + 2 * p, :],
                   ALU.mult).then_inc(*conv_vec.step(f"v{p}"))
                dve.wait_ge(*conv_vec.at(f"v{p}"))
                for j in (2 * p, 2 * p + 1):
                    ts_(conv_y[:, j, :], conv_v[:, j, PAD:ZW], V("conv", 16 + j), None, ALU.mult
                        ).then_inc(*conv_vec.step(f"a{j}"))
                for s in (1, 0):
                    for j in (2 * p, 2 * p + 1):
                        dve.wait_ge(*conv_vec.at(f"a{j}" if s else f"b{j}"))
                        o = PAD - 2 + s
                        stt(out=conv_y[:, j, :], in0=conv_v[:, j, o:o + TOK], scalar=V("conv", 8 * s + j),
                            in1=conv_y[:, j, :], op0=ALU.mult, op1=ALU.add
                            ).then_inc(*conv_vec.step(f"b{j}" if s else f"c{j}"))
                dve.wait_ge(*conv_vec.at(f"c{2 * p + 1}"))
                for j in (2 * p, 2 * p + 1):
                    tt(conv_y[:, j, :], conv_y[:, j, :], conv_z[:, j, :], ALU.mult).then_inc(*conv_vec.step(f"y{j}"))

            def conv(st):
                dve.wait_ge(*conv_pool.at("pad"))
                for t in range(12):
                    p, g = t // 3, t % 3
                    take(st, t, conv_z[:, 8 * g + 2 * p:8 * g + 2 * p + 2, :])
                    if g == 2 and p < 3:
                        dve.wait_ge(front_taken, st.front + t + 1)
                        conv_rows(p)

            def kv(st):
                for t in range(4):
                    f, s = st.front + t, t // 2
                    advance(st.half + 2 * t + 3)
                    dve.wait_ge(half_used, st.half + 2 * t + 2)
                    for gi in range(2):
                        g = 2 * (t % 2) + gi
                        for r in range(2):
                            rows_ = slice(r * DH, (r + 1) * DH)
                            src = half(FRONT[f % 2], gi).rearrange("p (m b r) -> p r b m", b=8, r=2)
                            for a in range(2):
                                kc = slice(8 * a, 8 * a + 8)
                                a0 = VEC["pos"][0] + 16 * s + 8 * a
                                ins = tt(blocks[rows_, s, kc, g * N_CMP:(g + 1) * N_CMP],
                                         src[rows_, r, :, a:a + N_CMP],
                                         vecs[rows_, a0:a0 + 8].unsqueeze(2).to_broadcast([DH, 8, N_CMP]), ALU.add)
                    ins.then_inc(front_taken, 1)
                dve.wait_ge(front_taken, st.front + 4)
                cp(small[:, 0:1], V("c")).then_inc(*kv_vec.step("blocks"))
                dve.wait_ge(*kv_pool.at("zero"))
                for t in range(4):
                    f, br = st.front + 4 + t, t // 2
                    advance(st.half + 2 * (4 + t) + 3)
                    dve.wait_ge(half_used, st.half + 2 * (4 + t) + 2)
                    for r in range(2):
                        rows_ = slice(r * DH, (r + 1) * DH)
                        g = 2 * (t % 2)
                        ins = cp(kz[rows_, br, g:g + 2, r, :], pair(FRONT[f % 2])[rows_, :, :])
                    ins.then_inc(front_taken, 1)
                for br in range(2):
                    f = st.front + 8 + br
                    advance(st.half + 2 * (8 + br) + 3)
                    dve.wait_ge(half_used, st.half + 2 * (8 + br) + 2)
                    for c in range(2):
                        src = half(FRONT[f % 2], c).rearrange("p (g d) -> p g d", g=NG)
                        for r in range(2):
                            i = (br * 2 + c) * NG
                            ins = cp(vz[:, i:i + NG, r, r * DH:(r + 1) * DH], src)
                    ins.then_inc(front_taken, 1)
                dve.wait_ge(*kv_pool.at("zero_cmp"))
                dve.wait_ge(halves_left, 2 * (st.tile + 15))
                for r in range(2):
                    rows_ = slice(r * DH, (r + 1) * DH)
                    cp(kcz[rows_, :, r, :], bank[7][rows_, 0:NG * N_CMP].rearrange("p (g n) -> p g n", g=NG)
                       ).then_inc(*kv_vec.step(f"kcz{r}"))
                for r in range(2):
                    cp(vcz[0:N_CMP, :, r, r * DH:(r + 1) * DH],
                       bank[7][0:N_CMP, 64:64 + NG * DH].rearrange("p (g n) -> p g n", g=NG)
                       ).then_inc(*kv_vec.step(f"vcz{r}"))

            def nsa(st):
                for t in range(4):
                    f = st.front + t
                    advance(st.half + 2 * t + 3)
                    dve.wait_ge(half_used, st.half + 2 * t + 2)
                    ts_(q_t[:, 2 * t:2 * t + 2, :], pair(FRONT[f % 2]), DH ** -0.5, None, ALU.mult
                        ).then_inc(front_taken, 1)
                dve.wait_ge(front_taken, st.front + 4)
                cp(small[:, 1:2], q_t[:, 7, 0:1]).then_inc(*at_vec.step("q3"))
                dve.wait_ge(front_taken, st.front + 5)
                for qt in range(2):
                    p = pc[:, qt, :, :]
                    dist = K("cmp_dist")[:, qt * N_CMP:(qt + 1) * N_CMP]
                    mask = K("cmp_mask").rearrange("p (q n) -> p q n", q=2)[:, qt:qt + 1, :].to_broadcast([P, NH, N_CMP])
                    src = bank[6 + qt][:, 0:256].rearrange("p (h n) -> p h n", h=NH)[:, :, 0:N_CMP]
                    m = at_small[:, 16 + 64 * qt:32 + 64 * qt]
                    z = at_small[:, 32 + 64 * qt:48 + 64 * qt]
                    dve.wait_ge(*at_pe.at(f"cmp_scores{qt}"))
                    for hd in range(NH):
                        ins = stt(out=p[:, hd, :], in0=dist, scalar=-slope(hd), in1=src[:, hd, :], op0=ALU.mult,
                                  op1=ALU.add)
                    ins.then_inc(*at_vec.step(f"cmp_biased{qt}"))
                    dve.wait_ge(*at_vec.at(f"cmp_biased{qt}"))
                    nc.vector.tensor_reduce(m, p, AX_X, ALU.max).then_inc(*at_vec.step(f"cmp_max{qt}"))
                    dve.wait_ge(*at_vec.at(f"cmp_max{qt}"))
                    tt(p, p, m.unsqueeze(2).to_broadcast([P, NH, N_CMP]), ALU.subtract
                       ).then_inc(*at_vec.step(f"cmp_centred{qt}"))
                    dve.wait_ge(*at_act.at(f"cmp_exp{qt}"))
                    tt(p, p, mask, ALU.mult).then_inc(*at_vec.step(f"cmp_masked{qt}"))
                    dve.wait_ge(*at_vec.at(f"cmp_masked{qt}"))
                    nc.vector.tensor_reduce(z, p, AX_X, ALU.add).then_inc(*at_vec.step(f"cmp_sum{qt}"))
                    dve.wait_ge(*at_vec.at(f"cmp_sum{qt}"))
                    ts_(z, z, 1e-30, None, ALU.max).then_inc(*at_vec.step(f"cmp_floor{qt}"))
                    dve.wait_ge(*at_vec.at(f"cmp_floor{qt}"))
                    nc.vector.reciprocal(m, z).then_inc(*at_vec.step(f"cmp_inv{qt}"))
                    dve.wait_ge(*at_vec.at(f"cmp_inv{qt}"))
                    tt(z, m, gate_tok[:, qt, 0:NH], ALU.mult).then_inc(*at_vec.step(f"cmp_gate{qt}"))
                    dve.wait_ge(*at_vec.at(f"cmp_gate{qt}"))
                    tt(p, p, z.unsqueeze(2).to_broadcast([P, NH, N_CMP]), ALU.mult).then_inc(*at_vec.step(f"pc{qt}"))
                for i in range(8):
                    dve.wait_ge(*at_pe.at(f"cmp_turned{i}"))
                    cp(pc_t[0:N_CMP, i // 4, 4 * (i % 4):4 * (i % 4) + 4, :], quad(2 + i % 2)[0:N_CMP, :, :]
                       ).then_inc(*at_vec.step(f"pcT{i}"))

                def first(u):
                    j, qt, r = u // 4, u // 2 % 2, u % 2
                    hd, nk = 2 * j + r, (qt + 1) * P
                    dist = K("dist")[:, TOK - nk:TOK].unsqueeze(1).to_broadcast([P, 2, nk])
                    s = s_buf[u % 3][:, :, 0:nk]
                    dve.wait_ge(*at_pe.at(f"scores{u}"))
                    if u >= 3:
                        dve.wait_ge(*at_pe.at(f"turned{u - 3}"))
                    stt(out=s, in0=dist, scalar=-slope(hd), in1=pair(u % 2)[:, :, 0:nk],
                        op0=ALU.mult, op1=ALU.add).then_inc(*at_vec.step(f"biased{u}"))
                    dve.wait_ge(*at_vec.at(f"biased{u}"))
                    m = at_small[:, 4 + 2 * (u % 2):6 + 2 * (u % 2)]
                    nc.vector.tensor_reduce(m, s, AX_X, ALU.max).then_inc(*at_vec.step(f"rawmax{u}"))
                    dve.wait_ge(*at_vec.at(f"rawmax{u}"))
                    ts_(at_small[:, 2 * (u % 2):2 * (u % 2) + 2], m, -1.0, None, ALU.mult
                        ).then_inc(*at_vec.step(f"max{u}"))

                def second(u):
                    j, qt, r = u // 4, u // 2 % 2, u % 2
                    hd, nk = 2 * j + r, (qt + 1) * P
                    z = at_small[:, 8 + 2 * (u % 2):10 + 2 * (u % 2)]
                    w = at_small[:, 12 + 2 * (u % 2):14 + 2 * (u % 2)]
                    dve.wait_ge(*at_act.at(f"exp{u}_1"))
                    nc.vector.reciprocal(w, z).then_inc(*at_vec.step(f"inv{u}"))
                    dve.wait_ge(*at_vec.at(f"inv{u}"))
                    gate = gate_tok[:, qt, :].rearrange("p (b h) -> p b h", b=3)[:, 1:3, hd]
                    tt(w, w, gate, ALU.mult).then_inc(*at_vec.step(f"weight{u}"))
                    dve.wait_ge(*at_vec.at(f"weight{u}"))
                    for br in range(2):
                        ins = ts_(s_buf[u % 3][:, br, 0:nk], s_buf[u % 3][:, br, 0:nk], w[:, br:br + 1], None, ALU.mult)
                    ins.then_inc(*at_vec.step(f"p{u}"))

                def out(i):
                    dve.wait_ge(*at_pe.at(f"values{2 * i + 1}"))
                    cp(o_t[:, i // 2, (i % 2) * P:(i % 2 + 1) * P], bank[4 + i % 2][:, 0:P]
                       ).then_inc(*at_vec.step(f"o{i}"))

                first(0)
                for v in range(32):
                    if v + 1 < 32:
                        first(v + 1)
                    second(v)
                    if v % 2 == 1 and v > 2:
                        out(v // 2 - 1)
                out(15)

            def mix(st):
                l, M, R = st.layer, ML[st.layer], RW[st.layer]
                Mv, Rv = M.vec, R.vec
                rt = row_tmp[64:68]
                gb = V(f"gbias{l}")

                def shift(t):
                    rows_ = slice(2 * t, min(2 * t + 2, NZ))
                    dve.wait_ge(front_taken, st.front + t + 1)
                    tt(diff[:, rows_, :], zp[:, rows_, PAD - 1:ZW - 1], zp[:, rows_, PAD:ZW], ALU.subtract
                       ).then_inc(*Mv.step(f"diff{t}"))
                    dve.wait_ge(*Mv.at(f"diff{t}"))
                    for i in range(rows_.start, rows_.stop):
                        ins = stt(out=zp[:, i, PAD:ZW], in0=diff[:, i, :], scalar=V(f"mu{l}", i), in1=zp[:, i, PAD:ZW],
                                  op0=ALU.mult, op1=ALU.add)
                    ins.then_inc(*Mv.step(f"shifted{t}"))

                def gate_inputs():
                    dve.wait_ge(*Mv.at("shifted7"))
                    ts_(rt[:, 0, :], zp[64:68, 14, PAD:ZW], gb[64:68], None, ALU.add).then_inc(*Mv.step("li"))
                    ts_(rt[:, 1, :], zp[96:100, 14, PAD:ZW], gb[96:100], None, ALU.add).then_inc(*Mv.step("xf"))
                    dve.wait_ge(*Mv.at("xf"))
                    stt(out=rt[:, 2, :], in0=rt[:, 1, :], scalar=-1.0, in1=rt[:, 1, :], op0=ALU.mult, op1=ALU.min
                        ).then_inc(*Mv.step("minus_abs"))

                def gate_sums():
                    dve.wait_ge(*M.act.at("ln_f"))
                    stt(out=rt[:, 1, :], in0=rt[:, 1, :], scalar=0.0, in1=rt[:, 2, :], op0=ALU.min, op1=ALU.subtract
                        ).then_inc(*Mv.step("lf"))
                    dve.wait_ge(*Mv.at("lf"))
                    nc.vector.tensor_tensor_scan(rt[:, 3, :], K("ones")[64:68, 0:1].to_broadcast([4, TOK]), rt[:, 1, :],
                                                 0.0, ALU.mult, ALU.add).then_inc(*Mv.step("F"))
                    dve.wait_ge(*Mv.at("F"))
                    dve.wait_ge(*M.pool.at("rows_zero"))
                    tt(rows[64:68, 0, :], rt[:, 0, :], rt[:, 3, :], ALU.subtract).then_inc(*Mv.step("g_row"))
                    dve.wait_ge(*Mv.at("g_row"))
                    nc.vector.tensor_tensor_scan(rows[64:68, 1, :], rows[64:68, 0, :], rows[64:68, 0, :], 0.0,
                                                 ALU.max, ALU.max).then_inc(*Mv.step("M_row"))
                    dve.wait_ge(*Mv.at("M_row"))
                    tt(rt[:, 4, :], rt[:, 3, :], rows[64:68, 1, :], ALU.add).then_inc(*Mv.step("F_plus_M"))

                def short_conv(t):
                    dve.wait_ge(front_taken, st.front + t + 1)
                    for i in range(4):
                        for j in (2 * t - 16, 2 * t - 15):
                            if i == 0:
                                ts_(qk[:, j, :], mqk[:, j, 1:1 + TOK], V(f"convw{l}", j), V(f"convb{l}", j), ALU.mult,
                                    ALU.add).then_inc(*Mv.step(f"tap0_{j}"))
                                continue
                            dve.wait_ge(*Mv.at(f"tap{i - 1}_{j}"))
                            stt(out=qk[:, j, :], in0=mqk[:, j, 1 + i:1 + i + TOK], scalar=V(f"convw{l}", 8 * i + j),
                                in1=qk[:, j, :], op0=ALU.mult, op1=ALU.add
                                ).then_inc(*Mv.step(f"tap{i}_{j}" if i < 3 else f"conv{j}"))

                dve.wait_ge(*M.pool.at("pads"))
                for t in range(16):
                    f = st.front + t
                    if t < 7:
                        take(st, t, zp[:, 2 * t:2 * t + 2, PAD:ZW])
                    elif t == 7:
                        take(st, t, zp[:, 14:15, PAD:ZW], 1)
                    elif t < 12:
                        take(st, t, mqk[:, 2 * t - 16:2 * t - 14, PAD:ZW])
                    elif t < 14:
                        take(st, t, v_tok[:, :, (t - 12) * TOK:(t - 11) * TOK])
                    else:
                        take(st, t, m_o[:, 2 * t - 28:2 * t - 26, :])
                    if t < 8:
                        shift(t)
                    if t == 7:
                        gate_inputs()
                    if t == 9:
                        gate_sums()
                    if 10 <= t < 14:
                        short_conv(t - 2)
                dve.wait_ge(front_taken, st.front + 16)
                cp(small[:, 0:1], m_o[:, 3, 0:1]).then_inc(*Mv.step("m_o"))
                dve.wait_ge(*M.pe.at("g_turned"))
                g_col = small[:, 8:16].rearrange("p (c h) -> p c h", c=2)
                cp(g_col, bank[7][:, 0:TOK].rearrange("p (c r) -> p c r", c=2)[:, :, 64:68]).then_inc(*Mv.step("g_col"))
                dve.wait_ge(*Mv.at("g_col"))
                dve.wait_ge(*M.pe.at("M_spread"))

                def gap(i):
                    hd, kt = i // 2, i % 2
                    ts_(w_buf[:, i % 4, kt * P:TOK], half(hd // 2, hd % 2)[:, kt * P:TOK], g_col[:, kt, hd:hd + 1], 0.0,
                        ALU.subtract, ALU.max).then_inc(*Mv.step(f"gap{i}"))

                def finish(hd):
                    b = FRONT[hd % 2]
                    dve.wait_ge(*M.pe.at(f"sums{hd}"))
                    if hd == 0:
                        dve.wait_ge(*M.act.at("em_copy"))
                    e = bc_e[:, hd, :]
                    stt(out=e, in0=half(b, 1), scalar=-1.0, in1=e, op0=ALU.mult, op1=ALU.max
                        ).then_inc(*Mv.step(f"floor{hd}"))
                    dve.wait_ge(*Mv.at(f"floor{hd}"))
                    tt(e, half(b, 1), e, ALU.max).then_inc(*Mv.step(f"den{hd}"))
                    dve.wait_ge(*Mv.at(f"den{hd}"))
                    nc.vector.reciprocal(e, e).then_inc(*Mv.step(f"inv{hd}"))
                    dve.wait_ge(*Mv.at(f"inv{hd}"))
                    tt(h_b[:, hd, :], half(b, 0), e, ALU.mult).then_inc(*Mv.step(f"h{hd}"))

                for i in range(3):
                    gap(i)
                for i in range(8):
                    hd, kt = i // 2, i % 2
                    dve.wait_ge(*M.pe.at(f"scores{i}"))
                    dve.wait_ge(*M.act.at(f"weight{i}"))
                    stt(out=sw[:, i, kt * P:TOK], in0=w_buf[:, i % 4, kt * P:TOK], scalar=float(P) ** -0.5,
                        in1=bank[6 + i % 2][:, kt * P:TOK], op0=ALU.mult, op1=ALU.mult).then_inc(*Mv.step(f"sw{i}"))
                    dve.wait_ge(*Mv.at(f"sw{i}"))
                    dg = sw[:, i, kt * P:(kt + 1) * P]
                    tt(dg, dg, K("causal"), ALU.mult).then_inc(*Mv.step(f"masked{i}"))
                    if i + 3 < 8:
                        gap(i + 3)
                    if i % 2 == 1 and i > 2:
                        finish(hd - 1)
                finish(3)
                dve.wait_ge(*M.pe.at("mean"))
                for i in range(2):
                    d = h_b[:, 2 * i:2 * i + 2, :]
                    stt(out=d, in0=pair(i), scalar=-1.0 / P, in1=d, op0=ALU.mult, op1=ALU.add
                        ).then_inc(*Mv.step(f"centred{i}"))
                nc.vector.memset(lora_in[:, 2:4, :], 0.0).then_inc(*Rv.step("lora_zero"))
                dve.wait_ge(*Rv.at("lora_zero"))
                cp(lora_in[32:64, 3, :], zp[32:64, 14, PAD:ZW]).then_inc(*Rv.step("lora_tail"))
                ts_(small[:, 16:20], V(f"ka{l}", 0, 4), -1.0, 1.0, ALU.mult, ALU.add).then_inc(*Rv.step("one_minus_ka"))
                for i in range(2):
                    dve.wait_ge(*M.act.at(f"root{i}"))
                    nc.vector.reciprocal(sw[:, 2 * i:2 * i + 2, :], sw[:, 2 * i:2 * i + 2, :]
                                         ).then_inc(*Mv.step(f"rstd{i}"))
                dve.wait_ge(*Mv.at("rstd1"))
                for j in range(4):
                    ins = stt(out=h_b[:, j, :], in0=h_b[:, j, :], scalar=V(f"mlnorm{l}", j), in1=sw[:, j, :],
                              op0=ALU.mult, op1=ALU.mult)
                ins.then_inc(*Mv.step("normed"))
                dve.wait_ge(*Mv.at("normed"))
                dve.wait_ge(*M.act.at("sig_o"))
                tt(y_b[:, :, :], h_b[:, :, :], m_o[:, :, :], ALU.mult).then_inc(*Mv.step("y_b"))
                dve.wait_ge(*Mv.at("y_b"))

                zr, zk, zv = zp[:, 0:4, PAD:ZW], zp[:, 4:8, PAD:ZW], zp[:, 8:12, PAD:ZW]
                for j in range(4):
                    ts_(e3[:, j, :], zp[:, 4 + j, PAD:ZW], V(f"kk{l}", j), None, ALU.mult
                        ).then_inc(*Rv.step(f"kk_raw{j}"))
                dve.wait_ge(*R.act.at("sig_w"))
                ts_(e1[:, :, :], e1[:, :, :], -EXP_MINUS_HALF, None, ALU.mult).then_inc(*Rv.step("lw"))
                dve.wait_ge(*Rv.at("lw"))
                for j in range(4):
                    ins = nc.vector.tensor_tensor_scan(e5[:, j, :], K("reset"), e1[:, j, :], 0.0, ALU.mult, ALU.add)
                ins.then_inc(*Rv.step("L"))
                dve.wait_ge(*Rv.at("L"))
                tt(e6[:, :, :], e5[:, :, :], e1[:, :, :], ALU.subtract).then_inc(*Rv.step("L_prev"))
                dve.wait_ge(*R.act.at("a"))
                dve.wait_ge(*Rv.at("one_minus_ka"))
                for j in range(4):
                    ins = ts_(e8[:, j, :], e4[:, j, :], V(f"ka{l}", j), small[:, 16 + j:17 + j], ALU.mult, ALU.add)
                ins.then_inc(*Rv.step("ka"))
                dve.wait_ge(*Rv.at("ka"))
                dve.wait_ge(*Rv.at("kk_raw3"))
                tt(zk, zk, e8[:, :, :], ALU.mult).then_inc(*Rv.step("k_mixed"))
                dve.wait_ge(*Rv.at("k_mixed"))
                tt(e8[:, :, :], zr, zk, ALU.mult).then_inc(*Rv.step("rk"))
                dve.wait_ge(*Rv.at("rk"))
                for j in range(4):
                    ts_(e8[:, j, :], e8[:, j, :], V(f"rk{l}", j), None, ALU.mult).then_inc(*Rv.step(f"rk{j}"))
                vf = tiles(v_first, 4)
                if l == 0:
                    cp(vf, zv).then_inc(*Rv.step("v_mixed"))
                else:
                    dve.wait_ge(*R.act.at("vg"))
                    tt(e1[:, :, :], vf, zv, ALU.subtract).then_inc(*Rv.step("v_gap"))
                    dve.wait_ge(*Rv.at("v_gap"))
                    tt(e1[:, :, :], e1[:, :, :], e7[:, :, :], ALU.mult).then_inc(*Rv.step("v_gated"))
                    dve.wait_ge(*Rv.at("v_gated"))
                    tt(zv, zv, e1[:, :, :], ALU.add).then_inc(*Rv.step("v_mixed"))
                dve.wait_ge(*Rv.at("v_mixed"))
                dve.wait_ge(*R.pe.at("kk_norm"))
                for i in range(2):
                    ts_(e2[:, 2 * i:2 * i + 2, :], pair(i), 1e-24, None, ALU.max).then_inc(*Rv.step(f"kk_floor{i}"))
                for i in range(2):
                    dve.wait_ge(*R.act.at(f"kk_root{i}"))
                    nc.vector.reciprocal(e2[:, 2 * i:2 * i + 2, :], e2[:, 2 * i:2 * i + 2, :]
                                         ).then_inc(*Rv.step(f"kk_rstd{i}"))
                dve.wait_ge(*Rv.at("kk_rstd1"))
                tt(e3[:, :, :], e3[:, :, :], e2[:, :, :], ALU.mult).then_inc(*Rv.step("kk"))
                dve.wait_ge(*Rv.at("kk"))
                dve.wait_ge(*R.pe.at("rk_sum"))
                for i in range(2):
                    tt(bonus[:, 2 * i:2 * i + 2, :], pair(2 + i), zp[:, 8 + 2 * i:10 + 2 * i, PAD:ZW], ALU.mult
                       ).then_inc(*Rv.step(f"bonus{i}"))
                tt(e4[:, :, :], e4[:, :, :], e3[:, :, :], ALU.mult).then_inc(*Rv.step("b"))
                dve.wait_ge(*R.act.at("E_prev"))
                tt(kap[:, :, :], e3[:, :, :], e6[:, :, :], ALU.mult).then_inc(*Rv.step("kap"))
                dve.wait_ge(*R.act.at("E"))
                tt(rho[:, :, :], zr, e8[:, :, :], ALU.mult).then_inc(*Rv.step("rho"))
                pcol = small[:, 20:36].rearrange("p (j c) -> p j c", j=4)
                cp(pcol, e8.rearrange("p j (c t) -> p j c t", t=CH)[:, :, :, CH - 1]).then_inc(*Rv.step("P"))
                dve.wait_ge(*Rv.at("b"))
                dve.wait_ge(*Rv.at("kap"))
                tt(e5[:, :, :], zk, e7[:, :, :], ALU.mult).then_inc(*Rv.step("khat"))
                tt(e6[:, :, :], e4[:, :, :], e7[:, :, :], ALU.mult).then_inc(*Rv.step("bhat"))
                dve.wait_ge(*Rv.at("bhat"))
                dve.wait_ge(*R.pool.at("z_zero"))
                for r in range(2):
                    rows_ = slice(r * CH, (r + 1) * CH)
                    cp(k_z[rows_, :, r, :], e5[rows_, :, :]).then_inc(*Rv.step(f"k_z{r}"))
                dve.wait_ge(*Rv.at("khat"))
                for s, src in enumerate((e5, e6)):
                    cp(keep[s], src[:, :, P:TOK]).then_inc(*Rv.step(f"keep{s}"))
                dve.wait_ge(*Rv.at("keep1"))
                dve.wait_ge(*R.pool.at("tok_zero"))

                def masked(name, hf, T, dst, b, mask, sign=None):
                    mk = K(mask).unsqueeze(1).to_broadcast([P, 4, P])
                    dve.wait_ge(*R.pe.at(f"{name}{hf}_{T}"))
                    d = dst[:, 4 * hf:4 * hf + 4, :]
                    if sign is None:
                        ins = tt(d, quad(b + hf), mk, ALU.mult)
                    else:
                        ins = stt(out=d, in0=quad(b + hf), scalar=sign, in1=mk, op0=ALU.mult, op1=ALU.mult)
                    return ins

                for T in range(2):
                    dve.wait_ge(*R.pe.at(f"turned0_{T}"))
                    for cl in range(2):
                        rows_ = slice(cl * CH, (cl + 1) * CH)
                        cp(ktok[rows_, cl, :], bank[4][rows_, :]).then_inc(*Rv.step(f"ktok{cl}_{T}"))
                    idn = K("ident").unsqueeze(1).to_broadcast([P, 4, P])
                    for hf in range(2):
                        masked("A_t", hf, T, A_t, 0, "strict").then_inc(*Rv.step(f"A_t{hf}_{T}"))
                    for hf in range(2):
                        d = X[:, 4 * hf:4 * hf + 4, :]
                        masked("A", hf, T, X, 2, "level0_ts").then_inc(*Rv.step(f"X_off{hf}_{T}"))
                        dve.wait_ge(*Rv.at(f"X_off{hf}_{T}"))
                        tt(d, idn, d, ALU.subtract).then_inc(*Rv.step(f"X0_{hf}_{T}"))
                        d, a = X_t[:, 4 * hf:4 * hf + 4, :], A_t[:, 4 * hf:4 * hf + 4, :]
                        dve.wait_ge(*Rv.at(f"A_t{hf}_{T}"))
                        tt(d, a, K("level0").unsqueeze(1).to_broadcast([P, 4, P]), ALU.mult
                           ).then_inc(*Rv.step(f"Xt_off{hf}_{T}"))
                        dve.wait_ge(*Rv.at(f"Xt_off{hf}_{T}"))
                        tt(d, idn, d, ALU.subtract).then_inc(*Rv.step(f"X_t0_{hf}_{T}"))
                    for hf in range(2):
                        masked("A_kk", hf, T, A_kk, 4, "strict").then_inc(*Rv.step(f"A_kk{hf}_{T}"))
                    for hf in range(2):
                        masked("A_rk", hf, T, A_rk, 6, "incl").then_inc(*Rv.step(f"A_rk{hf}_{T}"))
                    for hf in range(2):
                        masked("A_rb", hf, T, A_rb, 0, "incl", -1.0).then_inc(*Rv.step(f"A_rb{hf}_{T}"))
                    for lv in range(1, LEVELS):
                        for hf in range(2):
                            for nm, dst, b in (("", X, 2), ("_t", X_t, 6)):
                                if nm == "" and lv == LEVELS - 1:
                                    continue
                                dve.wait_ge(*R.pe.at(f"D{nm}{lv}_{hf}_{T}"))
                                d = dst[:, 4 * hf:4 * hf + 4, :]
                                tt(d, d, quad(b + hf), ALU.subtract).then_inc(*Rv.step(f"X{nm}{lv}_{hf}_{T}"))
                    for cl in range(2):
                        c = 2 * T + cl
                        if c == 0:
                            cp(small[:, 40:44], small[:, 16:20]).then_inc(*Rv.step("S0_3"))
                        if c == 2:
                            open_run()
                            advance(st.half + 34)
                        dve.wait_ge(*R.pe.at(f"G{c}"))
                        cp(gs[:, :], bank[0][:, :]).then_inc(*Rv.step(f"G{c}"))
                        dve.wait_ge(*R.pe.at(f"SA{c}"))
                        rows_ = slice(cl * CH, (cl + 1) * CH)
                        for r in range(2):
                            cp(sa_z[rows_, :, r, r * CH:(r + 1) * CH], quad(1)[rows_, :, r * CH:(r + 1) * CH]
                               ).then_inc(*Rv.step(f"SA{c}_{r}"))
                        dve.wait_ge(*R.pe.at(f"dS{c}"))
                        tt(S, S, quad(2), ALU.add).then_inc(*Rv.step(f"S_sum{c}"))
                        dve.wait_ge(*Rv.at(f"S_sum{c}"))
                        for j in range(4):
                            stt(out=S[:, j, :], in0=S[:, j, :], scalar=pcol[:, j, c:c + 1], in1=K("blk"), op0=ALU.mult,
                                op1=ALU.mult).then_inc(*Rv.step(f"S{c + 1}_{j}"))
                        dve.wait_ge(*Rv.at(f"S{c + 1}_3"))
                        dve.wait_ge(*R.pe.at(f"y{c}"))
                        cp(y_a[:, :, c * CH:(c + 1) * CH], bank[3][:, 0:TOK].rearrange("p (j t) -> p j t", j=4)
                           ).then_inc(*Rv.step(f"y{c}"))
                dve.wait_ge(*R.pe.at("gn_mean"))
                for i in range(2):
                    d = y_a[:, 2 * i:2 * i + 2, :]
                    stt(out=d, in0=pair(i), scalar=-1.0 / CH, in1=d, op0=ALU.mult, op1=ALU.add
                        ).then_inc(*Rv.step(f"gn_centred{i}"))
                for i in range(2):
                    dve.wait_ge(*R.act.at(f"gn_root{i}"))
                    nc.vector.reciprocal(e3[:, 2 * i:2 * i + 2, :], e3[:, 2 * i:2 * i + 2, :]
                                         ).then_inc(*Rv.step(f"gn_rstd{i}"))
                dve.wait_ge(*Rv.at("gn_rstd1"))
                for j in range(4):
                    stt(out=y_a[:, j, :], in0=y_a[:, j, :], scalar=V(f"gnw{l}", j), in1=e3[:, j, :], op0=ALU.mult,
                        op1=ALU.mult).then_inc(*Rv.step(f"gn{j}"))
                for j in range(4):
                    dve.wait_ge(*Rv.at(f"gn{j}"))
                    stt(out=y_a[:, j, :], in0=y_a[:, j, :], scalar=V(f"gnb{l}", j), in1=bonus[:, j, :], op0=ALU.add,
                        op1=ALU.add).then_inc(*Rv.step(f"with_bonus{j}"))
                for j in range(4):
                    dve.wait_ge(*Rv.at(f"with_bonus{j}"))
                    tt(y_a[:, j, :], y_a[:, j, :], g_up[:, j, :], ALU.mult).then_inc(*Rv.step(f"y_a{j}"))

            def branch(st):
                parts(st, lambda j: (y_a, y_b)[j // 4][:, j % 4, :])
                for ct in range(8):
                    f = st.front + ct
                    q = 8 * st.branch + ct
                    advance(st.half + ct + 2)
                    dve.wait_ge(half_used, st.half + ct + 1)
                    if ct == 0:
                        dve.wait_ge(front_taken, st.front)
                    tt(br_t[:, 0, :], sgate[:, ct, :], half(FRONT[f % 2], 0), ALU.mult).then_inc(br_product, 1)
                    tt(br_t[:, 1, :], sgate[:, 8 + ct, :], half(FRONT[f % 2], 1), ALU.mult).then_inc(front_taken, 1)
                    dve.wait_ge(br_product, q + 1)
                    dve.wait_ge(front_taken, f + 1)
                    tt(u[:, ct, :], br_t[:, 0, :], br_t[:, 1, :], ALU.add).then_inc(u_ready, 1)
                    dve.wait_ge(u_ready, q + 1)

            dve.wait_ge(vecs_landed, 16)
            for st in PLAN:
                if st.kind == "ada":
                    ada(st)
                elif st.kind == "norm":
                    if st.mod is None:
                        norm(st, y3, h_scaled, lambda j: V(st.gain, j), x3)
                    else:
                        q = 6 if st.mod == "kv" else 3 * st.mod[0] + st.mod[1]
                        sh = mod_col(*st.mod, 0) if st.mod != "kv" else 144
                        norm(st, y3, h_scaled, lambda j: pre_gain[:, 8 * q + j:8 * q + j + 1], x3,
                             lambda j: mods[:, sh + j:sh + j + 1])
                elif st.kind == "final":
                    norm(st, y3, out_ready, lambda j: V(st.gain, j), x3)
                elif st.kind == "post":
                    if st.source == "ffn":
                        if st.ffn <= 2:
                            mods_out(st.ffn)
                        ffn_out(st)
                    q = 3 * st.mod[0] + st.mod[1]
                    norm(st, y3, delta_ready, lambda j: post_gain[:, 8 * q + j:8 * q + j + 1], y3)
                elif st.kind in ("ffn", "ffn_ada"):
                    ffn(st)
                elif st.kind == "half":
                    half_add(st)
                elif st.kind == "conv":
                    conv(st)
                elif st.kind == "kv":
                    kv(st)
                elif st.kind == "nsa":
                    nsa(st)
                elif st.kind == "mix":
                    mix(st)
                elif st.kind == "branch":
                    branch(st)
                elif st.kind == "gates":
                    open_run()
                    advance(st.half + 15)
                elif st.kind == "lin4":
                    src = conv_y if st.rhs == "conv_y" else o_t if st.rhs == "o" else u
                    if st.rhs == "conv_y":
                        parts(st, lambda j: src[:, j, :], 0, 6)
                        dve.wait_ge(front_taken, st.front)
                        conv_rows(3)
                        parts(st, lambda j: src[:, j, :], 6, 8)
                    else:
                        parts(st, lambda j: src[:, j, :])
                    for t in range(4):
                        if st.rhs != "u":
                            take(st, t, y3[:, 2 * t:2 * t + 2, :])
                            continue
                        advance(st.half + 2 * t + 3)
                        dve.wait_ge(half_used, st.half + 2 * t + 2)
                        xp = x3[:, 2 * t:2 * t + 2, :]
                        tt(xp, pair(FRONT[(st.front + t) % 2]), xp, ALU.add).then_inc(front_taken, 1)


def constant_array():
    out = np.zeros((P, NCONST), np.float32)

    def put(name, a):
        s, n = CONST[name]
        out[:, s:s + n] = np.asarray(a, np.float32).reshape(a.shape[0], -1)

    i = np.arange(P)
    s, t = i[:, None], i[None, :]
    put("ident", np.eye(P))
    put("ones", np.ones((P, P)))
    same = s // CH == t // CH
    put("blk", same)
    for lv in range(LEVELS):
        b = 1 << lv
        m = (s // (2 * b) == t // (2 * b)) & (s // b % 2 == 0) & (t // b % 2 == 1)
        put(f"level{lv}", m)
        if lv == 0:
            put("level0_ts", m.T)
    put("strict", same & (s < t))
    put("incl", same & (s <= t))
    put("causal", s <= t)
    put("reset", np.broadcast_to(np.arange(TOK) % CH != 0, (P, TOK)))
    put("dist", np.concatenate([s - t + P, np.where(s >= t, s - t, 1e30)], axis=1))
    q = np.arange(TOK).reshape(2, P).T
    dc = q[:, :, None] - (np.arange(N_CMP) * CMP_STRIDE + CMP_LEN - 1)
    put("cmp_dist", np.where(dc >= 0, dc, 1e30))
    put("cmp_mask", dc >= 0)
    return out


def vector_array(a):
    out = np.zeros((P, NVEC), np.float32)

    def put(name, v):
        s, n = VEC[name]
        v = np.asarray(v).reshape(-1, P).T
        out[:, s:s + v.shape[1]] = v

    put("c", a["c"])
    put("mod_b", np.concatenate([a["ada_b"].reshape(-1), a["kv_ada_b"]]))
    put("norm_g", a["norm_g"])
    put("kv_norm", a["kv_norm_g"])
    put("conv", a["a_conv"])
    put("pos", a["cmp_pos"])
    for l in range(2):
        put(f"ffn1{l}", a["ffn1_norm_2"][l])
        put(f"mix{l}", a["mix_norm_2"][l])
        put(f"ffn2{l}", a["ffn2_norm_2"][l])
        put(f"mu{l}", np.concatenate([a["shift_mu_2"][l], np.zeros(96, np.float32)]))
        for name, key in (("w0", "rw_w0_2"), ("a0", "rw_a0_2"), ("kk", "rw_k_k_2"), ("ka", "rw_k_a_2"),
                          ("rk", "rw_r_k_2"), ("gnw", "rw_gn_w_2"), ("gnb", "rw_gn_b_2"), ("convw", "ml_conv_w_2"),
                          ("convb", "ml_conv_b_2"), ("mlnorm", "ml_norm_w_2")):
            put(f"{name}{l}", a[key][l])
        if l:
            put(f"vres{l}", a["vres_bias_2"][l - 1])
        g = VEC[f"gbias{l}"][0]
        out[64:68, g] = a["ml_i_bias_2"][l]
        out[96:100, g] = a["ml_f_bias_2"][l]
    put("final", a["final_norm_2"])
    return out


def weight_tiles(a):
    out = np.zeros((N_TILES, P, 2, KC, P), np.float32)
    n = 0

    def put(w):
        nonlocal n
        t = -(-w.shape[1] // TILE_COLS)
        for i in range(t):
            for c in range(2):
                v = w[:, (2 * i + c) * P:(2 * i + c + 1) * P]
                out[n, :, c, :, :v.shape[1]] = v.reshape(KC, P, -1).transpose(1, 0, 2)
            n += 1

    def put_flat(v):
        nonlocal n
        out[n].reshape(P, TILE)[:, :v.shape[1]] = v
        n += 1

    def put_ffn(w_in, w_out, riders=None):
        for hh in range(HALVES):
            c = slice(hh * P, (hh + 1) * P)
            put(np.concatenate([w_in[:, c], w_in[:, D_FF:][:, c]], axis=1))
            if riders is not None and hh:
                put_flat(riders.pop(0))
            if hh and (hh % 2 == 0 or hh == HALVES - 1):
                s = (hh - 1) // 2
                if hh == HALVES - 1:
                    s = FFN_STEPS - 1
                put_flat(w_out[s * TILE_COLS:(s + 1) * TILE_COLS].reshape(2, P, D).transpose(1, 0, 2).reshape(P, 2 * D))
                if riders is not None:
                    put_flat(riders.pop(0))

    def twice(w):
        return np.repeat(w.reshape(w.shape[0], -1, 1, DH), 2, axis=2).reshape(w.shape[0], -1)

    ada_w = np.concatenate([a["ada_w"][0], a["ada_w"][1], a["kv_ada_w"]], axis=1)
    ada = [ada_w[:, i:i + TILE_COLS].reshape(KC, P, TILE_COLS).transpose(1, 0, 2).reshape(P, TILE)
           for i in range(0, MOD_COLS * P, TILE_COLS)]
    for _ in range(ADA_FIRST):
        put_flat(ada.pop(0))
    put_ffn(a["ffn_w_in"][0, 0], a["ffn_w_out"][0, 0], ada)
    put(a["a_w_in"][0].reshape(D, 3, 4, TILE_COLS).transpose(0, 2, 1, 3).reshape(D, 3 * D))
    put(a["a_w_out"][0])
    put_ffn(a["ffn_w_in"][0, 1], a["ffn_w_out"][0, 1], ada)
    kv = a["kv_w"].reshape(D, 3, 2, NG * DH)
    for br, s in ((0, 0), (0, 1), (1, 0), (2, 0)):
        put(twice(kv[:, br, s]))
    put(kv[:, 1, 1])
    put(kv[:, 2, 1])
    for s in range(2):
        w1 = a["cmp_w1"][s].reshape(2, KC, P, 256)
        for i in range(2):
            put_flat(w1[i].reshape(KC, P, 2, P).transpose(1, 2, 0, 3).reshape(P, TILE))
    w2 = a["cmp_w2"].reshape(2, 2, P, DH)
    put_flat(np.concatenate([w2[0, 0], w2[0, 0], w2[0, 1], w2[0, 1], w2[1, 0], w2[1, 1]], axis=1))
    put_ffn(a["ffn_w_in"][1, 0], a["ffn_w_out"][1, 0])
    put(a["b_w_in"][0])
    put(a["b_w_out"][0])
    put_ffn(a["ffn_w_in"][1, 1], a["ffn_w_out"][1, 1])
    for l in range(2):
        put_ffn(a["ffn1_w_in_2"][l], a["ffn1_w_out_2"][l])
        w = a["w_in_2"][l]
        put(w[:, 0:1792])
        tail = np.zeros((D, TILE_COLS), np.float32)
        tail[:, 0:32] = w[:, 1792:1824]
        if l:
            tail[:, 32:64] = a["vres_down_2"][l - 1]
        tail[:, 64:68] = w[:, 3872:3876]
        tail[:, 96:100] = w[:, 3876:3880]
        put(tail)
        put(w[:, 1824:3872])
        lora = np.zeros((P, 4, 512), np.float32)
        lora[0:64, 0] = a["rw_w_up_2"][l]
        lora[64:128, 1] = a["rw_a_up_2"][l]
        lora[:, 2] = a["rw_g_up_2"][l][0:P]
        lora[0:32, 3] = a["rw_g_up_2"][l][P:]
        if l:
            lora[32:64, 3] = a["vres_up_2"][l - 1]
        put_flat(lora.reshape(P, TILE))
        put(w[:, 3880:])
        put(np.concatenate([a["br_a_2"][l], a["br_b_2"][l]], axis=0))
        put(a["w_out_2"][l])
        put_ffn(a["ffn2_w_in_2"][l], a["ffn2_w_out_2"][l])
    assert n == N_TILES, (n, N_TILES)
    return out.reshape(N_TILES, P, TILE)


def kernel(**inputs):
    import concourse.bacc as bacc
    from concourse.bass_utils import run_bass_kernel_spmd

    a = {k: np.asarray(v) for k, v in inputs.items()}
    x = a["x"].reshape(TOK, KC, P).transpose(2, 1, 0).reshape(P, KC * TOK)
    arrays = {"consts": constant_array(), "vecs": vector_array(a), "x_in": np.ascontiguousarray(x),
              "weights": weight_tiles(a)}
    nc = bacc.Bacc("TRN2", target_bir_lowering=False, num_devices=1)
    args = [nc.dram_tensor(k, v.shape, F32, kind="ExternalInput").ap() for k, v in arrays.items()]
    out = nc.dram_tensor("out", (P, KC * TOK), F32, kind="ExternalOutput").ap()
    build(nc, *args, out)
    got = run_bass_kernel_spmd(nc, [arrays], core_ids=[0]).results[0]["out"]
    return np.ascontiguousarray(got.reshape(P, KC, TOK).transpose(2, 1, 0).reshape(1, TOK, D))
```
